# Optimizing a Trainium2 kernel written in Bass

```python
import jax
import jax.numpy as jnp
from jax import lax
import numpy as np
import math
import jax, jax.numpy as jnp

D_MODEL = 1024
BATCH = 1
SEQ = 512
DEPTH = 1

GRID_W = 64
CTX_LEN = 256
HEAD_DIM = 64
ATT_HEADS = 8
ATT_KV_HEADS = 2
ATT_GROUPS = ATT_HEADS // ATT_KV_HEADS
ATT_DIM = ATT_HEADS * HEAD_DIM
KV_DIM = ATT_KV_HEADS * HEAD_DIM
WINDOW = 128
BLOCK = 128
ROPE_BASE = 10000.0
ATT_SCALE = HEAD_DIM ** -0.5
NEG_INF = -1e30
RWKV_HEADS = 8
RWKV_DIM = RWKV_HEADS * HEAD_DIM
DECAY_LORA = 64
ICL_LORA = 64
GATE_LORA = 128
GN_EPS = 64e-5
N_EXPERTS = 32
TOP_K = 4
D_EXPERT = D_MODEL
SWIGLU_LIMIT = 7.0
SWIGLU_ALPHA = 1.702
MOE_BLOCK = 128
RMS_EPS = 1e-6
ATT_COLS = ATT_DIM + 2 * KV_DIM
RWKV_SIZES = (RWKV_DIM, RWKV_DIM, RWKV_DIM, DECAY_LORA, DECAY_LORA, ICL_LORA, ICL_LORA, GATE_LORA)
RWKV_COLS = sum(RWKV_SIZES)
RWKV_OFFSETS = tuple(int(o) for o in np.cumsum(RWKV_SIZES)[:-1])
GATE_COLS = 2 * D_MODEL
PROJ_COLS = ATT_COLS + RWKV_COLS + GATE_COLS
F32 = jnp.float32


def rms_norm(x, g):
    xf = x.astype(F32)
    y = xf * lax.rsqrt(jnp.mean(xf * xf, axis=-1, keepdims=True) + RMS_EPS)
    return y.astype(x.dtype) * g

def modulate(h, shift, scale):
    return h * (1.0 + scale) + shift

def _rotate_half(t, ang):
    cos = jnp.cos(ang)[None, :, None, :].astype(t.dtype)
    sin = jnp.sin(ang)[None, :, None, :].astype(t.dtype)
    t1, t2 = jnp.split(t, 2, axis=-1)
    return jnp.concatenate([t1 * cos - t2 * sin, t2 * cos + t1 * sin], axis=-1)

def axial_rope(t):
    L = t.shape[1]
    n_rows = L // GRID_W
    row = jnp.repeat(jnp.arange(n_rows, dtype=F32), GRID_W, total_repeat_length=L)
    col = jnp.tile(jnp.arange(GRID_W, dtype=F32), n_rows)
    half = HEAD_DIM // 2
    inv_freq = ROPE_BASE ** (-jnp.arange(0, half, 2, dtype=F32) / half)
    t_row, t_col = jnp.split(t, 2, axis=-1)
    return jnp.concatenate([_rotate_half(t_row, row[:, None] * inv_freq[None, :]),
                            _rotate_half(t_col, col[:, None] * inv_freq[None, :])], axis=-1)

def token_shift(z, mu_prev, mu_next):
    prev = jnp.pad(z[:, :-1], ((0, 0), (1, 0), (0, 0)))
    nxt = jnp.pad(z[:, 1:], ((0, 0), (0, 1), (0, 0)))
    return z + mu_prev * (prev - z) + mu_next * (nxt - z)

def rwkv_features(z, p):
    B, L, _ = z.shape
    r, k, v, wl_f, wl_b, al_f, al_b, gl = jnp.split(z, RWKV_OFFSETS, axis=-1)

    def heads(t):
        return t.reshape(B, L, RWKV_HEADS, HEAD_DIM)

    def decay(w_low, w0, w2):
        w = (w0 + jnp.tanh(w_low) @ w2).astype(F32)
        w = -jax.nn.softplus(-w) - 0.5
        return heads(jnp.exp(-jnp.exp(w)))

    icl_f = jax.nn.sigmoid(p['a0_f'] + al_f @ p['a2_f'])
    icl_b = jax.nn.sigmoid(p['a0_b'] + al_b @ p['a2_b'])
    kk = heads(k * p['k_k']).astype(F32)
    kk = (kk / jnp.maximum(jnp.sqrt(jnp.sum(kk * kk, axis=-1, keepdims=True)), 1e-12)).astype(z.dtype)
    return dict(
        r=heads(r), v=heads(v),
        k_f=heads(k * (1.0 + (icl_f - 1.0) * p['k_a'])),
        k_b=heads(k * (1.0 + (icl_b - 1.0) * p['k_a'])),
        dec_f=decay(wl_f, p['w0_f'], p['w2_f']),
        dec_b=decay(wl_b, p['w0_b'], p['w2_b']),
        a=-kk, b_f=kk * heads(icl_f), b_b=kk * heads(icl_b),
        gate=jax.nn.sigmoid(gl) @ p['g2'])

def wkv_scan(r, w, k, v, a, b, state0, reverse):
    def step(S, inp):
        r_t, w_t, k_t, v_t, a_t, b_t = inp
        sa = jnp.einsum('bhij,bhj->bhi', S, a_t)
        S = S * w_t[:, :, None, :] + sa[..., None] * b_t[:, :, None, :] + v_t[..., None] * k_t[:, :, None, :]
        return S, jnp.einsum('bhij,bhj->bhi', S, r_t)

    xs = tuple(jnp.moveaxis(t.astype(F32), 1, 0) for t in (r, w, k, v, a, b))
    S, ys = lax.scan(step, state0, xs, reverse=reverse)
    return jnp.moveaxis(ys, 0, 1), S

def bidir_scan(f, s0_f, s0_b):
    y_f, s_f = wkv_scan(f['r'], f['dec_f'], f['k_f'], f['v'], f['a'], f['b_f'], s0_f, False)
    y_b, s_b = wkv_scan(f['r'], f['dec_b'], f['k_b'], f['v'], f['a'], f['b_b'], s0_b, True)
    return y_f + y_b, s_f, s_b

def rwkv_output(y, f, p):
    B, L = y.shape[:2]
    mean = jnp.mean(y, axis=-1, keepdims=True)
    var = jnp.mean(jnp.square(y - mean), axis=-1, keepdims=True)
    yn = ((y - mean) * lax.rsqrt(var + GN_EPS)).reshape(B, L, RWKV_DIM)
    yn = (yn * p['ln_x_w'] + p['ln_x_b']).astype(f['v'].dtype)
    bonus = jnp.sum(f['r'] * (f['k_f'] + f['k_b']) * p['r_k'], axis=-1, keepdims=True) * f['v']
    return (yn + bonus.reshape(B, L, RWKV_DIM)) * f['gate']

def project(h, p):
    B, L, _ = h.shape
    z = h @ p['w_in'] + p['b_in']
    z_att, z_rwkv, z_gate = jnp.split(z, [ATT_COLS, ATT_COLS + RWKV_COLS], axis=-1)
    q, k, v = jnp.split(z_att, [ATT_DIM, ATT_DIM + KV_DIM], axis=-1)
    q = q.reshape(B, L, ATT_HEADS, HEAD_DIM)
    k = k.reshape(B, L, ATT_KV_HEADS, HEAD_DIM)
    v = v.reshape(B, L, ATT_KV_HEADS, HEAD_DIM)
    feats = rwkv_features(token_shift(z_rwkv, p['mu_prev'], p['mu_next']), p)
    return q, k, v, feats, z_gate

def sink_softmax(logits, sinks):
    sink = jnp.broadcast_to(sinks.reshape(ATT_KV_HEADS, ATT_GROUPS, 1, 1).astype(F32), logits.shape[:-1] + (1,))
    return jax.nn.softmax(jnp.concatenate([logits, sink], axis=-1), axis=-1)[..., :-1]

def window_attention(q, k, v, k_ctx, v_ctx, sinks):
    B, L = q.shape[:2]
    nb = L // BLOCK
    band = BLOCK + 2 * WINDOW
    qb = jnp.moveaxis(q.reshape(B, nb, BLOCK, ATT_KV_HEADS, ATT_GROUPS, HEAD_DIM), 1, 0)
    kp = jnp.pad(k, ((0, 0), (WINDOW, WINDOW), (0, 0), (0, 0)))
    vp = jnp.pad(v, ((0, 0), (WINDOW, WINDOW), (0, 0), (0, 0)))
    k_off = jnp.arange(band) - WINDOW
    rel = k_off[None, :] - jnp.arange(BLOCK)[:, None]

    def one_block(args):
        n, q_n = args
        k_n = lax.dynamic_slice_in_dim(kp, n * BLOCK, band, axis=1)
        v_n = lax.dynamic_slice_in_dim(vp, n * BLOCK, band, axis=1)
        kpos = n * BLOCK + k_off
        valid = (jnp.abs(rel) <= WINDOW) & ((kpos >= 0) & (kpos < L))[None, :]
        s_lat = jnp.einsum('bqkgd,bskd->bkgqs', q_n, k_n).astype(F32) * ATT_SCALE
        s_lat = jnp.where(valid, s_lat, NEG_INF)
        s_ctx = jnp.einsum('bqkgd,bckd->bkgqc', q_n, k_ctx).astype(F32) * ATT_SCALE
        prob = sink_softmax(jnp.concatenate([s_lat, s_ctx], axis=-1), sinks).astype(v.dtype)
        return (jnp.einsum('bkgqs,bskd->bqkgd', prob[..., :band], v_n)
                + jnp.einsum('bkgqc,bckd->bqkgd', prob[..., band:], v_ctx))

    o = lax.map(one_block, (jnp.arange(nb), qb))
    return jnp.moveaxis(o, 0, 1).reshape(B, L, ATT_DIM)

def context_attention(q, k, v, sinks):
    B, C = q.shape[:2]
    qg = q.reshape(B, C, ATT_KV_HEADS, ATT_GROUPS, HEAD_DIM)
    s = jnp.einsum('bqkgd,bckd->bkgqc', qg, k).astype(F32) * ATT_SCALE
    prob = sink_softmax(s, sinks).astype(v.dtype)
    return jnp.einsum('bkgqc,bckd->bqkgd', prob, v).reshape(B, C, ATT_DIM)

def merge_branches(att, rwk, z_gate, p):
    g_att, g_rwkv = jnp.split(jax.nn.sigmoid(z_gate), 2, axis=-1)
    merged = g_att * (att @ p['w_up_att']) + g_rwkv * (rwk @ p['w_up_rwkv'])
    return merged @ p['w_out']

def moe_ffn(h, p):
    B, L, D = h.shape
    xt = h.reshape(-1, D)
    T = xt.shape[0]
    TK = T * TOP_K
    logits = (xt @ p['w_router'] + p['b_router']).astype(F32)
    top_val, top_idx = lax.top_k(logits, TOP_K)
    gates = jax.nn.softmax(top_val, axis=-1).astype(h.dtype)
    flat_e = top_idx.reshape(-1).astype(jnp.int32)
    flat_tok = jnp.repeat(jnp.arange(T, dtype=jnp.int32), TOP_K)
    order = jnp.argsort(flat_e)
    e_sorted = flat_e[order]
    counts = jnp.zeros((N_EXPERTS,), jnp.int32).at[flat_e].add(1)
    padded = ((counts + MOE_BLOCK - 1) // MOE_BLOCK) * MOE_BLOCK
    start = jnp.cumsum(counts) - counts
    p_end = jnp.cumsum(padded)
    p_start = p_end - padded
    dest = p_start[e_sorted] + jnp.arange(TK, dtype=jnp.int32) - start[e_sorted]
    n_blocks = -(-TK // MOE_BLOCK) + N_EXPERTS
    n_slots = n_blocks * MOE_BLOCK
    slot_tok = jnp.full((n_slots,), T, jnp.int32).at[dest].set(flat_tok[order])
    slot_g = jnp.zeros((n_slots,), h.dtype).at[dest].set(gates.reshape(-1)[order])
    block_exp = jnp.minimum(jnp.searchsorted(p_end, jnp.arange(n_blocks, dtype=jnp.int32) * MOE_BLOCK, side='right'),
                            N_EXPERTS - 1).astype(jnp.int32)
    x_pad = jnp.concatenate([xt, jnp.zeros((1, D), xt.dtype)], axis=0)
    xb = x_pad[slot_tok].reshape(n_blocks, MOE_BLOCK, D)
    w_gu, b_gu, w_dn, b_dn = p['w_gate_up'], p['b_gate_up'], p['w_down'], p['b_down']

    def expert_block(args):
        e, x_b = args
        gu = x_b @ w_gu[e] + b_gu[e]
        gate = jnp.minimum(gu[..., ::2], SWIGLU_LIMIT)
        up = jnp.clip(gu[..., 1::2], -SWIGLU_LIMIT, SWIGLU_LIMIT)
        return ((up + 1.0) * (gate * jax.nn.sigmoid(SWIGLU_ALPHA * gate))) @ w_dn[e] + b_dn[e]

    yb = lax.map(expert_block, (block_exp, xb)).reshape(n_slots, D)
    y = jnp.zeros((T + 1, D), yb.dtype).at[slot_tok].add(yb * slot_g[:, None])[:T]
    return y.reshape(B, L, D)

def first_inputs(seed: int = 0) -> dict:
    key = jax.random.key(seed)
    ks = iter(jax.random.split(key, 48))
    D = D_MODEL

    def nrm(shape, scale):
        return scale * jax.random.normal(next(ks), shape, F32)

    def gain(shape):
        return 1.0 + nrm(shape, 0.05)

    return {
        'x': nrm((BATCH, SEQ, D), 1.0),
        'c': nrm((BATCH, D), 1.0),
        'ctx': nrm((BATCH, CTX_LEN, D), 1.0),
        'c_ctx': nrm((D,), 1.0),
        'w_ada': nrm((DEPTH, D, 6 * D), 0.5 * D ** -0.5),
        'b_ada': nrm((DEPTH, 6 * D), 0.02),
        'g_pre_mix': gain((DEPTH, D)),
        'g_post_mix': gain((DEPTH, D)),
        'g_pre_ffn': gain((DEPTH, D)),
        'g_post_ffn': gain((DEPTH, D)),
        'w_in': nrm((DEPTH, D, PROJ_COLS), D ** -0.5),
        'b_in': nrm((DEPTH, PROJ_COLS), 0.02),
        'mu_prev': jax.random.uniform(next(ks), (DEPTH, RWKV_COLS), F32, 0.0, 0.5),
        'mu_next': jax.random.uniform(next(ks), (DEPTH, RWKV_COLS), F32, 0.0, 0.5),
        'att_sinks': nrm((DEPTH, ATT_HEADS), 0.5),
        'w0_f': jax.random.uniform(next(ks), (DEPTH, RWKV_DIM), F32, -5.0, 0.0),
        'w0_b': jax.random.uniform(next(ks), (DEPTH, RWKV_DIM), F32, -5.0, 0.0),
        'w2_f': nrm((DEPTH, DECAY_LORA, RWKV_DIM), 0.5 * DECAY_LORA ** -0.5),
        'w2_b': nrm((DEPTH, DECAY_LORA, RWKV_DIM), 0.5 * DECAY_LORA ** -0.5),
        'a0_f': nrm((DEPTH, RWKV_DIM), 0.5),
        'a0_b': nrm((DEPTH, RWKV_DIM), 0.5),
        'a2_f': nrm((DEPTH, ICL_LORA, RWKV_DIM), 0.5 * ICL_LORA ** -0.5),
        'a2_b': nrm((DEPTH, ICL_LORA, RWKV_DIM), 0.5 * ICL_LORA ** -0.5),
        'g2': nrm((DEPTH, GATE_LORA, RWKV_DIM), GATE_LORA ** -0.5),
        'k_k': 0.85 + nrm((DEPTH, RWKV_DIM), 0.05),
        'k_a': gain((DEPTH, RWKV_DIM)),
        'r_k': nrm((DEPTH, RWKV_HEADS, HEAD_DIM), 0.1),
        'ln_x_w': gain((DEPTH, RWKV_DIM)),
        'ln_x_b': nrm((DEPTH, RWKV_DIM), 0.02),
        'w_up_att': nrm((DEPTH, ATT_DIM, D), ATT_DIM ** -0.5),
        'w_up_rwkv': nrm((DEPTH, RWKV_DIM, D), RWKV_DIM ** -0.5),
        'w_out': nrm((DEPTH, D, D), D ** -0.5),
        'w_router': nrm((DEPTH, D, N_EXPERTS), D ** -0.5),
        'b_router': nrm((DEPTH, N_EXPERTS), 0.01),
        'w_gate_up': nrm((DEPTH, N_EXPERTS, D, 2 * D_EXPERT), D ** -0.5),
        'b_gate_up': nrm((DEPTH, N_EXPERTS, 2 * D_EXPERT), 0.02),
        'w_down': nrm((DEPTH, N_EXPERTS, D_EXPERT, D), D_EXPERT ** -0.5),
        'b_down': nrm((DEPTH, N_EXPERTS, D), 0.02),
    }

def first_block(x, c, ctx, c_ctx, w_ada, b_ada, g_pre_mix, g_post_mix, g_pre_ffn, g_post_ffn,
              w_in, b_in, mu_prev, mu_next, att_sinks, w0_f, w0_b, w2_f, w2_b, a0_f, a0_b,
              a2_f, a2_b, g2, k_k, k_a, r_k, ln_x_w, ln_x_b, w_up_att, w_up_rwkv, w_out,
              w_router, b_router, w_gate_up, b_gate_up, w_down, b_down):
    B = x.shape[0]
    silu_c = jax.nn.silu(c)
    silu_cc = jax.nn.silu(c_ctx)
    for l in range(DEPTH):
        p = dict(w_in=w_in[l], b_in=b_in[l], mu_prev=mu_prev[l], mu_next=mu_next[l], sinks=att_sinks[l],
                 w0_f=w0_f[l], w0_b=w0_b[l], w2_f=w2_f[l], w2_b=w2_b[l], a0_f=a0_f[l], a0_b=a0_b[l],
                 a2_f=a2_f[l], a2_b=a2_b[l], g2=g2[l], k_k=k_k[l], k_a=k_a[l], r_k=r_k[l],
                 ln_x_w=ln_x_w[l], ln_x_b=ln_x_b[l], w_up_att=w_up_att[l], w_up_rwkv=w_up_rwkv[l],
                 w_out=w_out[l], w_router=w_router[l], b_router=b_router[l], w_gate_up=w_gate_up[l],
                 b_gate_up=b_gate_up[l], w_down=w_down[l], b_down=b_down[l])
        mx = [m[:, None, :] for m in jnp.split(silu_c @ w_ada[l] + b_ada[l], 6, axis=-1)]
        mc = jnp.split(silu_cc @ w_ada[l] + b_ada[l], 6, axis=-1)
        hc = modulate(rms_norm(ctx, g_pre_mix[l]), mc[0], mc[1])
        qc, kc, vc, fc, zc_gate = project(hc, p)
        zero_state = jnp.zeros((B, RWKV_HEADS, HEAD_DIM, HEAD_DIM), F32)
        yc, sc_f, sc_b = bidir_scan(fc, zero_state, zero_state)
        hx = modulate(rms_norm(x, g_pre_mix[l]), mx[0], mx[1])
        q, k, v, fx, zx_gate = project(hx, p)
        att_x = window_attention(axial_rope(q), axial_rope(k), v, kc, vc, p['sinks'])
        yx, _, _ = bidir_scan(fx, sc_f, sc_b)
        mix_x = merge_branches(att_x, rwkv_output(yx, fx, p), zx_gate, p)
        x = x + mx[2] * rms_norm(mix_x, g_post_mix[l])
        hf = modulate(rms_norm(x, g_pre_ffn[l]), mx[3], mx[4])
        x = x + mx[5] * rms_norm(moe_ffn(hf, p), g_post_ffn[l])
        if l + 1 < DEPTH:
            mix_c = merge_branches(context_attention(qc, kc, vc, p['sinks']), rwkv_output(yc, fc, p), zc_gate, p)
            ctx = ctx + mc[2] * rms_norm(mix_c, g_post_mix[l])
            hcf = modulate(rms_norm(ctx, g_pre_ffn[l]), mc[3], mc[4])
            ctx = ctx + mc[5] * rms_norm(moe_ffn(hcf, p), g_post_ffn[l])
    return x


CHUNK = 64
Q_BLOCK = 128
N_HEADS_A = 8
NOPE_DIM = 64
ROPE_DIM = 32
V_DIM_A = 64
Q_LORA = 384
KV_LORA = 256
N_HEADS_B = 8
HEAD_DIM_B = 64
WIDTH_A = N_HEADS_A * V_DIM_A
WIDTH_B = N_HEADS_B * HEAD_DIM_B
ROPE_THETA = 10000.0
EPS = 1e-6
SPLITS = (Q_LORA, KV_LORA, ROPE_DIM, WIDTH_A, WIDTH_B, WIDTH_B, WIDTH_B,
          N_HEADS_B, WIDTH_B, D_MODEL, D_MODEL)
D_IN = sum(SPLITS)


def rms_norm_2(x, w):
    xf = x.astype(jnp.float32)
    y = xf * lax.rsqrt(jnp.mean(xf * xf, axis=-1, keepdims=True) + EPS)
    return (y * w.astype(jnp.float32)).astype(x.dtype)

def rope_angles(positions):
    inv_freq = ROPE_THETA ** (-jnp.arange(0, ROPE_DIM, 2, dtype=jnp.float32) / ROPE_DIM)
    ang = positions.astype(jnp.float32)[..., None] * inv_freq
    return jnp.cos(ang), jnp.sin(ang)

def apply_rope(x, cos, sin):
    x1, x2 = jnp.split(x.astype(jnp.float32), 2, axis=-1)
    y = jnp.concatenate([x1 * cos - x2 * sin, x2 * cos + x1 * sin], axis=-1)
    return y.astype(x.dtype)

def chunk_causal_mask(lo, hi):
    qp = lo + jnp.arange(Q_BLOCK)
    kp = jnp.arange(hi)
    return (kp[None, :] // CHUNK) <= (qp[:, None] // CHUNK)

def mla_attention(q_nope, q_rope, k_nope, k_rope, v):
    seq = q_nope.shape[1]
    scale = 1.0 / math.sqrt(NOPE_DIM + ROPE_DIM)
    outs = []
    for i in range(seq // Q_BLOCK):
        lo, hi = i * Q_BLOCK, (i + 1) * Q_BLOCK
        s = (jnp.einsum('bqhd,bkhd->bhqk', q_nope[:, lo:hi], k_nope[:, :hi],
                        preferred_element_type=jnp.float32)
             + jnp.einsum('bqhr,bkr->bhqk', q_rope[:, lo:hi], k_rope[:, :hi],
                          preferred_element_type=jnp.float32)) * scale
        s = jnp.where(chunk_causal_mask(lo, hi), s, -jnp.inf)
        p = jax.nn.softmax(s, axis=-1).astype(v.dtype)
        outs.append(jnp.einsum('bhqk,bkhd->bqhd', p, v[:, :hi]))
    return jnp.concatenate(outs, axis=1)

def fox_attention(q, k, v, log_f):
    seq = q.shape[1]
    scale = 1.0 / math.sqrt(HEAD_DIM_B)
    cum = jnp.swapaxes(jnp.cumsum(log_f, axis=1), 1, 2)
    outs = []
    for i in range(seq // Q_BLOCK):
        lo, hi = i * Q_BLOCK, (i + 1) * Q_BLOCK
        s = jnp.einsum('bqhd,bkhd->bhqk', q[:, lo:hi], k[:, :hi],
                       preferred_element_type=jnp.float32) * scale
        s = s + (cum[:, :, lo:hi, None] - cum[:, :, None, :hi])
        qp = lo + jnp.arange(Q_BLOCK)
        kp = jnp.arange(hi)
        s = jnp.where(kp[None, :] <= qp[:, None], s, -jnp.inf)
        p = jax.nn.softmax(s, axis=-1).astype(v.dtype)
        outs.append(jnp.einsum('bhqk,bkhd->bqhd', p, v[:, :hi]))
    return jnp.concatenate(outs, axis=1)

def second_inputs(seed: int = 0) -> dict:
    key = jax.random.key(seed)
    ks = jax.random.split(key, 24)
    f32 = jnp.float32
    nrm = lambda k, shape, s: jax.random.normal(k, shape, f32) * s
    gain = lambda k, n: 1.0 + 0.05 * jax.random.normal(k, (DEPTH, n), f32)
    x = jax.random.normal(ks[0], (BATCH, SEQ, D_MODEL), f32)
    c = jax.random.normal(ks[1], (BATCH, D_MODEL), f32)
    offset = jax.random.randint(ks[2], (BATCH, 1), 0, 4096, dtype=jnp.int32)
    positions = offset + jnp.arange(SEQ, dtype=jnp.int32)[None, :]
    return {
        "x": x,
        "c": c,
        "positions": positions,
        "w_ada": nrm(ks[3], (DEPTH, D_MODEL, 3 * D_MODEL), 0.5 * D_MODEL ** -0.5),
        "b_ada": nrm(ks[4], (DEPTH, 3 * D_MODEL), 0.02),
        "norm_w": gain(ks[5], D_MODEL),
        "w_in": nrm(ks[6], (DEPTH, D_MODEL, D_IN), D_MODEL ** -0.5),
        "b_f": jax.random.uniform(ks[7], (DEPTH, N_HEADS_B), f32, 1.0, 5.0),
        "q_lora_norm_w": gain(ks[8], Q_LORA),
        "kv_lora_norm_w": gain(ks[9], KV_LORA),
        "w_uq": nrm(ks[10], (DEPTH, Q_LORA, N_HEADS_A * (NOPE_DIM + ROPE_DIM)), Q_LORA ** -0.5),
        "w_ukv": nrm(ks[11], (DEPTH, KV_LORA, N_HEADS_A * (NOPE_DIM + V_DIM_A)), KV_LORA ** -0.5),
        "qn_nope_a": gain(ks[12], NOPE_DIM),
        "qn_rope_a": gain(ks[13], ROPE_DIM),
        "kn_nope_a": gain(ks[14], NOPE_DIM),
        "kn_rope_a": gain(ks[15], ROPE_DIM),
        "qn_b": gain(ks[16], HEAD_DIM_B),
        "kn_b": gain(ks[17], HEAD_DIM_B),
        "w_branch_a": nrm(ks[18], (DEPTH, WIDTH_A, D_MODEL), WIDTH_A ** -0.5),
        "w_branch_b": nrm(ks[19], (DEPTH, WIDTH_B, D_MODEL), WIDTH_B ** -0.5),
        "w_out": nrm(ks[20], (DEPTH, D_MODEL, D_MODEL), D_MODEL ** -0.5),
    }

def second_block(x, c, positions, w_ada, b_ada, norm_w, w_in, b_f, q_lora_norm_w,
              kv_lora_norm_w, w_uq, w_ukv, qn_nope_a, qn_rope_a, kn_nope_a,
              kn_rope_a, qn_b, kn_b, w_branch_a, w_branch_b, w_out):
    B, S, _ = x.shape
    cos, sin = rope_angles(positions)
    split_points = np.cumsum(SPLITS)[:-1].tolist()
    for l in range(DEPTH):
        ada = c @ w_ada[l] + b_ada[l]
        shift, scale, gate = jnp.split(ada, 3, axis=-1)
        h = rms_norm_2(x, norm_w[l]) * (1.0 + scale[:, None, :]) + shift[:, None, :]

        proj = h @ w_in[l]
        (cq, ckv, k_rope, gate_a, q_b, k_b, v_b, f_b, gate_b,
         mg_a, mg_b) = jnp.split(proj, split_points, axis=-1)

        q = (rms_norm_2(cq, q_lora_norm_w[l]) @ w_uq[l]).reshape(B, S, N_HEADS_A, NOPE_DIM + ROPE_DIM)
        q_nope, q_rope = q[..., :NOPE_DIM], q[..., NOPE_DIM:]
        kv = (rms_norm_2(ckv, kv_lora_norm_w[l]) @ w_ukv[l]).reshape(B, S, N_HEADS_A, NOPE_DIM + V_DIM_A)
        k_nope, v_a = kv[..., :NOPE_DIM], kv[..., NOPE_DIM:]
        q_nope = rms_norm_2(q_nope, qn_nope_a[l])
        q_rope = apply_rope(rms_norm_2(q_rope, qn_rope_a[l]), cos[:, :, None, :], sin[:, :, None, :])
        k_nope = rms_norm_2(k_nope, kn_nope_a[l])
        k_rope = apply_rope(rms_norm_2(k_rope, kn_rope_a[l]), cos, sin)
        o_a = mla_attention(q_nope, q_rope, k_nope, k_rope, v_a).reshape(B, S, WIDTH_A)
        y_a = o_a * jax.nn.silu(gate_a)

        qb = rms_norm_2(q_b.reshape(B, S, N_HEADS_B, HEAD_DIM_B), qn_b[l])
        kb = rms_norm_2(k_b.reshape(B, S, N_HEADS_B, HEAD_DIM_B), kn_b[l])
        vb = v_b.reshape(B, S, N_HEADS_B, HEAD_DIM_B)
        log_f = jax.nn.log_sigmoid(f_b.astype(jnp.float32) + b_f[l].astype(jnp.float32))
        o_b = fox_attention(qb, kb, vb, log_f).reshape(B, S, WIDTH_B)
        y_b = o_b * jax.nn.silu(gate_b)

        merged = (jax.nn.sigmoid(mg_a) * (y_a @ w_branch_a[l])
                  + jax.nn.sigmoid(mg_b) * (y_b @ w_branch_b[l]))
        x = x + gate[:, None, :] * (merged @ w_out[l])
    return x


def setup_inputs(seed=0):
    out = dict(first_inputs(seed))
    for name, value in second_inputs(seed + 1).items():
        if name != "x":
            out[name + "_2"] = value
    return out


def reference(
    x, c, ctx, c_ctx, w_ada, b_ada, g_pre_mix, g_post_mix, g_pre_ffn, g_post_ffn, w_in, b_in,
    mu_prev, mu_next, att_sinks, w0_f, w0_b, w2_f, w2_b, a0_f, a0_b, a2_f, a2_b, g2, k_k, k_a,
    r_k, ln_x_w, ln_x_b, w_up_att, w_up_rwkv, w_out, w_router, b_router, w_gate_up, b_gate_up,
    w_down, b_down, c_2, positions_2, w_ada_2, b_ada_2, norm_w_2, w_in_2, b_f_2,
    q_lora_norm_w_2, kv_lora_norm_w_2, w_uq_2, w_ukv_2, qn_nope_a_2, qn_rope_a_2, kn_nope_a_2,
    kn_rope_a_2, qn_b_2, kn_b_2, w_branch_a_2, w_branch_b_2, w_out_2,
):
    x = first_block(
        x, c, ctx, c_ctx, w_ada, b_ada, g_pre_mix, g_post_mix, g_pre_ffn, g_post_ffn, w_in,
        b_in, mu_prev, mu_next, att_sinks, w0_f, w0_b, w2_f, w2_b, a0_f, a0_b, a2_f, a2_b, g2,
        k_k, k_a, r_k, ln_x_w, ln_x_b, w_up_att, w_up_rwkv, w_out, w_router, b_router,
        w_gate_up, b_gate_up, w_down, b_down,
    )
    return second_block(
        x, c_2, positions_2, w_ada_2, b_ada_2, norm_w_2, w_in_2, b_f_2, q_lora_norm_w_2,
        kv_lora_norm_w_2, w_uq_2, w_ukv_2, qn_nope_a_2, qn_rope_a_2, kn_nope_a_2, kn_rope_a_2,
        qn_b_2, kn_b_2, w_branch_a_2, w_branch_b_2, w_out_2,
    )


_drawn_inputs = setup_inputs


def setup_inputs(seed=0):
    import zlib

    import numpy as np

    out = dict(_drawn_inputs(seed))
    spreads = {}
    factors = {'g_post_ffn': 3.739,
     'att_sinks': 8.0,
     'w2_f': 3.059,
     'ln_x_b': 3.232,
     'b_router': 3.149,
     'b_gate_up': 8.0,
     'b_down': 8.0,
     'b_ada_2': 6.592,
     'norm_w_2': 6.409,
     'b_f_2': 3.442,
     'q_lora_norm_w_2': 8.0,
     'kv_lora_norm_w_2': 8.0,
     'w_uq_2': 3.303,
     'qn_nope_a_2': 8.0,
     'qn_rope_a_2': 8.0,
     'kn_nope_a_2': 8.0,
     'kn_rope_a_2': 8.0,
     'qn_b_2': 8.0,
     'kn_b_2': 8.0}
    for name, (base, spread) in spreads.items():
        noise = np.random.default_rng([zlib.crc32(name.encode()), seed]).standard_normal(out[name].shape)
        drawn = base * np.exp(spread * noise) if base else spread * noise
        out[name] = jnp.asarray(drawn.astype(out[name].dtype))
    for name, factor in factors.items():
        out[name] = (out[name] * factor).astype(out[name].dtype)
    return out
```

```python
from contextlib import ExitStack, contextmanager

import numpy as np

import concourse.bass as bass
from concourse import mybir

F32 = mybir.dt.float32
I32 = mybir.dt.int32
U32 = mybir.dt.uint32
ALU = mybir.AluOpType
ACT = mybir.ActivationFunctionType
AX = mybir.AxisListType

P = 128
D = 1024
KD = D // P
SEQ = 512
CTX = 256
NT_X = SEQ // P
NT_C = CTX // P
NTOK = SEQ + CTX
HD = 64
NEG = -1e30
RMS_EPS = 1e-6


class Shared:

    def __init__(self, ident, vec, eps_col, ada, ada2):
        self.ident, self.vec, self.eps_col, self.ada, self.ada2 = ident, vec, eps_col, ada, ada2


@contextmanager
def stage(nc, name, *signals, clear=()):
    with ExitStack() as held:
        sems = {s: held.enter_context(nc.semaphore(f"{name}_{s}")) for s in signals}
        with nc.Block() as block:
            yield sems, block
        numbers = sorted([x.num for x in sems.values()] + [x.num for x in clear])
        starts = [i for i, x in enumerate(numbers) if i == 0 or x != numbers[i - 1] + 1] + [len(numbers)]
        for i, j in zip(starts[:-1], starts[1:]):
            nc.gpsimd.sem_clear(range(numbers[i], numbers[j - 1] + 1))
        nc.all_engine_barrier()


def chained(engine, signal):
    count = [0]

    def step(instruction):
        count[0] += 1
        instruction.then_inc(signal, 1)
        engine.wait_ge(signal, count[0])

    return step


def row_to_all(row, n):
    return bass.AP(tensor=row.tensor, offset=row.offset, ap=[[0, P], [1, n]])


def vector_columns():
    at, cols = 0, {}
    for name, n in (("c", 8), ("c_ctx", 8), ("c_2", 8), ("b_ada", 48), ("g_pre_mix", 8), ("g_post_mix", 8),
                    ("g_pre_ffn", 8), ("g_post_ffn", 8), ("b_ada_2", 24), ("norm_w_2", 8), ("lora_b_in", 3),
                    ("lora_mu_prev", 3), ("lora_mu_next", 3), ("lora_norms_2", 5)):
        cols[name] = slice(at, at + n)
        at += n
    return cols, at


VCOL, NVCOL = vector_columns()


def ada_stage(nc, name, cond, n_cond, w_dram, n_chunks, bias_cols, ada, first_chunk=0):
    chunk = 4
    wv = w_dram.rearrange("(k p) n -> p k n", p=P)
    with ExitStack() as held:
        w_sb = held.enter_context(nc.sbuf_tensor(f"{name}_w", [P, 3, KD, 512], F32))
        ps = held.enter_context(nc.psum_tensor(f"{name}_ps", [P, 2, chunk, 128], F32))
        with stage(nc, name, "w0", "w1", "w2", "columns", "evacuated") as (s, block):
            loaded = [s["w0"], s["w1"], s["w2"]]

            @block.sync
            def _(sp):
                for c in range(n_chunks):
                    if c >= 3:
                        sp.wait_ge(s["columns"], c - 2)
                    at = (first_chunk + c) * 512
                    sp.dma_start(w_sb[:, c % 3], wv[:, :, at:at + 512]).then_inc(loaded[c % 3], 16)

            @block.tensor
            def _(pe):
                for c in range(n_chunks):
                    pe.wait_ge(loaded[c % 3], 16 * (c // 3 + 1))
                    if c >= 2:
                        pe.wait_ge(s["evacuated"], c - 1)
                    for m in range(chunk):
                        for k in range(KD):
                            last = nc.tensor.matmul(ps[:, c % 2, m, 0:n_cond], w_sb[:, c % 3, k, m * P:(m + 1) * P],
                                                    cond[:, k, :], start=(k == 0), stop=(k == KD - 1))
                    last.then_inc(s["columns"], 1)

            @block.vector
            def _(dve):
                for c in range(n_chunks):
                    dve.wait_ge(s["columns"], c + 1)
                    m = (first_chunk + c) * chunk
                    bias = bias_cols[:, m:m + chunk].unsqueeze(2).to_broadcast([P, chunk, n_cond])
                    nc.vector.tensor_tensor(ada[:, m:m + chunk, :], ps[:, c % 2, :, 0:n_cond], bias,
                                            ALU.add).then_inc(s["evacuated"], 1)


def norm_turn_stage(nc, name, tiles, sources, xn, hT, affine, eps, ident):
    n = len(tiles)
    with ExitStack() as held:
        squares = held.enter_context(nc.sbuf_tensor(f"{name}_sq", [P, D], F32))
        stat = held.enter_context(nc.sbuf_tensor(f"{name}_stat", [P, 3, n], F32))
        ps = held.enter_context(nc.psum_tensor(f"{name}_ps", [P, 2, 2, 512], F32))
        with stage(nc, name, "x", "squared", "root", "inverse", "normed", "turned", "out_act", "out_dve") as (s, block):
            @block.sync
            def _(sp):
                if sources is not None:
                    for m in range(n):
                        sp.dma_start(tiles[m], sources[m]).then_inc(s["x"], 16)

            @block.scalar
            def _(act):
                if sources is not None:
                    act.wait_ge(s["x"], 16 * n)
                for m in range(n):
                    if m:
                        act.wait_ge(s["squared"], m)
                    nc.scalar.activation(squares[:, :], tiles[m], ACT.Square,
                                         accum_out=stat[:, 0, m:m + 1]).then_inc(s["squared"], 1)
                act.wait_ge(s["squared"], n)
                nc.scalar.activation(stat[:, 1, :], stat[:, 0, :], ACT.Sqrt, scale=1.0 / D,
                                     bias=eps).then_inc(s["root"], 1)
                for m in range(n):
                    act.wait_ge(s["turned"], m + 1)
                    for k in range(4):
                        gain, shift = affine(m, k)
                        last = nc.scalar.activation(hT[:, k, m * P:(m + 1) * P], ps[:, m % 2, 0, k * P:(k + 1) * P],
                                                    ACT.Identity, scale=gain, bias=shift)
                    last.then_inc(s["out_act"], 1)

            @block.vector
            def _(dve):
                dve.wait_ge(s["root"], 1)
                nc.vector.reciprocal(stat[:, 2, :], stat[:, 1, :]).then_inc(s["inverse"], 1)
                dve.wait_ge(s["inverse"], 1)
                for m in range(n):
                    nc.vector.tensor_scalar(xn[m], tiles[m], stat[:, 2, m:m + 1], None, ALU.mult).then_inc(s["normed"], 1)
                for m in range(n):
                    dve.wait_ge(s["turned"], m + 1)
                    for k in range(4, 8):
                        gain, shift = affine(m, k)
                        last = nc.vector.tensor_scalar(hT[:, k, m * P:(m + 1) * P],
                                                       ps[:, m % 2, 1, (k - 4) * P:(k - 3) * P],
                                                       gain, shift, ALU.mult, ALU.add)
                    last.then_inc(s["out_dve"], 1)

            @block.tensor
            def _(pe):
                for m in range(n):
                    pe.wait_ge(s["normed"], m + 1)
                    if m >= 2:
                        pe.wait_ge(s["out_act"], m - 1)
                        pe.wait_ge(s["out_dve"], m - 1)
                    for k in range(KD):
                        last = nc.tensor.transpose(ps[:, m % 2, k // 4, (k % 4) * P:(k % 4 + 1) * P],
                                                   xn[m][:, k * P:(k + 1) * P], ident)
                    last.then_inc(s["turned"], 1)


def token_gemm_stage(nc, name, chunks, w_slots, evacuate, extra=()):
    with ExitStack() as held:
        ps = held.enter_context(nc.psum_tensor(f"{name}_ps", [P, 4, 512], F32))
        with stage(nc, name, "w0", "w1", "tile", "free", "chain", "step2", *extra) as (s, block):
            loaded = [s["w0"], s["w1"]]
            firsts, tiles = [], []
            for c, chunk in enumerate(chunks):
                firsts.append(len(tiles))
                tiles += [(c, m) for m in range(len(chunk["lhs"]))]
            firsts.append(len(tiles))

            @block.sync
            def _(sp):
                for c, chunk in enumerate(chunks):
                    if c >= 2:
                        sp.wait_ge(s["tile"], firsts[c - 1])
                    sp.dma_start(w_slots[c % 2][:, 0:chunk["k"], 0:chunk["width"]],
                                 chunk["w"].rearrange("(k p) n -> p k n", p=P)).then_inc(loaded[c % 2], 16)

            @block.tensor
            def _(pe):
                for t, (c, m) in enumerate(tiles):
                    chunk = chunks[c]
                    if m == 0:
                        pe.wait_ge(loaded[c % 2], 16 * (c // 2 + 1))
                    if t >= 4:
                        pe.wait_ge(s["free"], t - 3)
                    for k in range(chunk["k"]):
                        last = nc.tensor.matmul(ps[:, t % 4, 0:chunk["width"]], chunk["lhs"][m](k),
                                                w_slots[c % 2][:, k, 0:chunk["width"]],
                                                start=(k == 0), stop=(k == chunk["k"] - 1))
                    last.then_inc(s["tile"], 1)

            work = [(t, chunks[c], m, ps[:, t % 4, 0:chunks[c]["width"]]) for t, (c, m) in enumerate(tiles)]
            evacuate(s, block, work)


def attention_stage(nc, name, items, scale):
    n = len(items)
    W = 640
    with ExitStack() as held:
        masked = held.enter_context(nc.sbuf_tensor(f"{name}_masked", [P, 2, W], F32))
        prob = held.enter_context(nc.sbuf_tensor(f"{name}_prob", [P, 2, W], F32))
        probT = held.enter_context(nc.sbuf_tensor(f"{name}_probT", [P, 2, W], F32))
        col = held.enter_context(nc.sbuf_tensor(f"{name}_col", [P, 3, 8], F32))
        ps_s = held.enter_context(nc.psum_tensor(f"{name}_s", [P, 2, 1024], F32))
        ps_t = held.enter_context(nc.psum_tensor(f"{name}_t", [P, 1024], F32))
        ps_o = held.enter_context(nc.psum_tensor(f"{name}_o", [P, 2, 512], F32))
        MAX, NEGMAX, SUM, SINK, DEN, INV = range(6)
        with stage(nc, name, "scores", "maxed", "negated", "probs", "turned", "probT", "values", "done",
                   "den") as (s, block):
            def c(i, what):
                return col[:, i % 3, what:what + 1]

            @block.tensor
            def _(pe):
                for i in range(n + 2):
                    if i < n:
                        if i >= 2:
                            pe.wait_ge(s["maxed"], i - 1)
                        it, at = items[i], 0
                        for keys in it["keys"]:
                            w = keys.shape[1]
                            done = 0
                            while done < w:
                                part = min(w - done, 512 - at % 512)
                                last = nc.tensor.matmul(ps_s[:, i % 2, at:at + part], it["q"],
                                                        keys[:, done:done + part], start=(at % 512 == 0),
                                                        stop=True, skip_group_check=True)
                                at, done = at + part, done + part
                        last.then_inc(s["scores"], 1)
                    if 1 <= i <= n:
                        j = i - 1
                        pe.wait_ge(s["probs"], j + 1)
                        if j >= 1:
                            pe.wait_ge(s["probT"], j)
                        for t in range(len(items[j]["v"])):
                            last = nc.tensor.transpose(ps_t[:, t * P:(t + 1) * P], prob[:, j % 2, t * P:(t + 1) * P],
                                                       items[j]["ident"])
                        last.then_inc(s["turned"], 1)
                    if i >= 2:
                        j = i - 2
                        pe.wait_ge(s["probT"], j + 1)
                        if j >= 2:
                            pe.wait_ge(s["done"], j - 1)
                        vs = items[j]["v"]
                        for t, v in enumerate(vs):
                            last = nc.tensor.matmul(ps_o[:, j % 2, 0:HD], probT[:, j % 2, t * P:(t + 1) * P], v,
                                                    start=(t == 0), stop=(t == len(vs) - 1))
                        last.then_inc(s["values"], 1)

            @block.vector
            def _(dve):
                for i in range(n + 2):
                    if i < n:
                        it = items[i]
                        w = P * len(it["v"])
                        dve.wait_ge(s["scores"], i + 1)
                        if i >= 2:
                            dve.wait_ge(s["probs"], i - 1)
                        if i >= 3:
                            dve.wait_ge(s["done"], i - 2)
                        start = it["sink"] if it["sink"] is not None else -3.0e38
                        nc.vector.tensor_tensor_reduce(masked[:, i % 2, 0:w], ps_s[:, i % 2, 0:w], it["mask"], scale,
                                                       start, ALU.add, ALU.max, c(i, MAX)).then_inc(s["maxed"], 1)
                        dve.wait_ge(s["maxed"], i + 1)
                        nc.vector.tensor_scalar(c(i, NEGMAX), c(i, MAX), -1.0, None, ALU.mult).then_inc(s["negated"], 1)
                    if 1 <= i <= n:
                        j = i - 1
                        w = P * len(items[j]["v"])
                        dve.wait_ge(s["turned"], j + 1)
                        if j >= 2:
                            dve.wait_ge(s["values"], j - 1)
                        nc.vector.tensor_copy(probT[:, j % 2, 0:w], ps_t[:, 0:w]).then_inc(s["probT"], 1)
                    if i >= 2:
                        j = i - 2
                        den = c(j, SUM)
                        if items[j]["sink"] is not None:
                            nc.vector.tensor_tensor(c(j, DEN), c(j, SUM), c(j, SINK), ALU.add).then_inc(s["den"], 1)
                            den = c(j, DEN)
                        else:
                            nc.vector.tensor_copy(c(j, DEN), c(j, SUM)).then_inc(s["den"], 1)
                            den = c(j, DEN)
                        dve.wait_ge(s["den"], 2 * j + 1)
                        nc.vector.reciprocal(c(j, INV), den).then_inc(s["den"], 1)
                        dve.wait_ge(s["den"], 2 * j + 2)
                        dve.wait_ge(s["values"], j + 1)
                        nc.vector.tensor_scalar(items[j]["out"], ps_o[:, j % 2, 0:HD], c(j, INV), None,
                                                ALU.mult).then_inc(s["done"], 1)

            @block.scalar
            def _(act):
                for i, it in enumerate(items):
                    w = P * len(it["v"])
                    act.wait_ge(s["negated"], i + 1)
                    if i >= 2:
                        act.wait_ge(s["turned"], i - 1)
                    if it["sink"] is not None:
                        nc.scalar.activation(c(i, SINK), c(i, NEGMAX), ACT.Exp, bias=it["sink"])
                    nc.scalar.activation(prob[:, i % 2, 0:w], masked[:, i % 2, 0:w], ACT.Exp, bias=c(i, NEGMAX),
                                         accum_out=c(i, SUM)).then_inc(s["probs"], 1)


def turn_stage(nc, name, sources, targets, ident):
    n = len(sources)
    groups = [list(range(a, min(a + 4, n))) for a in range(0, n, 4)]
    with ExitStack() as held:
        ps = held.enter_context(nc.psum_tensor(f"{name}_ps", [P, 4, 512], F32))
        with stage(nc, name, "turned", "even", "odd") as (s, block):
            @block.tensor
            def _(pe):
                for q, group in enumerate(groups):
                    if q >= 4:
                        pe.wait_ge(s["odd"] if q % 2 else s["even"], (q - 4) // 2 + 1)
                    for j, i in enumerate(group):
                        last = nc.tensor.transpose(ps[:, q % 4, j * P:(j + 1) * P], sources[i], ident)
                    last.then_inc(s["turned"], 1)

            def copies(engine, copy, odd, signal):
                for q, group in enumerate(groups):
                    if q % 2 == odd:
                        engine.wait_ge(s["turned"], q + 1)
                        for j, i in enumerate(group):
                            last = copy(targets[i], ps[:, q % 4, j * P:(j + 1) * P])
                        last.then_inc(signal, 1)

            @block.vector
            def _(dve):
                copies(dve, nc.vector.tensor_copy, 0, s["even"])

            @block.scalar
            def _(act):
                copies(act, nc.scalar.copy, 1, s["odd"])


def first_block(nc, d, g, x, row_cols, ones):
    with ExitStack() as mixing:
        rwkT = mixing.enter_context(nc.sbuf_tensor("rwkT", [P, 4, SEQ], F32))
        hT = mixing.enter_context(nc.sbuf_tensor("hT", [P, KD, NTOK], F32))
        mix_inputs(nc, d, g, hT)
        rwkv_branch(nc, d, g, hT, rwkT)
        attT = mixing.enter_context(nc.sbuf_tensor("attT", [P, 4, SEQ], F32))
        window_attention(nc, d, g, hT, attT)
        gates = mixing.enter_context(nc.sbuf_tensor("gates", [P, NT_X, 2 * D], F32))
        merge_gates(nc, d, hT, gates)
        mix = mixing.enter_context(nc.sbuf_tensor("mix", [P, NT_X, D], F32))
        merge_and_out(nc, d, g, "mix", (attT, rwkT), gates, (d["w_up_att"], d["w_up_rwkv"]), d["w_out"], mix)
        with stage(nc, "x_in", "x") as (s, block):
            @block.sync
            def _(sp):
                sp.dma_start(x[:, :, :], d["x"][0].rearrange("(m p) n -> p m n", p=P)).then_inc(s["x"], 16)
                sp.wait_ge(s["x"], 16)
        tiles = [x[:, m] for m in range(NT_X)]
        row = mixing.enter_context(nc.sbuf_tensor("mix_row", [P, D], F32))
        rows_stage(nc, g, "mix_rows", [row_cols[:, 0]], [row[:, :]], ones)
        add_normed_stage(nc, g, "post_mix", [mix[:, m] for m in range(NT_X)], tiles, row[:, :])
    with ExitStack() as ffn:
        def sb(name, shape, dtype=F32):
            return ffn.enter_context(nc.sbuf_tensor(name, shape, dtype))

        xn = sb("ffn_xn", [P, NT_X, D])
        gain = sb("ffn_gain", [P, KD])
        number, gate = sb("slot_of", [P, NT_X, N_EXP]), sb("gate_of", [P, NT_X, N_EXP])
        table, n_blocks = sb("table", [1, P], I32), sb("n_blocks", [1, 1], I32)
        with stage(nc, "ffn_gain", "done") as (s, block):
            @block.vector
            def _(dve):
                nc.vector.scalar_tensor_tensor(gain[:, :], g.ada[:, 32:40, 0], 1.0, g.vec[:, VCOL["g_pre_ffn"]],
                                               ALU.add, ALU.mult).then_inc(s["done"], 1)
        with nc.sbuf_tensor("ffn_hT", [P, KD, SEQ], F32) as hT:
            norm_turn_stage(nc, "ffn", tiles, None, [xn[:, m] for m in range(NT_X)], hT,
                            lambda m, k: (gain[:, k:k + 1], g.ada[:, 24 + k, 0:1]), g.eps_col[:, 0:1], g.ident[:, :])
            route_stage(nc, d, g, hT, ones, number, gate, table, n_blocks)
        y = sb("ffn_y", [P, NT_X, D])
        shift = sb("ffn_shift", [P, KD])
        with stage(nc, "ffn_shift", "done") as (s, block):
            @block.vector
            def _(dve):
                nc.vector.tensor_copy(shift[:, :], g.ada[:, 24:32, 0]).then_inc(s["done"], 1)
        experts(nc, d, g, xn, gain, shift, number, gate, table, n_blocks, y)
        row = sb("ffn_row", [P, D])
        rows_stage(nc, g, "ffn_rows", [row_cols[:, 1]], [row[:, :]], ones)
        add_normed_stage(nc, g, "post_ffn", [y[:, m] for m in range(NT_X)], tiles, row[:, :])


def mix_inputs(nc, d, g, hT):
    with ExitStack() as held:
        gain = held.enter_context(nc.sbuf_tensor("pre_gain", [P, 2, KD], F32))
        ctx_sb = held.enter_context(nc.sbuf_tensor("ctx_sb", [P, NT_C, D], F32))
        x_sb = held.enter_context(nc.sbuf_tensor("pre_x", [P, NT_X, D], F32))
        xn = held.enter_context(nc.sbuf_tensor("pre_xn", [P, 6, D], F32))
        with stage(nc, "pre_gain", "done") as (s, block):
            @block.vector
            def _(dve):
                for j in range(2):
                    nc.vector.scalar_tensor_tensor(gain[:, j, :], g.ada[:, 8:16, j], 1.0, g.vec[:, VCOL["g_pre_mix"]],
                                                   ALU.add, ALU.mult).then_inc(s["done"], 1)
        tiles = [ctx_sb[:, m] for m in range(NT_C)] + [x_sb[:, m] for m in range(NT_X)]
        sources = [d["ctx"][0, m * P:(m + 1) * P, :] for m in range(NT_C)]
        sources += [d["x"][0, m * P:(m + 1) * P, :] for m in range(NT_X)]

        def affine(m, k):
            j = 1 if m < NT_C else 0
            return gain[:, j, k:k + 1], g.ada[:, k, j:j + 1]

        norm_turn_stage(nc, "pre", tiles, sources, [xn[:, m] for m in range(6)], hT, affine, g.eps_col[:, 0:1],
                        g.ident[:, :])


def window_attention(nc, d, g, hT, attT):
    ident = g.ident[:, :]
    with ExitStack() as held:
        def sb(name, shape, dtype=F32):
            return held.enter_context(nc.sbuf_tensor(name, shape, dtype))

        qkv = sb("qkv", [P, NT_X, 768])
        kvc = sb("kvc", [P, NT_C, 256])
        rope = sb("rope", [P, NT_X, 2, 2, 16])
        masks = sb("win_masks", [P, 1152])
        sinks = sb("sinks", [P, 8])
        with ExitStack() as projecting:
            bias = projecting.enter_context(nc.sbuf_tensor("proj_bias", [P, 768], F32))
            slots = [projecting.enter_context(nc.sbuf_tensor(f"proj_w{i}", [P, KD, 512], F32)) for i in range(2)]
            w = d["w_in_tok"]

            def tok(t):
                return lambda k: hT[:, k, t * P:(t + 1) * P]

            chunks = [dict(w=w[:, 0:512], width=512, k=KD, lhs=[tok(NT_C + m) for m in range(NT_X)], col=0),
                      dict(w=w[:, 512:768], width=256, k=KD, lhs=[tok(NT_C + m) for m in range(NT_X)] +
                           [tok(m) for m in range(NT_C)], col=512)]

            def evacuate(s, block, work):
                def target(chunk, m):
                    a, b = chunk["col"], chunk["col"] + chunk["width"]
                    return qkv[:, m, a:b] if m < NT_X else kvc[:, m - NT_X, :]

                @block.scalar
                def _(act):
                    act.dma_start(bias[:, :], row_to_all(d["b_in_tok"], 768)).then_inc(s["side"], 16)
                    act.dma_start(rope[:, :, :, :, :], d["rope_axial"]).then_inc(s["side"], 16)
                    act.dma_start(masks[:, :], d["window_masks"]).then_inc(s["side"], 16)
                    act.dma_start(sinks[:, :], row_to_all(d["att_sinks"], 8)).then_inc(s["side"], 16)
                    act.wait_ge(s["side"], 64)

                @block.vector
                def _(dve):
                    dve.wait_ge(s["side"], 64)
                    for t, chunk, m, ps in work:
                        dve.wait_ge(s["tile"], t + 1)
                        a, b = chunk["col"], chunk["col"] + chunk["width"]
                        nc.vector.tensor_tensor(target(chunk, m), ps, bias[:, a:b], ALU.add).then_inc(s["free"], 1)

            token_gemm_stage(nc, "proj", chunks, slots, evacuate, extra=("side",))

        turned = sb("qk_turned", [P, 5, SEQ])
        kcT = sb("kcT", [P, CTX])
        rope_turn(nc, g, qkv, kvc, rope, turned, kcT)
        att = sb("att", [P, NT_X, 512])
        items = []
        for b in range(NT_X):
            for h in range(8):
                kv = h // 4
                rows = slice(HD * kv, HD * kv + HD)
                lo, hi = max(0, b - 1), min(NT_X, b + 2)
                mask = {0: masks[:, 640:1152], NT_X - 1: masks[:, 0:512]}.get(b, masks[:, 0:640])
                items.append(dict(
                    q=turned[rows, h % 4, b * P:(b + 1) * P],
                    keys=[kcT[rows, :], turned[rows, 4, lo * P:hi * P]],
                    v=[kvc[:, t, P + HD * kv:P + HD * kv + HD] for t in range(NT_C)] +
                      [qkv[:, t, 640 + HD * kv:640 + HD * kv + HD] for t in range(lo, hi)],
                    mask=mask, sink=sinks[:, h:h + 1], out=att[:, b, HD * h:HD * h + HD], ident=ident))
        attention_stage(nc, "window", items, HD ** -0.5)
        turn_stage(nc, "att_turn", [att[:, m, c * P:(c + 1) * P] for m in range(NT_X) for c in range(4)],
                   [attT[:, c, m * P:(m + 1) * P] for m in range(NT_X) for c in range(4)], ident)


def rope_turn(nc, g, qkv, kvc, rope, turned, kcT):
    ident = g.ident[:, :]
    with ExitStack() as held:
        rot = held.enter_context(nc.sbuf_tensor("rot", [P, NT_X, 640], F32))
        tmp = held.enter_context(nc.sbuf_tensor("rot_tmp", [P, 2, 4, 320], F32))
        ps = held.enter_context(nc.psum_tensor("rot_ps", [P, 2, 1024], F32))
        with stage(nc, "rot", "parts", "rotated", "turned", "copied") as (s, block):
            @block.vector
            def _(dve):
                for m in range(NT_X):
                    src = qkv[:, m, 0:640].rearrange("p (h a b c) -> p b h a c", h=10, a=2, b=2)
                    dst = rot[:, m, :].rearrange("p (h a b c) -> p b h a c", h=10, a=2, b=2)
                    cos = rope[:, m, 0].unsqueeze(1).to_broadcast([P, 10, 2, 16])
                    sin = rope[:, m, 1].unsqueeze(1).to_broadcast([P, 10, 2, 16])
                    if m >= 2:
                        dve.wait_ge(s["rotated"], 2 * (m - 1))
                    part = [tmp[:, m % 2, i, :].rearrange("p (h a c) -> p h a c", h=10, a=2) for i in range(4)]
                    for i, (x, y) in enumerate(((0, cos), (1, sin), (1, cos), (0, sin))):
                        nc.vector.tensor_tensor(part[i], src[:, x], y, ALU.mult).then_inc(s["parts"], 1)
                    dve.wait_ge(s["parts"], 4 * m + 4)
                    nc.vector.tensor_tensor(dst[:, 0], part[0], part[1], ALU.subtract).then_inc(s["rotated"], 1)
                    nc.vector.tensor_tensor(dst[:, 1], part[2], part[3], ALU.add).then_inc(s["rotated"], 1)

            @block.tensor
            def _(pe):
                for m in range(NT_X + 1):
                    if m >= 2:
                        pe.wait_ge(s["copied"], m - 1)
                    if m < NT_X:
                        pe.wait_ge(s["rotated"], 2 * m + 2)
                        for j in range(5):
                            last = nc.tensor.transpose(ps[:, m % 2, j * P:(j + 1) * P], rot[:, m, j * P:(j + 1) * P], ident)
                    else:
                        for t in range(NT_C):
                            last = nc.tensor.transpose(ps[:, m % 2, t * P:(t + 1) * P], kvc[:, t, 0:P], ident)
                    last.then_inc(s["turned"], 1)

            @block.scalar
            def _(act):
                for m in range(NT_X + 1):
                    act.wait_ge(s["turned"], m + 1)
                    if m < NT_X:
                        nc.scalar.copy(turned[:, :, m * P:(m + 1) * P],
                                       ps[:, m % 2, 0:640].rearrange("p (j t) -> p j t", j=5)).then_inc(s["copied"], 1)
                    else:
                        nc.scalar.copy(kcT[:, :], ps[:, m % 2, 0:CTX]).then_inc(s["copied"], 1)


def merge_gates(nc, d, hT, gates):
    with ExitStack() as held:
        bias = held.enter_context(nc.sbuf_tensor("gates_bias", [P, 2 * D], F32))
        slots = [held.enter_context(nc.sbuf_tensor(f"gates_w{i}", [P, KD, 512], F32)) for i in range(2)]

        def tok(t):
            return lambda k: hT[:, k, t * P:(t + 1) * P]

        chunks = [dict(w=d["w_in_tok"][:, 768 + 512 * c:1280 + 512 * c], width=512, k=KD,
                       lhs=[tok(NT_C + m) for m in range(NT_X)], col=512 * c) for c in range(4)]

        def evacuate(s, block, work):
            @block.vector
            def _(dve):
                dve.wait_ge(s["side"], 16)
                for t, chunk, m, ps in work:
                    dve.wait_ge(s["tile"], t + 1)
                    a = chunk["col"]
                    nc.vector.tensor_tensor(gates[:, m, a:a + 512], ps, bias[:, a:a + 512], ALU.add).then_inc(s["free"], 1)

            @block.scalar
            def _(act):
                act.dma_start(bias[:, :], row_to_all(d["b_gates"], 2 * D)).then_inc(s["side"], 16)
                for t, chunk, m, ps in work:
                    act.wait_ge(s["free"], t + 1)
                    gate = gates[:, m, chunk["col"]:chunk["col"] + 512]
                    nc.scalar.activation(gate, gate, ACT.Sigmoid)

        token_gemm_stage(nc, "gates", chunks, slots, evacuate, extra=("side",))


def rows_stage(nc, g, name, columns, rows, ones):
    with ExitStack() as held:
        diag = held.enter_context(nc.sbuf_tensor(f"{name}_diag", [P, 2, KD, P], F32))
        ps = held.enter_context(nc.psum_tensor(f"{name}_ps", [P, 2, 1024], F32))
        with stage(nc, name, "diag", "made", "copied") as (s, block):
            @block.vector
            def _(dve):
                for i, col in enumerate(columns):
                    if i >= 2:
                        dve.wait_ge(s["made"], i - 1)
                    for k in range(KD):
                        last = nc.vector.tensor_scalar(diag[:, i % 2, k, :], g.ident[:, :], col[:, k:k + 1], None, ALU.mult)
                    last.then_inc(s["diag"], 1)

            @block.tensor
            def _(pe):
                for i in range(len(columns)):
                    pe.wait_ge(s["diag"], i + 1)
                    if i >= 2:
                        pe.wait_ge(s["copied"], i - 1)
                    for half in range(2):
                        last = nc.tensor.matmul(ps[:, i % 2, 512 * half:512 * half + 512], ones,
                                                diag[:, i % 2, 4 * half:4 * half + 4, :].rearrange("p k n -> p (k n)"),
                                                start=True, stop=True)
                    last.then_inc(s["made"], 1)

            @block.scalar
            def _(act):
                for i, row in enumerate(rows):
                    act.wait_ge(s["made"], i + 1)
                    nc.scalar.copy(row, ps[:, i % 2, :]).then_inc(s["copied"], 1)


def add_normed_stage(nc, g, name, branch, x, row):
    n = len(x)
    with ExitStack() as held:
        squares = held.enter_context(nc.sbuf_tensor(f"{name}_sq", [P, D], F32))
        stat = held.enter_context(nc.sbuf_tensor(f"{name}_stat", [P, 3, n], F32))
        with stage(nc, name, "squared", "root", "chain", "scaled") as (s, block):
            @block.scalar
            def _(act):
                for m in range(n):
                    if m:
                        act.wait_ge(s["squared"], m)
                    nc.scalar.activation(squares[:, :], branch[m], ACT.Square,
                                         accum_out=stat[:, 0, m:m + 1]).then_inc(s["squared"], 1)
                act.wait_ge(s["squared"], n)
                nc.scalar.activation(stat[:, 1, :], stat[:, 0, :], ACT.Sqrt, scale=1.0 / D,
                                     bias=g.eps_col[:, 0:1]).then_inc(s["root"], 1)

            @block.vector
            def _(dve):
                step = chained(dve, s["chain"])
                dve.wait_ge(s["root"], 1)
                step(nc.vector.reciprocal(stat[:, 2, :], stat[:, 1, :]))
                for m in range(n):
                    nc.vector.scalar_tensor_tensor(branch[m], branch[m], stat[:, 2, m:m + 1], row, ALU.mult,
                                                   ALU.mult).then_inc(s["scaled"], 1)
                dve.wait_ge(s["scaled"], n)
                for m in range(n):
                    nc.vector.tensor_tensor(x[m], x[m], branch[m], ALU.add).then_inc(s["scaled"], 1)


def merge_and_out(nc, d, g, name, branches, gates, w_up, w_out, mix):
    with ExitStack() as held:
        merged = held.enter_context(nc.sbuf_tensor(f"{name}_merged", [P, NT_X, D], F32))
        tmp = held.enter_context(nc.sbuf_tensor(f"{name}_tmp", [P, 2, 512], F32))
        slots = [held.enter_context(nc.sbuf_tensor(f"{name}_w{i}", [P, KD, 512], F32)) for i in range(2)]

        def tok(t, m):
            return lambda k: t[:, k, m * P:(m + 1) * P]

        chunks = [dict(w=w_up[b][:, 512 * c:512 * c + 512], width=512, k=4, b=b, c=c,
                       lhs=[tok(branches[b], m) for m in range(NT_X)]) for b in range(2) for c in range(2)]

        def gated(s, block, work):
            @block.vector
            def _(dve):
                for t, chunk, m, ps in work:
                    dve.wait_ge(s["tile"], t + 1)
                    at = slice(512 * chunk["c"], 512 * chunk["c"] + 512)
                    gate = gates[:, m, D * chunk["b"] + at.start:D * chunk["b"] + at.stop]
                    if chunk["b"] == 0:
                        nc.vector.tensor_tensor(merged[:, m, at], ps, gate, ALU.mult).then_inc(s["free"], 1)
                    else:
                        if t > 8:
                            dve.wait_ge(s["chain"], t - 8)
                        nc.vector.tensor_tensor(tmp[:, t % 2, :], ps, gate, ALU.mult).then_inc(s["free"], 1)
                        dve.wait_ge(s["free"], t + 1)
                        nc.vector.tensor_tensor(merged[:, m, at], merged[:, m, at], tmp[:, t % 2, :],
                                                ALU.add).then_inc(s["chain"], 1)

        token_gemm_stage(nc, f"{name}_up", chunks, slots, gated)
        mergedT = held.enter_context(nc.sbuf_tensor(f"{name}_mergedT", [P, KD, SEQ], F32))
        turn_stage(nc, f"{name}_turn", [merged[:, m, k * P:(k + 1) * P] for m in range(NT_X) for k in range(KD)],
                   [mergedT[:, k, m * P:(m + 1) * P] for m in range(NT_X) for k in range(KD)], g.ident[:, :])
        chunks = [dict(w=w_out[:, 512 * c:512 * c + 512], width=512, k=KD, c=c,
                       lhs=[tok(mergedT, m) for m in range(NT_X)]) for c in range(2)]

        def keep(s, block, work):
            @block.vector
            def _(dve):
                for t, chunk, m, ps in work:
                    dve.wait_ge(s["tile"], t + 1)
                    nc.vector.tensor_copy(mix[:, m, 512 * chunk["c"]:512 * chunk["c"] + 512], ps).then_inc(s["free"], 1)

        token_gemm_stage(nc, f"{name}_out", chunks, slots, keep)


N_EXP = 32
TOP_K = 4
SLOTS = P
MAX_BLOCKS = 48
LIMIT, ALPHA = 7.0, 1.702


def route_stage(nc, d, g, hT, ones, number, gate, table, n_blocks):
    with ExitStack() as held:
        def sb(name, shape, dtype=F32):
            return held.enter_context(nc.sbuf_tensor(name, shape, dtype))

        w = sb("router_w", [P, KD, N_EXP])
        bias = sb("router_b", [P, N_EXP])
        iota = sb("router_iota", [P, P])
        part = sb("router_part", [P, 1])
        before = sb("router_before", [P, P])
        logits = sb("router_logits", [P, NT_X, N_EXP])
        top = sb("router_top", [P, NT_X, 8])
        index = sb("router_index", [P, NT_X, 8], U32)
        indexf = sb("router_indexf", [P, NT_X, 8])
        weight = sb("router_weight", [P, NT_X, TOP_K])
        negtop = sb("router_negtop", [P, NT_X])
        total = sb("router_total", [P, NT_X])
        chosen = sb("router_chosen", [P, NT_X, N_EXP])
        hit = sb("router_hit", [P, N_EXP])
        blocks, ends, starts, tmp = (sb(f"router_{x}", [P, N_EXP]) for x in ("blocks", "ends", "starts", "tmp"))
        expert = sb("router_expert", [P, 4])
        experti = sb("router_experti", [P, 1], I32)
        ps = held.enter_context(nc.psum_tensor("router_ps", [P, NT_X, 512], F32))
        ps_r = held.enter_context(nc.psum_tensor("router_rank", [P, 1, 512], F32))
        with stage(nc, "route", "loaded", "logits", "negtop", "weight", "chosen", "rank", "chain", "expert",
                   "table", "top") as (s, block):
            @block.sync
            def _(sp):
                sp.dma_start(w[:, :, :], d["w_router"].rearrange("(k p) e -> p k e", p=P)).then_inc(s["loaded"], 16)
                sp.dma_start(bias[:, :], row_to_all(d["b_router"], N_EXP)).then_inc(s["loaded"], 16)
                sp.dma_start(iota[:, :], row_to_all(d["iota"], P)).then_inc(s["loaded"], 16)
                sp.dma_start(part[:, :], d["iota"].rearrange("(p a) -> p a", a=1)).then_inc(s["loaded"], 16)
                sp.dma_start(before[:, :], d["before"]).then_inc(s["loaded"], 16)
                sp.wait_ge(s["expert"], 2)
                sp.dma_start(table[0:1, :], experti[:, 0:1]).then_inc(s["table"], 16)
                sp.wait_ge(s["table"], 16)

            @block.tensor
            def _(pe):
                pe.wait_ge(s["loaded"], 80)
                for m in range(NT_X):
                    for k in range(KD):
                        last = nc.tensor.matmul(ps[:, m, 0:N_EXP], hT[:, k, m * P:(m + 1) * P], w[:, k, :],
                                                start=(k == 0), stop=(k == KD - 1))
                    last.then_inc(s["logits"], 1)
                pe.wait_ge(s["chosen"], NT_X)
                for m in range(NT_X):
                    for q in range(m):
                        nc.tensor.matmul(ps_r[:, 0, m * N_EXP:(m + 1) * N_EXP], ones, chosen[:, q, :],
                                         start=(m == 0), stop=False, skip_group_check=True)
                    nc.tensor.matmul(ps_r[:, 0, m * N_EXP:(m + 1) * N_EXP], before[:, :], chosen[:, m, :],
                                     start=(m == 0), stop=True, skip_group_check=True)
                for q in range(NT_X):
                    last = nc.tensor.matmul(ps_r[:, 0, 128:160], ones, chosen[:, q, :], start=False,
                                            stop=(q == NT_X - 1), skip_group_check=True)
                last.then_inc(s["rank"], 1)

            @block.scalar
            def _(act):
                for m in range(NT_X):
                    act.wait_ge(s["negtop"], m + 1)
                    nc.scalar.activation(weight[:, m, :], top[:, m, 0:TOP_K], ACT.Exp, bias=negtop[:, m:m + 1],
                                         accum_out=total[:, m:m + 1]).then_inc(s["weight"], 1)

            @block.vector
            def _(dve):
                step = chained(dve, s["chain"])
                dve.wait_ge(s["loaded"], 80)
                for m in range(NT_X):
                    dve.wait_ge(s["logits"], m + 1)
                    step(nc.vector.tensor_tensor(logits[:, m, :], ps[:, m, 0:N_EXP], bias[:, :], ALU.add))
                    step(nc.vector.max(top[:, m, :], logits[:, m, :]))
                    nc.vector.tensor_scalar(negtop[:, m:m + 1], top[:, m, 0:1], -1.0, None, ALU.mult) \
                        .then_inc(s["negtop"], 1)
                    step(nc.vector.max_index(index[:, m, :], top[:, m, :], logits[:, m, :]))
                    step(nc.vector.tensor_copy(indexf[:, m, :], index[:, m, :]))
                dve.wait_ge(s["weight"], NT_X)
                step(nc.vector.reciprocal(total[:, :], total[:, :]))
                for m in range(NT_X):
                    step(nc.vector.tensor_scalar(weight[:, m, :], weight[:, m, :], total[:, m:m + 1], None, ALU.mult))
                    for j in range(TOP_K):
                        if j == 0:
                            step(nc.vector.tensor_scalar(chosen[:, m, :], iota[:, 0:N_EXP], indexf[:, m, 0:1], None,
                                                         ALU.is_equal))
                            step(nc.vector.tensor_scalar(gate[:, m, :], chosen[:, m, :], weight[:, m, 0:1], None,
                                                         ALU.mult))
                        else:
                            step(nc.vector.tensor_scalar(hit[:, :], iota[:, 0:N_EXP], indexf[:, m, j:j + 1], None,
                                                         ALU.is_equal))
                            step(nc.vector.scalar_tensor_tensor(gate[:, m, :], hit[:, :], weight[:, m, j:j + 1],
                                                                gate[:, m, :], ALU.mult, ALU.add))
                            step(nc.vector.tensor_tensor(chosen[:, m, :], chosen[:, m, :], hit[:, :], ALU.add))
                    nc.vector.tensor_copy(hit[:, :], hit[:, :]).then_inc(s["chosen"], 1)
                dve.wait_ge(s["chosen"], NT_X)
                dve.wait_ge(s["rank"], 1)
                counts = ps_r[:, 0, 128:160]
                step(nc.vector.tensor_scalar(blocks[:, :], counts, 0.0, None, ALU.is_gt))
                for j in range(1, SEQ // SLOTS):
                    step(nc.vector.scalar_tensor_tensor(blocks[:, :], counts, float(SLOTS * j), blocks[:, :],
                                                        ALU.is_gt, ALU.add))
                step(nc.vector.memset(tmp[:, :], 1.0))
                step(nc.vector.tensor_tensor_scan(ends[:, :], tmp[:, :], blocks[:, :], 0.0, ALU.mult, ALU.add))
                step(nc.vector.tensor_tensor(starts[:, :], ends[:, :], blocks[:, :], ALU.subtract))
                step(nc.vector.tensor_scalar(starts[:, :], starts[:, :], float(SLOTS), 1.0, ALU.mult, ALU.add))
                for m in range(NT_X):
                    step(nc.vector.tensor_tensor(tmp[:, :], ps_r[:, 0, m * N_EXP:(m + 1) * N_EXP], starts[:, :], ALU.add))
                    step(nc.vector.tensor_tensor(tmp[:, :], tmp[:, :], chosen[:, m, :], ALU.mult))
                    step(nc.vector.tensor_scalar(number[:, m, :], tmp[:, :], -1.0, None, ALU.add))
                step(nc.vector.tensor_scalar(tmp[:, :], ends[:, :], part[:, 0:1], None, ALU.is_le))
                step(nc.vector.tensor_reduce(expert[:, 0:1], tmp[:, :], AX.X, ALU.add))
                step(nc.vector.tensor_scalar(expert[:, 0:1], expert[:, 0:1], float(N_EXP - 1), None, ALU.min))
                nc.vector.tensor_copy(experti[:, :], expert[:, 0:1]).then_inc(s["expert"], 1)
                step(nc.vector.tensor_scalar(tmp[:, :], iota[:, 0:N_EXP], 2.0, None, ALU.mult))
                step(nc.vector.tensor_scalar(tmp[:, :], tmp[:, :], ends[:, N_EXP - 1:N_EXP], None, ALU.is_lt))
                step(nc.vector.tensor_reduce(expert[:, 1:2], tmp[:, :], AX.X, ALU.add))
                nc.vector.tensor_copy(n_blocks[0:1, :], expert[0:1, 1:2]).then_inc(s["expert"], 1)


def spread(row, n):
    return row.unsqueeze(0).to_broadcast([P, n])


def experts(nc, d, g, xn, gain, shift, number, gate, table, n_blocks, y):
    ident = g.ident[:, :]
    GROUPS = 4
    with ExitStack() as held:
        def sb(name, shape, dtype=F32):
            return held.enter_context(nc.sbuf_tensor(name, shape, dtype))

        gu = sb("w_gu", [P, KD, 2 * D])
        dn = sb("w_dn", [P, KD, D])
        b_gu = sb("b_gu", [P, 2 * D])
        b_dn = sb("b_dn", [P, D])
        slot = sb("slot_numbers", [P, SLOTS])
        sel = sb("selected", [P, NT_X, 2])
        pick = sb("pick", [P, NT_X, SLOTS])
        put = sb("put", [P, NT_X, SLOTS])
        putT = sb("putT", [P, NT_X, P])
        xgT = sb("xgT", [P, KD, SLOTS])
        biased = sb("biased", [P, 512])
        ga, up, sg = (sb(x, [P, 256]) for x in ("ga", "up", "sg"))
        act_sb = sb("act_sb", [P, D])
        actT = sb("actT", [P, KD, SLOTS])
        yb = sb("yb", [P, D])
        arrived = {p: [held.enter_context(nc.semaphore(f"w_{p}{i}")) for i in range(3 * GROUPS)] for p in "ab"}
        gu_v = d["w_gate_up"].rearrange("e (k p) n -> e p k n", p=P)
        dn_v = d["w_down"].rearrange("e (k p) n -> e p k n", p=P)

        def load(sp, expert, what, parity):
            k = slice(2 * (what % 4), 2 * (what % 4) + 2)
            if what < 8:
                half = slice(D * (what // 4), D * (what // 4) + D)
                to, src = gu[:, k, half], gu_v[expert][:, k, half]
            else:
                to, src = dn[:, k, :], dn_v[expert][:, k, :]
            sp.dma_start(to, src).then_inc(arrived[parity][what], 16)

        def expert_block(parity, other, v):
            w_here = arrived[parity]
            with nc.psum_tensor(f"moe_ps_{parity}", [P, 8, 512], F32) as ps, \
                    stage(nc, f"moe_{parity}", "bias", "sel", "pick", "put", "putT", "put_out", "gathered", "xg_act", "xg_dve",
                          "gu", "gu_used", "chain", "ga", "sig", "acted", "turned", "actT", "dn", "dn_used", "yb", "sc",
                          "added", clear=w_here) as (s, block):
                @block.sync
                def _(sp):
                    here = sp.value_load(table[0:1, bass.ds(v, 1)], min_val=0, max_val=N_EXP - 1)
                    sp.dma_start(b_gu[:, :], spread(d["b_gate_up"][here], 2 * D)).then_inc(s["bias"], 16)
                    sp.dma_start(b_dn[:, :], spread(d["b_down"][here], D)).then_inc(s["bias"], 16)
                    after = sp.value_load(table[0:1, bass.ds(v + 1, 1)], min_val=0, max_val=N_EXP - 1)
                    for what in range(3 * GROUPS):
                        if what < 2 * GROUPS:
                            sp.wait_ge(s["gu_used"], what + 1)
                        else:
                            sp.wait_ge(s["dn_used"], what - 2 * GROUPS + 1)
                        load(sp, after, what, other)

                @block.tensor
                def _(pe):
                    pe.wait_ge(s["pick"], NT_X)
                    for k in range(KD):
                        for m in range(NT_X):
                            last = nc.tensor.matmul(ps[:, k // 4, (k % 4) * P:(k % 4 + 1) * P], xn[:, m, k * P:(k + 1) * P],
                                                    pick[:, m, :], start=(m == 0), stop=(m == NT_X - 1),
                                                    skip_group_check=True)
                        if k % 4 == 3:
                            last.then_inc(s["gathered"], 1)
                    pe.wait_ge(s["put"], NT_X)
                    for m in range(NT_X):
                        last = nc.tensor.transpose(ps[:, 6, m * P:(m + 1) * P], put[:, m, :], ident)
                    last.then_inc(s["putT"], 1)
                    for half in range(2):
                        for k in range(KD):
                            if k % 2 == 0:
                                pe.wait_ge(w_here[half * GROUPS + k // 2], 16)
                            if half == 0:
                                pe.wait_ge(s["xg_act"] if k < 4 else s["xg_dve"], k % 4 + 1)
                            for n in range(2):
                                at = D * half + 512 * n
                                last = nc.tensor.matmul(ps[:, 2 + 2 * half + n, :], xgT[:, k, :], gu[:, k, at:at + 512],
                                                        start=(k == 0), stop=(k == KD - 1))
                            if k % 2:
                                last.then_inc(s["gu_used"], 1)
                    for half in range(2):
                        pe.wait_ge(s["acted"], 2 * half + 2)
                        for k in range(4):
                            last = nc.tensor.transpose(ps[:, half, k * P:(k + 1) * P],
                                                       act_sb[:, (4 * half + k) * P:(4 * half + k + 1) * P], ident)
                        last.then_inc(s["turned"], 1)
                    pe.wait_ge(s["put_out"], 1)
                    for k in range(KD):
                        if k % 2 == 0:
                            pe.wait_ge(w_here[2 * GROUPS + k // 2], 16)
                        if k % 4 == 0:
                            pe.wait_ge(s["actT"], k // 4 + 1)
                        for n in range(2):
                            last = nc.tensor.matmul(ps[:, 6 + n, :], actT[:, k, :], dn[:, k, 512 * n:512 * n + 512],
                                                    start=(k == 0), stop=(k == KD - 1))
                        if k % 2:
                            last.then_inc(s["dn_used"], 1)
                    t = 0
                    for n in range(2):
                        pe.wait_ge(s["yb"], n + 1)
                        for m in range(NT_X):
                            if t >= 4:
                                pe.wait_ge(s["added"], t - 3)
                            nc.tensor.matmul(ps[:, 2 + t % 4, :], putT[:, m, :], yb[:, 512 * n:512 * n + 512], start=True,
                                             stop=True).then_inc(s["sc"], 1)
                            t += 1

                @block.scalar
                def _(act):
                    act.wait_ge(s["gathered"], 1)
                    for k in range(4):
                        nc.scalar.activation(xgT[:, k, :], ps[:, 0, k * P:(k + 1) * P], ACT.Identity,
                                             scale=gain[:, k:k + 1], bias=shift[:, k:k + 1]).then_inc(s["xg_act"], 1)
                    act.wait_ge(s["putT"], 1)
                    nc.scalar.copy(putT[:, :, :], ps[:, 6, :].rearrange("p (m t) -> p m t", m=NT_X)).then_inc(s["put_out"], 1)
                    for n in range(4):
                        act.wait_ge(s["ga"], n + 1)
                        nc.scalar.activation(sg[:, :], ga[:, :], ACT.Sigmoid, scale=ALPHA).then_inc(s["sig"], 1)
                    for half in range(2):
                        act.wait_ge(s["turned"], half + 1)
                        nc.scalar.copy(actT[:, 4 * half:4 * half + 4, :],
                                       ps[:, half, :].rearrange("p (k t) -> p k t", k=4)).then_inc(s["actT"], 1)

                @block.vector
                def _(dve):
                    step = chained(dve, s["chain"])
                    here = dve.value_load(table[0:1, bass.ds(v, 1)], min_val=0, max_val=N_EXP - 1)
                    step(nc.vector.tensor_copy(sel[:, :, 0:1], number[:, :, bass.ds(here, 1)]))
                    step(nc.vector.tensor_copy(sel[:, :, 1:2], gate[:, :, bass.ds(here, 1)]))
                    for m in range(NT_X):
                        nc.vector.tensor_scalar(pick[:, m, :], slot[:, :], sel[:, m, 0:1], None,
                                                ALU.is_equal).then_inc(s["pick"], 1)
                    for m in range(NT_X):
                        nc.vector.tensor_scalar(put[:, m, :], slot[:, :], sel[:, m, 0:1], sel[:, m, 1:2],
                                                ALU.is_equal, ALU.mult).then_inc(s["put"], 1)
                    dve.wait_ge(s["put"], NT_X)
                    step(nc.vector.tensor_scalar(slot[:, :], slot[:, :], float(SLOTS), None, ALU.add))
                    dve.wait_ge(s["gathered"], 2)
                    for k in range(4, 8):
                        nc.vector.tensor_scalar(xgT[:, k, :], ps[:, 1, (k - 4) * P:(k - 3) * P], gain[:, k:k + 1],
                                                shift[:, k:k + 1], ALU.mult, ALU.add).then_inc(s["xg_dve"], 1)
                    dve.wait_ge(s["bias"], 32)
                    for n in range(4):
                        dve.wait_ge(s["gu_used"], GROUPS * (n // 2 + 1))
                        pairs = biased[:, :].rearrange("p (c a) -> p c a", a=2)
                        step(nc.vector.tensor_tensor(biased[:, :], ps[:, 2 + n, :], b_gu[:, 512 * n:512 * n + 512], ALU.add))
                        nc.vector.tensor_scalar(ga[:, :], pairs[:, :, 0], LIMIT, None, ALU.min).then_inc(s["ga"], 1)
                        step(nc.vector.tensor_scalar(up[:, :], pairs[:, :, 1], LIMIT, -LIMIT, ALU.min, ALU.max))
                        dve.wait_ge(s["ga"], n + 1)
                        step(nc.vector.scalar_tensor_tensor(up[:, :], up[:, :], 1.0, ga[:, :], ALU.add, ALU.mult))
                        dve.wait_ge(s["sig"], n + 1)
                        nc.vector.tensor_tensor(act_sb[:, 256 * n:256 * n + 256], up[:, :], sg[:, :],
                                                ALU.mult).then_inc(s["acted"], 1)
                        dve.wait_ge(s["acted"], n + 1)
                    dve.wait_ge(s["dn_used"], GROUPS)
                    for n in range(2):
                        nc.vector.tensor_tensor(yb[:, 512 * n:512 * n + 512], ps[:, 6 + n, :],
                                                b_dn[:, 512 * n:512 * n + 512], ALU.add).then_inc(s["yb"], 1)
                    for t in range(8):
                        n, m = t // NT_X, t % NT_X
                        dve.wait_ge(s["sc"], t + 1)
                        nc.vector.tensor_tensor(y[:, m, 512 * n:512 * n + 512], y[:, m, 512 * n:512 * n + 512],
                                                ps[:, 2 + t % 4, :], ALU.add).then_inc(s["added"], 1)

        with stage(nc, "moe_start", "slot", "zero") as (s, block):
            @block.sync
            def _(sp):
                sp.dma_start(slot[:, :], row_to_all(d["iota"], SLOTS)).then_inc(s["slot"], 16)
                sp.wait_ge(s["slot"], 16)
                first = sp.value_load(table[0:1, 0:1], min_val=0, max_val=N_EXP - 1)
                for what in range(12):
                    load(sp, first, what, "a")

            @block.gpsimd
            def _(pool):
                for m in range(NT_X):
                    nc.gpsimd.memset(y[:, m, :], 0.0).then_inc(s["zero"], 1)

        turns = nc.values_load(n_blocks[0:1, 0:1], min_val=1, max_val=MAX_BLOCKS // 2)
        with nc.Fori(0, turns) as turn:
            for parity, other in ("ab", "ba"):
                v = turn * 2 + (parity == "b")
                expert_block(parity, other, v)
        with stage(nc, "moe_end", "none", clear=arrived["a"]) as (s, block):
            @block.sync
            def _(sp):
                for w in arrived["a"]:
                    sp.wait_ge(w, 16)


CH = 64
N_CHUNKS = NTOK // CH
SEG = 4
SEG_TOK = SEG * CH
LEVELS = 6
DECAY = float(-np.exp(np.float32(-0.5)))
GN_EPS = 64e-5
PAIR_COLS = ("b_r", "b_k", "b_v", "prev_r", "prev_k", "prev_v", "next_r", "next_k", "next_v", "w0_f", "w0_b",
             "a0_f", "a0_b", "k_k", "k_a", "r_k", "ln_w", "ln_b")
PC = {name: i for i, name in enumerate(PAIR_COLS)}


def shift_tokens(nc, step, zp, out_ctx, out_x, tmp, keep, prev, nxt):
    step(nc.vector.tensor_scalar(tmp[:, 0:769], zp[:, 1:770], keep, None, ALU.mult))
    step(nc.vector.scalar_tensor_tensor(tmp[:, 0:769], zp[:, 0:769], prev, tmp[:, 0:769], ALU.mult, ALU.add))
    nc.vector.scalar_tensor_tensor(out_ctx, zp[:, 2:258], nxt, tmp[:, 0:256], ALU.mult, ALU.add)
    step(nc.vector.scalar_tensor_tensor(out_x, zp[:, 259:771], nxt, tmp[:, 257:769], ALU.mult, ALU.add))


def channel_project(nc, name, w_dram, loads, hT, bias, finish):
    with nc.psum_tensor(f"{name}_ps", [P, 3, 1024], F32) as ps, \
            nc.sbuf_tensor(f"{name}_w", [P, KD, 384], F32) as w_sb, \
            nc.sbuf_tensor(f"{name}_padded", [P, 3, NTOK + 4], F32) as zp, \
            nc.sbuf_tensor(f"{name}_tmp", [P, NTOK + 4], F32) as tmp, \
            nc.sbuf_tensor(f"{name}_keep", [P, 3], F32) as keep, \
            stage(nc, name, "w", "made", "biased", "chain") as (s, block):
        @block.sync
        def _(sp):
            sp.dma_start(w_sb[:, :, :], w_dram).then_inc(s["w"], 16)
            for to, what in loads:
                sp.dma_start(to, what).then_inc(s["w"], 16)

        @block.tensor
        def _(pe):
            pe.wait_ge(s["w"], 16 * (1 + len(loads)))
            for i in range(3):
                for lo, n, at in ((0, CTX, 0), (CTX, SEQ, 512)):
                    for k in range(KD):
                        last = nc.tensor.matmul(ps[:, i, at:at + n], w_sb[:, k, i * P:(i + 1) * P],
                                                hT[:, k, lo:lo + n], start=(k == 0), stop=(k == KD - 1))
                last.then_inc(s["made"], 1)

        @block.scalar
        def _(act):
            for i in range(3):
                act.wait_ge(s["made"], i + 1)
                nc.scalar.activation(zp[:, i, 1:1 + CTX], ps[:, i, 0:CTX], ACT.Identity, bias=bias(i))
                nc.scalar.activation(zp[:, i, 2 + CTX:2 + NTOK], ps[:, i, 512:1024], ACT.Identity,
                                     bias=bias(i)).then_inc(s["biased"], 1)

        @block.vector
        def _(dve):
            step = chained(dve, s["chain"])
            for zero in (0, 1 + CTX, 2 + NTOK):
                step(nc.vector.memset(zp[:, :, zero:zero + 1], 0.0))
            dve.wait_ge(s["w"], 16 * (1 + len(loads)))
            finish(dve, step, s, zp, tmp, keep)


def rwkv_branch(nc, d, g, hT, rwkT):
    ident = g.ident[:, :]
    with ExitStack() as held:
        def sb(name, shape, dtype=F32):
            return held.enter_context(nc.sbuf_tensor(name, shape, dtype))

        lora = sb("lora", [P, 3, NTOK])
        segment = sb("segment", [P, NTOK])
        tri = sb("tri", [P, 2, 2, P])
        off = sb("off", [P, 2, LEVELS, P])
        heads = sb("heads", [P, 2, P])
        eps = sb("gn_eps", [P, 1])

        def lora_finish(dve, step, s, zp, tmp, keep):
            v = g.vec
            step(nc.vector.tensor_tensor(keep[:, :], v[:, VCOL["lora_mu_prev"]], v[:, VCOL["lora_mu_next"]], ALU.add))
            step(nc.vector.tensor_scalar(keep[:, :], keep[:, :], -1.0, 1.0, ALU.mult, ALU.add))
            step(nc.vector.memset(eps[:, :], GN_EPS))
            for i in range(3):
                dve.wait_ge(s["biased"], i + 1)
                p0, n0 = VCOL["lora_mu_prev"].start + i, VCOL["lora_mu_next"].start + i
                shift_tokens(nc, step, zp[:, i], lora[:, i, 0:CTX], lora[:, i, CTX:NTOK], tmp, keep[:, i:i + 1],
                             v[:, p0:p0 + 1], v[:, n0:n0 + 1])

        b0 = VCOL["lora_b_in"].start
        channel_project(nc, "lora_z", d["w_lora_in"],
                        [(segment[:, :], d["segment"]), (tri[:, :, :, :], d["tri"]), (off[:, :, :, :], d["off"]), (heads[:, :, :], d["heads"])],
                        hT, lambda i: g.vec[:, b0 + i:b0 + i + 1], lora_finish)
        with stage(nc, "lora_act", "done") as (s, block):
            @block.scalar
            def _(act):
                nc.scalar.activation(lora[:, 0, :], lora[:, 0, :], ACT.Tanh).then_inc(s["done"], 1)
                nc.scalar.activation(lora[:, 2, :], lora[:, 2, :], ACT.Sigmoid).then_inc(s["done"], 1)

        f = {n: sb(f"f_{n}", [P, NTOK]) for n in
             ("r", "k", "v", "a", "k0", "k1", "b0", "b1", "excl0", "excl1", "incl0", "incl1", "neg0", "neg1",
              "tail0", "tail1")}
        cols = sb("pair_cols", [P, len(PAIR_COLS)])
        low = sb("pair_low", [P, 3, P])
        bonus = sb("bonus", [P, SEQ])
        gate = sb("gate", [P, SEQ])
        total = sb("total_decay", [P, 2, N_CHUNKS])
        y = sb("y", [P, SEQ])
        state = sb("state", [P, 2, 2, P])
        seg = {n: sb(f"bd_{n}", [P, 2, SEG, P]) for n in ("b", "k", "bt", "kt", "v")}
        seg["ar"] = sb("bd_ar", [P, 2, SEG, 2, P])
        with stage(nc, "bd_zero", "done") as (s, block):
            @block.gpsimd
            def _(pool):
                for t in seg.values():
                    nc.gpsimd.memset(t[:], 0.0).then_inc(s["done"], 1)

        with nc.Fori(0, 4) as pair:
            def pair_finish(dve, step, s, zp, tmp, keep):
                step(nc.vector.tensor_tensor(keep[:, :], cols[:, 3:6], cols[:, 6:9], ALU.add))
                step(nc.vector.tensor_scalar(keep[:, :], keep[:, :], -1.0, 1.0, ALU.mult, ALU.add))
                for i, n in enumerate("rkv"):
                    dve.wait_ge(s["biased"], i + 1)
                    shift_tokens(nc, step, zp[:, i], f[n][:, 0:CTX], f[n][:, CTX:NTOK], tmp, keep[:, i:i + 1],
                                 cols[:, 3 + i:4 + i], cols[:, 6 + i:7 + i])

            channel_project(nc, "pair_z", d["w_rkv"][pair],
                            [(cols[:, :], d["pair_cols"][pair]), (low[:, :, :], d["pair_low"][pair])],
                            hT, lambda i: cols[:, i:i + 1], pair_finish)
            pair_features(nc, g, f, cols, low, lora, heads, segment, bonus, gate, total)
            with stage(nc, "state0", "done") as (s, block):
                @block.gpsimd
                def _(pool):
                    nc.gpsimd.memset(state[:, :, 0, :], 0.0).then_inc(s["done"], 1)
            for n in range(3):
                pair_segment(nc, g, n, f, seg, tri, off, total, state, y)
            pair_output(nc, g, pair, y, bonus, gate, cols, heads, eps, rwkT)


def pair_features(nc, g, f, cols, low, lora, heads, segment, bonus, gate, total):
    def col(n):
        return cols[:, PC[n]:PC[n] + 1]

    halves = ((0, 512), (512, 256))
    with ExitStack() as held:
        ps = held.enter_context(nc.psum_tensor("feat_ps", [P, 4, 1024], F32))
        one_ka = held.enter_context(nc.sbuf_tensor("one_ka", [P, 1], F32))
        t1 = held.enter_context(nc.sbuf_tensor("feat_t1", [P, NTOK], F32))
        t2 = held.enter_context(nc.sbuf_tensor("feat_t2", [P, SEQ], F32))
        sg = [held.enter_context(nc.sbuf_tensor(f"feat_sg{i}", [P, NTOK], F32)) for i in range(2)]
        with stage(nc, "feat", "low", "rates", "squares", "sums", "rooted", "chain", "rk", "bonus", "gate", "gated",
                   "sums_in", "prep", "exped") as (s, block):
            @block.tensor
            def _(pe):
                for q in range(4):
                    rows = slice(64 * (q % 2), 64 * (q % 2) + 64)
                    for at, n in halves:
                        last = nc.tensor.matmul(ps[:, q, at:at + n], low[rows, q // 2, :],
                                                lora[rows, q // 2, at:at + n], start=True, stop=True)
                    last.then_inc(s["low"], 1)
                pe.wait_ge(s["rates"], 2)
                pe.wait_ge(s["squares"], 1)
                for at, n in halves:
                    last = nc.tensor.matmul(ps[:, 0, at:at + n], heads[:, 0, :], t1[:, at:at + n], start=True, stop=True)
                last.then_inc(s["sums"], 1)
                nc.tensor.matmul(ps[:, 1, 0:SEQ], low[:, 2, :], lora[:, 2, CTX:NTOK], start=True,
                                 stop=True).then_inc(s["gate"], 1)
                pe.wait_ge(s["rates"], 4)
                pe.wait_ge(s["rk"], 1)
                nc.tensor.matmul(ps[:, 2, 0:SEQ], heads[:, 0, :], t2[:, :], start=True, stop=True).then_inc(s["bonus"], 1)

            @block.scalar
            def _(act):
                rate = (sg[0], sg[1], f["b0"], f["b1"])
                for q, (to, bias) in enumerate(zip(rate, ("w0_f", "w0_b", "a0_f", "a0_b"))):
                    act.wait_ge(s["low"], q + 1)
                    nc.scalar.activation(to[:, :], ps[:, q, 0:NTOK], ACT.Sigmoid, bias=col(bias)).then_inc(s["rates"], 1)
                act.wait_ge(s["gate"], 1)
                nc.scalar.copy(gate[:, :], ps[:, 1, 0:SEQ]).then_inc(s["gated"], 1)
                act.wait_ge(s["sums"], 1)
                nc.scalar.activation(t1[:, :], ps[:, 0, 0:NTOK], ACT.Sqrt).then_inc(s["rooted"], 1)
                for i in range(2):
                    act.wait_ge(s["prep"], 1 + i)
                    for to, sign in ((f["neg%d" % i], -1.0),):
                        nc.scalar.activation(to[:, :], f["incl%d" % i][:, :], ACT.Exp, scale=-DECAY).then_inc(s["exped"], 1)
                    act.wait_ge(s["exped"], 4 * i + 1)
                    for n in ("incl%d" % i, "excl%d" % i, "tail%d" % i):
                        nc.scalar.activation(f[n][:, :], f[n][:, :], ACT.Exp, scale=DECAY).then_inc(s["exped"], 1)
                    nc.scalar.activation(total[:, i, :], total[:, i, :], ACT.Exp, scale=DECAY)

            @block.vector
            def _(dve):
                step = chained(dve, s["chain"])
                step(nc.vector.tensor_scalar(one_ka[:, :], col("k_a"), -1.0, 1.0, ALU.mult, ALU.add))
                step(nc.vector.tensor_scalar(f["a"][:, :], f["k"][:, :], col("k_k"), None, ALU.mult))
                nc.vector.tensor_tensor(t1[:, :], f["a"][:, :], f["a"][:, :], ALU.mult).then_inc(s["squares"], 1)
                for i in range(2):
                    dve.wait_ge(s["rates"], i + 1)
                    cp = f["incl0" if i == 0 else "tail1"]
                    step(nc.vector.tensor_tensor_scan(cp[:, :], segment[:, :], sg[i][:, :], 0.0, ALU.mult, ALU.add))
                    cp3 = cp[:, :].rearrange("p (c t) -> p c t", t=CH)
                    end = cp3[:, :, CH - 1:CH]
                    step(nc.vector.tensor_copy(total[:, i, :].unsqueeze(2), end))
                    tot = total[:, i, :].unsqueeze(2).to_broadcast([P, N_CHUNKS, CH])
                    rest = f["tail0" if i == 0 else "excl1"]
                    step(nc.vector.tensor_tensor(rest[:, :].rearrange("p (c t) -> p c t", t=CH), tot, cp3, ALU.subtract))
                    if i == 0:
                        nc.vector.tensor_tensor(f["excl0"][:, :], cp[:, :], sg[0][:, :], ALU.subtract).then_inc(s["prep"], 1)
                    else:
                        step(nc.vector.tensor_tensor(f["incl1"][:, :], rest[:, :], sg[1][:, :], ALU.add))
                        nc.vector.tensor_tensor(cp[:, :], cp[:, :], sg[1][:, :], ALU.subtract).then_inc(s["prep"], 1)
                dve.wait_ge(s["rates"], 4)
                for i in range(2):
                    kd = f["k%d" % i]
                    step(nc.vector.tensor_scalar(kd[:, :], f["b%d" % i][:, :], col("k_a"), one_ka[:, :], ALU.mult, ALU.add))
                    step(nc.vector.tensor_tensor(kd[:, :], kd[:, :], f["k"][:, :], ALU.mult))
                x = slice(CTX, NTOK)
                step(nc.vector.tensor_tensor(t2[:, :], f["k0"][:, x], f["k1"][:, x], ALU.add))
                nc.vector.scalar_tensor_tensor(t2[:, :], t2[:, :], col("r_k"), f["r"][:, x], ALU.mult,
                                               ALU.mult).then_inc(s["rk"], 1)
                dve.wait_ge(s["rooted"], 1)
                step(nc.vector.tensor_scalar(t1[:, :], t1[:, :], 1e-12, None, ALU.max))
                step(nc.vector.reciprocal(t1[:, :], t1[:, :]))
                step(nc.vector.tensor_tensor(f["a"][:, :], f["a"][:, :], t1[:, :], ALU.mult))
                for i in range(2):
                    step(nc.vector.tensor_tensor(f["b%d" % i][:, :], f["b%d" % i][:, :], f["a"][:, :], ALU.mult))
                step(nc.vector.tensor_scalar(f["a"][:, :], f["a"][:, :], -1.0, None, ALU.mult))
                dve.wait_ge(s["bonus"], 1)
                nc.vector.tensor_tensor(bonus[:, :], f["v"][:, x], ps[:, 2, 0:SEQ], ALU.mult).then_inc(s["sums_in"], 1)


def segment_tokens(n, direction):
    return (0, (CTX, CTX + SEG_TOK)[direction], (CTX + SEG_TOK, CTX)[direction])[n]


def pair_segment(nc, g, n, f, seg, tri, off, total, state, y):
    ident = g.ident[:, :]
    has_y = n > 0
    start = [segment_tokens(n, i) for i in range(2)]
    last_level = LEVELS - 1
    with ExitStack() as held:
        def sb(name, shape):
            return held.enter_context(nc.sbuf_tensor(f"{name}_{n}", shape, F32))

        gb, gk = sb("gb", [P, 2, SEG, 2, P]), sb("gk", [P, 2, SEG, 2, P])
        aoff = sb("aoff", [P, 2, 2, SEG, P])
        tmat, qmat, wmat = (sb(x, [P, 2, SEG, P]) for x in ("tmat", "qmat", "wmat"))
        btT, ktT, vbd = (sb(x, [P, 2, SEG, P]) for x in ("btT", "ktT", "vbd"))
        xs, us = sb("xs", [P, 2, P]), sb("us", [P, 2, P])
        with nc.psum_tensor(f"seg_ps{n}", [P, 2, 4, 512], F32) as ps, \
                stage(nc, f"seg{n}", "built0", "built1", "v0", "v1", "made0", "made1", "dve0", "dve1", "act0", "act1",
                      "off0", "off1", "t_in", "chain", "q_in") as (s, block):
            built, vin, made = (s["built0"], s["built1"]), (s["v0"], s["v1"]), (s["made0"], s["made1"])
            out = {"dve": (s["dve0"], s["dve1"]), "act": (s["act0"], s["act1"])}
            offs = (s["off0"], s["off1"])
            jobs = [("gb0", "dve"), ("gb1", "dve"), ("gk0", "dve"), ("gk1", "dve"), ("n", "dve"), ("bt", "act"),
                    ("kt", "act"), ("v", "act")]
            for l in range(1, last_level):
                jobs += [(f"w{l}", "act"), (f"t{l}", "dve"), (f"q{l}", "act")]
            jobs += [(f"w{last_level}", "act"), (f"q{last_level}", "dve")]
            names = [j for j, _ in jobs]

            def evacuated(j):
                who = jobs[j][1]
                return who, sum(w == who for _, w in jobs[:j + 1])

            def wait_out(engine, name, i):
                who, count = evacuated(names.index(name))
                engine.wait_ge(out[who][i], count)

            arrays = [("b", "b", "neg"), ("ar0", "a", "excl"), ("ar1", "r", "incl"), ("k", "k", "neg"),
                      ("bt", "b", "tail"), ("kt", "k", "tail")]
            if not has_y:
                arrays.pop(2)
            order = [x[0] for x in arrays]

            def build(engine, ops, i):
                for n_array, (to, what, decay) in enumerate(arrays):
                    src = f[what if what in "ar" else what + str(i)]
                    dec = f[decay + str(i)]
                    for h in range(2):
                        rows = slice(64 * h, 64 * h + 64)
                        dst = seg[to][rows, i, :, 64 * h:64 * h + 64] if to[:2] != "ar" else \
                            seg["ar"][rows, i, :, int(to[2]), 64 * h:64 * h + 64]
                        cut = slice(start[i], start[i] + SEG_TOK)
                        ops.tensor_tensor(dst, src[rows, cut].rearrange("p (c t) -> p c t", t=CH),
                                          dec[rows, cut].rearrange("p (c t) -> p c t", t=CH),
                                          ALU.mult).then_inc(built[i], 1)
                        if ops is nc.gpsimd:
                            engine.wait_ge(built[i], 2 * n_array + h + 1)

            def wait_built(pe, i, *which):
                pe.wait_ge(built[i], 2 * (1 + max(order.index(w) for w in which)))

            @block.tensor
            def _(pe):
                width = 256 if has_y else P
                for j, name in enumerate(names):
                    for i in range(2):
                        bank = ps[:, i, j % 4, :]
                        if j >= 4:
                            who, count = evacuated(j - 4)
                            pe.wait_ge(out[who][i], count)
                        if name[:2] in ("gb", "gk"):
                            wait_built(pe, i, "b", "ar1" if has_y else "ar0", "k" if name[1] == "k" else "b")
                            for c2 in range(2):
                                c = 2 * int(name[2]) + c2
                                last = nc.tensor.matmul(bank[:, 256 * c2:256 * c2 + width], seg[name[1]][:, i, c, :],
                                                        seg["ar"][:, i, c, 0:width // P, :], start=True, stop=True)
                        elif name == "n":
                            for c in range(SEG):
                                last = nc.tensor.matmul(bank[:, c * P:(c + 1) * P], seg["ar"][:, i, c, 0, :],
                                                        seg["b"][:, i, c, :], start=True, stop=True)
                        elif name in ("bt", "kt", "v"):
                            if name == "v":
                                pe.wait_ge(vin[i], 2)
                            else:
                                wait_built(pe, i, name)
                            for c in range(SEG):
                                last = nc.tensor.transpose(bank[:, c * P:(c + 1) * P], seg[name][:, i, c, :], ident)
                        elif name[0] == "w":
                            l = int(name[1:])
                            pe.wait_ge(offs[i], l + 1)
                            wait_out(pe, "n" if l == 1 else f"t{l - 1}", i)
                            for c in range(SEG):
                                last = nc.tensor.matmul(bank[:, c * P:(c + 1) * P], aoff[:, i, l % 2, c, :],
                                                        tmat[:, i, c, :], start=True, stop=True)
                        elif name[0] == "t":
                            l = int(name[1:])
                            wait_out(pe, f"w{l}", i)
                            if l > 1:
                                wait_out(pe, f"q{l - 1}", i)
                            for c in range(SEG):
                                last = nc.tensor.matmul(bank[:, c * P:(c + 1) * P], qmat[:, i, c, :],
                                                        wmat[:, i, c, :], start=True, stop=True)
                        else:
                            l = int(name[1:])
                            if l < last_level:
                                wait_out(pe, f"t{l}", i)
                            else:
                                wait_out(pe, f"w{l}", i)
                                wait_out(pe, f"q{l - 1}", i)
                            for c in range(SEG):
                                if l < last_level:
                                    last = nc.tensor.transpose(bank[:, c * P:(c + 1) * P], tmat[:, i, c, :], ident)
                                else:
                                    last = nc.tensor.matmul(bank[:, c * P:(c + 1) * P], wmat[:, i, c, :],
                                                            qmat[:, i, c, :], start=True, stop=True)
                        last.then_inc(made[i], 1)

            def four(t):
                return t.unsqueeze(1).to_broadcast([P, SEG, P])

            @block.vector
            def _(dve):
                step = chained(dve, s["chain"])
                build(dve, nc.vector, 0)
                for j, (name, who) in enumerate(jobs):
                    if who != "dve":
                        continue
                    for i in range(2):
                        bank = ps[:, i, j % 4, :]
                        dve.wait_ge(made[i], j + 1)
                        if name[:2] in ("gb", "gk"):
                            to = gb if name[1] == "b" else gk
                            c = 2 * int(name[2])
                            if has_y:
                                mask = tri[:, i].rearrange("p a t -> p (a t)").unsqueeze(1).to_broadcast([P, 2, 256])
                                nc.vector.tensor_tensor(to[:, i, c:c + 2].rearrange("p c a t -> p c (a t)"),
                                                        bank.rearrange("p (c t) -> p c t", c=2), mask,
                                                        ALU.mult).then_inc(s_out(out, i), 1)
                            else:
                                mask = tri[:, i, 0, :].unsqueeze(1).to_broadcast([P, 2, P])
                                nc.vector.tensor_tensor(to[:, i, c:c + 2, 0, :],
                                                        bank.rearrange("p (c t) -> p c t", c=2)[:, :, 0:P], mask,
                                                        ALU.mult).then_inc(s_out(out, i), 1)
                        elif name == "n":
                            step(nc.vector.tensor_tensor(tmat[:, i], bank.rearrange("p (c t) -> p c t", c=SEG),
                                                         four(off[:, 1 - i, 0, :]), ALU.mult))
                            nc.vector.tensor_tensor(tmat[:, i], tmat[:, i], four(ident), ALU.add).then_inc(s_out(out, i), 1)
                        elif name[0] == "t":
                            nc.vector.tensor_tensor(tmat[:, i], bank.rearrange("p (c t) -> p c t", c=SEG), tmat[:, i],
                                                    ALU.add).then_inc(s_out(out, i), 1)
                        else:
                            nc.vector.tensor_tensor(qmat[:, i], bank.rearrange("p (c t) -> p c t", c=SEG), qmat[:, i],
                                                    ALU.add).then_inc(s_out(out, i), 1)

            @block.scalar
            def _(act):
                for i in range(2):
                    for h in range(2):
                        rows = slice(64 * h, 64 * h + 64)
                        nc.scalar.copy(seg["v"][rows, i, :, 64 * h:64 * h + 64],
                                       f["v"][rows, start[i]:start[i] + SEG_TOK].rearrange("p (c t) -> p c t", t=CH)) \
                            .then_inc(vin[i], 1)
                for j, (name, who) in enumerate(jobs):
                    if who != "act":
                        continue
                    for i in range(2):
                        act.wait_ge(made[i], j + 1)
                        to = {"bt": btT, "kt": ktT, "v": vbd}.get(name) or {"w": wmat, "q": qmat}[name[0]]
                        nc.scalar.copy(to[:, i], ps[:, i, j % 4, :].rearrange("p (c t) -> p c t", c=SEG)) \
                            .then_inc(out["act"][i], 1)

            @block.gpsimd
            def _(pool):
                build(pool, nc.gpsimd, 1)
                for i in range(2):
                    pool.wait_ge(out["dve"][i], 2)
                    nc.gpsimd.tensor_tensor(qmat[:, i], gb[:, i, :, 0, :], four(off[:, i, 0, :]), ALU.mult) \
                        .then_inc(s["t_in"], 1)
                    pool.wait_ge(s["t_in"], i + 1)
                    nc.gpsimd.tensor_tensor(qmat[:, i], qmat[:, i], four(ident), ALU.add).then_inc(offs[i], 1)
                for l in range(1, LEVELS):
                    for i in range(2):
                        if l > 2:
                            pool.wait_ge(made[i], names.index(f"w{l - 2}") + 1)
                        nc.gpsimd.tensor_tensor(aoff[:, i, l % 2], gb[:, i, :, 0, :], four(off[:, i, l, :]), ALU.mult) \
                            .then_inc(offs[i], 1)

        scan_segment(nc, n, start, seg, gb, gk, qmat, btT, ktT, vbd, xs, us, total, state, y)


def s_out(out, i):
    return out["dve"][i]


def scan_segment(nc, n, start, seg, gb, gk, qmat, btT, ktT, vbd, xs, us, total, state, y):
    has_y = n > 0
    with nc.psum_tensor(f"scan_ps{n}", [P, 2, 4, 512], F32) as ps, \
            stage(nc, f"scan{n}", "x0", "x1", "xs0", "xs1", "u0", "u1", "us0", "us1", "s0", "s1", "st0", "st1", "y0", "y1",
                  "yo0", "yo1") as (s, block):
        X, XS, U, US = (s["x0"], s["x1"]), (s["xs0"], s["xs1"]), (s["u0"], s["u1"]), (s["us0"], s["us1"])
        S_, ST, Y, YO = (s["s0"], s["s1"]), (s["st0"], s["st1"]), (s["y0"], s["y1"]), (s["yo0"], s["yo1"])

        def chunk(step_no, i):
            return step_no if i == 0 else SEG - 1 - step_no

        @block.tensor
        def _(pe):
            for q in range(SEG):
                for i in range(2):
                    c = chunk(q, i)
                    if q:
                        pe.wait_ge(ST[i], q)
                    nc.tensor.matmul(ps[:, i, 0, 0:P], gk[:, i, c, 0, :], vbd[:, i, c, :], start=True, stop=False)
                    nc.tensor.matmul(ps[:, i, 0, 0:P], seg["ar"][:, i, c, 0, :], state[:, i, q % 2, :], start=False,
                                     stop=True).then_inc(X[i], 1)
                for i in range(2):
                    c = chunk(q, i)
                    pe.wait_ge(XS[i], q + 1)
                    nc.tensor.matmul(ps[:, i, 1, 0:P], qmat[:, i, c, :], xs[:, i, :], start=True,
                                     stop=True).then_inc(U[i], 1)
                for i in range(2):
                    c = chunk(q, i)
                    nc.tensor.matmul(ps[:, i, 2, 0:P], ktT[:, i, c, :], vbd[:, i, c, :], start=True, stop=False)
                    pe.wait_ge(US[i], q + 1)
                    nc.tensor.matmul(ps[:, i, 2, 0:P], btT[:, i, c, :], us[:, i, :], start=False,
                                     stop=True).then_inc(S_[i], 1)
                if has_y:
                    for i in range(2):
                        c = chunk(q, i)
                        if q:
                            pe.wait_ge(YO[i], 2 * q)
                        nc.tensor.matmul(ps[:, i, 3, 0:P], vbd[:, i, c, :], gk[:, i, c, 1, :], start=True, stop=False)
                        nc.tensor.matmul(ps[:, i, 3, 0:P], state[:, i, q % 2, :], seg["ar"][:, i, c, 1, :], start=False,
                                         stop=False)
                        nc.tensor.matmul(ps[:, i, 3, 0:P], us[:, i, :], gb[:, i, c, 1, :], start=False,
                                         stop=True).then_inc(Y[i], 1)

        def put_y(ops, copy, i, q, signal):
            c = chunk(q, i)
            at = start[i] - CTX + c * CH
            for h in range(2):
                rows = slice(64 * h, 64 * h + 64)
                src = ps[rows, i, 3, 64 * h:64 * h + 64]
                if n == 1:
                    copy(y[rows, at:at + CH], src).then_inc(signal, 1)
                else:
                    ops.tensor_tensor(y[rows, at:at + CH], src, y[rows, at:at + CH], ALU.add).then_inc(signal, 1)

        @block.vector
        def _(dve):
            for q in range(SEG):
                dve.wait_ge(X[0], q + 1)
                if q:
                    dve.wait_ge(U[0], q)
                nc.vector.tensor_copy(xs[:, 0, :], ps[:, 0, 0, 0:P]).then_inc(XS[0], 1)
                dve.wait_ge(U[0], q + 1)
                if has_y and q:
                    dve.wait_ge(Y[0], q)
                nc.vector.tensor_copy(us[:, 0, :], ps[:, 0, 1, 0:P]).then_inc(US[0], 1)
                for i in range(2):
                    c = start[i] // CH + chunk(q, i)
                    dve.wait_ge(S_[i], q + 1)
                    if has_y and q:
                        dve.wait_ge(Y[i], q)
                    nc.vector.scalar_tensor_tensor(state[:, i, (q + 1) % 2, :], state[:, i, q % 2, :],
                                                   total[:, i, c:c + 1], ps[:, i, 2, 0:P], ALU.mult,
                                                   ALU.add).then_inc(ST[i], 1)
                if has_y:
                    for i in range(2):
                        if n == 2 or i == 0:
                            dve.wait_ge(Y[i], q + 1)
                            put_y(nc.vector, nc.vector.tensor_copy, i, q, YO[i])

        @block.scalar
        def _(act):
            for q in range(SEG):
                act.wait_ge(X[1], q + 1)
                if q:
                    act.wait_ge(U[1], q)
                nc.scalar.copy(xs[:, 1, :], ps[:, 1, 0, 0:P]).then_inc(XS[1], 1)
                act.wait_ge(U[1], q + 1)
                if has_y and q:
                    act.wait_ge(Y[1], q)
                nc.scalar.copy(us[:, 1, :], ps[:, 1, 1, 0:P]).then_inc(US[1], 1)
                if n == 1:
                    act.wait_ge(Y[1], q + 1)
                    put_y(None, nc.scalar.copy, 1, q, YO[1])


def pair_output(nc, g, pair, y, bonus, gate, cols, heads, eps, rwkT):
    with ExitStack() as held:
        t = held.enter_context(nc.sbuf_tensor("out_t", [P, SEQ], F32))
        u = held.enter_context(nc.sbuf_tensor("out_u", [P, SEQ], F32))
        ps = held.enter_context(nc.psum_tensor("out_ps", [P, 2, 512], F32))
        with stage(nc, "out", "mean", "centred", "squared", "var", "root", "chain") as (s, block):
            @block.tensor
            def _(pe):
                nc.tensor.matmul(ps[:, 0, :], heads[:, 1, :], y[:, :], start=True, stop=True).then_inc(s["mean"], 1)
                pe.wait_ge(s["squared"], 1)
                nc.tensor.matmul(ps[:, 1, :], heads[:, 1, :], t[:, :], start=True, stop=True).then_inc(s["var"], 1)

            @block.scalar
            def _(act):
                act.wait_ge(s["centred"], 1)
                nc.scalar.activation(t[:, :], y[:, :], ACT.Square).then_inc(s["squared"], 1)
                act.wait_ge(s["var"], 1)
                nc.scalar.activation(u[:, :], ps[:, 1, :], ACT.Sqrt, bias=eps[:, 0:1]).then_inc(s["root"], 1)

            @block.vector
            def _(dve):
                step = chained(dve, s["chain"])
                dve.wait_ge(s["mean"], 1)
                nc.vector.tensor_tensor(y[:, :], y[:, :], ps[:, 0, :], ALU.subtract).then_inc(s["centred"], 1)
                dve.wait_ge(s["root"], 1)
                step(nc.vector.reciprocal(u[:, :], u[:, :]))
                step(nc.vector.tensor_tensor(u[:, :], u[:, :], y[:, :], ALU.mult))
                step(nc.vector.tensor_scalar(u[:, :], u[:, :], cols[:, PC["ln_w"]:PC["ln_w"] + 1],
                                             cols[:, PC["ln_b"]:PC["ln_b"] + 1], ALU.mult, ALU.add))
                step(nc.vector.tensor_tensor(u[:, :], u[:, :], bonus[:, :], ALU.add))
                step(nc.vector.tensor_tensor(rwkT[:, bass.ds(pair, 1), :].rearrange("p a t -> p (a t)"), u[:, :],
                                             gate[:, :], ALU.mult))


NH = 8
QL, KVL, RD = 384, 256, 32
LOWW = QL + KVL + RD + NH
TWO_PI_HI, TWO_PI_MID = 6.28125, 0.0019350051879882812
TWO_PI_LO = float(2 * np.pi - TWO_PI_HI - TWO_PI_MID)
ROUND = 12582912.0


def head_norm_stage(nc, g, name, jobs):
    with ExitStack() as held:
        sq = held.enter_context(nc.sbuf_tensor(f"{name}_sq", [P, 2, 512], F32))
        tmp = held.enter_context(nc.sbuf_tensor(f"{name}_tmp", [P, 2, 512], F32))
        ss = held.enter_context(nc.sbuf_tensor(f"{name}_ss", [P, 3, len(jobs), NH], F32))
        with stage(nc, name, "set", "square", "sum", "root", "inverse", "scaled", "normed") as (s, block):
            def view(t, src):
                return t[:, 0:src.shape[1] * src.shape[2]].rearrange("p (h n) -> p h n", n=src.shape[2])

            @block.scalar
            def _(act):
                for j, (src, _, _) in enumerate(jobs):
                    if j >= 2:
                        act.wait_ge(s["sum"], j - 1)
                    nc.scalar.activation(view(sq[:, j % 2], src), src, ACT.Square).then_inc(s["square"], 1)
                act.wait_ge(s["sum"], len(jobs))
                act.wait_ge(s["set"], 1)
                for j, (src, _, _) in enumerate(jobs):
                    nc.scalar.activation(ss[:, 1, j, :], ss[:, 0, j, :], ACT.Sqrt, scale=1.0 / src.shape[2],
                                         bias=g.eps_col[:, 0:1]).then_inc(s["root"], 1)

            @block.vector
            def _(dve):
                nc.vector.memset(ss[:, 0], 1.0).then_inc(s["set"], 1)
                dve.wait_ge(s["set"], 1)
                for j, (src, _, _) in enumerate(jobs):
                    dve.wait_ge(s["square"], j + 1)
                    nc.vector.tensor_reduce(ss[:, 0, j, 0:src.shape[1]], view(sq[:, j % 2], src), AX.X,
                                            ALU.add).then_inc(s["sum"], 1)
                dve.wait_ge(s["root"], len(jobs))
                nc.vector.reciprocal(ss[:, 2], ss[:, 1]).then_inc(s["inverse"], 1)
                dve.wait_ge(s["inverse"], 1)
                for j, (src, dst, w) in enumerate(jobs):
                    h, n = src.shape[1], src.shape[2]
                    if j >= 2:
                        dve.wait_ge(s["normed"], j - 1)
                    nc.vector.tensor_tensor(view(tmp[:, j % 2], src), src,
                                            ss[:, 2, j, 0:h].unsqueeze(2).to_broadcast([P, h, n]),
                                            ALU.mult).then_inc(s["scaled"], 1)
                    dve.wait_ge(s["scaled"], j + 1)
                    nc.vector.tensor_tensor(dst, view(tmp[:, j % 2], src), w.unsqueeze(1).to_broadcast([P, h, n]),
                                            ALU.mult).then_inc(s["normed"], 1)


def second_block(nc, d, g, x, row_cols, ones, out):
    ident = g.ident[:, :]
    tiles = [x[:, m] for m in range(NT_X)]
    with ExitStack() as held:
        def sb(name, shape, dtype=F32):
            return held.enter_context(nc.sbuf_tensor(name, shape, dtype))

        hT = sb("b2_hT", [P, KD, SEQ])
        yT = [sb(f"y{i}T", [P, 4, SEQ]) for i in range(2)]
        with ExitStack() as branches:
            def bb(name, shape, dtype=F32):
                return branches.enter_context(nc.sbuf_tensor(name, shape, dtype))

            low = bb("b2_low", [P, NT_X, LOWW])
            wide = bb("b2_wide", [P, NT_X, 5, 512])
            norm_rows = bb("norm_rows", [P, 320])
            causal = bb("causal", [P, 2, SEQ])
            rope = bb("b2_rope", [P, 2, NT_X, 16])
            b_f = bb("b_f", [P, NH])
            project_second(nc, d, g, tiles, hT, low, wide, norm_rows, causal, b_f)
            rope_tables(nc, d, g, rope)
            mla(nc, d, g, low, wide, norm_rows, causal, rope, yT[0])
            fox(nc, d, g, low, wide, norm_rows, causal, b_f, ones, yT[1])
        mg = sb("b2_mg", [P, NT_X, 2 * D])
        second_gates(nc, d, hT, mg)
        mix = sb("b2_mix", [P, NT_X, D])
        merge_and_out(nc, d, g, "b2m", yT, mg, (d["w_branch_a_2"], d["w_branch_b_2"]), d["w_out_2"], mix)
        row = sb("b2_row", [P, D])
        rows_stage(nc, g, "b2_rows", [row_cols[:, 2]], [row[:, :]], ones)
        with stage(nc, "last", "scaled", "added", "out") as (s, block):
            @block.vector
            def _(dve):
                for m in range(NT_X):
                    nc.vector.tensor_tensor(mix[:, m], mix[:, m], row[:, :], ALU.mult).then_inc(s["scaled"], 1)
                for m in range(NT_X):
                    dve.wait_ge(s["scaled"], m + 1)
                    nc.vector.tensor_tensor(x[:, m], x[:, m], mix[:, m], ALU.add).then_inc(s["added"], 1)

            @block.sync
            def _(sp):
                for m in range(NT_X):
                    sp.wait_ge(s["added"], m + 1)
                    sp.dma_start(out[0, m * P:(m + 1) * P, :], x[:, m]).then_inc(s["out"], 16)
                sp.wait_ge(s["out"], 16 * NT_X)


def project_second(nc, d, g, tiles, hT, low, wide, norm_rows, causal, b_f):
    with ExitStack() as held:
        def sb(name, shape, dtype=F32):
            return held.enter_context(nc.sbuf_tensor(name, shape, dtype))

        gain = sb("b2_gain", [P, KD])
        with stage(nc, "b2_gain", "done") as (s, block):
            @block.vector
            def _(dve):
                nc.vector.scalar_tensor_tensor(gain[:, :], g.ada2[:, 8:16, 0], 1.0, g.vec[:, VCOL["norm_w_2"]],
                                               ALU.add, ALU.mult).then_inc(s["done"], 1)
        with nc.sbuf_tensor("b2_xn", [P, NT_X, D], F32) as xn:
            norm_turn_stage(nc, "b2n", tiles, None, [xn[:, m] for m in range(NT_X)], hT,
                            lambda m, k: (gain[:, k:k + 1], g.ada2[:, k, 0:1]), g.eps_col[:, 0:1], g.ident[:, :])
        slots = [sb(f"b2_w{i}", [P, KD, 512]) for i in range(2)]
        sig = sb("b2_sig", [P, 2, 512])

        def tok(m):
            return lambda k: hT[:, k, m * P:(m + 1) * P]

        lhs = [tok(m) for m in range(NT_X)]
        w = d["w_in_2"]
        chunks = [dict(to="low", at=0, width=512), dict(to="low", at=512, width=LOWW - 512)]
        chunks += [dict(to="wide", at=i, width=512) for i in range(5)]
        at = 0
        for c in chunks:
            c.update(w=w[:, at:at + c["width"]], k=KD, lhs=lhs)
            at += c["width"]

        def evacuate(s, block, work):
            silu = [t for t, c, m, ps in work if c["to"] == "wide" and c["at"] < 2]

            @block.vector
            def _(dve):
                for t, c, m, ps in work:
                    dve.wait_ge(s["tile"], t + 1)
                    if t in silu:
                        dve.wait_ge(s["step2"], silu.index(t) + 1)
                        nc.vector.tensor_tensor(wide[:, m, c["at"], :], ps, sig[:, t % 2, :], ALU.mult).then_inc(s["free"], 1)
                    else:
                        to = wide[:, m, c["at"], :] if c["to"] == "wide" else low[:, m, c["at"]:c["at"] + c["width"]]
                        nc.vector.tensor_copy(to, ps).then_inc(s["free"], 1)

            @block.scalar
            def _(act):
                act.dma_start(norm_rows[:, :], row_to_all(d["norm_rows_2"], 320)).then_inc(s["side"], 16)
                act.dma_start(causal[:, :, :], d["causal_masks"]).then_inc(s["side"], 16)
                act.dma_start(b_f[:, :], row_to_all(d["b_f_2"], NH)).then_inc(s["side"], 16)
                act.wait_ge(s["side"], 48)
                for t, c, m, ps in work:
                    if t in silu:
                        act.wait_ge(s["tile"], t + 1)
                        if t >= silu[0] + 2:
                            act.wait_ge(s["free"], t - 1)
                        nc.scalar.activation(sig[:, t % 2, :], ps, ACT.Sigmoid).then_inc(s["step2"], 1)

        token_gemm_stage(nc, "b2p", chunks, slots, evacuate, extra=("side",))


def second_gates(nc, d, hT, mg):
    with ExitStack() as held:
        slots = [held.enter_context(nc.sbuf_tensor(f"b2g_w{i}", [P, KD, 512], F32)) for i in range(2)]

        def tok(m):
            return lambda k: hT[:, k, m * P:(m + 1) * P]

        at = LOWW + 5 * 512
        chunks = [dict(w=d["w_in_2"][:, at + 512 * c:at + 512 * c + 512], width=512, k=KD,
                       lhs=[tok(m) for m in range(NT_X)], col=512 * c) for c in range(4)]

        def evacuate(s, block, work):
            @block.scalar
            def _(act):
                for t, chunk, m, ps in work:
                    act.wait_ge(s["tile"], t + 1)
                    a = chunk["col"]
                    nc.scalar.activation(mg[:, m, a:a + 512], ps, ACT.Sigmoid).then_inc(s["free"], 1)

        token_gemm_stage(nc, "b2g", chunks, slots, evacuate)


def rope_tables(nc, d, g, rope):
    with ExitStack() as held:
        def sb(name, shape, dtype=F32):
            return held.enter_context(nc.sbuf_tensor(name, shape, dtype))

        pos, posf = sb("pos", [P, NT_X], I32), sb("posf", [P, NT_X])
        freq = sb("freq", [P, 16])
        ang, n, r, a = (sb(f"rope_{x}", [P, NT_X, 16]) for x in ("ang", "n", "r", "abs"))
        half_pi = sb("half_pi", [P, 1])
        with stage(nc, "rope2", "loaded", "chain", "angle") as (s, block):
            @block.sync
            def _(sp):
                sp.dma_start(pos[:, :], d["positions_2"]).then_inc(s["loaded"], 16)
                sp.dma_start(freq[:, :], row_to_all(d["rope_freq"], 16)).then_inc(s["loaded"], 16)

            @block.vector
            def _(dve):
                step = chained(dve, s["chain"])
                step(nc.vector.memset(half_pi[:, :], float(np.pi / 2)))
                dve.wait_ge(s["loaded"], 32)
                step(nc.vector.tensor_copy(posf[:, :], pos[:, :]))
                for m in range(NT_X):
                    step(nc.vector.tensor_scalar(ang[:, m, :], freq[:, :], posf[:, m:m + 1], None, ALU.mult))
                step(nc.vector.tensor_scalar(n[:, :, :], ang[:, :, :], float(1 / (2 * np.pi)), ROUND, ALU.mult, ALU.add))
                step(nc.vector.tensor_scalar(n[:, :, :], n[:, :, :], -ROUND, None, ALU.add))
                step(nc.vector.scalar_tensor_tensor(r[:, :, :], n[:, :, :], -TWO_PI_HI, ang[:, :, :], ALU.mult, ALU.add))
                step(nc.vector.scalar_tensor_tensor(r[:, :, :], n[:, :, :], -TWO_PI_MID, r[:, :, :], ALU.mult, ALU.add))
                step(nc.vector.scalar_tensor_tensor(r[:, :, :], n[:, :, :], -TWO_PI_LO, r[:, :, :], ALU.mult, ALU.add))
                for beyond, edge, turn in ((ALU.is_gt, np.pi, -2 * np.pi), (ALU.is_lt, -np.pi, 2 * np.pi)):
                    step(nc.vector.tensor_scalar(n[:, :, :], r[:, :, :], float(edge), None, beyond))
                    step(nc.vector.scalar_tensor_tensor(r[:, :, :], n[:, :, :], float(turn), r[:, :, :], ALU.mult, ALU.add))
                step(nc.vector.tensor_scalar(r[:, :, :], r[:, :, :], 3.1415925, -3.1415925, ALU.min, ALU.max))
                nc.vector.scalar_tensor_tensor(a[:, :, :], r[:, :, :], -1.0, r[:, :, :], ALU.mult,
                                               ALU.max).then_inc(s["angle"], 1)

            @block.scalar
            def _(act):
                act.wait_ge(s["angle"], 1)
                nc.scalar.activation(rope[:, 0], a[:, :, :], ACT.Sin, scale=-1.0, bias=half_pi[:, 0:1])
                nc.scalar.activation(rope[:, 1], r[:, :, :], ACT.Sin)


def turn_gate(nc, name, o, gate_of, yT, ident):
    with stage(nc, f"{name}_gate", "done") as (s, block):
        @block.vector
        def _(dve):
            for m in range(NT_X):
                nc.vector.tensor_tensor(o[:, m, :], o[:, m, :], gate_of(m), ALU.mult).then_inc(s["done"], 1)
    turn_stage(nc, f"{name}_turn", [o[:, m, c * P:(c + 1) * P] for m in range(NT_X) for c in range(4)],
               [yT[:, c, m * P:(m + 1) * P] for m in range(NT_X) for c in range(4)], ident)


def mla(nc, d, g, low, wide, norm_rows, causal, rope, yT):
    ident = g.ident[:, :]
    K = HD + RD
    with ExitStack() as held:
        def sb(name, shape, dtype=F32):
            return held.enter_context(nc.sbuf_tensor(name, shape, dtype))

        qT, kT = sb("mla_qT", [P, NH, SEQ]), sb("mla_kT", [P, NH, SEQ])
        v = sb("mla_v", [P, NT_X, 512])
        with ExitStack() as making:
            def tb(name, shape, dtype=F32):
                return making.enter_context(nc.sbuf_tensor(name, shape, dtype))

            qn, kn = tb("mla_qn", [P, NT_X, 512]), tb("mla_kn", [P, NT_X, 512])
            rr = tb("mla_rr", [P, NT_X, 9, RD])
            with ExitStack() as lowering:
                lowT = lowering.enter_context(nc.sbuf_tensor("lowT", [P, 5, SEQ], F32))
                low_norm_turn(nc, g, low, lowT)
                slots = [lowering.enter_context(nc.sbuf_tensor(f"mla_w{i}", [P, 3, 512], F32)) for i in range(2)]

                def tok(m, k0):
                    return lambda k: lowT[:, k0 + k, m * P:(m + 1) * P]

                uq, ukv = d["w_uq_2"], d["w_ukv_2"]
                chunks = [dict(w=uq[:, 0:512], width=512, k=3, lhs=[tok(m, 0) for m in range(NT_X)], to="qn"),
                          dict(w=uq[:, 512:768], width=256, k=3, lhs=[tok(m, 0) for m in range(NT_X)], to="qr"),
                          dict(w=ukv[:, 0:512], width=512, k=2, lhs=[tok(m, 3) for m in range(NT_X)], to="kn"),
                          dict(w=ukv[:, 512:1024], width=512, k=2, lhs=[tok(m, 3) for m in range(NT_X)], to="v")]

                def evacuate(s, block, work):
                    @block.vector
                    def _(dve):
                        for t, c, m, ps in work:
                            dve.wait_ge(s["tile"], t + 1)
                            if c["to"] == "qr":
                                nc.vector.tensor_copy(rr[:, m, 0:NH, :],
                                                      ps.rearrange("p (h n) -> p h n", n=RD)).then_inc(s["free"], 1)
                            else:
                                nc.vector.tensor_copy({"qn": qn, "kn": kn, "v": v}[c["to"]][:, m, :], ps) \
                                    .then_inc(s["free"], 1)

                    @block.scalar
                    def _(act):
                        for m in range(NT_X):
                            nc.scalar.copy(rr[:, m, NH, :], low[:, m, QL + KVL:QL + KVL + RD])

                token_gemm_stage(nc, "mla_up", chunks, slots, evacuate)
            qcat, kcat = tb("qcat", [P, NT_X, NH, K]), tb("kcat", [P, NT_X, NH, K])
            rn = tb("mla_rn", [P, NT_X, 9, RD])

            def heads(t, m):
                return t[:, m, :].rearrange("p (h n) -> p h n", n=HD)

            jobs = [(heads(qn, m), qcat[:, m, :, 0:HD], norm_rows[:, 0:64]) for m in range(NT_X)]
            jobs += [(heads(kn, m), kcat[:, m, :, 0:HD], norm_rows[:, 64:128]) for m in range(NT_X)]
            jobs += [(rr[:, m, 0:NH, :], rn[:, m, 0:NH, :], norm_rows[:, 256:288]) for m in range(NT_X)]
            jobs += [(rr[:, m, NH:NH + 1, :], rn[:, m, NH:NH + 1, :], norm_rows[:, 288:320]) for m in range(NT_X)]
            head_norm_stage(nc, g, "mla_norm", jobs)
            rotate_second(nc, rn, rope, rr, qcat, kcat)
            turn_heads(nc, "mla_turn", [(qcat, qT), (kcat, kT)], K, ident)
        o = sb("mla_att", [P, NT_X, 512])
        items = [dict(q=qT[0:K, h, b * P:(b + 1) * P], keys=[kT[0:K, h, 0:(b + 1) * P]],
                      v=[v[:, t, HD * h:HD * h + HD] for t in range(b + 1)], mask=causal[:, 0, (3 - b) * P:SEQ],
                      sink=None, out=o[:, b, HD * h:HD * h + HD], ident=ident) for b in range(NT_X) for h in range(NH)]
        attention_stage(nc, "mla", items, float(1.0 / np.sqrt(K)))
        turn_gate(nc, "mla_o", o, lambda m: wide[:, m, 0, :], yT, ident)


def rotate_second(nc, rn, rope, rr, qcat, kcat):
    with nc.sbuf_tensor("rot2", [P, 4, NT_X, 9, 16], F32) as part, \
            stage(nc, "rot2", "parts", "rotated", "copied") as (s, block):
        @block.vector
        def _(dve):
            n = 0
            for m in range(NT_X):
                cos = rope[:, 0, m].unsqueeze(1).to_broadcast([P, 9, 16])
                sin = rope[:, 1, m].unsqueeze(1).to_broadcast([P, 9, 16])
                for i, (x, y) in enumerate(((0, cos), (16, sin), (16, cos), (0, sin))):
                    nc.vector.tensor_tensor(part[:, i, m], rn[:, m, :, x:x + 16], y, ALU.mult).then_inc(s["parts"], 1)
            for m in range(NT_X):
                dve.wait_ge(s["parts"], 4 * m + 4)
                nc.vector.tensor_tensor(rr[:, m, :, 0:16], part[:, 0, m], part[:, 1, m], ALU.subtract).then_inc(s["rotated"], 1)
                nc.vector.tensor_tensor(rr[:, m, :, 16:32], part[:, 2, m], part[:, 3, m], ALU.add).then_inc(s["rotated"], 1)

        @block.scalar
        def _(act):
            for m in range(NT_X):
                act.wait_ge(s["rotated"], 2 * m + 2)
                nc.scalar.copy(qcat[:, m, :, HD:HD + RD], rr[:, m, 0:NH, :])
                nc.scalar.copy(kcat[:, m, :, HD:HD + RD], rr[:, m, NH:NH + 1, :].to_broadcast([P, NH, RD]))


def turn_heads(nc, name, pairs, K, ident):
    groups = [(src, dst, m, h) for src, dst in pairs for m in range(NT_X) for h in (0, 4)]
    with nc.psum_tensor(f"{name}_ps", [P, 4, 512], F32) as ps, stage(nc, name, "turned", "even", "odd") as (s, block):
        @block.tensor
        def _(pe):
            for q, (src, dst, m, h) in enumerate(groups):
                if q >= 4:
                    pe.wait_ge(s["odd"] if q % 2 else s["even"], (q - 4) // 2 + 1)
                for j in range(4):
                    last = nc.tensor.transpose(ps[0:K, q % 4, j * P:(j + 1) * P], src[:, m, h + j, :], ident)
                last.then_inc(s["turned"], 1)

        def copies(engine, copy, odd, signal):
            for q, (src, dst, m, h) in enumerate(groups):
                if q % 2 == odd:
                    engine.wait_ge(s["turned"], q + 1)
                    copy(dst[0:K, h:h + 4, m * P:(m + 1) * P],
                         ps[0:K, q % 4, :].rearrange("p (j t) -> p j t", j=4)).then_inc(signal, 1)

        @block.vector
        def _(dve):
            copies(dve, nc.vector.tensor_copy, 0, s["even"])

        @block.scalar
        def _(act):
            copies(act, nc.scalar.copy, 1, s["odd"])


def low_norm_turn(nc, g, low, lowT):
    parts = ((0, QL), (QL, KVL))
    gains = VCOL["lora_norms_2"].start
    with ExitStack() as held:
        def sb(name, shape):
            return held.enter_context(nc.sbuf_tensor(name, shape, F32))

        sq, xn, stat = sb("low_sq", [P, QL]), sb("low_xn", [P, NT_X, QL + KVL]), sb("low_stat", [P, 3, 2, NT_X])
        ps = held.enter_context(nc.psum_tensor("low_ps", [P, 2, 1024], F32))
        with stage(nc, "low", "squared", "root", "inverse", "normed", "turned", "out") as (s, block):
            @block.scalar
            def _(act):
                n = 0
                for i, (at, w) in enumerate(parts):
                    for m in range(NT_X):
                        if n:
                            act.wait_ge(s["squared"], n)
                        nc.scalar.activation(sq[:, 0:w], low[:, m, at:at + w], ACT.Square,
                                             accum_out=stat[:, 0, i, m:m + 1]).then_inc(s["squared"], 1)
                        n += 1
                act.wait_ge(s["squared"], n)
                for i, (at, w) in enumerate(parts):
                    nc.scalar.activation(stat[:, 1, i, :], stat[:, 0, i, :], ACT.Sqrt, scale=1.0 / w,
                                         bias=g.eps_col[:, 0:1]).then_inc(s["root"], 1)
                for m in range(NT_X):
                    act.wait_ge(s["turned"], m + 1)
                    for k in range(5):
                        last = nc.scalar.activation(lowT[:, k, m * P:(m + 1) * P], ps[:, m % 2, k * P:(k + 1) * P],
                                                    ACT.Copy, scale=g.vec[:, gains + k:gains + k + 1])
                    last.then_inc(s["out"], 1)

            @block.vector
            def _(dve):
                dve.wait_ge(s["root"], 2)
                nc.vector.reciprocal(stat[:, 2], stat[:, 1]).then_inc(s["inverse"], 1)
                dve.wait_ge(s["inverse"], 1)
                for m in range(NT_X):
                    for i, (at, w) in enumerate(parts):
                        nc.vector.tensor_scalar(xn[:, m, at:at + w], low[:, m, at:at + w], stat[:, 2, i, m:m + 1], None,
                                                ALU.mult).then_inc(s["normed"], 1)

            @block.tensor
            def _(pe):
                for m in range(NT_X):
                    pe.wait_ge(s["normed"], 2 * m + 2)
                    if m >= 2:
                        pe.wait_ge(s["out"], m - 1)
                    for k in range(5):
                        last = nc.tensor.transpose(ps[:, m % 2, k * P:(k + 1) * P], xn[:, m, k * P:(k + 1) * P],
                                                   g.ident[:, :])
                    last.then_inc(s["turned"], 1)


def fox(nc, d, g, low, wide, norm_rows, causal, b_f, ones, yT):
    ident = g.ident[:, :]
    K = HD + 2
    scale = HD ** -0.5
    with ExitStack() as held:
        def sb(name, shape, dtype=F32):
            return held.enter_context(nc.sbuf_tensor(name, shape, dtype))

        qT, kT = sb("fox_qT", [P, NH, SEQ]), sb("fox_kT", [P, NH, SEQ])
        with ExitStack() as making:
            def tb(name, shape, dtype=F32):
                return making.enter_context(nc.sbuf_tensor(name, shape, dtype))

            qcat, kcat = tb("fox_qcat", [P, NT_X, NH, K]), tb("fox_kcat", [P, NT_X, NH, K])

            def heads(i, m):
                return wide[:, m, i, :].rearrange("p (h n) -> p h n", n=HD)

            jobs = [(heads(2, m), qcat[:, m, :, 0:HD], norm_rows[:, 128:192]) for m in range(NT_X)]
            jobs += [(heads(3, m), kcat[:, m, :, 0:HD], norm_rows[:, 192:256]) for m in range(NT_X)]
            head_norm_stage(nc, g, "fox_norm", jobs)
            z, e, lf = (tb(f"fox_{x}", [P, NT_X, NH]) for x in ("z", "e", "lf"))
            upto = tb("upto", [P, P])
            with nc.psum_tensor("cum_ps", [P, 512], F32) as ps, \
                    stage(nc, "cum", "chain", "loaded", "abs", "log", "lf", "summed", "done") as (s, block):
                @block.sync
                def _(sp):
                    sp.dma_start(upto[:, :], d["before"]).then_inc(s["loaded"], 16)

                @block.vector
                def _(dve):
                    step = chained(dve, s["chain"])
                    for m in range(NT_X):
                        step(nc.vector.tensor_tensor(z[:, m, :], low[:, m, LOWW - NH:LOWW], b_f[:, :], ALU.add))
                    nc.vector.scalar_tensor_tensor(e[:, :, :], z[:, :, :], -1.0, z[:, :, :], ALU.mult,
                                                   ALU.max).then_inc(s["abs"], 1)
                    dve.wait_ge(s["log"], 2)
                    step(nc.vector.tensor_scalar(z[:, :, :], z[:, :, :], 0.0, None, ALU.min))
                    step(nc.vector.tensor_tensor(lf[:, :, :], z[:, :, :], e[:, :, :], ALU.subtract))
                    dve.wait_ge(s["loaded"], 16)
                    nc.vector.tensor_tensor(upto[:, :], upto[:, :], ident, ALU.add).then_inc(s["lf"], 1)
                    for cat, at in ((qcat, HD + 1), (kcat, HD)):
                        for m in range(NT_X):
                            nc.vector.memset(cat[:, m, :, at:at + 1], 1.0).then_inc(s["done"], 1)
                    dve.wait_ge(s["summed"], 1)
                    for m in range(NT_X):
                        cum = ps[:, m * NH:(m + 1) * NH].unsqueeze(2)
                        nc.vector.tensor_scalar(qcat[:, m, :, HD:HD + 1], cum, 1.0 / scale, None,
                                                ALU.mult).then_inc(s["done"], 1)
                        nc.vector.tensor_scalar(kcat[:, m, :, HD + 1:HD + 2], cum, -1.0 / scale, None,
                                                ALU.mult).then_inc(s["done"], 1)

                @block.scalar
                def _(act):
                    act.wait_ge(s["abs"], 1)
                    nc.scalar.activation(e[:, :, :], e[:, :, :], ACT.Exp, scale=-1.0).then_inc(s["log"], 1)
                    act.wait_ge(s["log"], 1)
                    nc.scalar.activation(e[:, :, :], e[:, :, :], ACT.Ln, bias=1.0).then_inc(s["log"], 1)

                @block.tensor
                def _(pe):
                    pe.wait_ge(s["lf"], 1)
                    for m in range(NT_X):
                        for q in range(m):
                            nc.tensor.matmul(ps[:, m * NH:(m + 1) * NH], ones, lf[:, q, :], start=(q == 0), stop=False,
                                             skip_group_check=True)
                        last = nc.tensor.matmul(ps[:, m * NH:(m + 1) * NH], upto[:, :], lf[:, m, :], start=(m == 0),
                                                stop=True, skip_group_check=True)
                    last.then_inc(s["summed"], 1)
            turn_heads(nc, "fox_turn", [(qcat, qT), (kcat, kT)], K, ident)
        o = sb("fox_att", [P, NT_X, 512])
        items = [dict(q=qT[0:K, h, b * P:(b + 1) * P], keys=[kT[0:K, h, 0:(b + 1) * P]],
                      v=[wide[:, t, 4, HD * h:HD * h + HD] for t in range(b + 1)], mask=causal[:, 1, (3 - b) * P:SEQ],
                      sink=None, out=o[:, b, HD * h:HD * h + HD], ident=ident) for b in range(NT_X) for h in range(NH)]
        attention_stage(nc, "fox", items, scale)
        turn_gate(nc, "fox_o", o, lambda m: wide[:, m, 1, :], yT, ident)


def build_program(nc, d, out):
    with ExitStack() as whole:
        def sb(name, shape, dtype=F32):
            return whole.enter_context(nc.sbuf_tensor(name, shape, dtype))

        ident = sb("ident", [P, P])
        vec = sb("vec", [P, NVCOL])
        eps_col = sb("eps_col", [P, 1])
        ada = sb("ada", [P, 48, 2])
        ada2 = sb("ada2", [P, 24, 1])
        g = Shared(ident=ident, vec=vec, eps_col=eps_col, ada=ada, ada2=ada2)

        cond = sb("cond", [P, KD, 2])
        sig = sb("sig", [P, 2, KD])
        with stage(nc, "start", "loaded", "set", "sig", "cond") as (s, block):
            @block.sync
            def _(sp):
                sp.dma_start(ident[:, :], d["ident"]).then_inc(s["loaded"], 16)
                sp.dma_start(vec[:, :], d["vectors"]).then_inc(s["loaded"], 16)
                sp.wait_ge(s["loaded"], 32)

            @block.vector
            def _(dve):
                nc.vector.memset(eps_col[:, :], RMS_EPS).then_inc(s["set"], 1)
                dve.wait_ge(s["sig"], 1)
                for j, name in enumerate(("c", "c_ctx")):
                    nc.vector.tensor_tensor(cond[:, :, j], vec[:, VCOL[name]], sig[:, j, :], ALU.mult).then_inc(s["cond"], 1)

            @block.scalar
            def _(act):
                act.wait_ge(s["loaded"], 32)
                nc.scalar.activation(sig[:, :, :].rearrange("p a k -> p (a k)"),
                                     vec[:, VCOL["c"].start:VCOL["c_ctx"].stop], ACT.Sigmoid).then_inc(s["sig"], 1)

        ada_stage(nc, "ada", cond, 2, d["w_ada"], 12, vec[:, VCOL["b_ada"]], ada)
        ada_stage(nc, "ada2", vec[:, VCOL["c_2"]].unsqueeze(2), 1, d["w_ada_2"], 6, vec[:, VCOL["b_ada_2"]], ada2)
        row_cols = sb("row_cols", [P, 3, KD])
        ones = sb("ones", [P, P])
        with stage(nc, "row_cols", "done") as (s, block):
            @block.vector
            def _(dve):
                nc.vector.memset(ones[:, :], 1.0).then_inc(s["done"], 1)
                nc.vector.tensor_tensor(row_cols[:, 0, :], ada[:, 16:24, 0], vec[:, VCOL["g_post_mix"]],
                                        ALU.mult).then_inc(s["done"], 1)
                nc.vector.tensor_tensor(row_cols[:, 1, :], ada[:, 40:48, 0], vec[:, VCOL["g_post_ffn"]],
                                        ALU.mult).then_inc(s["done"], 1)
                nc.vector.tensor_copy(row_cols[:, 2, :], ada2[:, 16:24, 0]).then_inc(s["done"], 1)
        x = sb("x", [P, NT_X, D])
        first_block(nc, d, g, x, row_cols, ones[:, :])
        second_block(nc, d, g, x, row_cols, ones[:, :], out)


def axial_tables():
    t = np.arange(SEQ)
    half = HD // 2
    inv = (np.float32(10000.0) ** (-np.arange(0, half, 2, dtype=np.float32) / np.float32(half))).astype(np.float32)
    ang = np.stack([(t // 64).astype(np.float32)[:, None] * inv, (t % 64).astype(np.float32)[:, None] * inv], 1)
    tab = np.stack([np.cos(ang), np.sin(ang)], 1).astype(np.float32)
    return np.ascontiguousarray(tab.reshape(NT_X, P, 2, 2, 16).transpose(1, 0, 2, 3, 4))


def window_mask_table():
    q, k = np.arange(P)[:, None], np.arange(P)[None, :]
    before = np.where(k >= q, 0.0, NEG)
    after = np.where(k <= q, 0.0, NEG)
    z = np.zeros((P, P))
    return np.concatenate([z, z, before, z, after, z, z, z, after], 1).astype(np.float32)


def rwkv_tables():
    s, t = np.arange(P)[:, None], np.arange(P)[None, :]
    same = s // CH == t // CH
    tri = np.zeros((P, 2, 2, P), np.float32)
    off = np.zeros((P, 2, LEVELS, P), np.float32)
    for i, (before, upto) in enumerate(((s < t, s <= t), (s > t, s >= t))):
        tri[:, i, 0], tri[:, i, 1] = same & before, same & upto
        for l in range(LEVELS):
            off[:, i, l] = before & (s // (2 << l) == t // (2 << l)) & (s // (1 << l) != t // (1 << l))
    heads = np.stack([same.astype(np.float32), same / np.float32(CH)], 1).astype(np.float32)
    segment = np.tile((np.arange(NTOK) % CH != 0).astype(np.float32), (P, 1))
    return {"tri": tri, "off": off, "heads": heads, "segment": segment}


def rwkv_layout(a):
    w, b, mp, mn = a["w_in"][0], a["b_in"][0], a["mu_prev"][0], a["mu_next"][0]

    def slices(m):
        return m.reshape(KD, P, -1).transpose(1, 0, 2)

    d = dict(rwkv_tables())
    d["w_lora_in"] = slices(w[:, 768 + 1536:768 + 1920])
    rkv, cols, low = [], [], []
    for pair in range(4):
        c = slice(P * pair, P * pair + P)
        at = [768 + 512 * i + P * pair for i in range(3)]
        rkv.append(slices(np.concatenate([w[:, x:x + P] for x in at], 1)))
        here = [b[x:x + P] for x in at] + [m[x - 768:x - 768 + P] for m in (mp, mn) for x in at]
        here += [a[n][0, c] for n in ("w0_f", "w0_b", "a0_f", "a0_b", "k_k", "k_a")]
        here += [a["r_k"][0].reshape(-1)[c], a["ln_x_w"][0, c], a["ln_x_b"][0, c]]
        cols.append(np.stack(here, 1))
        low.append(np.stack([np.concatenate([a["w2_f"][0][:, c], a["w2_b"][0][:, c]], 0),
                             np.concatenate([a["a2_f"][0][:, c], a["a2_b"][0][:, c]], 0), a["g2"][0][:, c]], 1))
    d["w_rkv"], d["pair_cols"], d["pair_low"] = np.stack(rkv), np.stack(cols), np.stack(low)
    return d


def second_layout(a):
    at = dict(zip(("cq", "ckv", "kr", "ga", "q", "k", "v", "f", "gb", "mg"),
                  (0, 384, 640, 672, 1184, 1696, 2208, 2720, 2728, 3240)))
    size = dict(cq=384, ckv=256, kr=32, ga=512, q=512, k=512, v=512, f=8, gb=512, mg=2048)
    order = np.concatenate([np.arange(at[n], at[n] + size[n]) for n in
                            ("cq", "ckv", "kr", "f", "ga", "gb", "q", "k", "v", "mg")])
    uq = np.arange(NH * (HD + RD)).reshape(NH, HD + RD)
    ukv = np.arange(NH * 2 * HD).reshape(NH, 2 * HD)
    q, k = np.arange(P)[:, None], np.arange(P)[None, :]
    causal = np.zeros((P, 2, SEQ), np.float32)
    causal[:, 0, 384:] = np.where(k // 64 <= q // 64, 0.0, NEG)
    causal[:, 1, 384:] = np.where(k <= q, 0.0, NEG)
    half = np.arange(0, RD, 2, dtype=np.float32)
    return {"w_in_2": a["w_in_2"][0][:, order],
            "w_uq_2": a["w_uq_2"][0][:, np.concatenate([uq[:, :HD].ravel(), uq[:, HD:].ravel()])],
            "w_ukv_2": a["w_ukv_2"][0][:, np.concatenate([ukv[:, :HD].ravel(), ukv[:, HD:].ravel()])],
            "norm_rows_2": np.concatenate([a[n + "_2"][0] for n in ("qn_nope_a", "kn_nope_a", "qn_b", "kn_b",
                                                                    "qn_rope_a", "kn_rope_a")]),
            "b_f_2": a["b_f_2"][0], "w_branch_a_2": a["w_branch_a_2"][0], "w_branch_b_2": a["w_branch_b_2"][0],
            "w_out_2": a["w_out_2"][0], "causal_masks": causal,
            "positions_2": np.ascontiguousarray(a["positions_2"].reshape(NT_X, P).T),
            "rope_freq": (np.float32(10000.0) ** (-half / np.float32(RD))).astype(np.float32)}


def host_layout(inputs):
    a = {k: np.asarray(v) for k, v in inputs.items()}

    def columns(v):
        return np.ascontiguousarray(v.reshape(-1, P).T)

    lora = slice(768 + 1536, 768 + 1920)
    parts = {"c": a["c"][0], "c_ctx": a["c_ctx"], "c_2": a["c_2"][0], "b_ada": a["b_ada"][0],
             "g_pre_mix": a["g_pre_mix"][0], "g_post_mix": a["g_post_mix"][0], "g_pre_ffn": a["g_pre_ffn"][0],
             "g_post_ffn": a["g_post_ffn"][0], "b_ada_2": a["b_ada_2"][0], "norm_w_2": a["norm_w_2"][0],
             "lora_b_in": a["b_in"][0, lora], "lora_mu_prev": a["mu_prev"][0, 1536:], "lora_mu_next": a["mu_next"][0, 1536:],
             "lora_norms_2": np.concatenate([a["q_lora_norm_w_2"][0], a["kv_lora_norm_w_2"][0]])}
    d = {"vectors": np.concatenate([columns(parts[n]) for n in VCOL], 1)}
    d["ident"] = np.eye(P, dtype=np.float32)
    d["x"], d["ctx"] = a["x"], a["ctx"]
    d["w_ada"], d["w_ada_2"] = a["w_ada"][0], a["w_ada_2"][0]
    w, b = a["w_in"][0], a["b_in"][0]
    order = np.concatenate([np.arange(HD) + HD * h for h in (0, 4, 1, 5, 2, 6, 3, 7)])
    tok = np.concatenate([order, np.arange(512, 768), np.arange(2688, 4736)])
    d["w_in_tok"], d["b_in_tok"], d["b_gates"] = w[:, tok], b[tok[:768]], b[tok[768:]]
    d["rope_axial"], d["window_masks"] = axial_tables(), window_mask_table()
    d.update(rwkv_layout(a))
    for n in ("w_up_att", "w_up_rwkv", "w_out", "w_router", "b_router", "w_gate_up", "b_gate_up", "w_down", "b_down"):
        d[n] = a[n][0]
    d.update(second_layout(a))
    d["iota"] = np.arange(P, dtype=np.float32)
    d["before"] = np.triu(np.ones((P, P), np.float32), 1)
    d["att_sinks"] = a["att_sinks"][0]
    return d


def kernel(**inputs):
    import numpy as _np
    import concourse.bacc as _bacc
    from concourse import mybir as _mybir
    from concourse.bass_utils import run_bass_kernel_spmd as _run

    nc = _bacc.Bacc("TRN2", target_bir_lowering=False, num_devices=1)
    arrays, d = {}, {}
    for name, array in host_layout(inputs).items():
        array = _np.ascontiguousarray(array)
        arrays[f"in_{name}"] = array
        d[name] = nc.dram_tensor(f"in_{name}", array.shape, _mybir.dt.from_np(array.dtype), kind="ExternalInput").ap()
    out = nc.dram_tensor("out_0", (1, SEQ, D), F32, kind="ExternalOutput").ap()
    build_program(nc, d, out)
    r = _run(nc, [arrays], core_ids=[0])
    return r.results[0]["out_0"]
```

```python
from contextlib import ExitStack, contextmanager

import numpy as np

import concourse.bass as bass
from concourse import mybir

F32 = mybir.dt.float32
I32 = mybir.dt.int32
U32 = mybir.dt.uint32
ALU = mybir.AluOpType
ACT = mybir.ActivationFunctionType
AX = mybir.AxisListType

P = 128
D = 1024
KD = D // P
SEQ = 512
CTX = 256
NT_X = SEQ // P
NT_C = CTX // P
NTOK = SEQ + CTX
HD = 64
NEG = -1e30
ROUND = 12582912.0
RMS_EPS = 1e-6


class Shared:

    def __init__(self, ident, vec, eps_col, ada, ada2):
        self.ident, self.vec, self.eps_col, self.ada, self.ada2 = ident, vec, eps_col, ada, ada2


@contextmanager
def stage(nc, name, *signals, clear=(), pool_dma=()):
    with ExitStack() as held:
        sems = {s: held.enter_context(nc.semaphore(f"{name}_{s}")) for s in signals}
        with nc.Block() as block:
            yield sems, block
        for x in pool_dma:
            nc.gpsimd.dma_reset(range(x.num, x.num + 1))
        numbers = sorted([x.num for x in sems.values()] + [x.num for x in clear] + [x.num for x in pool_dma])
        starts = [i for i, x in enumerate(numbers) if i == 0 or x != numbers[i - 1] + 1] + [len(numbers)]
        for i, j in zip(starts[:-1], starts[1:]):
            nc.gpsimd.sem_clear(range(numbers[i], numbers[j - 1] + 1))
        nc.all_engine_barrier()


def chained(engine, signal):
    count = [0]

    def step(instruction):
        count[0] += 1
        instruction.then_inc(signal, 1)
        engine.wait_ge(signal, count[0])

    return step


def row_to_all(row, n):
    return bass.AP(tensor=row.tensor, offset=row.offset, ap=[[0, P], [1, n]])


def vector_columns():
    at, cols = 0, {}
    for name, n in (("c", 8), ("c_ctx", 8), ("c_2", 8), ("b_ada", 48), ("g_pre_mix", 8), ("g_post_mix", 8),
                    ("g_pre_ffn", 8), ("g_post_ffn", 8), ("b_ada_2", 24), ("norm_w_2", 8), ("lora_b_in", 3),
                    ("lora_mu_prev", 3), ("lora_mu_next", 3), ("lora_norms_2", 5)):
        cols[name] = slice(at, at + n)
        at += n
    return cols, at


VCOL, NVCOL = vector_columns()


def ada_stage(nc, name, cond, n_cond, w_dram, n_chunks, bias_cols, ada, ident):
    chunk, slots = 4, 4
    wv = w_dram.rearrange("(k p) n -> p k n", p=P)
    with ExitStack() as held:
        w_sb = held.enter_context(nc.sbuf_tensor(f"{name}_w", [P, slots, KD, 512], F32))
        row = held.enter_context(nc.sbuf_tensor(f"{name}_row", [n_cond, 2, 512], F32))
        ps = held.enter_context(nc.psum_tensor(f"{name}_ps", [P, 2, 512], F32))
        ps_c = held.enter_context(nc.psum_tensor(f"{name}_columns", [P, 2, 512], F32))
        with stage(nc, name, "w0", "w1", "w2", "w3", "product", "row", "columns", "out") as (s, block):
            loaded = [s["w0"], s["w1"], s["w2"], s["w3"]]

            @block.sync
            def _(sp):
                for c in range(n_chunks):
                    if c >= slots:
                        sp.wait_ge(s["product"], c - slots + 1)
                    sp.dma_start(w_sb[:, c % slots], wv[:, :, c * 512:c * 512 + 512]).then_inc(loaded[c % slots], 16)

            @block.tensor
            def _(pe):
                for c in range(n_chunks + 1):
                    if c < n_chunks:
                        pe.wait_ge(loaded[c % slots], 16 * (c // slots + 1))
                        if c >= 2:
                            pe.wait_ge(s["row"], c - 1)
                        for k in range(KD):
                            last = nc.tensor.matmul(ps[0:n_cond, c % 2, :], cond[:, k, :], w_sb[:, c % slots, k, :],
                                                    start=(k == 0), stop=(k == KD - 1))
                        last.then_inc(s["product"], 1)
                    if c >= 1:
                        b = c - 1
                        pe.wait_ge(s["row"], b + 1)
                        if b >= 2:
                            pe.wait_ge(s["out"], b - 1)
                        for m in range(chunk):
                            last = nc.tensor.transpose(ps_c[:, b % 2, m * n_cond:(m + 1) * n_cond],
                                                       row[:, b % 2, m * P:(m + 1) * P], ident[0:n_cond, 0:n_cond])
                        last.then_inc(s["columns"], 1)

            @block.scalar
            def _(act):
                for c in range(n_chunks):
                    act.wait_ge(s["product"], c + 1)
                    if c >= 2:
                        act.wait_ge(s["columns"], c - 1)
                    nc.scalar.copy(row[:, c % 2, :], ps[0:n_cond, c % 2, :]).then_inc(s["row"], 1)

            @block.vector
            def _(dve):
                for c in range(n_chunks):
                    dve.wait_ge(s["columns"], c + 1)
                    bias = bias_cols[:, c * chunk:(c + 1) * chunk].unsqueeze(2).to_broadcast([P, chunk, n_cond])
                    nc.vector.tensor_tensor(ada[:, c * chunk:(c + 1) * chunk, :],
                                            ps_c[:, c % 2, 0:chunk * n_cond].rearrange("p (m j) -> p m j", j=n_cond),
                                            bias, ALU.add).then_inc(s["out"], 1)


def norm_turn_stage(nc, name, tiles, sources, xn, hT, affine, eps, ident):
    n = len(tiles)
    with ExitStack() as held:
        squares = held.enter_context(nc.sbuf_tensor(f"{name}_sq", [P, D], F32))
        stat = held.enter_context(nc.sbuf_tensor(f"{name}_stat", [P, 3, n], F32))
        ps = held.enter_context(nc.psum_tensor(f"{name}_ps", [P, 2, 2, 512], F32))
        with stage(nc, name, "x", "squared", "root", "inverse", "normed", "turned", "out_act", "out_dve") as (s, block):
            @block.sync
            def _(sp):
                if sources is not None:
                    for m in range(n):
                        sp.dma_start(tiles[m], sources[m]).then_inc(s["x"], 16)

            @block.scalar
            def _(act):
                if sources is not None:
                    act.wait_ge(s["x"], 16 * n)
                for m in range(n):
                    if m:
                        act.wait_ge(s["squared"], m)
                    nc.scalar.activation(squares[:, :], tiles[m], ACT.Square,
                                         accum_out=stat[:, 0, m:m + 1]).then_inc(s["squared"], 1)
                act.wait_ge(s["squared"], n)
                nc.scalar.activation(stat[:, 1, :], stat[:, 0, :], ACT.Sqrt, scale=1.0 / D,
                                     bias=eps).then_inc(s["root"], 1)
                for m in range(n):
                    act.wait_ge(s["turned"], m + 1)
                    for k in range(4):
                        gain, shift = affine(m, k)
                        last = nc.scalar.activation(hT[:, k, m * P:(m + 1) * P], ps[:, m % 2, 0, k * P:(k + 1) * P],
                                                    ACT.Identity, scale=gain, bias=shift)
                    last.then_inc(s["out_act"], 1)

            @block.vector
            def _(dve):
                dve.wait_ge(s["root"], 1)
                nc.vector.reciprocal(stat[:, 2, :], stat[:, 1, :]).then_inc(s["inverse"], 1)
                dve.wait_ge(s["inverse"], 1)
                for m in range(n):
                    nc.vector.tensor_scalar(xn[m], tiles[m], stat[:, 2, m:m + 1], None, ALU.mult).then_inc(s["normed"], 1)
                for m in range(n):
                    dve.wait_ge(s["turned"], m + 1)
                    for k in range(4, 8):
                        gain, shift = affine(m, k)
                        last = nc.vector.tensor_scalar(hT[:, k, m * P:(m + 1) * P],
                                                       ps[:, m % 2, 1, (k - 4) * P:(k - 3) * P],
                                                       gain, shift, ALU.mult, ALU.add)
                    last.then_inc(s["out_dve"], 1)

            @block.tensor
            def _(pe):
                for m in range(n):
                    pe.wait_ge(s["normed"], m + 1)
                    if m >= 2:
                        pe.wait_ge(s["out_act"], m - 1)
                        pe.wait_ge(s["out_dve"], m - 1)
                    for k in range(KD):
                        last = nc.tensor.transpose(ps[:, m % 2, k // 4, (k % 4) * P:(k % 4 + 1) * P],
                                                   xn[m][:, k * P:(k + 1) * P], ident)
                    last.then_inc(s["turned"], 1)


def token_gemm_stage(nc, name, chunks, w_slots, evacuate, extra=()):
    with ExitStack() as held:
        ps = held.enter_context(nc.psum_tensor(f"{name}_ps", [P, 4, 512], F32))
        with stage(nc, name, "w0", "w1", "tile", "free", "chain", "step2", *extra) as (s, block):
            loaded = [s["w0"], s["w1"]]
            firsts, tiles = [], []
            for c, chunk in enumerate(chunks):
                firsts.append(len(tiles))
                tiles += [(c, m) for m in range(4 if "rhs" in chunk else len(chunk["lhs"]))]
            firsts.append(len(tiles))

            @block.sync
            def _(sp):
                for c, chunk in enumerate(chunks):
                    if c >= 2:
                        sp.wait_ge(s["tile"], firsts[c - 1])
                    sp.dma_start(w_slots[c % 2][:, 0:chunk["k"], 0:chunk["width"]],
                                 chunk["w"].rearrange("(k p) n -> p k n", p=P)).then_inc(loaded[c % 2], 16)

            @block.tensor
            def _(pe):
                for t, (c, m) in enumerate(tiles):
                    chunk = chunks[c]
                    if m == 0:
                        pe.wait_ge(loaded[c % 2], 16 * (c // 2 + 1))
                    if t >= 4:
                        pe.wait_ge(s["free"], t - 3)
                    for k in range(chunk["k"]):
                        start, stop = k == 0, k == chunk["k"] - 1
                        if "rhs" in chunk:
                            last = nc.tensor.matmul(ps[:, t % 4, :], w_slots[c % 2][:, k, m * P:(m + 1) * P],
                                                    chunk["rhs"](k), start=start, stop=stop)
                        else:
                            last = nc.tensor.matmul(ps[:, t % 4, 0:chunk["width"]], chunk["lhs"][m](k),
                                                    w_slots[c % 2][:, k, 0:chunk["width"]], start=start, stop=stop)
                    last.then_inc(s["tile"], 1)

            work = [(t, chunks[c], m, ps[:, t % 4, 0:chunks[c]["width"]]) for t, (c, m) in enumerate(tiles)]
            evacuate(s, block, work)


def attention_stage(nc, name, items, scale, ident):
    n = len(items)
    W = 640
    with ExitStack() as held:
        masked = held.enter_context(nc.sbuf_tensor(f"{name}_masked", [P, 2, W], F32))
        prob = held.enter_context(nc.sbuf_tensor(f"{name}_prob", [P, 3, W], F32))
        probT = held.enter_context(nc.sbuf_tensor(f"{name}_probT", [P, 2, W], F32))
        diag = held.enter_context(nc.sbuf_tensor(f"{name}_diag", [P, 2, P], F32))
        col = held.enter_context(nc.sbuf_tensor(f"{name}_col", [P, 3, 8], F32))
        ps_s = held.enter_context(nc.psum_tensor(f"{name}_s", [P, 2, 1024], F32))
        ps_t = held.enter_context(nc.psum_tensor(f"{name}_t", [P, 1024], F32))
        ps_o = held.enter_context(nc.psum_tensor(f"{name}_o", [P, 2, 512], F32))
        MAX, NEGMAX, SUM, SINK, DEN, INV = range(6)
        with stage(nc, name, "scores", "maxed", "negated", "probs", "turned", "probT", "values", "done", "den",
                   "diag") as (s, block):
            def c(i, what):
                return col[:, i % 3, what:what + 1]

            def rows(i):
                return slice(HD * items[i]["half"], HD * items[i]["half"] + HD)

            @block.tensor
            def _(pe):
                for i in range(n + 3):
                    if i < n:
                        if i >= 2:
                            pe.wait_ge(s["maxed"], i - 1)
                        it, at = items[i], 0
                        for keys in it["keys"]:
                            w = keys.shape[1]
                            done = 0
                            while done < w:
                                part = min(w - done, 512 - at % 512)
                                last = nc.tensor.matmul(ps_s[:, i % 2, at:at + part], it["q"],
                                                        keys[:, done:done + part], start=(at % 512 == 0),
                                                        stop=True, skip_group_check=True)
                                at, done = at + part, done + part
                        last.then_inc(s["scores"], 1)
                    if 2 <= i <= n + 1:
                        j = i - 2
                        pe.wait_ge(s["diag"], j + 1)
                        if j >= 1:
                            pe.wait_ge(s["probT"], j)
                        for t in range(len(items[j]["v"])):
                            last = nc.tensor.matmul(ps_t[:, t * P:(t + 1) * P], prob[:, j % 3, t * P:(t + 1) * P],
                                                    diag[:, j % 2, :], start=True, stop=True)
                        last.then_inc(s["turned"], 1)
                    if i >= 3:
                        j = i - 3
                        pe.wait_ge(s["probT"], j + 1)
                        if j >= 2:
                            pe.wait_ge(s["done"], j - 1)
                        vs = items[j]["v"]
                        for t, v in enumerate(vs):
                            last = nc.tensor.matmul(ps_o[rows(j), j % 2, 0:P], v, probT[:, j % 2, t * P:(t + 1) * P],
                                                    start=(t == 0), stop=(t == len(vs) - 1))
                        last.then_inc(s["values"], 1)

            @block.vector
            def _(dve):
                for i in range(n + 3):
                    if i < n:
                        it = items[i]
                        w = P * len(it["v"])
                        dve.wait_ge(s["scores"], i + 1)
                        if i >= 2:
                            dve.wait_ge(s["probs"], i - 1)
                        start = it["sink"] if it["sink"] is not None else -3.0e38
                        nc.vector.tensor_tensor_reduce(masked[:, i % 2, 0:w], ps_s[:, i % 2, 0:w], it["mask"], scale,
                                                       start, ALU.add, ALU.max, c(i, MAX)).then_inc(s["maxed"], 1)
                        dve.wait_ge(s["maxed"], i + 1)
                        nc.vector.tensor_scalar(c(i, NEGMAX), c(i, MAX), -1.0, None, ALU.mult) \
                            .then_inc(s["negated"], 1)
                    if 1 <= i <= n:
                        j = i - 1
                        dve.wait_ge(s["probs"], j + 1)
                        sink = c(j, SINK) if items[j]["sink"] is not None else 0.0
                        nc.vector.tensor_scalar(c(j, DEN), c(j, SUM), sink, None, ALU.add).then_inc(s["den"], 1)
                        dve.wait_ge(s["den"], 2 * j + 1)
                        nc.vector.reciprocal(c(j, INV), c(j, DEN)).then_inc(s["den"], 1)
                        dve.wait_ge(s["den"], 2 * j + 2)
                        if j >= 2:
                            dve.wait_ge(s["turned"], j - 1)
                        nc.vector.tensor_scalar(diag[:, j % 2, :], ident, c(j, INV), None, ALU.mult) \
                            .then_inc(s["diag"], 1)
                    if i >= 3:
                        j = i - 3
                        dve.wait_ge(s["values"], j + 1)
                        if items[j]["gate"] is None:
                            nc.vector.tensor_copy(items[j]["out"], ps_o[rows(j), j % 2, 0:P]).then_inc(s["done"], 1)
                        else:
                            nc.vector.tensor_tensor(items[j]["out"], ps_o[rows(j), j % 2, 0:P], items[j]["gate"],
                                                    ALU.mult).then_inc(s["done"], 1)

            @block.scalar
            def _(act):
                for i in range(n + 2):
                    if i < n:
                        w = P * len(items[i]["v"])
                        act.wait_ge(s["negated"], i + 1)
                        if i >= 3:
                            act.wait_ge(s["turned"], i - 2)
                        if i >= 3:
                            act.wait_ge(s["diag"], i - 2)
                        if items[i]["sink"] is not None:
                            nc.scalar.activation(c(i, SINK), c(i, NEGMAX), ACT.Exp, bias=items[i]["sink"])
                        nc.scalar.activation(prob[:, i % 3, 0:w], masked[:, i % 2, 0:w], ACT.Exp, bias=c(i, NEGMAX),
                                             accum_out=c(i, SUM)).then_inc(s["probs"], 1)
                    if i >= 2:
                        j = i - 2
                        w = P * len(items[j]["v"])
                        act.wait_ge(s["turned"], j + 1)
                        if j >= 2:
                            act.wait_ge(s["values"], j - 1)
                        nc.scalar.copy(probT[:, j % 2, 0:w], ps_t[:, 0:w]).then_inc(s["probT"], 1)


def turn_stage(nc, name, sources, targets, ident):
    n = len(sources)
    groups = [list(range(a, min(a + 4, n))) for a in range(0, n, 4)]
    with ExitStack() as held:
        ps = held.enter_context(nc.psum_tensor(f"{name}_ps", [P, 4, 512], F32))
        with stage(nc, name, "turned", "even", "odd") as (s, block):
            @block.tensor
            def _(pe):
                for q, group in enumerate(groups):
                    if q >= 4:
                        pe.wait_ge(s["odd"] if q % 2 else s["even"], (q - 4) // 2 + 1)
                    for j, i in enumerate(group):
                        last = nc.tensor.transpose(ps[:, q % 4, j * P:(j + 1) * P], sources[i], ident)
                    last.then_inc(s["turned"], 1)

            def copies(engine, copy, odd, signal):
                for q, group in enumerate(groups):
                    if q % 2 == odd:
                        engine.wait_ge(s["turned"], q + 1)
                        for j, i in enumerate(group):
                            last = copy(targets[i], ps[:, q % 4, j * P:(j + 1) * P])
                        last.then_inc(signal, 1)

            @block.vector
            def _(dve):
                copies(dve, nc.vector.tensor_copy, 0, s["even"])

            @block.scalar
            def _(act):
                copies(act, nc.scalar.copy, 1, s["odd"])


def first_block(nc, d, g, x, row_cols, ones):
    with ExitStack() as mixing:
        rwkT = mixing.enter_context(nc.sbuf_tensor("rwkT", [P, 4, SEQ], F32))
        hT = mixing.enter_context(nc.sbuf_tensor("hT", [P, KD, NTOK], F32))
        mix_inputs(nc, d, g, hT)
        rwkv_branch(nc, d, g, hT, rwkT)
        attT = mixing.enter_context(nc.sbuf_tensor("attT", [P, 4, SEQ], F32))
        window_attention(nc, d, g, hT, attT)
        gates = mixing.enter_context(nc.sbuf_tensor("gates", [P, NT_X, 2 * D], F32))
        merge_gates(nc, d, hT, gates)
        mix = mixing.enter_context(nc.sbuf_tensor("mix", [P, NT_X, D], F32))
        merge_and_out(nc, d, g, "mix", (attT, rwkT), gates, (d["w_up_att"], d["w_up_rwkv"]), d["w_out"], mix)
        with stage(nc, "x_in", "x") as (s, block):
            @block.sync
            def _(sp):
                sp.dma_start(x[:, :, :], d["x"][0].rearrange("(m p) n -> p m n", p=P)).then_inc(s["x"], 16)
                sp.wait_ge(s["x"], 16)
        tiles = [x[:, m] for m in range(NT_X)]
        row = mixing.enter_context(nc.sbuf_tensor("mix_row", [P, D], F32))
        rows_stage(nc, g, "mix_rows", [row_cols[:, 0]], [row[:, :]], ones)
        add_normed_stage(nc, g, "post_mix", [mix[:, m] for m in range(NT_X)], tiles, row[:, :])
    with ExitStack() as ffn:
        def sb(name, shape, dtype=F32):
            return ffn.enter_context(nc.sbuf_tensor(name, shape, dtype))

        gain, shift = sb("ffn_gain", [P, KD]), sb("ffn_shift", [P, KD])
        weight, slot_of = sb("weight_of", [P, NT_X, TOP_K]), sb("slot_of", [P, NT_X, TOP_K], U32)
        token_of = sb("token_of", [P, LISTED], U32)
        table, n_blocks = sb("table", [1, P], I32), sb("n_blocks", [1, 1], I32)
        rows = nc.dram_tensor("normed_rows", (SEQ, D), F32).ap()
        with stage(nc, "ffn_gain", "done") as (s, block):
            @block.vector
            def _(dve):
                nc.vector.scalar_tensor_tensor(gain[:, :], g.ada[:, 32:40, 0], 1.0, g.vec[:, VCOL["g_pre_ffn"]],
                                               ALU.add, ALU.mult).then_inc(s["done"], 1)
                nc.vector.tensor_copy(shift[:, :], g.ada[:, 24:32, 0]).then_inc(s["done"], 1)
        weights = ExpertWeights(nc, d, ffn)
        with nc.sbuf_tensor("ffn_hT", [P, KD, SEQ], F32) as hT, nc.sbuf_tensor("ffn_xn", [P, NT_X, D], F32) as xn:
            norm_turn_stage(nc, "ffn", tiles, None, [xn[:, m] for m in range(NT_X)], hT,
                            lambda m, k: (gain[:, k:k + 1], shift[:, k:k + 1]), g.eps_col[:, 0:1], g.ident[:, :])
            route_stage(nc, d, g, hT, ones, weights, xn, rows, weight, slot_of, token_of, table, n_blocks)
        y = sb("ffn_y", [P, NT_X, D])
        experts(nc, d, g, weights, rows, gain, shift, weight, slot_of, token_of, table, n_blocks, y)
        row = sb("ffn_row", [P, D])
        rows_stage(nc, g, "ffn_rows", [row_cols[:, 1]], [row[:, :]], ones)
        add_normed_stage(nc, g, "post_ffn", [y[:, m] for m in range(NT_X)], tiles, row[:, :])


def mix_inputs(nc, d, g, hT):
    with ExitStack() as held:
        gain = held.enter_context(nc.sbuf_tensor("pre_gain", [P, 2, KD], F32))
        ctx_sb = held.enter_context(nc.sbuf_tensor("ctx_sb", [P, NT_C, D], F32))
        x_sb = held.enter_context(nc.sbuf_tensor("pre_x", [P, NT_X, D], F32))
        xn = held.enter_context(nc.sbuf_tensor("pre_xn", [P, 6, D], F32))
        with stage(nc, "pre_gain", "done") as (s, block):
            @block.vector
            def _(dve):
                for j in range(2):
                    nc.vector.scalar_tensor_tensor(gain[:, j, :], g.ada[:, 8:16, j], 1.0, g.vec[:, VCOL["g_pre_mix"]],
                                                   ALU.add, ALU.mult).then_inc(s["done"], 1)
        tiles = [ctx_sb[:, m] for m in range(NT_C)] + [x_sb[:, m] for m in range(NT_X)]
        sources = [d["ctx"][0, m * P:(m + 1) * P, :] for m in range(NT_C)]
        sources += [d["x"][0, m * P:(m + 1) * P, :] for m in range(NT_X)]

        def affine(m, k):
            j = 1 if m < NT_C else 0
            return gain[:, j, k:k + 1], g.ada[:, k, j:j + 1]

        norm_turn_stage(nc, "pre", tiles, sources, [xn[:, m] for m in range(6)], hT, affine, g.eps_col[:, 0:1],
                        g.ident[:, :])


def window_attention(nc, d, g, hT, attT):
    ident = g.ident[:, :]
    with ExitStack() as held:
        def sb(name, shape, dtype=F32):
            return held.enter_context(nc.sbuf_tensor(name, shape, dtype))

        qkv = sb("qkv", [P, NT_X, 768])
        kvc = sb("kvc", [P, NT_C, 256])
        rope = sb("rope", [P, NT_X, 2, 2, 16])
        masks = sb("win_masks", [P, 1152])
        sinks = sb("sinks", [P, 8])
        with ExitStack() as projecting:
            bias = projecting.enter_context(nc.sbuf_tensor("proj_bias", [P, 768], F32))
            slots = [projecting.enter_context(nc.sbuf_tensor(f"proj_w{i}", [P, KD, 512], F32)) for i in range(2)]
            w = d["w_in_tok"]

            def tok(t):
                return lambda k: hT[:, k, t * P:(t + 1) * P]

            chunks = [dict(w=w[:, 0:512], width=512, k=KD, lhs=[tok(NT_C + m) for m in range(NT_X)], col=0),
                      dict(w=w[:, 512:768], width=256, k=KD, lhs=[tok(NT_C + m) for m in range(NT_X)] +
                           [tok(m) for m in range(NT_C)], col=512)]

            def evacuate(s, block, work):
                def target(chunk, m):
                    a, b = chunk["col"], chunk["col"] + chunk["width"]
                    return qkv[:, m, a:b] if m < NT_X else kvc[:, m - NT_X, :]

                @block.scalar
                def _(act):
                    act.dma_start(bias[:, :], row_to_all(d["b_in_tok"], 768)).then_inc(s["side"], 16)
                    act.dma_start(rope[:, :, :, :, :], d["rope_axial"]).then_inc(s["side"], 16)
                    act.dma_start(masks[:, :], d["window_masks"]).then_inc(s["side"], 16)
                    act.dma_start(sinks[:, :], row_to_all(d["att_sinks"], 8)).then_inc(s["side"], 16)
                    act.wait_ge(s["side"], 64)

                @block.vector
                def _(dve):
                    dve.wait_ge(s["side"], 64)
                    for t, chunk, m, ps in work:
                        dve.wait_ge(s["tile"], t + 1)
                        a, b = chunk["col"], chunk["col"] + chunk["width"]
                        nc.vector.tensor_tensor(target(chunk, m), ps, bias[:, a:b], ALU.add).then_inc(s["free"], 1)

            token_gemm_stage(nc, "proj", chunks, slots, evacuate, extra=("side",))

        qT = sb("q_turned", [P, 2, 4, SEQ])
        keyT = sb("k_turned", [P, SEQ])
        kcT = sb("kcT", [P, CTX])
        rope_turn(nc, g, qkv, kvc, rope, qT, keyT, kcT)
        items = []
        for b in range(NT_X):
            for h in range(8):
                kv = h // 4
                lo, hi = max(0, b - 1), min(NT_X, b + 2)
                mask = {0: masks[:, 640:1152], NT_X - 1: masks[:, 0:512]}.get(b, masks[:, 0:640])
                items.append(dict(
                    q=qT[:, kv, h % 4, b * P:(b + 1) * P], keys=[kcT[:, :], keyT[:, lo * P:hi * P]],
                    v=[kvc[:, t, P + HD * kv:P + HD * kv + HD] for t in range(NT_C)] +
                      [qkv[:, t, 640 + HD * kv:640 + HD * kv + HD] for t in range(lo, hi)],
                    mask=mask, sink=sinks[:, h:h + 1], half=h % 2,
                    out=attT[HD * (h % 2):HD * (h % 2) + HD, h // 2, b * P:(b + 1) * P], gate=None))
        attention_stage(nc, "window", items, HD ** -0.5, ident)


def rope_turn(nc, g, qkv, kvc, rope, qT, keyT, kcT):
    ident = g.ident[:, :]
    with ExitStack() as held:
        rot = held.enter_context(nc.sbuf_tensor("rot", [P, NT_X, 640], F32))
        tmp = held.enter_context(nc.sbuf_tensor("rot_tmp", [P, 2, 4, 320], F32))
        ps = held.enter_context(nc.psum_tensor("rot_ps", [P, 2, 1024], F32))
        with stage(nc, "rot", "parts", "rotated", "turned", "copied", "zero") as (s, block):
            @block.vector
            def _(dve):
                for m in range(NT_X):
                    src = qkv[:, m, 0:640].rearrange("p (h a b c) -> p b h a c", h=10, a=2, b=2)
                    dst = rot[:, m, :].rearrange("p (h a b c) -> p b h a c", h=10, a=2, b=2)
                    cos = rope[:, m, 0].unsqueeze(1).to_broadcast([P, 10, 2, 16])
                    sin = rope[:, m, 1].unsqueeze(1).to_broadcast([P, 10, 2, 16])
                    if m >= 2:
                        dve.wait_ge(s["rotated"], 2 * (m - 1))
                    part = [tmp[:, m % 2, i, :].rearrange("p (h a c) -> p h a c", h=10, a=2) for i in range(4)]
                    for i, (x, y) in enumerate(((0, cos), (1, sin), (1, cos), (0, sin))):
                        nc.vector.tensor_tensor(part[i], src[:, x], y, ALU.mult).then_inc(s["parts"], 1)
                    dve.wait_ge(s["parts"], 4 * m + 4)
                    nc.vector.tensor_tensor(dst[:, 0], part[0], part[1], ALU.subtract).then_inc(s["rotated"], 1)
                    nc.vector.tensor_tensor(dst[:, 1], part[2], part[3], ALU.add).then_inc(s["rotated"], 1)

            @block.gpsimd
            def _(pool):
                for kv in range(2):
                    rows = slice(HD * (1 - kv), HD * (1 - kv) + HD)
                    nc.gpsimd.memset(qT[rows, kv], 0.0).then_inc(s["zero"], 1)
                    pool.wait_ge(s["zero"], kv + 1)

            @block.tensor
            def _(pe):
                for m in range(NT_X + 1):
                    if m >= 2:
                        pe.wait_ge(s["copied"], m - 1)
                    if m < NT_X:
                        pe.wait_ge(s["rotated"], 2 * m + 2)
                        for j in range(5):
                            last = nc.tensor.transpose(ps[:, m % 2, j * P:(j + 1) * P], rot[:, m, j * P:(j + 1) * P], ident)
                    else:
                        for t in range(NT_C):
                            last = nc.tensor.transpose(ps[:, m % 2, t * P:(t + 1) * P], kvc[:, t, 0:P], ident)
                    last.then_inc(s["turned"], 1)

            @block.scalar
            def _(act):
                for m in range(NT_X + 1):
                    act.wait_ge(s["turned"], m + 1)
                    if m < NT_X:
                        for kv in range(2):
                            rows = slice(HD * kv, HD * kv + HD)
                            nc.scalar.copy(qT[rows, kv, :, m * P:(m + 1) * P],
                                           ps[rows, m % 2, 0:512].rearrange("p (j t) -> p j t", j=4))
                        nc.scalar.copy(keyT[:, m * P:(m + 1) * P], ps[:, m % 2, 512:640]).then_inc(s["copied"], 1)
                    else:
                        nc.scalar.copy(kcT[:, :], ps[:, m % 2, 0:CTX]).then_inc(s["copied"], 1)


def merge_gates(nc, d, hT, gates):
    with ExitStack() as held:
        bias = held.enter_context(nc.sbuf_tensor("gates_bias", [P, 2 * D], F32))
        slots = [held.enter_context(nc.sbuf_tensor(f"gates_w{i}", [P, KD, 512], F32)) for i in range(2)]

        def tok(t):
            return lambda k: hT[:, k, t * P:(t + 1) * P]

        chunks = [dict(w=d["w_in_tok"][:, 768 + 512 * c:1280 + 512 * c], width=512, k=KD,
                       lhs=[tok(NT_C + m) for m in range(NT_X)], col=512 * c) for c in range(4)]

        def evacuate(s, block, work):
            @block.vector
            def _(dve):
                dve.wait_ge(s["side"], 16)
                for t, chunk, m, ps in work:
                    dve.wait_ge(s["tile"], t + 1)
                    a = chunk["col"]
                    nc.vector.tensor_tensor(gates[:, m, a:a + 512], ps, bias[:, a:a + 512], ALU.add).then_inc(s["free"], 1)

            @block.scalar
            def _(act):
                act.dma_start(bias[:, :], row_to_all(d["b_gates"], 2 * D)).then_inc(s["side"], 16)
                for t, chunk, m, ps in work:
                    act.wait_ge(s["free"], t + 1)
                    gate = gates[:, m, chunk["col"]:chunk["col"] + 512]
                    nc.scalar.activation(gate, gate, ACT.Sigmoid)

        token_gemm_stage(nc, "gates", chunks, slots, evacuate, extra=("side",))


def rows_stage(nc, g, name, columns, rows, ones):
    with ExitStack() as held:
        diag = held.enter_context(nc.sbuf_tensor(f"{name}_diag", [P, 2, KD, P], F32))
        ps = held.enter_context(nc.psum_tensor(f"{name}_ps", [P, 2, 1024], F32))
        with stage(nc, name, "diag", "made", "copied") as (s, block):
            @block.vector
            def _(dve):
                for i, col in enumerate(columns):
                    if i >= 2:
                        dve.wait_ge(s["made"], i - 1)
                    for k in range(KD):
                        last = nc.vector.tensor_scalar(diag[:, i % 2, k, :], g.ident[:, :], col[:, k:k + 1], None, ALU.mult)
                    last.then_inc(s["diag"], 1)

            @block.tensor
            def _(pe):
                for i in range(len(columns)):
                    pe.wait_ge(s["diag"], i + 1)
                    if i >= 2:
                        pe.wait_ge(s["copied"], i - 1)
                    for half in range(2):
                        last = nc.tensor.matmul(ps[:, i % 2, 512 * half:512 * half + 512], ones,
                                                diag[:, i % 2, 4 * half:4 * half + 4, :].rearrange("p k n -> p (k n)"),
                                                start=True, stop=True)
                    last.then_inc(s["made"], 1)

            @block.scalar
            def _(act):
                for i, row in enumerate(rows):
                    act.wait_ge(s["made"], i + 1)
                    nc.scalar.copy(row, ps[:, i % 2, :]).then_inc(s["copied"], 1)


def add_normed_stage(nc, g, name, branch, x, row):
    n = len(x)
    with ExitStack() as held:
        squares = held.enter_context(nc.sbuf_tensor(f"{name}_sq", [P, D], F32))
        stat = held.enter_context(nc.sbuf_tensor(f"{name}_stat", [P, 3, n], F32))
        with stage(nc, name, "squared", "root", "chain", "scaled") as (s, block):
            @block.scalar
            def _(act):
                for m in range(n):
                    if m:
                        act.wait_ge(s["squared"], m)
                    nc.scalar.activation(squares[:, :], branch[m], ACT.Square,
                                         accum_out=stat[:, 0, m:m + 1]).then_inc(s["squared"], 1)
                act.wait_ge(s["squared"], n)
                nc.scalar.activation(stat[:, 1, :], stat[:, 0, :], ACT.Sqrt, scale=1.0 / D,
                                     bias=g.eps_col[:, 0:1]).then_inc(s["root"], 1)

            @block.vector
            def _(dve):
                step = chained(dve, s["chain"])
                dve.wait_ge(s["root"], 1)
                step(nc.vector.reciprocal(stat[:, 2, :], stat[:, 1, :]))
                for m in range(n):
                    nc.vector.scalar_tensor_tensor(branch[m], branch[m], stat[:, 2, m:m + 1], row, ALU.mult,
                                                   ALU.mult).then_inc(s["scaled"], 1)
                dve.wait_ge(s["scaled"], n)
                for m in range(n):
                    nc.vector.tensor_tensor(x[m], x[m], branch[m], ALU.add).then_inc(s["scaled"], 1)


def merge_and_out(nc, d, g, name, branches, gates, w_up, w_out, mix):
    with ExitStack() as held:
        merged = held.enter_context(nc.sbuf_tensor(f"{name}_merged", [P, NT_X, D], F32))
        tmp = held.enter_context(nc.sbuf_tensor(f"{name}_tmp", [P, 2, 512], F32))
        slots = [held.enter_context(nc.sbuf_tensor(f"{name}_w{i}", [P, KD, 512], F32)) for i in range(2)]

        def tok(t, m):
            return lambda k: t[:, k, m * P:(m + 1) * P]

        chunks = [dict(w=w_up[b][:, 512 * c:512 * c + 512], width=512, k=4, b=b, c=c,
                       lhs=[tok(branches[b], m) for m in range(NT_X)]) for b in range(2) for c in range(2)]

        def gated(s, block, work):
            @block.vector
            def _(dve):
                for t, chunk, m, ps in work:
                    dve.wait_ge(s["tile"], t + 1)
                    at = slice(512 * chunk["c"], 512 * chunk["c"] + 512)
                    gate = gates[:, m, D * chunk["b"] + at.start:D * chunk["b"] + at.stop]
                    if chunk["b"] == 0:
                        nc.vector.tensor_tensor(merged[:, m, at], ps, gate, ALU.mult).then_inc(s["free"], 1)
                    else:
                        if t > 8:
                            dve.wait_ge(s["chain"], t - 8)
                        nc.vector.tensor_tensor(tmp[:, t % 2, :], ps, gate, ALU.mult).then_inc(s["free"], 1)
                        dve.wait_ge(s["free"], t + 1)
                        nc.vector.tensor_tensor(merged[:, m, at], merged[:, m, at], tmp[:, t % 2, :],
                                                ALU.add).then_inc(s["chain"], 1)

        token_gemm_stage(nc, f"{name}_up", chunks, slots, gated)
        mergedT = held.enter_context(nc.sbuf_tensor(f"{name}_mergedT", [P, KD, SEQ], F32))
        turn_stage(nc, f"{name}_turn", [merged[:, m, k * P:(k + 1) * P] for m in range(NT_X) for k in range(KD)],
                   [mergedT[:, k, m * P:(m + 1) * P] for m in range(NT_X) for k in range(KD)], g.ident[:, :])
        chunks = [dict(w=w_out[:, 512 * c:512 * c + 512], width=512, k=KD, c=c,
                       lhs=[tok(mergedT, m) for m in range(NT_X)]) for c in range(2)]

        def keep(s, block, work):
            @block.vector
            def _(dve):
                for t, chunk, m, ps in work:
                    dve.wait_ge(s["tile"], t + 1)
                    nc.vector.tensor_copy(mix[:, m, 512 * chunk["c"]:512 * chunk["c"] + 512], ps).then_inc(s["free"], 1)

        token_gemm_stage(nc, f"{name}_out", chunks, slots, keep)


N_EXP = 32
TOP_K = 4
SLOTS = P
MAX_BLOCKS = 48
LISTED = 50
LIMIT, ALPHA = 7.0, 1.702


def route_stage(nc, d, g, hT, ones, weights, xn, rows, weight, slot_of, token_of, table, n_blocks):
    with ExitStack() as held:
        def sb(name, shape, dtype=F32):
            return held.enter_context(nc.sbuf_tensor(name, shape, dtype))

        w = sb("router_w", [P, KD, N_EXP])
        bias = sb("router_b", [P, N_EXP])
        iota = sb("router_iota", [P, P])
        part = sb("router_part", [P, 1])
        before = sb("router_before", [P, P])
        logits = sb("router_logits", [P, NT_X, N_EXP])
        top = sb("router_top", [P, NT_X, 8])
        index = sb("router_index", [P, NT_X, 8], U32)
        indexf = sb("router_indexf", [P, NT_X, 8])
        number = sb("router_number", [P, NT_X, N_EXP])
        at_choice = sb("router_at_choice", [P, TOP_K, N_EXP])
        slotf = sb("router_slotf", [P, NT_X, TOP_K])
        place, home = (sb(f"router_{x}", [P, NT_X, TOP_K]) for x in ("place", "home"))
        in_block = sb("router_in_block", [P, NT_X * TOP_K, SLOTS])
        of_block = sb("router_of_block", [P, NT_X * TOP_K, LISTED])
        tokenf = sb("router_tokenf", [P, NT_X])
        negtop = sb("router_negtop", [P, NT_X])
        total = sb("router_total", [P, NT_X])
        chosen = sb("router_chosen", [P, NT_X, N_EXP])
        blocks, ends, starts, tmp = (sb(f"router_{x}", [P, N_EXP]) for x in ("blocks", "ends", "starts", "tmp"))
        expert = sb("router_expert", [P, 4])
        experti = sb("router_experti", [P, 1], I32)
        ps = held.enter_context(nc.psum_tensor("router_ps", [P, NT_X, 512], F32))
        ps_r = held.enter_context(nc.psum_tensor("router_rank", [P, 1, 512], F32))
        with stage(nc, "route", "loaded", "logits", "negtop", "weight", "chosen", "rank", "chain", "expert",
                   "table", "slots", "hot", "listed", "rows") as (s, block):
            @block.sync
            def _(sp):
                sp.dma_start(w[:, :, :], d["w_router"].rearrange("(k p) e -> p k e", p=P)).then_inc(s["loaded"], 16)
                sp.dma_start(bias[:, :], row_to_all(d["b_router"], N_EXP)).then_inc(s["loaded"], 16)
                sp.dma_start(iota[:, :], row_to_all(d["iota"], P)).then_inc(s["loaded"], 16)
                sp.dma_start(part[:, :], d["iota"].rearrange("(p a) -> p a", a=1)).then_inc(s["loaded"], 16)
                sp.dma_start(before[:, :], d["before"]).then_inc(s["loaded"], 16)
                sp.wait_ge(s["expert"], 2)
                sp.dma_start(table[0:1, :], experti[:, 0:1]).then_inc(s["table"], 16)
                sp.wait_ge(s["table"], 16)
                first = sp.value_load(table[0:1, 0:1], min_val=0, max_val=N_EXP - 1)
                for what in range(3 * GROUPS):
                    weights.load(sp, first, what, "a")

            @block.tensor
            def _(pe):
                pe.wait_ge(s["loaded"], 80)
                for m in range(NT_X):
                    for k in range(KD):
                        last = nc.tensor.matmul(ps[:, m, 0:N_EXP], hT[:, k, m * P:(m + 1) * P], w[:, k, :],
                                                start=(k == 0), stop=(k == KD - 1))
                    last.then_inc(s["logits"], 1)
                pe.wait_ge(s["chosen"], NT_X)
                for m in range(NT_X):
                    for q in range(m):
                        nc.tensor.matmul(ps_r[:, 0, m * N_EXP:(m + 1) * N_EXP], ones, chosen[:, q, :],
                                         start=(m == 0), stop=False, skip_group_check=True)
                    nc.tensor.matmul(ps_r[:, 0, m * N_EXP:(m + 1) * N_EXP], before[:, :], chosen[:, m, :],
                                     start=(m == 0), stop=True, skip_group_check=True)
                for q in range(NT_X):
                    last = nc.tensor.matmul(ps_r[:, 0, 128:160], ones, chosen[:, q, :], start=False,
                                            stop=(q == NT_X - 1), skip_group_check=True)
                last.then_inc(s["rank"], 1)
                pe.wait_ge(s["hot"], 1)
                for c in range(NT_X * TOP_K):
                    last = nc.tensor.matmul(ps[:, 0, 0:LISTED], in_block[:, c, :], of_block[:, c, :], start=(c == 0),
                                            stop=(c == NT_X * TOP_K - 1))
                last.then_inc(s["listed"], 1)

            @block.scalar
            def _(act):
                act.dma_start(rows.rearrange("(m p) n -> p m n", p=P), xn[:, :, :]).then_inc(s["rows"], 16)
                for m in range(NT_X):
                    act.wait_ge(s["negtop"], m + 1)
                    nc.scalar.activation(weight[:, m, :], top[:, m, 0:TOP_K], ACT.Exp, bias=negtop[:, m:m + 1],
                                         accum_out=total[:, m:m + 1]).then_inc(s["weight"], 1)
                act.wait_ge(s["rows"], 16)

            @block.vector
            def _(dve):
                step = chained(dve, s["chain"])
                dve.wait_ge(s["loaded"], 80)
                for m in range(NT_X):
                    dve.wait_ge(s["logits"], m + 1)
                    step(nc.vector.tensor_tensor(logits[:, m, :], ps[:, m, 0:N_EXP], bias[:, :], ALU.add))
                    step(nc.vector.max(top[:, m, :], logits[:, m, :]))
                    nc.vector.tensor_scalar(negtop[:, m:m + 1], top[:, m, 0:1], -1.0, None, ALU.mult) \
                        .then_inc(s["negtop"], 1)
                    step(nc.vector.max_index(index[:, m, :], top[:, m, :], logits[:, m, :]))
                    step(nc.vector.tensor_copy(indexf[:, m, :], index[:, m, :]))
                dve.wait_ge(s["weight"], NT_X)
                step(nc.vector.reciprocal(total[:, :], total[:, :]))
                for m in range(NT_X):
                    step(nc.vector.tensor_scalar(weight[:, m, :], weight[:, m, :], total[:, m:m + 1], None, ALU.mult))
                    for j in range(TOP_K):
                        if j == 0:
                            step(nc.vector.tensor_scalar(chosen[:, m, :], iota[:, 0:N_EXP], indexf[:, m, 0:1], None,
                                                         ALU.is_equal))
                        elif j < TOP_K - 1:
                            step(nc.vector.scalar_tensor_tensor(chosen[:, m, :], iota[:, 0:N_EXP],
                                                                indexf[:, m, j:j + 1], chosen[:, m, :],
                                                                ALU.is_equal, ALU.add))
                        else:
                            nc.vector.scalar_tensor_tensor(chosen[:, m, :], iota[:, 0:N_EXP], indexf[:, m, j:j + 1],
                                                           chosen[:, m, :], ALU.is_equal, ALU.add) \
                                .then_inc(s["chosen"], 1)
                dve.wait_ge(s["chosen"], NT_X)
                dve.wait_ge(s["rank"], 1)
                counts = ps_r[:, 0, 128:160]
                step(nc.vector.tensor_scalar(blocks[:, :], counts, 0.0, None, ALU.is_gt))
                for j in range(1, SEQ // SLOTS):
                    step(nc.vector.scalar_tensor_tensor(blocks[:, :], counts, float(SLOTS * j), blocks[:, :],
                                                        ALU.is_gt, ALU.add))
                step(nc.vector.memset(tmp[:, :], 1.0))
                step(nc.vector.tensor_tensor_scan(ends[:, :], tmp[:, :], blocks[:, :], 0.0, ALU.mult, ALU.add))
                step(nc.vector.tensor_tensor(starts[:, :], ends[:, :], blocks[:, :], ALU.subtract))
                step(nc.vector.tensor_scalar(tmp[:, :], ends[:, :], part[:, 0:1], None, ALU.is_le))
                step(nc.vector.tensor_reduce(expert[:, 0:1], tmp[:, :], AX.X, ALU.add))
                step(nc.vector.tensor_scalar(expert[:, 0:1], expert[:, 0:1], float(N_EXP - 1), None, ALU.min))
                nc.vector.tensor_copy(experti[:, :], expert[:, 0:1]).then_inc(s["expert"], 1)
                step(nc.vector.tensor_scalar(tmp[:, :], iota[:, 0:N_EXP], 2.0, None, ALU.mult))
                step(nc.vector.tensor_scalar(tmp[:, :], tmp[:, :], ends[:, N_EXP - 1:N_EXP], None, ALU.is_lt))
                step(nc.vector.tensor_reduce(expert[:, 1:2], tmp[:, :], AX.X, ALU.add))
                nc.vector.tensor_copy(n_blocks[0:1, :], expert[0:1, 1:2]).then_inc(s["expert"], 1)
                step(nc.vector.tensor_scalar(starts[:, :], starts[:, :], float(SLOTS), float(SLOTS), ALU.mult, ALU.add))
                for m in range(NT_X):
                    step(nc.vector.tensor_tensor(tmp[:, :], ps_r[:, 0, m * N_EXP:(m + 1) * N_EXP], starts[:, :], ALU.add))
                    step(nc.vector.tensor_tensor(number[:, m, :], tmp[:, :], chosen[:, m, :], ALU.mult))
                    step(nc.vector.tensor_tensor(at_choice[:, :, :],
                                                 iota[:, 0:N_EXP].unsqueeze(1).to_broadcast([P, TOP_K, N_EXP]),
                                                 indexf[:, m, 0:TOP_K].unsqueeze(2).to_broadcast([P, TOP_K, N_EXP]),
                                                 ALU.is_equal))
                    step(nc.vector.tensor_tensor(at_choice[:, :, :], at_choice[:, :, :],
                                                 number[:, m, :].unsqueeze(1).to_broadcast([P, TOP_K, N_EXP]), ALU.mult))
                    step(nc.vector.tensor_reduce(slotf[:, m, :], at_choice[:, :, :], AX.X, ALU.add))
                    step(nc.vector.tensor_scalar(tokenf[:, m:m + 1], part[:, 0:1], float(P * m), None, ALU.add))
                step(nc.vector.tensor_scalar(home[:, :, :], slotf[:, :, :], 1.0 / SLOTS, -(SLOTS - 1) / (2.0 * SLOTS),
                                             ALU.mult, ALU.add))
                step(nc.vector.tensor_scalar(home[:, :, :], home[:, :, :], ROUND, None, ALU.add))
                step(nc.vector.tensor_scalar(home[:, :, :], home[:, :, :], -ROUND, None, ALU.add))
                step(nc.vector.scalar_tensor_tensor(place[:, :, :], home[:, :, :], -float(SLOTS), slotf[:, :, :],
                                                    ALU.mult, ALU.add))
                step(nc.vector.tensor_scalar(home[:, :, :], home[:, :, :], -1.0, None, ALU.add))
                step(nc.vector.tensor_tensor(in_block[:, :, :],
                                             iota[:, :].unsqueeze(1).to_broadcast([P, NT_X * TOP_K, SLOTS]),
                                             place[:, :, :].rearrange("p m j -> p (m j)").unsqueeze(2)
                                             .to_broadcast([P, NT_X * TOP_K, SLOTS]), ALU.is_equal))
                step(nc.vector.tensor_tensor(of_block[:, :, :],
                                             iota[:, 0:LISTED].unsqueeze(1).to_broadcast([P, NT_X * TOP_K, LISTED]),
                                             home[:, :, :].rearrange("p m j -> p (m j)").unsqueeze(2)
                                             .to_broadcast([P, NT_X * TOP_K, LISTED]), ALU.is_equal))
                for m in range(NT_X):
                    part_of = of_block[:, m * TOP_K:(m + 1) * TOP_K, :]
                    step(nc.vector.tensor_scalar(part_of, part_of, tokenf[:, m:m + 1], None, ALU.mult))
                nc.vector.tensor_copy(slot_of[:, :, :], slotf[:, :, :]).then_inc(s["hot"], 1)
                dve.wait_ge(s["listed"], 1)
                nc.vector.tensor_copy(token_of[:, :], ps[:, 0, 0:LISTED]).then_inc(s["slots"], 1)


def spread(row, n):
    return row.unsqueeze(0).to_broadcast([P, n])


GROUPS = 4


class ExpertWeights:

    def __init__(self, nc, d, held):
        self.gu = held.enter_context(nc.sbuf_tensor("w_gu", [P, KD, 2 * D], F32))
        self.dn = held.enter_context(nc.sbuf_tensor("w_dn", [P, KD, D], F32))
        self.arrived = {p: [held.enter_context(nc.semaphore(f"w_{p}{i}")) for i in range(3 * GROUPS)] for p in "ab"}
        self.gu_v = d["w_gate_up"].rearrange("e (k p) n -> e p k n", p=P)
        self.dn_v = d["w_down"].rearrange("e (k p) n -> e p k n", p=P)

    def load(self, sp, expert, what, parity):
        k = slice(2 * (what % 4), 2 * (what % 4) + 2)
        if what < 8:
            half = slice(D * (what // 4), D * (what // 4) + D)
            to, src = self.gu[:, k, half], self.gu_v[expert][:, k, half]
        else:
            to, src = self.dn[:, k, :], self.dn_v[expert][:, k, :]
        sp.dma_start(to, src).then_inc(self.arrived[parity][what], 16)


def experts(nc, d, g, weights, rows, gain, shift, weight, slot_of, token_of, table, n_blocks, y):
    ident = g.ident[:, :]
    gu, dn, arrived, load = weights.gu, weights.dn, weights.arrived, weights.load
    slot_rows = nc.dram_tensor("slot_rows", ((MAX_BLOCKS + 1) * SLOTS, D), I32).ap()
    with ExitStack() as held:
        def sb(name, shape, dtype=F32):
            return held.enter_context(nc.sbuf_tensor(name, shape, dtype))

        b_gu = sb("b_gu", [P, 2 * D])
        b_dn = {p: sb(f"b_dn_{p}", [P, D]) for p in "ab"}
        tokens = sb("tokens", [P, 1], U32)
        xg = sb("xg", [P, D])
        xgT = sb("xgT", [P, KD, SLOTS])
        biased = sb("biased", [P, 512])
        ga, up, sg = (sb(x, [P, 256]) for x in ("ga", "up", "sg"))
        act_sb = sb("act_sb", [P, D])
        actT = sb("actT", [P, KD, SLOTS])
        yb = sb("yb", [P, D])
        ps_dn = held.enter_context(nc.psum_tensor("moe_down_ps", [P, 2, 512], F32))
        gathered = held.enter_context(nc.semaphore("gathered"))
        stored = {p: held.enter_context(nc.semaphore(f"rows_stored_{p}")) for p in "ab"}
        def turn_gathered(ps, half, signal):
            for k in range(4):
                last = nc.tensor.transpose(ps[:, 1 - half, k * P:(k + 1) * P],
                                           xg[:, (4 * half + k) * P:(4 * half + k + 1) * P], ident)
            last.then_inc(signal, 1)

        def modulate(ps, half, signal):
            for k in range(4 * half, 4 * half + 4):
                last = nc.scalar.activation(xgT[:, k, :], ps[:, 1 - half, (k % 4) * P:(k % 4 + 1) * P], ACT.Identity,
                                            scale=gain[:, k:k + 1], bias=shift[:, k:k + 1])
            last.then_inc(signal, 1)

        def keep_rows(dve, before, signal):
            dve.wait_ge(stored[before], 32)
            for n in range(2):
                nc.vector.tensor_tensor(yb[:, 512 * n:512 * n + 512], ps_dn[:, n, :],
                                        b_dn[before][:, 512 * n:512 * n + 512], ALU.add).then_inc(signal, 1)

        def store_rows(act, v, signal, parity):
            for n in range(2):
                act.wait_ge(signal, n + 1)
                act.dma_start(slot_rows[bass.ds(v * SLOTS, SLOTS), 512 * n:512 * n + 512],
                              yb[:, 512 * n:512 * n + 512].bitcast(I32)).then_inc(stored[parity], 16)

        def expert_block(parity, other, v):
            w_here = arrived[parity]
            with nc.psum_tensor(f"moe_ps_{parity}", [P, 6, 512], F32) as ps, \
                    stage(nc, f"moe_{parity}", "bias", "tokens", "gu_used", "chain", "ga", "sig", "acted", "turned", "actT",
                          "dn_used", "yb", "xg_turned", "xgT", clear=w_here + [stored[other]], pool_dma=(gathered,)) as (s, block):
                @block.sync
                def _(sp):
                    after = sp.value_load(table[0:1, bass.ds(v + 1, 1)], min_val=0, max_val=N_EXP - 1)
                    for what in range(3 * GROUPS):
                        if what < 2 * GROUPS:
                            sp.wait_ge(s["gu_used"], what + 1)
                        else:
                            sp.wait_ge(s["dn_used"], what - 2 * GROUPS + 1)
                        load(sp, after, what, other)

                @block.gpsimd
                def _(pool):
                    pool.wait_ge(s["tokens"], 1)
                    nc.gpsimd.indirect_dma_start(xg[:, :], None, rows,
                                                 bass.IndirectOffsetOnAxis(ap=tokens[:, 0:1], axis=0)) \
                        .then_inc(gathered, 16)
                    pool.wait_ge(gathered, 16)

                @block.tensor
                def _(pe):
                    for half in range(2):
                        for k in range(KD):
                            if k % 2 == 0:
                                pe.wait_ge(w_here[half * GROUPS + k // 2], 16)
                            for n in range(2):
                                at = D * half + 512 * n
                                last = nc.tensor.matmul(ps[:, 2 + 2 * half + n, :], xgT[:, k, :], gu[:, k, at:at + 512],
                                                        start=(k == 0), stop=(k == KD - 1))
                            if k % 2:
                                last.then_inc(s["gu_used"], 1)

                    def turn_act(half):
                        pe.wait_ge(s["acted"], 2 * half + 2)
                        for k in range(4):
                            last = nc.tensor.transpose(ps[:, half, k * P:(k + 1) * P],
                                                       act_sb[:, (4 * half + k) * P:(4 * half + k + 1) * P], ident)
                        last.then_inc(s["turned"], 1)

                    def down(half):
                        pe.wait_ge(s["actT"], half + 1)
                        for k in range(4 * half, 4 * half + 4):
                            if k % 2 == 0:
                                pe.wait_ge(w_here[2 * GROUPS + k // 2], 16)
                            for n in range(2):
                                last = nc.tensor.matmul(ps_dn[:, n, :], actT[:, k, :], dn[:, k, 512 * n:512 * n + 512],
                                                        start=(k == 0), stop=(k == KD - 1))
                            if k % 2:
                                last.then_inc(s["dn_used"], 1)

                    turn_act(0)
                    pe.wait_ge(gathered, 16)
                    turn_gathered(ps, 0, s["xg_turned"])
                    pe.wait_ge(s["yb"], 2)
                    down(0)
                    pe.wait_ge(s["xgT"], 1)
                    turn_act(1)
                    turn_gathered(ps, 1, s["xg_turned"])
                    down(1)

                @block.scalar
                def _(act):
                    here = act.value_load(table[0:1, bass.ds(v, 1)], min_val=0, max_val=N_EXP - 1)
                    act.dma_start(b_gu[:, :], spread(d["b_gate_up"][here], 2 * D)).then_inc(s["bias"], 16)
                    act.dma_start(b_dn[parity][:, :], spread(d["b_down"][here], D)).then_inc(s["bias"], 16)
                    store_rows(act, v, s["yb"], parity)
                    for n in range(2):
                        act.wait_ge(s["ga"], n + 1)
                        nc.scalar.activation(sg[:, :], ga[:, :], ACT.Sigmoid, scale=ALPHA).then_inc(s["sig"], 1)

                    def keep_turned(half):
                        act.wait_ge(s["turned"], half + 1)
                        nc.scalar.copy(actT[:, 4 * half:4 * half + 4, :],
                                       ps[:, half, :].rearrange("p (k t) -> p k t", k=4)).then_inc(s["actT"], 1)

                    keep_turned(0)
                    act.wait_ge(s["ga"], 3)
                    nc.scalar.activation(sg[:, :], ga[:, :], ACT.Sigmoid, scale=ALPHA).then_inc(s["sig"], 1)
                    act.wait_ge(s["ga"], 4)
                    nc.scalar.activation(sg[:, :], ga[:, :], ACT.Sigmoid, scale=ALPHA).then_inc(s["sig"], 1)
                    act.wait_ge(s["xg_turned"], 1)
                    modulate(ps, 0, s["xgT"])
                    keep_turned(1)
                    act.wait_ge(s["xg_turned"], 2)
                    modulate(ps, 1, s["xgT"])

                @block.vector
                def _(dve):
                    step = chained(dve, s["chain"])
                    nc.vector.tensor_copy(tokens[:, :], token_of[:, bass.ds(v + 1, 1)]).then_inc(s["tokens"], 1)
                    keep_rows(dve, other, s["yb"])
                    dve.wait_ge(s["bias"], 32)
                    for n in range(4):
                        dve.wait_ge(s["gu_used"], GROUPS * (n // 2 + 1))
                        pairs = biased[:, :].rearrange("p (c a) -> p c a", a=2)
                        step(nc.vector.tensor_tensor(biased[:, :], ps[:, 2 + n, :], b_gu[:, 512 * n:512 * n + 512], ALU.add))
                        nc.vector.tensor_scalar(ga[:, :], pairs[:, :, 0], LIMIT, None, ALU.min).then_inc(s["ga"], 1)
                        step(nc.vector.tensor_scalar(up[:, :], pairs[:, :, 1], LIMIT, -LIMIT, ALU.min, ALU.max))
                        dve.wait_ge(s["ga"], n + 1)
                        step(nc.vector.scalar_tensor_tensor(up[:, :], up[:, :], 1.0, ga[:, :], ALU.add, ALU.mult))
                        dve.wait_ge(s["sig"], n + 1)
                        nc.vector.tensor_tensor(act_sb[:, 256 * n:256 * n + 256], up[:, :], sg[:, :],
                                                ALU.mult).then_inc(s["acted"], 1)
                        dve.wait_ge(s["acted"], n + 1)

        with nc.psum_tensor("moe_ps_start", [P, 2, 512], F32) as ps, \
                stage(nc, "moe_start", "tokens", "zero", "xg_turned", "xgT", pool_dma=(gathered,)) as (s, block):
            @block.vector
            def _(dve):
                nc.vector.tensor_copy(tokens[:, :], token_of[:, 0:1]).then_inc(s["tokens"], 1)
                nc.vector.memset(ps_dn[:, :, :], 0.0).then_inc(s["zero"], 1)
                nc.vector.memset(b_dn["b"][:, :], 0.0).then_inc(s["zero"], 1)

            @block.gpsimd
            def _(pool):
                pool.wait_ge(s["tokens"], 1)
                nc.gpsimd.indirect_dma_start(xg[:, :], None, rows,
                                             bass.IndirectOffsetOnAxis(ap=tokens[:, 0:1], axis=0)).then_inc(gathered, 16)
                pool.wait_ge(gathered, 16)

            @block.tensor
            def _(pe):
                pe.wait_ge(gathered, 16)
                turn_gathered(ps, 0, s["xg_turned"])
                turn_gathered(ps, 1, s["xg_turned"])

            @block.scalar
            def _(act):
                for half in range(2):
                    act.wait_ge(s["xg_turned"], half + 1)
                    modulate(ps, half, s["xgT"])
                nc.scalar.copy(yb[:, 0:1], shift[:, 0:1]).then_inc(stored["b"], 32)

        turns = nc.values_load(n_blocks[0:1, 0:1], min_val=1, max_val=MAX_BLOCKS // 2)
        with nc.Fori(0, turns) as turn:
            for parity, other in ("ab", "ba"):
                expert_block(parity, other, turn * 2 + (parity == "b"))
        with stage(nc, "moe_end", "yb", clear=arrived["a"] + [stored["a"], stored["b"]]) as (s, block):
            @block.vector
            def _(dve):
                keep_rows(dve, "b", s["yb"])

            @block.scalar
            def _(act):
                store_rows(act, turns * 2, s["yb"], "a")
                act.wait_ge(stored["a"], 32)

            @block.sync
            def _(sp):
                for w in arrived["a"]:
                    sp.wait_ge(w, 16)
    combine(nc, slot_rows, weight, slot_of, y)


def combine(nc, slot_rows, weight, slot_of, y):
    n = NT_X * TOP_K
    with nc.sbuf_tensor("slot_in", [P, n, D], F32) as taken, ExitStack() as held:
        arrived = [held.enter_context(nc.semaphore(f"slot_rows_of_tile{m}")) for m in range(NT_X)]
        s, block = held.enter_context(stage(nc, "combine", "summed", pool_dma=arrived))

        @block.gpsimd
        def _(pool):
            for i in range(n):
                nc.gpsimd.indirect_dma_start(
                    taken[:, i, :].bitcast(I32), None, slot_rows,
                    bass.IndirectOffsetOnAxis(ap=slot_of[:, i // TOP_K, i % TOP_K:i % TOP_K + 1], axis=0)) \
                    .then_inc(arrived[i // TOP_K], 16)
            for m in range(NT_X):
                pool.wait_ge(arrived[m], 16 * TOP_K)

        @block.vector
        def _(dve):
            for m in range(NT_X):
                dve.wait_ge(arrived[m], 16 * TOP_K)
                for j in range(TOP_K):
                    row, w = taken[:, m * TOP_K + j, :], weight[:, m, j:j + 1]
                    if j == 0:
                        nc.vector.tensor_scalar(y[:, m, :], row, w, None, ALU.mult).then_inc(s["summed"], 1)
                    else:
                        dve.wait_ge(s["summed"], m * TOP_K + j)
                        nc.vector.scalar_tensor_tensor(y[:, m, :], row, w, y[:, m, :], ALU.mult,
                                                       ALU.add).then_inc(s["summed"], 1)


CH = 64
N_CHUNKS = NTOK // CH
SEG = 4
SEG_TOK = SEG * CH
LEVELS = 6
DECAY = float(-np.exp(np.float32(-0.5)))
GN_EPS = 64e-5
PAIR_COLS = ("b_r", "b_k", "b_v", "prev_r", "prev_k", "prev_v", "next_r", "next_k", "next_v", "w0_f", "w0_b",
             "a0_f", "a0_b", "k_k", "k_a", "r_k", "ln_w", "ln_b")
PC = {name: i for i, name in enumerate(PAIR_COLS)}


def shift_tokens(nc, step, zp, out_ctx, out_x, tmp, keep, prev, nxt):
    step(nc.vector.tensor_scalar(tmp[:, 0:769], zp[:, 1:770], keep, None, ALU.mult))
    step(nc.vector.scalar_tensor_tensor(tmp[:, 0:769], zp[:, 0:769], prev, tmp[:, 0:769], ALU.mult, ALU.add))
    nc.vector.scalar_tensor_tensor(out_ctx, zp[:, 2:258], nxt, tmp[:, 0:256], ALU.mult, ALU.add)
    step(nc.vector.scalar_tensor_tensor(out_x, zp[:, 259:771], nxt, tmp[:, 257:769], ALU.mult, ALU.add))


def channel_project(nc, name, w_dram, loads, hT, bias, finish):
    with nc.psum_tensor(f"{name}_ps", [P, 3, 1024], F32) as ps, \
            nc.sbuf_tensor(f"{name}_w", [P, KD, 384], F32) as w_sb, \
            nc.sbuf_tensor(f"{name}_padded", [P, 3, NTOK + 4], F32) as zp, \
            nc.sbuf_tensor(f"{name}_tmp", [P, NTOK + 4], F32) as tmp, \
            nc.sbuf_tensor(f"{name}_keep", [P, 3], F32) as keep, \
            stage(nc, name, "w", "made", "biased", "chain") as (s, block):
        @block.sync
        def _(sp):
            sp.dma_start(w_sb[:, :, :], w_dram).then_inc(s["w"], 16)
            for to, what in loads:
                sp.dma_start(to, what).then_inc(s["w"], 16)

        @block.tensor
        def _(pe):
            pe.wait_ge(s["w"], 16 * (1 + len(loads)))
            for i in range(3):
                for lo, n, at in ((0, CTX, 0), (CTX, SEQ, 512)):
                    for k in range(KD):
                        last = nc.tensor.matmul(ps[:, i, at:at + n], w_sb[:, k, i * P:(i + 1) * P],
                                                hT[:, k, lo:lo + n], start=(k == 0), stop=(k == KD - 1))
                last.then_inc(s["made"], 1)

        @block.scalar
        def _(act):
            for i in range(3):
                act.wait_ge(s["made"], i + 1)
                nc.scalar.activation(zp[:, i, 1:1 + CTX], ps[:, i, 0:CTX], ACT.Identity, bias=bias(i))
                nc.scalar.activation(zp[:, i, 2 + CTX:2 + NTOK], ps[:, i, 512:1024], ACT.Identity,
                                     bias=bias(i)).then_inc(s["biased"], 1)

        @block.vector
        def _(dve):
            step = chained(dve, s["chain"])
            for zero in (0, 1 + CTX, 2 + NTOK):
                step(nc.vector.memset(zp[:, :, zero:zero + 1], 0.0))
            dve.wait_ge(s["w"], 16 * (1 + len(loads)))
            finish(dve, step, s, zp, tmp, keep)


def rwkv_branch(nc, d, g, hT, rwkT):
    ident = g.ident[:, :]
    with ExitStack() as held:
        def sb(name, shape, dtype=F32):
            return held.enter_context(nc.sbuf_tensor(name, shape, dtype))

        lora = sb("lora", [P, 3, NTOK])
        segment = sb("segment", [P, NTOK])
        tri = sb("tri", [P, 2, 2, P])
        off = sb("off", [P, 2, LEVELS, P])
        heads = sb("heads", [P, 2, P])
        eps = sb("gn_eps", [P, 1])

        def lora_finish(dve, step, s, zp, tmp, keep):
            v = g.vec
            step(nc.vector.tensor_tensor(keep[:, :], v[:, VCOL["lora_mu_prev"]], v[:, VCOL["lora_mu_next"]], ALU.add))
            step(nc.vector.tensor_scalar(keep[:, :], keep[:, :], -1.0, 1.0, ALU.mult, ALU.add))
            step(nc.vector.memset(eps[:, :], GN_EPS))
            for i in range(3):
                dve.wait_ge(s["biased"], i + 1)
                p0, n0 = VCOL["lora_mu_prev"].start + i, VCOL["lora_mu_next"].start + i
                shift_tokens(nc, step, zp[:, i], lora[:, i, 0:CTX], lora[:, i, CTX:NTOK], tmp, keep[:, i:i + 1],
                             v[:, p0:p0 + 1], v[:, n0:n0 + 1])

        b0 = VCOL["lora_b_in"].start
        channel_project(nc, "lora_z", d["w_lora_in"],
                        [(segment[:, :], d["segment"]), (tri[:, :, :, :], d["tri"]), (off[:, :, :, :], d["off"]), (heads[:, :, :], d["heads"])],
                        hT, lambda i: g.vec[:, b0 + i:b0 + i + 1], lora_finish)
        with stage(nc, "lora_act", "done") as (s, block):
            @block.scalar
            def _(act):
                nc.scalar.activation(lora[:, 0, :], lora[:, 0, :], ACT.Tanh).then_inc(s["done"], 1)
                nc.scalar.activation(lora[:, 2, :], lora[:, 2, :], ACT.Sigmoid).then_inc(s["done"], 1)

        f = {n: sb(f"f_{n}", [P, NTOK]) for n in
             ("r", "k", "v", "a", "k0", "k1", "b0", "b1", "excl0", "excl1", "incl0", "incl1", "neg0", "neg1",
              "tail0", "tail1")}
        cols = sb("pair_cols", [P, len(PAIR_COLS)])
        low = sb("pair_low", [P, 3, P])
        bonus = sb("bonus", [P, SEQ])
        gate = sb("gate", [P, SEQ])
        total = sb("total_decay", [P, 2, N_CHUNKS])
        y = sb("y", [P, SEQ])
        state = sb("state", [P, 2, 2, P])
        seg = {n: sb(f"bd_{n}", [P, 2, SEG, P]) for n in ("b", "k", "bt", "kt", "v")}
        seg["ar"] = sb("bd_ar", [P, 2, SEG, 2, P])
        with stage(nc, "bd_zero", "done") as (s, block):
            @block.gpsimd
            def _(pool):
                for t in seg.values():
                    nc.gpsimd.memset(t[:], 0.0).then_inc(s["done"], 1)

        with nc.Fori(0, 4) as pair:
            def pair_finish(dve, step, s, zp, tmp, keep):
                step(nc.vector.tensor_tensor(keep[:, :], cols[:, 3:6], cols[:, 6:9], ALU.add))
                step(nc.vector.tensor_scalar(keep[:, :], keep[:, :], -1.0, 1.0, ALU.mult, ALU.add))
                for i, n in enumerate("rkv"):
                    dve.wait_ge(s["biased"], i + 1)
                    shift_tokens(nc, step, zp[:, i], f[n][:, 0:CTX], f[n][:, CTX:NTOK], tmp, keep[:, i:i + 1],
                                 cols[:, 3 + i:4 + i], cols[:, 6 + i:7 + i])

            channel_project(nc, "pair_z", d["w_rkv"][pair],
                            [(cols[:, :], d["pair_cols"][pair]), (low[:, :, :], d["pair_low"][pair])],
                            hT, lambda i: cols[:, i:i + 1], pair_finish)
            pair_features(nc, g, f, cols, low, lora, heads, segment, bonus, gate, total)
            with stage(nc, "state0", "done") as (s, block):
                @block.gpsimd
                def _(pool):
                    nc.gpsimd.memset(state[:, :, 0, :], 0.0).then_inc(s["done"], 1)
            for n in range(3):
                pair_segment(nc, g, n, f, seg, tri, off, total, state, y)
            pair_output(nc, g, pair, y, bonus, gate, cols, heads, eps, rwkT)


def pair_features(nc, g, f, cols, low, lora, heads, segment, bonus, gate, total):
    def col(n):
        return cols[:, PC[n]:PC[n] + 1]

    halves = ((0, 512), (512, 256))
    with ExitStack() as held:
        ps = held.enter_context(nc.psum_tensor("feat_ps", [P, 4, 1024], F32))
        one_ka = held.enter_context(nc.sbuf_tensor("one_ka", [P, 1], F32))
        t1 = held.enter_context(nc.sbuf_tensor("feat_t1", [P, NTOK], F32))
        t2 = held.enter_context(nc.sbuf_tensor("feat_t2", [P, SEQ], F32))
        sg = [held.enter_context(nc.sbuf_tensor(f"feat_sg{i}", [P, NTOK], F32)) for i in range(2)]
        with stage(nc, "feat", "low", "rates", "squares", "sums", "rooted", "chain", "rk", "bonus", "gate", "gated",
                   "sums_in", "prep", "exped") as (s, block):
            @block.tensor
            def _(pe):
                for q in range(4):
                    rows = slice(64 * (q % 2), 64 * (q % 2) + 64)
                    for at, n in halves:
                        last = nc.tensor.matmul(ps[:, q, at:at + n], low[rows, q // 2, :],
                                                lora[rows, q // 2, at:at + n], start=True, stop=True)
                    last.then_inc(s["low"], 1)
                pe.wait_ge(s["rates"], 2)
                pe.wait_ge(s["squares"], 1)
                for at, n in halves:
                    last = nc.tensor.matmul(ps[:, 0, at:at + n], heads[:, 0, :], t1[:, at:at + n], start=True, stop=True)
                last.then_inc(s["sums"], 1)
                nc.tensor.matmul(ps[:, 1, 0:SEQ], low[:, 2, :], lora[:, 2, CTX:NTOK], start=True,
                                 stop=True).then_inc(s["gate"], 1)
                pe.wait_ge(s["rates"], 4)
                pe.wait_ge(s["rk"], 1)
                nc.tensor.matmul(ps[:, 2, 0:SEQ], heads[:, 0, :], t2[:, :], start=True, stop=True).then_inc(s["bonus"], 1)

            @block.scalar
            def _(act):
                rate = (sg[0], sg[1], f["b0"], f["b1"])
                for q, (to, bias) in enumerate(zip(rate, ("w0_f", "w0_b", "a0_f", "a0_b"))):
                    act.wait_ge(s["low"], q + 1)
                    nc.scalar.activation(to[:, :], ps[:, q, 0:NTOK], ACT.Sigmoid, bias=col(bias)).then_inc(s["rates"], 1)
                act.wait_ge(s["gate"], 1)
                nc.scalar.copy(gate[:, :], ps[:, 1, 0:SEQ]).then_inc(s["gated"], 1)
                act.wait_ge(s["sums"], 1)
                nc.scalar.activation(t1[:, :], ps[:, 0, 0:NTOK], ACT.Sqrt).then_inc(s["rooted"], 1)
                for i in range(2):
                    act.wait_ge(s["prep"], 1 + i)
                    for to, sign in ((f["neg%d" % i], -1.0),):
                        nc.scalar.activation(to[:, :], f["incl%d" % i][:, :], ACT.Exp, scale=-DECAY).then_inc(s["exped"], 1)
                    act.wait_ge(s["exped"], 4 * i + 1)
                    for n in ("incl%d" % i, "excl%d" % i, "tail%d" % i):
                        nc.scalar.activation(f[n][:, :], f[n][:, :], ACT.Exp, scale=DECAY).then_inc(s["exped"], 1)
                    nc.scalar.activation(total[:, i, :], total[:, i, :], ACT.Exp, scale=DECAY)

            @block.vector
            def _(dve):
                step = chained(dve, s["chain"])
                step(nc.vector.tensor_scalar(one_ka[:, :], col("k_a"), -1.0, 1.0, ALU.mult, ALU.add))
                step(nc.vector.tensor_scalar(f["a"][:, :], f["k"][:, :], col("k_k"), None, ALU.mult))
                nc.vector.tensor_tensor(t1[:, :], f["a"][:, :], f["a"][:, :], ALU.mult).then_inc(s["squares"], 1)
                for i in range(2):
                    dve.wait_ge(s["rates"], i + 1)
                    cp = f["incl0" if i == 0 else "tail1"]
                    step(nc.vector.tensor_tensor_scan(cp[:, :], segment[:, :], sg[i][:, :], 0.0, ALU.mult, ALU.add))
                    cp3 = cp[:, :].rearrange("p (c t) -> p c t", t=CH)
                    end = cp3[:, :, CH - 1:CH]
                    step(nc.vector.tensor_copy(total[:, i, :].unsqueeze(2), end))
                    tot = total[:, i, :].unsqueeze(2).to_broadcast([P, N_CHUNKS, CH])
                    rest = f["tail0" if i == 0 else "excl1"]
                    step(nc.vector.tensor_tensor(rest[:, :].rearrange("p (c t) -> p c t", t=CH), tot, cp3, ALU.subtract))
                    if i == 0:
                        nc.vector.tensor_tensor(f["excl0"][:, :], cp[:, :], sg[0][:, :], ALU.subtract).then_inc(s["prep"], 1)
                    else:
                        step(nc.vector.tensor_tensor(f["incl1"][:, :], rest[:, :], sg[1][:, :], ALU.add))
                        nc.vector.tensor_tensor(cp[:, :], cp[:, :], sg[1][:, :], ALU.subtract).then_inc(s["prep"], 1)
                dve.wait_ge(s["rates"], 4)
                for i in range(2):
                    kd = f["k%d" % i]
                    step(nc.vector.tensor_scalar(kd[:, :], f["b%d" % i][:, :], col("k_a"), one_ka[:, :], ALU.mult, ALU.add))
                    step(nc.vector.tensor_tensor(kd[:, :], kd[:, :], f["k"][:, :], ALU.mult))
                x = slice(CTX, NTOK)
                step(nc.vector.tensor_tensor(t2[:, :], f["k0"][:, x], f["k1"][:, x], ALU.add))
                nc.vector.scalar_tensor_tensor(t2[:, :], t2[:, :], col("r_k"), f["r"][:, x], ALU.mult,
                                               ALU.mult).then_inc(s["rk"], 1)
                dve.wait_ge(s["rooted"], 1)
                step(nc.vector.tensor_scalar(t1[:, :], t1[:, :], 1e-12, None, ALU.max))
                step(nc.vector.reciprocal(t1[:, :], t1[:, :]))
                step(nc.vector.tensor_tensor(f["a"][:, :], f["a"][:, :], t1[:, :], ALU.mult))
                for i in range(2):
                    step(nc.vector.tensor_tensor(f["b%d" % i][:, :], f["b%d" % i][:, :], f["a"][:, :], ALU.mult))
                step(nc.vector.tensor_scalar(f["a"][:, :], f["a"][:, :], -1.0, None, ALU.mult))
                dve.wait_ge(s["bonus"], 1)
                nc.vector.tensor_tensor(bonus[:, :], f["v"][:, x], ps[:, 2, 0:SEQ], ALU.mult).then_inc(s["sums_in"], 1)


def segment_tokens(n, direction):
    return (0, (CTX, CTX + SEG_TOK)[direction], (CTX + SEG_TOK, CTX)[direction])[n]


def pair_segment(nc, g, n, f, seg, tri, off, total, state, y):
    ident = g.ident[:, :]
    has_y = n > 0
    start = [segment_tokens(n, i) for i in range(2)]
    last_level = LEVELS - 1
    with ExitStack() as held:
        def sb(name, shape):
            return held.enter_context(nc.sbuf_tensor(f"{name}_{n}", shape, F32))

        gb, gk = sb("gb", [P, 2, SEG, 2, P]), sb("gk", [P, 2, SEG, 2, P])
        aoff = sb("aoff", [P, 2, 2, SEG, P])
        tmat, qmat, wmat = (sb(x, [P, 2, SEG, P]) for x in ("tmat", "qmat", "wmat"))
        btT, ktT, vbd = (sb(x, [P, 2, SEG, P]) for x in ("btT", "ktT", "vbd"))
        xs, us = sb("xs", [P, 2, P]), sb("us", [P, 2, P])
        with nc.psum_tensor(f"seg_ps{n}", [P, 2, 4, 512], F32) as ps, \
                stage(nc, f"seg{n}", "built0", "built1", "v0", "v1", "made0", "made1", "dve0", "dve1", "act0", "act1",
                      "off0", "off1", "t_in", "chain", "q_in") as (s, block):
            built, vin, made = (s["built0"], s["built1"]), (s["v0"], s["v1"]), (s["made0"], s["made1"])
            out = {"dve": (s["dve0"], s["dve1"]), "act": (s["act0"], s["act1"])}
            offs = (s["off0"], s["off1"])
            jobs = [("gb0", "dve"), ("gb1", "dve"), ("gk0", "dve"), ("gk1", "dve"), ("n", "dve"), ("bt", "act"),
                    ("kt", "act"), ("v", "act")]
            for l in range(1, last_level):
                jobs += [(f"w{l}", "act"), (f"t{l}", "dve"), (f"q{l}", "act")]
            jobs += [(f"w{last_level}", "act"), (f"q{last_level}", "dve")]
            names = [j for j, _ in jobs]

            def evacuated(j):
                who = jobs[j][1]
                return who, sum(w == who for _, w in jobs[:j + 1])

            def wait_out(engine, name, i):
                who, count = evacuated(names.index(name))
                engine.wait_ge(out[who][i], count)

            arrays = [("b", "b", "neg"), ("ar0", "a", "excl"), ("ar1", "r", "incl"), ("k", "k", "neg"),
                      ("bt", "b", "tail"), ("kt", "k", "tail")]
            if not has_y:
                arrays.pop(2)
            order = [x[0] for x in arrays]

            def build(engine, ops, i):
                for n_array, (to, what, decay) in enumerate(arrays):
                    src = f[what if what in "ar" else what + str(i)]
                    dec = f[decay + str(i)]
                    for h in range(2):
                        rows = slice(64 * h, 64 * h + 64)
                        dst = seg[to][rows, i, :, 64 * h:64 * h + 64] if to[:2] != "ar" else \
                            seg["ar"][rows, i, :, int(to[2]), 64 * h:64 * h + 64]
                        cut = slice(start[i], start[i] + SEG_TOK)
                        ops.tensor_tensor(dst, src[rows, cut].rearrange("p (c t) -> p c t", t=CH),
                                          dec[rows, cut].rearrange("p (c t) -> p c t", t=CH),
                                          ALU.mult).then_inc(built[i], 1)
                        if ops is nc.gpsimd:
                            engine.wait_ge(built[i], 2 * n_array + h + 1)

            def wait_built(pe, i, *which):
                pe.wait_ge(built[i], 2 * (1 + max(order.index(w) for w in which)))

            @block.tensor
            def _(pe):
                width = 256 if has_y else P
                for j, name in enumerate(names):
                    for i in range(2):
                        bank = ps[:, i, j % 4, :]
                        if j >= 4:
                            who, count = evacuated(j - 4)
                            pe.wait_ge(out[who][i], count)
                        if name[:2] in ("gb", "gk"):
                            wait_built(pe, i, "b", "ar1" if has_y else "ar0", "k" if name[1] == "k" else "b")
                            for c2 in range(2):
                                c = 2 * int(name[2]) + c2
                                last = nc.tensor.matmul(bank[:, 256 * c2:256 * c2 + width], seg[name[1]][:, i, c, :],
                                                        seg["ar"][:, i, c, 0:width // P, :], start=True, stop=True)
                        elif name == "n":
                            for c in range(SEG):
                                last = nc.tensor.matmul(bank[:, c * P:(c + 1) * P], seg["ar"][:, i, c, 0, :],
                                                        seg["b"][:, i, c, :], start=True, stop=True)
                        elif name in ("bt", "kt", "v"):
                            if name == "v":
                                pe.wait_ge(vin[i], 2)
                            else:
                                wait_built(pe, i, name)
                            for c in range(SEG):
                                last = nc.tensor.transpose(bank[:, c * P:(c + 1) * P], seg[name][:, i, c, :], ident)
                        elif name[0] == "w":
                            l = int(name[1:])
                            pe.wait_ge(offs[i], l + 1)
                            wait_out(pe, "n" if l == 1 else f"t{l - 1}", i)
                            for c in range(SEG):
                                last = nc.tensor.matmul(bank[:, c * P:(c + 1) * P], aoff[:, i, l % 2, c, :],
                                                        tmat[:, i, c, :], start=True, stop=True)
                        elif name[0] == "t":
                            l = int(name[1:])
                            wait_out(pe, f"w{l}", i)
                            if l > 1:
                                wait_out(pe, f"q{l - 1}", i)
                            for c in range(SEG):
                                last = nc.tensor.matmul(bank[:, c * P:(c + 1) * P], qmat[:, i, c, :],
                                                        wmat[:, i, c, :], start=True, stop=True)
                        else:
                            l = int(name[1:])
                            if l < last_level:
                                wait_out(pe, f"t{l}", i)
                            else:
                                wait_out(pe, f"w{l}", i)
                                wait_out(pe, f"q{l - 1}", i)
                            for c in range(SEG):
                                if l < last_level:
                                    last = nc.tensor.transpose(bank[:, c * P:(c + 1) * P], tmat[:, i, c, :], ident)
                                else:
                                    last = nc.tensor.matmul(bank[:, c * P:(c + 1) * P], wmat[:, i, c, :],
                                                            qmat[:, i, c, :], start=True, stop=True)
                        last.then_inc(made[i], 1)

            def four(t):
                return t.unsqueeze(1).to_broadcast([P, SEG, P])

            @block.vector
            def _(dve):
                step = chained(dve, s["chain"])
                build(dve, nc.vector, 0)
                for j, (name, who) in enumerate(jobs):
                    if who != "dve":
                        continue
                    for i in range(2):
                        bank = ps[:, i, j % 4, :]
                        dve.wait_ge(made[i], j + 1)
                        if name[:2] in ("gb", "gk"):
                            to = gb if name[1] == "b" else gk
                            c = 2 * int(name[2])
                            if has_y:
                                mask = tri[:, i].rearrange("p a t -> p (a t)").unsqueeze(1).to_broadcast([P, 2, 256])
                                nc.vector.tensor_tensor(to[:, i, c:c + 2].rearrange("p c a t -> p c (a t)"),
                                                        bank.rearrange("p (c t) -> p c t", c=2), mask,
                                                        ALU.mult).then_inc(s_out(out, i), 1)
                            else:
                                mask = tri[:, i, 0, :].unsqueeze(1).to_broadcast([P, 2, P])
                                nc.vector.tensor_tensor(to[:, i, c:c + 2, 0, :],
                                                        bank.rearrange("p (c t) -> p c t", c=2)[:, :, 0:P], mask,
                                                        ALU.mult).then_inc(s_out(out, i), 1)
                        elif name == "n":
                            step(nc.vector.tensor_tensor(tmat[:, i], bank.rearrange("p (c t) -> p c t", c=SEG),
                                                         four(off[:, 1 - i, 0, :]), ALU.mult))
                            nc.vector.tensor_tensor(tmat[:, i], tmat[:, i], four(ident), ALU.add).then_inc(s_out(out, i), 1)
                        elif name[0] == "t":
                            nc.vector.tensor_tensor(tmat[:, i], bank.rearrange("p (c t) -> p c t", c=SEG), tmat[:, i],
                                                    ALU.add).then_inc(s_out(out, i), 1)
                        else:
                            nc.vector.tensor_tensor(qmat[:, i], bank.rearrange("p (c t) -> p c t", c=SEG), qmat[:, i],
                                                    ALU.add).then_inc(s_out(out, i), 1)

            @block.scalar
            def _(act):
                for i in range(2):
                    for h in range(2):
                        rows = slice(64 * h, 64 * h + 64)
                        nc.scalar.copy(seg["v"][rows, i, :, 64 * h:64 * h + 64],
                                       f["v"][rows, start[i]:start[i] + SEG_TOK].rearrange("p (c t) -> p c t", t=CH)) \
                            .then_inc(vin[i], 1)
                for j, (name, who) in enumerate(jobs):
                    if who != "act":
                        continue
                    for i in range(2):
                        act.wait_ge(made[i], j + 1)
                        to = {"bt": btT, "kt": ktT, "v": vbd}.get(name) or {"w": wmat, "q": qmat}[name[0]]
                        nc.scalar.copy(to[:, i], ps[:, i, j % 4, :].rearrange("p (c t) -> p c t", c=SEG)) \
                            .then_inc(out["act"][i], 1)

            @block.gpsimd
            def _(pool):
                build(pool, nc.gpsimd, 1)
                for i in range(2):
                    pool.wait_ge(out["dve"][i], 2)
                    nc.gpsimd.tensor_tensor(qmat[:, i], gb[:, i, :, 0, :], four(off[:, i, 0, :]), ALU.mult) \
                        .then_inc(s["t_in"], 1)
                    pool.wait_ge(s["t_in"], i + 1)
                    nc.gpsimd.tensor_tensor(qmat[:, i], qmat[:, i], four(ident), ALU.add).then_inc(offs[i], 1)
                for l in range(1, LEVELS):
                    for i in range(2):
                        if l > 2:
                            pool.wait_ge(made[i], names.index(f"w{l - 2}") + 1)
                        nc.gpsimd.tensor_tensor(aoff[:, i, l % 2], gb[:, i, :, 0, :], four(off[:, i, l, :]), ALU.mult) \
                            .then_inc(offs[i], 1)

        scan_segment(nc, n, start, seg, gb, gk, qmat, btT, ktT, vbd, xs, us, total, state, y)


def s_out(out, i):
    return out["dve"][i]


def scan_segment(nc, n, start, seg, gb, gk, qmat, btT, ktT, vbd, xs, us, total, state, y):
    has_y = n > 0
    with nc.psum_tensor(f"scan_ps{n}", [P, 2, 4, 512], F32) as ps, \
            stage(nc, f"scan{n}", "x0", "x1", "xs0", "xs1", "u0", "u1", "us0", "us1", "s0", "s1", "st0", "st1", "y0", "y1",
                  "yo0", "yo1") as (s, block):
        X, XS, U, US = (s["x0"], s["x1"]), (s["xs0"], s["xs1"]), (s["u0"], s["u1"]), (s["us0"], s["us1"])
        S_, ST, Y, YO = (s["s0"], s["s1"]), (s["st0"], s["st1"]), (s["y0"], s["y1"]), (s["yo0"], s["yo1"])

        def chunk(step_no, i):
            return step_no if i == 0 else SEG - 1 - step_no

        @block.tensor
        def _(pe):
            for q in range(SEG):
                for i in range(2):
                    c = chunk(q, i)
                    if q:
                        pe.wait_ge(ST[i], q)
                    nc.tensor.matmul(ps[:, i, 0, 0:P], gk[:, i, c, 0, :], vbd[:, i, c, :], start=True, stop=False)
                    nc.tensor.matmul(ps[:, i, 0, 0:P], seg["ar"][:, i, c, 0, :], state[:, i, q % 2, :], start=False,
                                     stop=True).then_inc(X[i], 1)
                for i in range(2):
                    c = chunk(q, i)
                    pe.wait_ge(XS[i], q + 1)
                    nc.tensor.matmul(ps[:, i, 1, 0:P], qmat[:, i, c, :], xs[:, i, :], start=True,
                                     stop=True).then_inc(U[i], 1)
                for i in range(2):
                    c = chunk(q, i)
                    nc.tensor.matmul(ps[:, i, 2, 0:P], ktT[:, i, c, :], vbd[:, i, c, :], start=True, stop=False)
                    pe.wait_ge(US[i], q + 1)
                    nc.tensor.matmul(ps[:, i, 2, 0:P], btT[:, i, c, :], us[:, i, :], start=False,
                                     stop=True).then_inc(S_[i], 1)
                if has_y:
                    for i in range(2):
                        c = chunk(q, i)
                        if q:
                            pe.wait_ge(YO[i], 2 * q)
                        nc.tensor.matmul(ps[:, i, 3, 0:P], vbd[:, i, c, :], gk[:, i, c, 1, :], start=True, stop=False)
                        nc.tensor.matmul(ps[:, i, 3, 0:P], state[:, i, q % 2, :], seg["ar"][:, i, c, 1, :], start=False,
                                         stop=False)
                        nc.tensor.matmul(ps[:, i, 3, 0:P], us[:, i, :], gb[:, i, c, 1, :], start=False,
                                         stop=True).then_inc(Y[i], 1)

        def put_y(ops, copy, i, q, signal):
            c = chunk(q, i)
            at = start[i] - CTX + c * CH
            for h in range(2):
                rows = slice(64 * h, 64 * h + 64)
                src = ps[rows, i, 3, 64 * h:64 * h + 64]
                if n == 1:
                    copy(y[rows, at:at + CH], src).then_inc(signal, 1)
                else:
                    ops.tensor_tensor(y[rows, at:at + CH], src, y[rows, at:at + CH], ALU.add).then_inc(signal, 1)

        @block.vector
        def _(dve):
            for q in range(SEG):
                dve.wait_ge(X[0], q + 1)
                if q:
                    dve.wait_ge(U[0], q)
                nc.vector.tensor_copy(xs[:, 0, :], ps[:, 0, 0, 0:P]).then_inc(XS[0], 1)
                dve.wait_ge(U[0], q + 1)
                if has_y and q:
                    dve.wait_ge(Y[0], q)
                nc.vector.tensor_copy(us[:, 0, :], ps[:, 0, 1, 0:P]).then_inc(US[0], 1)
                for i in range(2):
                    c = start[i] // CH + chunk(q, i)
                    dve.wait_ge(S_[i], q + 1)
                    if has_y and q:
                        dve.wait_ge(Y[i], q)
                    nc.vector.scalar_tensor_tensor(state[:, i, (q + 1) % 2, :], state[:, i, q % 2, :],
                                                   total[:, i, c:c + 1], ps[:, i, 2, 0:P], ALU.mult,
                                                   ALU.add).then_inc(ST[i], 1)
                if has_y:
                    for i in range(2):
                        if n == 2 or i == 0:
                            dve.wait_ge(Y[i], q + 1)
                            put_y(nc.vector, nc.vector.tensor_copy, i, q, YO[i])

        @block.scalar
        def _(act):
            for q in range(SEG):
                act.wait_ge(X[1], q + 1)
                if q:
                    act.wait_ge(U[1], q)
                nc.scalar.copy(xs[:, 1, :], ps[:, 1, 0, 0:P]).then_inc(XS[1], 1)
                act.wait_ge(U[1], q + 1)
                if has_y and q:
                    act.wait_ge(Y[1], q)
                nc.scalar.copy(us[:, 1, :], ps[:, 1, 1, 0:P]).then_inc(US[1], 1)
                if n == 1:
                    act.wait_ge(Y[1], q + 1)
                    put_y(None, nc.scalar.copy, 1, q, YO[1])


def pair_output(nc, g, pair, y, bonus, gate, cols, heads, eps, rwkT):
    with ExitStack() as held:
        t = held.enter_context(nc.sbuf_tensor("out_t", [P, SEQ], F32))
        u = held.enter_context(nc.sbuf_tensor("out_u", [P, SEQ], F32))
        ps = held.enter_context(nc.psum_tensor("out_ps", [P, 2, 512], F32))
        with stage(nc, "out", "mean", "centred", "squared", "var", "root", "chain") as (s, block):
            @block.tensor
            def _(pe):
                nc.tensor.matmul(ps[:, 0, :], heads[:, 1, :], y[:, :], start=True, stop=True).then_inc(s["mean"], 1)
                pe.wait_ge(s["squared"], 1)
                nc.tensor.matmul(ps[:, 1, :], heads[:, 1, :], t[:, :], start=True, stop=True).then_inc(s["var"], 1)

            @block.scalar
            def _(act):
                act.wait_ge(s["centred"], 1)
                nc.scalar.activation(t[:, :], y[:, :], ACT.Square).then_inc(s["squared"], 1)
                act.wait_ge(s["var"], 1)
                nc.scalar.activation(u[:, :], ps[:, 1, :], ACT.Sqrt, bias=eps[:, 0:1]).then_inc(s["root"], 1)

            @block.vector
            def _(dve):
                step = chained(dve, s["chain"])
                dve.wait_ge(s["mean"], 1)
                nc.vector.tensor_tensor(y[:, :], y[:, :], ps[:, 0, :], ALU.subtract).then_inc(s["centred"], 1)
                dve.wait_ge(s["root"], 1)
                step(nc.vector.reciprocal(u[:, :], u[:, :]))
                step(nc.vector.tensor_tensor(u[:, :], u[:, :], y[:, :], ALU.mult))
                step(nc.vector.tensor_scalar(u[:, :], u[:, :], cols[:, PC["ln_w"]:PC["ln_w"] + 1],
                                             cols[:, PC["ln_b"]:PC["ln_b"] + 1], ALU.mult, ALU.add))
                step(nc.vector.tensor_tensor(u[:, :], u[:, :], bonus[:, :], ALU.add))
                step(nc.vector.tensor_tensor(rwkT[:, bass.ds(pair, 1), :].rearrange("p a t -> p (a t)"), u[:, :],
                                             gate[:, :], ALU.mult))


NH = 8
QL, KVL, RD = 384, 256, 32
LOWW = QL + KVL + RD + NH
TWO_PI_HI, TWO_PI_MID = 6.28125, 0.0019350051879882812
TWO_PI_LO = float(2 * np.pi - TWO_PI_HI - TWO_PI_MID)



def head_norm_stage(nc, g, name, jobs):
    with ExitStack() as held:
        sq = held.enter_context(nc.sbuf_tensor(f"{name}_sq", [P, 2, 512], F32))
        tmp = held.enter_context(nc.sbuf_tensor(f"{name}_tmp", [P, 2, 512], F32))
        ss = held.enter_context(nc.sbuf_tensor(f"{name}_ss", [P, 3, len(jobs), NH], F32))
        with stage(nc, name, "set", "square", "sum", "root", "inverse", "scaled", "normed") as (s, block):
            def view(t, src):
                return t[:, 0:src.shape[1] * src.shape[2]].rearrange("p (h n) -> p h n", n=src.shape[2])

            @block.scalar
            def _(act):
                for j, (src, _, _) in enumerate(jobs):
                    if j >= 2:
                        act.wait_ge(s["sum"], j - 1)
                    nc.scalar.activation(view(sq[:, j % 2], src), src, ACT.Square).then_inc(s["square"], 1)
                act.wait_ge(s["sum"], len(jobs))
                act.wait_ge(s["set"], 1)
                for j, (src, _, _) in enumerate(jobs):
                    nc.scalar.activation(ss[:, 1, j, :], ss[:, 0, j, :], ACT.Sqrt, scale=1.0 / src.shape[2],
                                         bias=g.eps_col[:, 0:1]).then_inc(s["root"], 1)

            @block.vector
            def _(dve):
                nc.vector.memset(ss[:, 0], 1.0).then_inc(s["set"], 1)
                dve.wait_ge(s["set"], 1)
                for j, (src, _, _) in enumerate(jobs):
                    dve.wait_ge(s["square"], j + 1)
                    nc.vector.tensor_reduce(ss[:, 0, j, 0:src.shape[1]], view(sq[:, j % 2], src), AX.X,
                                            ALU.add).then_inc(s["sum"], 1)
                dve.wait_ge(s["root"], len(jobs))
                nc.vector.reciprocal(ss[:, 2], ss[:, 1]).then_inc(s["inverse"], 1)
                dve.wait_ge(s["inverse"], 1)
                for j, (src, dst, w) in enumerate(jobs):
                    h, n = src.shape[1], src.shape[2]
                    if j >= 2:
                        dve.wait_ge(s["normed"], j - 1)
                    nc.vector.tensor_tensor(view(tmp[:, j % 2], src), src,
                                            ss[:, 2, j, 0:h].unsqueeze(2).to_broadcast([P, h, n]),
                                            ALU.mult).then_inc(s["scaled"], 1)
                    dve.wait_ge(s["scaled"], j + 1)
                    nc.vector.tensor_tensor(dst, view(tmp[:, j % 2], src), w.unsqueeze(1).to_broadcast([P, h, n]),
                                            ALU.mult).then_inc(s["normed"], 1)


def second_block(nc, d, g, x, row_cols, ones, out):
    ident = g.ident[:, :]
    tiles = [x[:, m] for m in range(NT_X)]
    with ExitStack() as held:
        def sb(name, shape, dtype=F32):
            return held.enter_context(nc.sbuf_tensor(name, shape, dtype))

        hT = sb("b2_hT", [P, KD, SEQ])
        yT = [sb(f"y{i}T", [P, 4, SEQ]) for i in range(2)]
        with ExitStack() as branches:
            def bb(name, shape, dtype=F32):
                return branches.enter_context(nc.sbuf_tensor(name, shape, dtype))

            low = bb("b2_low", [P, NT_X, LOWW])
            wide = bb("b2_wide", [P, NT_X, 3, 512])
            gateT = bb("b2_gateT", [P, 2, 4, SEQ])
            norm_rows = bb("norm_rows", [P, 320])
            causal = bb("causal", [P, 2, SEQ])
            rope = bb("b2_rope", [P, 2, NT_X, 16])
            b_f = bb("b_f", [P, NH])
            project_second(nc, d, g, tiles, hT, low, wide, gateT, norm_rows, causal, b_f)
            rope_tables(nc, d, g, rope)
            mla(nc, d, g, low, gateT, norm_rows, causal, rope, yT[0])
            fox(nc, d, g, low, wide, gateT, norm_rows, causal, b_f, ones, yT[1])
        mg = sb("b2_mg", [P, NT_X, 2 * D])
        second_gates(nc, d, hT, mg)
        mix = sb("b2_mix", [P, NT_X, D])
        merge_and_out(nc, d, g, "b2m", yT, mg, (d["w_branch_a_2"], d["w_branch_b_2"]), d["w_out_2"], mix)
        row = sb("b2_row", [P, D])
        rows_stage(nc, g, "b2_rows", [row_cols[:, 2]], [row[:, :]], ones)
        with stage(nc, "last", "scaled", "added", "out") as (s, block):
            @block.vector
            def _(dve):
                for m in range(NT_X):
                    nc.vector.tensor_tensor(mix[:, m], mix[:, m], row[:, :], ALU.mult).then_inc(s["scaled"], 1)
                for m in range(NT_X):
                    dve.wait_ge(s["scaled"], m + 1)
                    nc.vector.tensor_tensor(x[:, m], x[:, m], mix[:, m], ALU.add).then_inc(s["added"], 1)

            @block.sync
            def _(sp):
                for m in range(NT_X):
                    sp.wait_ge(s["added"], m + 1)
                    sp.dma_start(out[0, m * P:(m + 1) * P, :], x[:, m]).then_inc(s["out"], 16)
                sp.wait_ge(s["out"], 16 * NT_X)


def project_second(nc, d, g, tiles, hT, low, wide, gateT, norm_rows, causal, b_f):
    with ExitStack() as held:
        def sb(name, shape, dtype=F32):
            return held.enter_context(nc.sbuf_tensor(name, shape, dtype))

        gain = sb("b2_gain", [P, KD])
        with stage(nc, "b2_gain", "done") as (s, block):
            @block.vector
            def _(dve):
                nc.vector.scalar_tensor_tensor(gain[:, :], g.ada2[:, 8:16, 0], 1.0, g.vec[:, VCOL["norm_w_2"]],
                                               ALU.add, ALU.mult).then_inc(s["done"], 1)
        with nc.sbuf_tensor("b2_xn", [P, NT_X, D], F32) as xn:
            norm_turn_stage(nc, "b2n", tiles, None, [xn[:, m] for m in range(NT_X)], hT,
                            lambda m, k: (gain[:, k:k + 1], g.ada2[:, k, 0:1]), g.eps_col[:, 0:1], g.ident[:, :])
        slots = [sb(f"b2_w{i}", [P, KD, 512]) for i in range(2)]
        sig = sb("b2_sig", [P, 2, 512])

        def tok(m):
            return lambda k: hT[:, k, m * P:(m + 1) * P]

        lhs = [tok(m) for m in range(NT_X)]
        w = d["w_in_2"]
        chunks = [dict(to="low", at=0, width=512), dict(to="low", at=512, width=LOWW - 512)]
        chunks += [dict(to="gate", at=i, width=512, rhs=lambda k: hT[:, k, :]) for i in range(2)]
        chunks += [dict(to="wide", at=i, width=512) for i in range(3)]
        at = 0
        for c in chunks:
            c.update(w=w[:, at:at + c["width"]], k=KD, lhs=lhs)
            at += c["width"]

        def evacuate(s, block, work):
            silu = [t for t, c, m, ps in work if c["to"] == "gate"]

            @block.vector
            def _(dve):
                for t, c, m, ps in work:
                    dve.wait_ge(s["tile"], t + 1)
                    if t in silu:
                        dve.wait_ge(s["step2"], silu.index(t) + 1)
                        nc.vector.tensor_tensor(gateT[:, c["at"], m, :], ps, sig[:, t % 2, :], ALU.mult).then_inc(s["free"], 1)
                    else:
                        to = wide[:, m, c["at"], :] if c["to"] == "wide" else low[:, m, c["at"]:c["at"] + c["width"]]
                        nc.vector.tensor_copy(to, ps).then_inc(s["free"], 1)

            @block.scalar
            def _(act):
                act.dma_start(norm_rows[:, :], row_to_all(d["norm_rows_2"], 320)).then_inc(s["side"], 16)
                act.dma_start(causal[:, :, :], d["causal_masks"]).then_inc(s["side"], 16)
                act.dma_start(b_f[:, :], row_to_all(d["b_f_2"], NH)).then_inc(s["side"], 16)
                act.wait_ge(s["side"], 48)
                for t, c, m, ps in work:
                    if t in silu:
                        act.wait_ge(s["tile"], t + 1)
                        if t >= silu[0] + 2:
                            act.wait_ge(s["free"], t - 1)
                        nc.scalar.activation(sig[:, t % 2, :], ps, ACT.Sigmoid).then_inc(s["step2"], 1)

        token_gemm_stage(nc, "b2p", chunks, slots, evacuate, extra=("side",))


def second_gates(nc, d, hT, mg):
    with ExitStack() as held:
        slots = [held.enter_context(nc.sbuf_tensor(f"b2g_w{i}", [P, KD, 512], F32)) for i in range(2)]

        def tok(m):
            return lambda k: hT[:, k, m * P:(m + 1) * P]

        at = LOWW + 5 * 512
        chunks = [dict(w=d["w_in_2"][:, at + 512 * c:at + 512 * c + 512], width=512, k=KD,
                       lhs=[tok(m) for m in range(NT_X)], col=512 * c) for c in range(4)]

        def evacuate(s, block, work):
            @block.scalar
            def _(act):
                for t, chunk, m, ps in work:
                    act.wait_ge(s["tile"], t + 1)
                    a = chunk["col"]
                    nc.scalar.activation(mg[:, m, a:a + 512], ps, ACT.Sigmoid).then_inc(s["free"], 1)

        token_gemm_stage(nc, "b2g", chunks, slots, evacuate)


def rope_tables(nc, d, g, rope):
    with ExitStack() as held:
        def sb(name, shape, dtype=F32):
            return held.enter_context(nc.sbuf_tensor(name, shape, dtype))

        pos, posf = sb("pos", [P, NT_X], I32), sb("posf", [P, NT_X])
        freq = sb("freq", [P, 16])
        ang, n, r, a = (sb(f"rope_{x}", [P, NT_X, 16]) for x in ("ang", "n", "r", "abs"))
        half_pi = sb("half_pi", [P, 1])
        with stage(nc, "rope2", "loaded", "chain", "angle") as (s, block):
            @block.sync
            def _(sp):
                sp.dma_start(pos[:, :], d["positions_2"]).then_inc(s["loaded"], 16)
                sp.dma_start(freq[:, :], row_to_all(d["rope_freq"], 16)).then_inc(s["loaded"], 16)

            @block.vector
            def _(dve):
                step = chained(dve, s["chain"])
                step(nc.vector.memset(half_pi[:, :], float(np.pi / 2)))
                dve.wait_ge(s["loaded"], 32)
                step(nc.vector.tensor_copy(posf[:, :], pos[:, :]))
                for m in range(NT_X):
                    step(nc.vector.tensor_scalar(ang[:, m, :], freq[:, :], posf[:, m:m + 1], None, ALU.mult))
                step(nc.vector.tensor_scalar(n[:, :, :], ang[:, :, :], float(1 / (2 * np.pi)), ROUND, ALU.mult, ALU.add))
                step(nc.vector.tensor_scalar(n[:, :, :], n[:, :, :], -ROUND, None, ALU.add))
                step(nc.vector.scalar_tensor_tensor(r[:, :, :], n[:, :, :], -TWO_PI_HI, ang[:, :, :], ALU.mult, ALU.add))
                step(nc.vector.scalar_tensor_tensor(r[:, :, :], n[:, :, :], -TWO_PI_MID, r[:, :, :], ALU.mult, ALU.add))
                step(nc.vector.scalar_tensor_tensor(r[:, :, :], n[:, :, :], -TWO_PI_LO, r[:, :, :], ALU.mult, ALU.add))
                for beyond, edge, turn in ((ALU.is_gt, np.pi, -2 * np.pi), (ALU.is_lt, -np.pi, 2 * np.pi)):
                    step(nc.vector.tensor_scalar(n[:, :, :], r[:, :, :], float(edge), None, beyond))
                    step(nc.vector.scalar_tensor_tensor(r[:, :, :], n[:, :, :], float(turn), r[:, :, :], ALU.mult, ALU.add))
                step(nc.vector.tensor_scalar(r[:, :, :], r[:, :, :], 3.1415925, -3.1415925, ALU.min, ALU.max))
                nc.vector.scalar_tensor_tensor(a[:, :, :], r[:, :, :], -1.0, r[:, :, :], ALU.mult,
                                               ALU.max).then_inc(s["angle"], 1)

            @block.scalar
            def _(act):
                act.wait_ge(s["angle"], 1)
                nc.scalar.activation(rope[:, 0], a[:, :, :], ACT.Sin, scale=-1.0, bias=half_pi[:, 0:1])
                nc.scalar.activation(rope[:, 1], r[:, :, :], ACT.Sin)


def heads_at(t, b, h):
    return t[HD * (h % 2):HD * (h % 2) + HD, h // 2, b * P:(b + 1) * P]


def mla(nc, d, g, low, gateT, norm_rows, causal, rope, yT):
    ident = g.ident[:, :]
    K = HD + RD
    with ExitStack() as held:
        def sb(name, shape, dtype=F32):
            return held.enter_context(nc.sbuf_tensor(name, shape, dtype))

        qT, kT = sb("mla_qT", [P, NH, SEQ]), sb("mla_kT", [P, NH, SEQ])
        v = sb("mla_v", [P, NT_X, 512])
        with ExitStack() as making:
            def tb(name, shape, dtype=F32):
                return making.enter_context(nc.sbuf_tensor(name, shape, dtype))

            qn, kn = tb("mla_qn", [P, NT_X, 512]), tb("mla_kn", [P, NT_X, 512])
            rr = tb("mla_rr", [P, NT_X, 9, RD])
            with ExitStack() as lowering:
                lowT = lowering.enter_context(nc.sbuf_tensor("lowT", [P, 5, SEQ], F32))
                low_norm_turn(nc, g, low, lowT)
                slots = [lowering.enter_context(nc.sbuf_tensor(f"mla_w{i}", [P, 3, 512], F32)) for i in range(2)]

                def tok(m, k0):
                    return lambda k: lowT[:, k0 + k, m * P:(m + 1) * P]

                uq, ukv = d["w_uq_2"], d["w_ukv_2"]
                chunks = [dict(w=uq[:, 0:512], width=512, k=3, lhs=[tok(m, 0) for m in range(NT_X)], to="qn"),
                          dict(w=uq[:, 512:768], width=256, k=3, lhs=[tok(m, 0) for m in range(NT_X)], to="qr"),
                          dict(w=ukv[:, 0:512], width=512, k=2, lhs=[tok(m, 3) for m in range(NT_X)], to="kn"),
                          dict(w=ukv[:, 512:1024], width=512, k=2, lhs=[tok(m, 3) for m in range(NT_X)], to="v")]

                def evacuate(s, block, work):
                    @block.vector
                    def _(dve):
                        for t, c, m, ps in work:
                            dve.wait_ge(s["tile"], t + 1)
                            if c["to"] == "qr":
                                nc.vector.tensor_copy(rr[:, m, 0:NH, :],
                                                      ps.rearrange("p (h n) -> p h n", n=RD)).then_inc(s["free"], 1)
                            else:
                                nc.vector.tensor_copy({"qn": qn, "kn": kn, "v": v}[c["to"]][:, m, :], ps) \
                                    .then_inc(s["free"], 1)

                    @block.scalar
                    def _(act):
                        for m in range(NT_X):
                            nc.scalar.copy(rr[:, m, NH, :], low[:, m, QL + KVL:QL + KVL + RD])

                token_gemm_stage(nc, "mla_up", chunks, slots, evacuate)
            qcat, kcat = tb("qcat", [P, NT_X, NH, K]), tb("kcat", [P, NT_X, NH, K])
            rn = tb("mla_rn", [P, NT_X, 9, RD])

            def heads(t, m):
                return t[:, m, :].rearrange("p (h n) -> p h n", n=HD)

            jobs = [(heads(qn, m), qcat[:, m, :, 0:HD], norm_rows[:, 0:64]) for m in range(NT_X)]
            jobs += [(heads(kn, m), kcat[:, m, :, 0:HD], norm_rows[:, 64:128]) for m in range(NT_X)]
            jobs += [(rr[:, m, 0:NH, :], rn[:, m, 0:NH, :], norm_rows[:, 256:288]) for m in range(NT_X)]
            jobs += [(rr[:, m, NH:NH + 1, :], rn[:, m, NH:NH + 1, :], norm_rows[:, 288:320]) for m in range(NT_X)]
            head_norm_stage(nc, g, "mla_norm", jobs)
            rotate_second(nc, rn, rope, rr, qcat, kcat)
            turn_heads(nc, "mla_turn", [(qcat, qT), (kcat, kT)], K, ident)
        items = [dict(q=qT[0:K, h, b * P:(b + 1) * P], keys=[kT[0:K, h, 0:(b + 1) * P]],
                      v=[v[:, t, HD * h:HD * h + HD] for t in range(b + 1)], mask=causal[:, 0, (3 - b) * P:SEQ],
                      sink=None, half=h % 2, out=heads_at(yT, b, h), gate=heads_at(gateT[:, 0], b, h)) for b in range(NT_X) for h in range(NH)]
        attention_stage(nc, "mla", items, float(1.0 / np.sqrt(K)), ident)


def rotate_second(nc, rn, rope, rr, qcat, kcat):
    with nc.sbuf_tensor("rot2", [P, 4, NT_X, 9, 16], F32) as part, \
            stage(nc, "rot2", "parts", "rotated", "copied") as (s, block):
        @block.vector
        def _(dve):
            n = 0
            for m in range(NT_X):
                cos = rope[:, 0, m].unsqueeze(1).to_broadcast([P, 9, 16])
                sin = rope[:, 1, m].unsqueeze(1).to_broadcast([P, 9, 16])
                for i, (x, y) in enumerate(((0, cos), (16, sin), (16, cos), (0, sin))):
                    nc.vector.tensor_tensor(part[:, i, m], rn[:, m, :, x:x + 16], y, ALU.mult).then_inc(s["parts"], 1)
            for m in range(NT_X):
                dve.wait_ge(s["parts"], 4 * m + 4)
                nc.vector.tensor_tensor(rr[:, m, :, 0:16], part[:, 0, m], part[:, 1, m], ALU.subtract).then_inc(s["rotated"], 1)
                nc.vector.tensor_tensor(rr[:, m, :, 16:32], part[:, 2, m], part[:, 3, m], ALU.add).then_inc(s["rotated"], 1)

        @block.scalar
        def _(act):
            for m in range(NT_X):
                act.wait_ge(s["rotated"], 2 * m + 2)
                nc.scalar.copy(qcat[:, m, :, HD:HD + RD], rr[:, m, 0:NH, :])
                nc.scalar.copy(kcat[:, m, :, HD:HD + RD], rr[:, m, NH:NH + 1, :].to_broadcast([P, NH, RD]))


def turn_heads(nc, name, pairs, K, ident):
    groups = [(src, dst, m, h) for src, dst in pairs for m in range(NT_X) for h in (0, 4)]
    with nc.psum_tensor(f"{name}_ps", [P, 4, 512], F32) as ps, stage(nc, name, "turned", "even", "odd") as (s, block):
        @block.tensor
        def _(pe):
            for q, (src, dst, m, h) in enumerate(groups):
                if q >= 4:
                    pe.wait_ge(s["odd"] if q % 2 else s["even"], (q - 4) // 2 + 1)
                for j in range(4):
                    last = nc.tensor.transpose(ps[0:K, q % 4, j * P:(j + 1) * P], src[:, m, h + j, :], ident)
                last.then_inc(s["turned"], 1)

        def copies(engine, copy, odd, signal):
            for q, (src, dst, m, h) in enumerate(groups):
                if q % 2 == odd:
                    engine.wait_ge(s["turned"], q + 1)
                    copy(dst[0:K, h:h + 4, m * P:(m + 1) * P],
                         ps[0:K, q % 4, :].rearrange("p (j t) -> p j t", j=4)).then_inc(signal, 1)

        @block.vector
        def _(dve):
            copies(dve, nc.vector.tensor_copy, 0, s["even"])

        @block.scalar
        def _(act):
            copies(act, nc.scalar.copy, 1, s["odd"])


def low_norm_turn(nc, g, low, lowT):
    parts = ((0, QL), (QL, KVL))
    gains = VCOL["lora_norms_2"].start
    with ExitStack() as held:
        def sb(name, shape):
            return held.enter_context(nc.sbuf_tensor(name, shape, F32))

        sq, xn, stat = sb("low_sq", [P, QL]), sb("low_xn", [P, NT_X, QL + KVL]), sb("low_stat", [P, 3, 2, NT_X])
        ps = held.enter_context(nc.psum_tensor("low_ps", [P, 2, 1024], F32))
        with stage(nc, "low", "squared", "root", "inverse", "normed", "turned", "out") as (s, block):
            @block.scalar
            def _(act):
                n = 0
                for i, (at, w) in enumerate(parts):
                    for m in range(NT_X):
                        if n:
                            act.wait_ge(s["squared"], n)
                        nc.scalar.activation(sq[:, 0:w], low[:, m, at:at + w], ACT.Square,
                                             accum_out=stat[:, 0, i, m:m + 1]).then_inc(s["squared"], 1)
                        n += 1
                act.wait_ge(s["squared"], n)
                for i, (at, w) in enumerate(parts):
                    nc.scalar.activation(stat[:, 1, i, :], stat[:, 0, i, :], ACT.Sqrt, scale=1.0 / w,
                                         bias=g.eps_col[:, 0:1]).then_inc(s["root"], 1)
                for m in range(NT_X):
                    act.wait_ge(s["turned"], m + 1)
                    for k in range(5):
                        last = nc.scalar.activation(lowT[:, k, m * P:(m + 1) * P], ps[:, m % 2, k * P:(k + 1) * P],
                                                    ACT.Copy, scale=g.vec[:, gains + k:gains + k + 1])
                    last.then_inc(s["out"], 1)

            @block.vector
            def _(dve):
                dve.wait_ge(s["root"], 2)
                nc.vector.reciprocal(stat[:, 2], stat[:, 1]).then_inc(s["inverse"], 1)
                dve.wait_ge(s["inverse"], 1)
                for m in range(NT_X):
                    for i, (at, w) in enumerate(parts):
                        nc.vector.tensor_scalar(xn[:, m, at:at + w], low[:, m, at:at + w], stat[:, 2, i, m:m + 1], None,
                                                ALU.mult).then_inc(s["normed"], 1)

            @block.tensor
            def _(pe):
                for m in range(NT_X):
                    pe.wait_ge(s["normed"], 2 * m + 2)
                    if m >= 2:
                        pe.wait_ge(s["out"], m - 1)
                    for k in range(5):
                        last = nc.tensor.transpose(ps[:, m % 2, k * P:(k + 1) * P], xn[:, m, k * P:(k + 1) * P],
                                                   g.ident[:, :])
                    last.then_inc(s["turned"], 1)


def fox(nc, d, g, low, wide, gateT, norm_rows, causal, b_f, ones, yT):
    ident = g.ident[:, :]
    K = HD + 2
    scale = HD ** -0.5
    with ExitStack() as held:
        def sb(name, shape, dtype=F32):
            return held.enter_context(nc.sbuf_tensor(name, shape, dtype))

        qT, kT = sb("fox_qT", [P, NH, SEQ]), sb("fox_kT", [P, NH, SEQ])
        with ExitStack() as making:
            def tb(name, shape, dtype=F32):
                return making.enter_context(nc.sbuf_tensor(name, shape, dtype))

            qcat, kcat = tb("fox_qcat", [P, NT_X, NH, K]), tb("fox_kcat", [P, NT_X, NH, K])

            def heads(i, m):
                return wide[:, m, i, :].rearrange("p (h n) -> p h n", n=HD)

            jobs = [(heads(0, m), qcat[:, m, :, 0:HD], norm_rows[:, 128:192]) for m in range(NT_X)]
            jobs += [(heads(1, m), kcat[:, m, :, 0:HD], norm_rows[:, 192:256]) for m in range(NT_X)]
            head_norm_stage(nc, g, "fox_norm", jobs)
            z, e, lf = (tb(f"fox_{x}", [P, NT_X, NH]) for x in ("z", "e", "lf"))
            upto = tb("upto", [P, P])
            with nc.psum_tensor("cum_ps", [P, 512], F32) as ps, \
                    stage(nc, "cum", "chain", "loaded", "abs", "log", "lf", "summed", "done") as (s, block):
                @block.sync
                def _(sp):
                    sp.dma_start(upto[:, :], d["before"]).then_inc(s["loaded"], 16)

                @block.vector
                def _(dve):
                    step = chained(dve, s["chain"])
                    for m in range(NT_X):
                        step(nc.vector.tensor_tensor(z[:, m, :], low[:, m, LOWW - NH:LOWW], b_f[:, :], ALU.add))
                    nc.vector.scalar_tensor_tensor(e[:, :, :], z[:, :, :], -1.0, z[:, :, :], ALU.mult,
                                                   ALU.max).then_inc(s["abs"], 1)
                    dve.wait_ge(s["log"], 2)
                    step(nc.vector.tensor_scalar(z[:, :, :], z[:, :, :], 0.0, None, ALU.min))
                    step(nc.vector.tensor_tensor(lf[:, :, :], z[:, :, :], e[:, :, :], ALU.subtract))
                    dve.wait_ge(s["loaded"], 16)
                    nc.vector.tensor_tensor(upto[:, :], upto[:, :], ident, ALU.add).then_inc(s["lf"], 1)
                    for cat, at in ((qcat, HD + 1), (kcat, HD)):
                        for m in range(NT_X):
                            nc.vector.memset(cat[:, m, :, at:at + 1], 1.0).then_inc(s["done"], 1)
                    dve.wait_ge(s["summed"], 1)
                    for m in range(NT_X):
                        cum = ps[:, m * NH:(m + 1) * NH].unsqueeze(2)
                        nc.vector.tensor_scalar(qcat[:, m, :, HD:HD + 1], cum, 1.0 / scale, None,
                                                ALU.mult).then_inc(s["done"], 1)
                        nc.vector.tensor_scalar(kcat[:, m, :, HD + 1:HD + 2], cum, -1.0 / scale, None,
                                                ALU.mult).then_inc(s["done"], 1)

                @block.scalar
                def _(act):
                    act.wait_ge(s["abs"], 1)
                    nc.scalar.activation(e[:, :, :], e[:, :, :], ACT.Exp, scale=-1.0).then_inc(s["log"], 1)
                    act.wait_ge(s["log"], 1)
                    nc.scalar.activation(e[:, :, :], e[:, :, :], ACT.Ln, bias=1.0).then_inc(s["log"], 1)

                @block.tensor
                def _(pe):
                    pe.wait_ge(s["lf"], 1)
                    for m in range(NT_X):
                        for q in range(m):
                            nc.tensor.matmul(ps[:, m * NH:(m + 1) * NH], ones, lf[:, q, :], start=(q == 0), stop=False,
                                             skip_group_check=True)
                        last = nc.tensor.matmul(ps[:, m * NH:(m + 1) * NH], upto[:, :], lf[:, m, :], start=(m == 0),
                                                stop=True, skip_group_check=True)
                    last.then_inc(s["summed"], 1)
            turn_heads(nc, "fox_turn", [(qcat, qT), (kcat, kT)], K, ident)
        items = [dict(q=qT[0:K, h, b * P:(b + 1) * P], keys=[kT[0:K, h, 0:(b + 1) * P]],
                      v=[wide[:, t, 2, HD * h:HD * h + HD] for t in range(b + 1)], mask=causal[:, 1, (3 - b) * P:SEQ],
                      sink=None, half=h % 2, out=heads_at(yT, b, h), gate=heads_at(gateT[:, 1], b, h)) for b in range(NT_X) for h in range(NH)]
        attention_stage(nc, "fox", items, scale, ident)


def build_program(nc, d, out):
    with ExitStack() as whole:
        def sb(name, shape, dtype=F32):
            return whole.enter_context(nc.sbuf_tensor(name, shape, dtype))

        ident = sb("ident", [P, P])
        vec = sb("vec", [P, NVCOL])
        eps_col = sb("eps_col", [P, 1])
        ada = sb("ada", [P, 48, 2])
        ada2 = sb("ada2", [P, 24, 1])
        g = Shared(ident=ident, vec=vec, eps_col=eps_col, ada=ada, ada2=ada2)

        cond = sb("cond", [P, KD, 2])
        sig = sb("sig", [P, 2, KD])
        with stage(nc, "start", "loaded", "set", "sig", "cond") as (s, block):
            @block.sync
            def _(sp):
                sp.dma_start(ident[:, :], d["ident"]).then_inc(s["loaded"], 16)
                sp.dma_start(vec[:, :], d["vectors"]).then_inc(s["loaded"], 16)
                sp.wait_ge(s["loaded"], 32)

            @block.vector
            def _(dve):
                nc.vector.memset(eps_col[:, :], RMS_EPS).then_inc(s["set"], 1)
                dve.wait_ge(s["sig"], 1)
                for j, name in enumerate(("c", "c_ctx")):
                    nc.vector.tensor_tensor(cond[:, :, j], vec[:, VCOL[name]], sig[:, j, :], ALU.mult).then_inc(s["cond"], 1)

            @block.scalar
            def _(act):
                act.wait_ge(s["loaded"], 32)
                nc.scalar.activation(sig[:, :, :].rearrange("p a k -> p (a k)"),
                                     vec[:, VCOL["c"].start:VCOL["c_ctx"].stop], ACT.Sigmoid).then_inc(s["sig"], 1)

        ada_stage(nc, "ada", cond, 2, d["w_ada"], 12, vec[:, VCOL["b_ada"]], ada, ident[:, :])
        ada_stage(nc, "ada2", vec[:, VCOL["c_2"]].unsqueeze(2), 1, d["w_ada_2"], 6, vec[:, VCOL["b_ada_2"]], ada2,
                  ident[:, :])
        row_cols = sb("row_cols", [P, 3, KD])
        ones = sb("ones", [P, P])
        with stage(nc, "row_cols", "done") as (s, block):
            @block.vector
            def _(dve):
                nc.vector.memset(ones[:, :], 1.0).then_inc(s["done"], 1)
                nc.vector.tensor_tensor(row_cols[:, 0, :], ada[:, 16:24, 0], vec[:, VCOL["g_post_mix"]],
                                        ALU.mult).then_inc(s["done"], 1)
                nc.vector.tensor_tensor(row_cols[:, 1, :], ada[:, 40:48, 0], vec[:, VCOL["g_post_ffn"]],
                                        ALU.mult).then_inc(s["done"], 1)
                nc.vector.tensor_copy(row_cols[:, 2, :], ada2[:, 16:24, 0]).then_inc(s["done"], 1)
        x = sb("x", [P, NT_X, D])
        first_block(nc, d, g, x, row_cols, ones[:, :])
        second_block(nc, d, g, x, row_cols, ones[:, :], out)


def axial_tables():
    t = np.arange(SEQ)
    half = HD // 2
    inv = (np.float32(10000.0) ** (-np.arange(0, half, 2, dtype=np.float32) / np.float32(half))).astype(np.float32)
    ang = np.stack([(t // 64).astype(np.float32)[:, None] * inv, (t % 64).astype(np.float32)[:, None] * inv], 1)
    tab = np.stack([np.cos(ang), np.sin(ang)], 1).astype(np.float32)
    return np.ascontiguousarray(tab.reshape(NT_X, P, 2, 2, 16).transpose(1, 0, 2, 3, 4))


def window_mask_table():
    q, k = np.arange(P)[:, None], np.arange(P)[None, :]
    before = np.where(k >= q, 0.0, NEG)
    after = np.where(k <= q, 0.0, NEG)
    z = np.zeros((P, P))
    return np.concatenate([z, z, before, z, after, z, z, z, after], 1).astype(np.float32)


def rwkv_tables():
    s, t = np.arange(P)[:, None], np.arange(P)[None, :]
    same = s // CH == t // CH
    tri = np.zeros((P, 2, 2, P), np.float32)
    off = np.zeros((P, 2, LEVELS, P), np.float32)
    for i, (before, upto) in enumerate(((s < t, s <= t), (s > t, s >= t))):
        tri[:, i, 0], tri[:, i, 1] = same & before, same & upto
        for l in range(LEVELS):
            off[:, i, l] = before & (s // (2 << l) == t // (2 << l)) & (s // (1 << l) != t // (1 << l))
    heads = np.stack([same.astype(np.float32), same / np.float32(CH)], 1).astype(np.float32)
    segment = np.tile((np.arange(NTOK) % CH != 0).astype(np.float32), (P, 1))
    return {"tri": tri, "off": off, "heads": heads, "segment": segment}


def rwkv_layout(a):
    w, b, mp, mn = a["w_in"][0], a["b_in"][0], a["mu_prev"][0], a["mu_next"][0]

    def slices(m):
        return m.reshape(KD, P, -1).transpose(1, 0, 2)

    d = dict(rwkv_tables())
    d["w_lora_in"] = slices(w[:, 768 + 1536:768 + 1920])
    rkv, cols, low = [], [], []
    for pair in range(4):
        c = slice(P * pair, P * pair + P)
        at = [768 + 512 * i + P * pair for i in range(3)]
        rkv.append(slices(np.concatenate([w[:, x:x + P] for x in at], 1)))
        here = [b[x:x + P] for x in at] + [m[x - 768:x - 768 + P] for m in (mp, mn) for x in at]
        here += [a[n][0, c] for n in ("w0_f", "w0_b", "a0_f", "a0_b", "k_k", "k_a")]
        here += [a["r_k"][0].reshape(-1)[c], a["ln_x_w"][0, c], a["ln_x_b"][0, c]]
        cols.append(np.stack(here, 1))
        low.append(np.stack([np.concatenate([a["w2_f"][0][:, c], a["w2_b"][0][:, c]], 0),
                             np.concatenate([a["a2_f"][0][:, c], a["a2_b"][0][:, c]], 0), a["g2"][0][:, c]], 1))
    d["w_rkv"], d["pair_cols"], d["pair_low"] = np.stack(rkv), np.stack(cols), np.stack(low)
    return d


def second_layout(a):
    at = dict(zip(("cq", "ckv", "kr", "ga", "q", "k", "v", "f", "gb", "mg"),
                  (0, 384, 640, 672, 1184, 1696, 2208, 2720, 2728, 3240)))
    size = dict(cq=384, ckv=256, kr=32, ga=512, q=512, k=512, v=512, f=8, gb=512, mg=2048)
    order = np.concatenate([np.arange(at[n], at[n] + size[n]) for n in
                            ("cq", "ckv", "kr", "f", "ga", "gb", "q", "k", "v", "mg")])
    uq = np.arange(NH * (HD + RD)).reshape(NH, HD + RD)
    ukv = np.arange(NH * 2 * HD).reshape(NH, 2 * HD)
    q, k = np.arange(P)[:, None], np.arange(P)[None, :]
    causal = np.zeros((P, 2, SEQ), np.float32)
    causal[:, 0, 384:] = np.where(k // 64 <= q // 64, 0.0, NEG)
    causal[:, 1, 384:] = np.where(k <= q, 0.0, NEG)
    half = np.arange(0, RD, 2, dtype=np.float32)
    return {"w_in_2": a["w_in_2"][0][:, order],
            "w_uq_2": a["w_uq_2"][0][:, np.concatenate([uq[:, :HD].ravel(), uq[:, HD:].ravel()])],
            "w_ukv_2": a["w_ukv_2"][0][:, np.concatenate([ukv[:, :HD].ravel(), ukv[:, HD:].ravel()])],
            "norm_rows_2": np.concatenate([a[n + "_2"][0] for n in ("qn_nope_a", "kn_nope_a", "qn_b", "kn_b",
                                                                    "qn_rope_a", "kn_rope_a")]),
            "b_f_2": a["b_f_2"][0], "w_branch_a_2": a["w_branch_a_2"][0], "w_branch_b_2": a["w_branch_b_2"][0],
            "w_out_2": a["w_out_2"][0], "causal_masks": causal,
            "positions_2": np.ascontiguousarray(a["positions_2"].reshape(NT_X, P).T),
            "rope_freq": (np.float32(10000.0) ** (-half / np.float32(RD))).astype(np.float32)}


def host_layout(inputs):
    a = {k: np.asarray(v) for k, v in inputs.items()}

    def columns(v):
        return np.ascontiguousarray(v.reshape(-1, P).T)

    lora = slice(768 + 1536, 768 + 1920)
    parts = {"c": a["c"][0], "c_ctx": a["c_ctx"], "c_2": a["c_2"][0], "b_ada": a["b_ada"][0],
             "g_pre_mix": a["g_pre_mix"][0], "g_post_mix": a["g_post_mix"][0], "g_pre_ffn": a["g_pre_ffn"][0],
             "g_post_ffn": a["g_post_ffn"][0], "b_ada_2": a["b_ada_2"][0], "norm_w_2": a["norm_w_2"][0],
             "lora_b_in": a["b_in"][0, lora], "lora_mu_prev": a["mu_prev"][0, 1536:], "lora_mu_next": a["mu_next"][0, 1536:],
             "lora_norms_2": np.concatenate([a["q_lora_norm_w_2"][0], a["kv_lora_norm_w_2"][0]])}
    d = {"vectors": np.concatenate([columns(parts[n]) for n in VCOL], 1)}
    d["ident"] = np.eye(P, dtype=np.float32)
    d["x"], d["ctx"] = a["x"], a["ctx"]
    d["w_ada"], d["w_ada_2"] = a["w_ada"][0], a["w_ada_2"][0]
    w, b = a["w_in"][0], a["b_in"][0]
    order = np.concatenate([np.arange(HD) + HD * h for h in (0, 4, 1, 5, 2, 6, 3, 7)])
    tok = np.concatenate([order, np.arange(512, 768), np.arange(2688, 4736)])
    d["w_in_tok"], d["b_in_tok"], d["b_gates"] = w[:, tok], b[tok[:768]], b[tok[768:]]
    d["rope_axial"], d["window_masks"] = axial_tables(), window_mask_table()
    d.update(rwkv_layout(a))
    for n in ("w_up_att", "w_up_rwkv", "w_out", "w_router", "b_router", "w_gate_up", "b_gate_up", "w_down", "b_down"):
        d[n] = a[n][0]
    d.update(second_layout(a))
    d["iota"] = np.arange(P, dtype=np.float32)
    d["before"] = np.triu(np.ones((P, P), np.float32), 1)
    d["att_sinks"] = a["att_sinks"][0]
    return d


def kernel(**inputs):
    import numpy as _np
    import concourse.bacc as _bacc
    from concourse import mybir as _mybir
    from concourse.bass_utils import run_bass_kernel_spmd as _run

    nc = _bacc.Bacc("TRN2", target_bir_lowering=False, num_devices=1)
    arrays, d = {}, {}
    for name, array in host_layout(inputs).items():
        array = _np.ascontiguousarray(array)
        arrays[f"in_{name}"] = array
        d[name] = nc.dram_tensor(f"in_{name}", array.shape, _mybir.dt.from_np(array.dtype), kind="ExternalInput").ap()
    out = nc.dram_tensor("out_0", (1, SEQ, D), F32, kind="ExternalOutput").ap()
    build_program(nc, d, out)
    r = _run(nc, [arrays], core_ids=[0])
    return r.results[0]["out_0"]
```

```python
from contextlib import ExitStack, contextmanager

import numpy as np

import concourse.bass as bass
from concourse import mybir

F32 = mybir.dt.float32
I32 = mybir.dt.int32
U32 = mybir.dt.uint32
ALU = mybir.AluOpType
ACT = mybir.ActivationFunctionType
AX = mybir.AxisListType

P = 128
D = 1024
KD = D // P
SEQ = 512
CTX = 256
NT_X = SEQ // P
NT_C = CTX // P
NTOK = SEQ + CTX
HD = 64
NEG = -1e30
ROUND = 12582912.0
RMS_EPS = 1e-6


class Shared:

    def __init__(self, ident, vec, eps_col, ada, ada2):
        self.ident, self.vec, self.eps_col, self.ada, self.ada2 = ident, vec, eps_col, ada, ada2


RESTING = []


@contextmanager
def stage(nc, name, *signals, clear=(), pool_dma=(), repeats=False):
    held = ExitStack()
    sems = {s: held.enter_context(nc.semaphore(f"{name}_{s}")) for s in signals}
    with nc.Block() as block:
        yield sems, block
    for x in pool_dma:
        nc.gpsimd.dma_reset(range(x.num, x.num + 1))
    numbers = sorted([x.num for x in sems.values()] + [x.num for x in clear] + [x.num for x in pool_dma])
    starts = [i for i, x in enumerate(numbers) if i == 0 or x != numbers[i - 1] + 1] + [len(numbers)]
    for i, j in zip(starts[:-1], starts[1:]):
        nc.gpsimd.sem_clear(range(numbers[i], numbers[j - 1] + 1))
    if clear or pool_dma or repeats:
        nc.all_engine_barrier()
    while RESTING:
        RESTING.pop().close()
    RESTING.append(held)


def chained(engine, signal):
    count = [0]

    def step(instruction):
        count[0] += 1
        instruction.then_inc(signal, 1)
        engine.wait_ge(signal, count[0])

    return step


def row_to_all(row, n):
    return bass.AP(tensor=row.tensor, offset=row.offset, ap=[[0, P], [1, n]])


def vector_columns():
    at, cols = 0, {}
    for name, n in (("c", 8), ("c_ctx", 8), ("c_2", 8), ("b_ada", 48), ("g_pre_mix", 8), ("g_post_mix", 8),
                    ("g_pre_ffn", 8), ("g_post_ffn", 8), ("b_ada_2", 24), ("norm_w_2", 8), ("lora_b_in", 3),
                    ("lora_mu_prev", 3), ("lora_mu_next", 3), ("lora_norms_2", 5)):
        cols[name] = slice(at, at + n)
        at += n
    return cols, at


VCOL, NVCOL = vector_columns()


def ada_stage(nc, name, cond, n_cond, w_dram, n_chunks, bias_cols, ada, ident):
    chunk, slots = 4, 4
    wv = w_dram.rearrange("(k p) n -> p k n", p=P)
    with ExitStack() as held:
        w_sb = held.enter_context(nc.sbuf_tensor(f"{name}_w", [P, slots, KD, 512], F32))
        row = held.enter_context(nc.sbuf_tensor(f"{name}_row", [n_cond, 2, 512], F32))
        ps = held.enter_context(nc.psum_tensor(f"{name}_ps", [P, 2, 512], F32))
        ps_c = held.enter_context(nc.psum_tensor(f"{name}_columns", [P, 2, 512], F32))
        with stage(nc, name, "w0", "w1", "w2", "w3", "product", "row", "columns", "out") as (s, block):
            loaded = [s["w0"], s["w1"], s["w2"], s["w3"]]

            @block.sync
            def _(sp):
                for c in range(n_chunks):
                    if c >= slots:
                        sp.wait_ge(s["product"], c - slots + 1)
                    sp.dma_start(w_sb[:, c % slots], wv[:, :, c * 512:c * 512 + 512]).then_inc(loaded[c % slots], 16)

            @block.tensor
            def _(pe):
                for c in range(n_chunks + 1):
                    if c < n_chunks:
                        pe.wait_ge(loaded[c % slots], 16 * (c // slots + 1))
                        if c >= 2:
                            pe.wait_ge(s["row"], c - 1)
                        for k in range(KD):
                            last = nc.tensor.matmul(ps[0:n_cond, c % 2, :], cond[:, k, :], w_sb[:, c % slots, k, :],
                                                    start=(k == 0), stop=(k == KD - 1))
                        last.then_inc(s["product"], 1)
                    if c >= 1:
                        b = c - 1
                        pe.wait_ge(s["row"], b + 1)
                        if b >= 2:
                            pe.wait_ge(s["out"], b - 1)
                        for m in range(chunk):
                            last = nc.tensor.transpose(ps_c[:, b % 2, m * n_cond:(m + 1) * n_cond],
                                                       row[:, b % 2, m * P:(m + 1) * P], ident[0:n_cond, 0:n_cond])
                        last.then_inc(s["columns"], 1)

            @block.scalar
            def _(act):
                for c in range(n_chunks):
                    act.wait_ge(s["product"], c + 1)
                    if c >= 2:
                        act.wait_ge(s["columns"], c - 1)
                    nc.scalar.copy(row[:, c % 2, :], ps[0:n_cond, c % 2, :]).then_inc(s["row"], 1)

            @block.vector
            def _(dve):
                for c in range(n_chunks):
                    dve.wait_ge(s["columns"], c + 1)
                    bias = bias_cols[:, c * chunk:(c + 1) * chunk].unsqueeze(2).to_broadcast([P, chunk, n_cond])
                    nc.vector.tensor_tensor(ada[:, c * chunk:(c + 1) * chunk, :],
                                            ps_c[:, c % 2, 0:chunk * n_cond].rearrange("p (m j) -> p m j", j=n_cond),
                                            bias, ALU.add).then_inc(s["out"], 1)


EARLY = 6
LATE = 12
LATE_A_TURN = LATE // 4


class LateModulation:
    SIGNALS = ("late_w0", "late_w1", "late_cond", "late_sum", "late_read", "late_made")

    def __init__(self, nc, held, ones):
        self.nc, self.ones = nc, ones
        self.cond = held.enter_context(nc.sbuf_tensor("late_cond_cols", [P, LATE, KD], F32))
        self.columns = held.enter_context(nc.sbuf_tensor("late_columns", [P, LATE * 4], F32))

    def open(self, d, turn, held):
        nc = self.nc
        self.turn, self.w_dram = turn, d["w_late"]
        self.w = held.enter_context(nc.sbuf_tensor("late_w", [P, 2, KD, 512], F32))
        self.sum = held.enter_context(nc.sbuf_tensor("late_sums", [P, LATE_A_TURN, 512], F32))
        self.here = held.enter_context(nc.sbuf_tensor("late_here", [P, LATE_A_TURN, KD], F32))
        self.ps = held.enter_context(nc.psum_tensor("late_ps", [P, 512], F32))

    def loads(self, sp, s):
        for q in range(LATE_A_TURN):
            if q >= 2:
                sp.wait_ge(s["late_sum"], KD * (q - 1))
            sp.dma_start(self.w[:, q % 2], self.w_dram[self.turn * LATE_A_TURN + q]).then_inc(s[f"late_w{q % 2}"], 16)

    def sums(self, dve, s, chunks):
        nc = self.nc
        for q in chunks:
            if q == 0:
                nc.vector.tensor_copy(self.here[:, :, :],
                                      self.cond[:, bass.ds(self.turn * LATE_A_TURN, LATE_A_TURN), :]) \
                    .then_inc(s["late_cond"], 1)
                dve.wait_ge(s["late_cond"], 1)
            dve.wait_ge(s[f"late_w{q % 2}"], 16 * (q // 2 + 1))
            for k in range(KD):
                w, c, out = self.w[:, q % 2, k, :], self.here[:, q, k:k + 1], self.sum[:, q, :]
                if k == 0:
                    nc.vector.tensor_scalar(out, w, c, None, ALU.mult).then_inc(s["late_sum"], 1)
                else:
                    dve.wait_ge(s["late_sum"], KD * q + k)
                    nc.vector.scalar_tensor_tensor(out, w, c, out, ALU.mult, ALU.add).then_inc(s["late_sum"], 1)

    def products(self, pe, s):
        pe.wait_ge(s["late_sum"], KD * LATE_A_TURN)
        for m in range(4 * LATE_A_TURN):
            last = self.nc.tensor.matmul(self.ps[:, m:m + 1], self.sum[:, m // 4, (m % 4) * P:(m % 4 + 1) * P],
                                         self.ones[:, 0:1], start=True, stop=True, skip_group_check=True)
        last.then_inc(s["late_made"], 1)

    def keep(self, act, s):
        act.wait_ge(s["late_made"], 1)
        n = 4 * LATE_A_TURN
        self.nc.scalar.copy(self.columns[:, bass.ds(self.turn * n, n)], self.ps[:, 0:n]).then_inc(s["late_read"], 1)


def norm_turn_stage(nc, name, tiles, sources, xn, hT, affine, eps, ident):
    n = len(tiles)
    with ExitStack() as held:
        squares = held.enter_context(nc.sbuf_tensor(f"{name}_sq", [P, D], F32))
        stat = held.enter_context(nc.sbuf_tensor(f"{name}_stat", [P, 3, n], F32))
        ps = held.enter_context(nc.psum_tensor(f"{name}_ps", [P, 2, 2, 512], F32))
        loads = [f"x{m}" for m in range(n)] if sources is not None else []
        with stage(nc, name, *loads, "squared", "root", "inverse", "normed", "turned", "out_act", "out_dve") as (s, block):
            here = [s[f"x{m}"] for m in range(n)] if sources is not None else None

            @block.sync
            def _(sp):
                if sources is not None:
                    for m in range(n):
                        sp.dma_start(tiles[m], sources[m]).then_inc(here[m], 16)

            @block.scalar
            def _(act):
                for m in range(n + 1):
                    if m < n:
                        if here is not None:
                            act.wait_ge(here[m], 16)
                        if m:
                            act.wait_ge(s["squared"], m)
                        nc.scalar.activation(squares[:, :], tiles[m], ACT.Square,
                                             accum_out=stat[:, 0, m:m + 1]).then_inc(s["squared"], 1)
                    if m >= 1:
                        act.wait_ge(s["squared"], m)
                        nc.scalar.activation(stat[:, 1, m - 1:m], stat[:, 0, m - 1:m], ACT.Sqrt, scale=1.0 / D,
                                             bias=eps).then_inc(s["root"], 1)
                for m in range(n):
                    act.wait_ge(s["turned"], m + 1)
                    for k in range(4):
                        gain, shift = affine(m, k)
                        last = nc.scalar.activation(hT[:, k, m * P:(m + 1) * P], ps[:, m % 2, 0, k * P:(k + 1) * P],
                                                    ACT.Identity, scale=gain, bias=shift)
                    last.then_inc(s["out_act"], 1)

            @block.vector
            def _(dve):
                for m in range(n):
                    dve.wait_ge(s["root"], m + 1)
                    nc.vector.reciprocal(stat[:, 2, m:m + 1], stat[:, 1, m:m + 1]).then_inc(s["inverse"], 1)
                    dve.wait_ge(s["inverse"], m + 1)
                    nc.vector.tensor_scalar(xn[m], tiles[m], stat[:, 2, m:m + 1], None, ALU.mult).then_inc(s["normed"], 1)
                for m in range(n):
                    dve.wait_ge(s["turned"], m + 1)
                    for k in range(4, 8):
                        gain, shift = affine(m, k)
                        last = nc.vector.tensor_scalar(hT[:, k, m * P:(m + 1) * P],
                                                       ps[:, m % 2, 1, (k - 4) * P:(k - 3) * P],
                                                       gain, shift, ALU.mult, ALU.add)
                    last.then_inc(s["out_dve"], 1)

            @block.tensor
            def _(pe):
                for m in range(n):
                    pe.wait_ge(s["normed"], m + 1)
                    if m >= 2:
                        pe.wait_ge(s["out_act"], m - 1)
                        pe.wait_ge(s["out_dve"], m - 1)
                    for k in range(KD):
                        last = nc.tensor.transpose(ps[:, m % 2, k // 4, (k % 4) * P:(k % 4 + 1) * P],
                                                   xn[m][:, k * P:(k + 1) * P], ident)
                    last.then_inc(s["turned"], 1)


class WeightRing:

    def __init__(self, nc, name, held, depth=KD):
        self.slots = [held.enter_context(nc.sbuf_tensor(f"{name}{i}", [P, depth, 512], F32)) for i in range(2)]
        self.arrived = [[held.enter_context(nc.semaphore(f"{name}_stage{j}_slot{i}")) for i in range(2)]
                        for j in range(2)]
        self.first = 0
        self.turn = 0
        self.called = 0

    def slot(self, c):
        return self.slots[(self.first + c) % 2]

    def load(self, engine, c, chunk, ahead=0):
        engine.dma_start(self.slot(c)[:, 0:chunk["k"], 0:chunk["width"]],
                         chunk["w"].rearrange("(k p) n -> p k n", p=P)) \
            .then_inc(self.arrived[(self.turn + ahead) % 2][(self.first + c) % 2], 16)

    def call_first(self, engine, chunks):
        for c, chunk in enumerate(chunks[0:2]):
            self.load(engine, c, chunk)
        self.called = min(2, len(chunks))

    def wait(self, pe, c):
        pe.wait_ge(self.arrived[self.turn][(self.first + c) % 2], 16 * (c // 2 + 1))

    def finish(self, n_chunks, n_called):
        self.first, self.turn, self.called = (self.first + n_chunks) % 2, 1 - self.turn, n_called


def token_gemm_stage(nc, name, chunks, ring, evacuate, extra=(), then=()):
    with ExitStack() as held:
        ps = held.enter_context(nc.psum_tensor(f"{name}_ps", [P, 4, 512], F32))
        with stage(nc, name, "tile", "free", "chain", "step2", *extra, clear=ring.arrived[ring.turn]) as (s, block):
            firsts, tiles = [], []
            for c, chunk in enumerate(chunks):
                firsts.append(len(tiles))
                tiles += [(c, m) for m in range(4 if "rhs" in chunk else len(chunk["lhs"]))]
            firsts.append(len(tiles))

            @block.sync
            def _(sp):
                n = len(chunks)
                for c, chunk in list(enumerate(chunks + list(then[0:2])))[ring.called:]:
                    if c >= 2:
                        sp.wait_ge(s["tile"], firsts[c - 1])
                    ring.load(sp, c, chunk, ahead=c >= n)

            @block.tensor
            def _(pe):
                for t, (c, m) in enumerate(tiles):
                    chunk = chunks[c]
                    if m == 0:
                        ring.wait(pe, c)
                    if t >= 4:
                        pe.wait_ge(s["free"], t - 3)
                    for k in range(chunk["k"]):
                        start, stop = k == 0, k == chunk["k"] - 1
                        if "rhs" in chunk:
                            last = nc.tensor.matmul(ps[:, t % 4, :], ring.slot(c)[:, k, m * P:(m + 1) * P],
                                                    chunk["rhs"](k), start=start, stop=stop)
                        else:
                            last = nc.tensor.matmul(ps[:, t % 4, 0:chunk["width"]], chunk["lhs"][m](k),
                                                    ring.slot(c)[:, k, 0:chunk["width"]], start=start, stop=stop)
                    last.then_inc(s["tile"], 1)

            work = [(t, chunks[c], m, ps[:, t % 4, 0:chunks[c]["width"]]) for t, (c, m) in enumerate(tiles)]
            evacuate(s, block, work)
    ring.finish(len(chunks), len(then[0:2]))


def attention_stage(nc, name, items, scale, ident, early=None):
    n = len(items)
    W = 640
    with ExitStack() as held:
        masked = held.enter_context(nc.sbuf_tensor(f"{name}_masked", [P, 2, W], F32))
        prob = held.enter_context(nc.sbuf_tensor(f"{name}_prob", [P, 3, W], F32))
        probT = held.enter_context(nc.sbuf_tensor(f"{name}_probT", [P, 2, W], F32))
        diag = held.enter_context(nc.sbuf_tensor(f"{name}_diag", [P, 2, P], F32))
        col = held.enter_context(nc.sbuf_tensor(f"{name}_col", [P, 3, 8], F32))
        ps_s = held.enter_context(nc.psum_tensor(f"{name}_s", [P, 2, 1024], F32))
        ps_t = held.enter_context(nc.psum_tensor(f"{name}_t", [P, 1024], F32))
        ps_o = held.enter_context(nc.psum_tensor(f"{name}_o", [P, 2, 512], F32))
        MAX, NEGMAX, SUM, SINK, DEN, INV = range(6)
        with stage(nc, name, "scores", "maxed", "negated", "probs", "turned", "probT", "values", "done", "den",
                   "diag") as (s, block):
            if early is not None:
                @block.sync
                def _(sp):
                    early(sp)

            def c(i, what):
                return col[:, i % 3, what:what + 1]

            def rows(i):
                return slice(HD * items[i]["half"], HD * items[i]["half"] + HD)

            @block.tensor
            def _(pe):
                for i in range(n + 3):
                    if i < n:
                        if i >= 2:
                            pe.wait_ge(s["maxed"], i - 1)
                        it, at = items[i], 0
                        for keys in it["keys"]:
                            w = keys.shape[1]
                            done = 0
                            while done < w:
                                part = min(w - done, 512 - at % 512)
                                last = nc.tensor.matmul(ps_s[:, i % 2, at:at + part], it["q"],
                                                        keys[:, done:done + part], start=(at % 512 == 0),
                                                        stop=True, skip_group_check=True)
                                at, done = at + part, done + part
                        last.then_inc(s["scores"], 1)
                    if 2 <= i <= n + 1:
                        j = i - 2
                        pe.wait_ge(s["diag"], j + 1)
                        if j >= 1:
                            pe.wait_ge(s["probT"], j)
                        for t in range(len(items[j]["v"])):
                            last = nc.tensor.matmul(ps_t[:, t * P:(t + 1) * P], prob[:, j % 3, t * P:(t + 1) * P],
                                                    diag[:, j % 2, :], start=True, stop=True)
                        last.then_inc(s["turned"], 1)
                    if i >= 3:
                        j = i - 3
                        pe.wait_ge(s["probT"], j + 1)
                        if j >= 2:
                            pe.wait_ge(s["done"], j - 1)
                        vs = items[j]["v"]
                        for t, v in enumerate(vs):
                            last = nc.tensor.matmul(ps_o[rows(j), j % 2, 0:P], v, probT[:, j % 2, t * P:(t + 1) * P],
                                                    start=(t == 0), stop=(t == len(vs) - 1))
                        last.then_inc(s["values"], 1)

            @block.vector
            def _(dve):
                for i in range(n + 3):
                    if i < n:
                        it = items[i]
                        w = P * len(it["v"])
                        dve.wait_ge(s["scores"], i + 1)
                        if i >= 2:
                            dve.wait_ge(s["probs"], i - 1)
                        start = it["sink"] if it["sink"] is not None else -3.0e38
                        nc.vector.tensor_tensor_reduce(masked[:, i % 2, 0:w], ps_s[:, i % 2, 0:w], it["mask"], scale,
                                                       start, ALU.add, ALU.max, c(i, MAX)).then_inc(s["maxed"], 1)
                        dve.wait_ge(s["maxed"], i + 1)
                        nc.vector.tensor_scalar(c(i, NEGMAX), c(i, MAX), -1.0, None, ALU.mult) \
                            .then_inc(s["negated"], 1)
                    if 1 <= i <= n:
                        j = i - 1
                        dve.wait_ge(s["probs"], j + 1)
                        sink = c(j, SINK) if items[j]["sink"] is not None else 0.0
                        nc.vector.tensor_scalar(c(j, DEN), c(j, SUM), sink, None, ALU.add).then_inc(s["den"], 1)
                        dve.wait_ge(s["den"], 2 * j + 1)
                        nc.vector.reciprocal(c(j, INV), c(j, DEN)).then_inc(s["den"], 1)
                        dve.wait_ge(s["den"], 2 * j + 2)
                        if j >= 2:
                            dve.wait_ge(s["turned"], j - 1)
                        nc.vector.tensor_scalar(diag[:, j % 2, :], ident, c(j, INV), None, ALU.mult) \
                            .then_inc(s["diag"], 1)
                    if i >= 3:
                        j = i - 3
                        dve.wait_ge(s["values"], j + 1)
                        if items[j]["gate"] is None:
                            nc.vector.tensor_copy(items[j]["out"], ps_o[rows(j), j % 2, 0:P]).then_inc(s["done"], 1)
                        else:
                            nc.vector.tensor_tensor(items[j]["out"], ps_o[rows(j), j % 2, 0:P], items[j]["gate"],
                                                    ALU.mult).then_inc(s["done"], 1)

            @block.scalar
            def _(act):
                for i in range(n + 2):
                    if i < n:
                        w = P * len(items[i]["v"])
                        act.wait_ge(s["negated"], i + 1)
                        if i >= 3:
                            act.wait_ge(s["turned"], i - 2)
                        if i >= 3:
                            act.wait_ge(s["diag"], i - 2)
                        if items[i]["sink"] is not None:
                            nc.scalar.activation(c(i, SINK), c(i, NEGMAX), ACT.Exp, bias=items[i]["sink"])
                        nc.scalar.activation(prob[:, i % 3, 0:w], masked[:, i % 2, 0:w], ACT.Exp, bias=c(i, NEGMAX),
                                             accum_out=c(i, SUM)).then_inc(s["probs"], 1)
                    if i >= 2:
                        j = i - 2
                        w = P * len(items[j]["v"])
                        act.wait_ge(s["turned"], j + 1)
                        if j >= 2:
                            act.wait_ge(s["values"], j - 1)
                        nc.scalar.copy(probT[:, j % 2, 0:w], ps_t[:, 0:w]).then_inc(s["probT"], 1)


def turn_stage(nc, name, sources, targets, ident):
    n = len(sources)
    groups = [list(range(a, min(a + 4, n))) for a in range(0, n, 4)]
    with ExitStack() as held:
        ps = held.enter_context(nc.psum_tensor(f"{name}_ps", [P, 4, 512], F32))
        with stage(nc, name, "turned", "even", "odd") as (s, block):
            @block.tensor
            def _(pe):
                for q, group in enumerate(groups):
                    if q >= 4:
                        pe.wait_ge(s["odd"] if q % 2 else s["even"], (q - 4) // 2 + 1)
                    for j, i in enumerate(group):
                        last = nc.tensor.transpose(ps[:, q % 4, j * P:(j + 1) * P], sources[i], ident)
                    last.then_inc(s["turned"], 1)

            def copies(engine, copy, odd, signal):
                for q, group in enumerate(groups):
                    if q % 2 == odd:
                        engine.wait_ge(s["turned"], q + 1)
                        for j, i in enumerate(group):
                            last = copy(targets[i], ps[:, q % 4, j * P:(j + 1) * P])
                        last.then_inc(signal, 1)

            @block.vector
            def _(dve):
                copies(dve, nc.vector.tensor_copy, 0, s["even"])

            @block.scalar
            def _(act):
                copies(act, nc.scalar.copy, 1, s["odd"])


def mixing_block(nc, d, g, late, x, row_cols, ones):
    with ExitStack() as mixing:
        rwkT = mixing.enter_context(nc.sbuf_tensor("rwkT", [P, 4, SEQ], F32))
        hT = mixing.enter_context(nc.sbuf_tensor("hT", [P, KD, NTOK], F32))
        mix_inputs(nc, d, g, hT)
        scratch = x[:, :, :].rearrange("p m n -> p (m n)")
        rwkv_branch(nc, d, g, late, hT, scratch, rwkT)
        finish_modulation(nc, g, late, row_cols)
        attT = mixing.enter_context(nc.sbuf_tensor("attT", [P, 4, SEQ], F32))
        ring = WeightRing(nc, "mix_w", mixing)
        x_here = mixing.enter_context(nc.semaphore("x_here"))
        window_attention(nc, d, g, ring, hT, attT, lambda sp: sp.dma_start(
            x[:, :, :], d["x"][0].rearrange("(m p) n -> p m n", p=P)).then_inc(x_here, 16))
        gates = mixing.enter_context(nc.sbuf_tensor("gates", [P, NT_X, 2 * D], F32))
        merge_gates(nc, d, ring, hT, gates)
        mix = mixing.enter_context(nc.sbuf_tensor("mix", [P, NT_X, D], F32))
        merge_and_out(nc, d, g, "mix", ring, (attT, rwkT), gates, (d["w_up_att"], d["w_up_rwkv"]), d["w_out"], mix)
        tiles = [x[:, m] for m in range(NT_X)]
        with stage(nc, "x_in", "none", clear=(x_here,)) as (s, block):
            @block.sync
            def _(sp):
                sp.wait_ge(x_here, 16)
        row = mixing.enter_context(nc.sbuf_tensor("mix_row", [P, D], F32))
        rows_stage(nc, g, "mix_rows", [row_cols[:, 0]], [row[:, :]], ones)
        add_normed_stage(nc, g, "post_mix", [mix[:, m] for m in range(NT_X)], tiles, row[:, :])


def finish_modulation(nc, g, late, row_cols):
    half, vec = 4 * LATE // 2, g.vec
    at = VCOL["b_ada"].start + 4 * EARLY
    with stage(nc, "row_cols", "biased", "done") as (s, block):
        @block.vector
        def _(dve):
            nc.vector.tensor_tensor(g.ada[:, 4 * EARLY:48, 0], late.columns[:, 0:half], vec[:, at:at + half],
                                    ALU.add).then_inc(s["biased"], 1)
            nc.vector.tensor_tensor(g.ada2[:, :, 0], late.columns[:, half:2 * half], vec[:, VCOL["b_ada_2"]],
                                    ALU.add).then_inc(s["biased"], 1)
            dve.wait_ge(s["biased"], 2)
            nc.vector.tensor_tensor(row_cols[:, 0, :], g.ada[:, 16:24, 0], vec[:, VCOL["g_post_mix"]],
                                    ALU.mult).then_inc(s["done"], 1)
            nc.vector.tensor_tensor(row_cols[:, 1, :], g.ada[:, 40:48, 0], vec[:, VCOL["g_post_ffn"]],
                                    ALU.mult).then_inc(s["done"], 1)
            nc.vector.tensor_copy(row_cols[:, 2, :], g.ada2[:, 16:24, 0]).then_inc(s["done"], 1)


def ffn_block(nc, d, g, ring, x, row_cols, ones):
    tiles = [x[:, m] for m in range(NT_X)]
    with ExitStack() as ffn:
        def sb(name, shape, dtype=F32):
            return ffn.enter_context(nc.sbuf_tensor(name, shape, dtype))

        gain, shift = sb("ffn_gain", [P, KD]), sb("ffn_shift", [P, KD])
        weight, slot_of = sb("weight_of", [P, NT_X, TOP_K]), sb("slot_of", [P, NT_X, TOP_K], U32)
        token_of = sb("token_of", [P, LISTED], U32)
        table, n_blocks = sb("table", [1, P], I32), sb("n_blocks", [1, 1], I32)
        rows = nc.dram_tensor("normed_rows", (SEQ, D), F32).ap()
        with stage(nc, "ffn_gain", "done") as (s, block):
            @block.vector
            def _(dve):
                nc.vector.scalar_tensor_tensor(gain[:, :], g.ada[:, 32:40, 0], 1.0, g.vec[:, VCOL["g_pre_ffn"]],
                                               ALU.add, ALU.mult).then_inc(s["done"], 1)
                nc.vector.tensor_copy(shift[:, :], g.ada[:, 24:32, 0]).then_inc(s["done"], 1)
        y = sb("ffn_y", [P, NT_X, D])
        moving = ffn.enter_context(ExitStack())
        weights = ExpertWeights(nc, d, moving)
        with nc.sbuf_tensor("ffn_hT", [P, KD, SEQ], F32) as hT:
            norm_turn_stage(nc, "ffn", tiles, None, [y[:, m] for m in range(NT_X)], hT,
                            lambda m, k: (gain[:, k:k + 1], shift[:, k:k + 1]), g.eps_col[:, 0:1], g.ident[:, :])
            route_stage(nc, d, g, hT, ones, weights, y, rows, weight, slot_of, token_of, table, n_blocks)
        slot_rows = experts(nc, d, g, weights, rows, gain, shift, token_of, table, n_blocks)
        moving.close()
        combine(nc, slot_rows, weight, slot_of, y)
        row = sb("ffn_row", [P, D])
        rows_stage(nc, g, "ffn_rows", [row_cols[:, 1]], [row[:, :]], ones)
        add_normed_stage(nc, g, "post_ffn", [y[:, m] for m in range(NT_X)], tiles, row[:, :],
                         early=lambda sp: ring.call_first(sp, second_weights(d)))


def mix_inputs(nc, d, g, hT):
    with ExitStack() as held:
        gain = held.enter_context(nc.sbuf_tensor("pre_gain", [P, 2, KD], F32))
        ctx_sb = held.enter_context(nc.sbuf_tensor("ctx_sb", [P, NT_C, D], F32))
        x_sb = held.enter_context(nc.sbuf_tensor("pre_x", [P, NT_X, D], F32))
        xn = held.enter_context(nc.sbuf_tensor("pre_xn", [P, 6, D], F32))
        with stage(nc, "pre_gain", "done") as (s, block):
            @block.vector
            def _(dve):
                for j in range(2):
                    nc.vector.scalar_tensor_tensor(gain[:, j, :], g.ada[:, 8:16, j], 1.0, g.vec[:, VCOL["g_pre_mix"]],
                                                   ALU.add, ALU.mult).then_inc(s["done"], 1)
        tiles = [ctx_sb[:, m] for m in range(NT_C)] + [x_sb[:, m] for m in range(NT_X)]
        sources = [d["ctx"][0, m * P:(m + 1) * P, :] for m in range(NT_C)]
        sources += [d["x"][0, m * P:(m + 1) * P, :] for m in range(NT_X)]

        def affine(m, k):
            j = 1 if m < NT_C else 0
            return gain[:, j, k:k + 1], g.ada[:, k, j:j + 1]

        norm_turn_stage(nc, "pre", tiles, sources, [xn[:, m] for m in range(6)], hT, affine, g.eps_col[:, 0:1],
                        g.ident[:, :])


def gate_weights(d):
    return [dict(w=d["w_in_tok"][:, 768 + 512 * c:1280 + 512 * c], width=512, k=KD, col=512 * c) for c in range(4)]


def window_attention(nc, d, g, ring, hT, attT, early):
    ident = g.ident[:, :]
    with ExitStack() as held:
        def sb(name, shape, dtype=F32):
            return held.enter_context(nc.sbuf_tensor(name, shape, dtype))

        qkv = sb("qkv", [P, NT_X, 768])
        kvc = sb("kvc", [P, NT_C, 256])
        rope = sb("rope", [P, NT_X, 2, 2, 16])
        masks = sb("win_masks", [P, 1152])
        sinks = sb("sinks", [P, 8])
        with ExitStack() as projecting:
            bias = projecting.enter_context(nc.sbuf_tensor("proj_bias", [P, 768], F32))
            w = d["w_in_tok"]

            def tok(t):
                return lambda k: hT[:, k, t * P:(t + 1) * P]

            chunks = [dict(w=w[:, 0:512], width=512, k=KD, lhs=[tok(NT_C + m) for m in range(NT_X)], col=0),
                      dict(w=w[:, 512:768], width=256, k=KD, lhs=[tok(NT_C + m) for m in range(NT_X)] +
                           [tok(m) for m in range(NT_C)], col=512)]

            def evacuate(s, block, work):
                def target(chunk, m):
                    a, b = chunk["col"], chunk["col"] + chunk["width"]
                    return qkv[:, m, a:b] if m < NT_X else kvc[:, m - NT_X, :]

                @block.scalar
                def _(act):
                    act.dma_start(bias[:, :], row_to_all(d["b_in_tok"], 768)).then_inc(s["side"], 16)
                    act.dma_start(rope[:, :, :, :, :], d["rope_axial"]).then_inc(s["side"], 16)
                    act.dma_start(masks[:, :], d["window_masks"]).then_inc(s["side"], 16)
                    act.dma_start(sinks[:, :], row_to_all(d["att_sinks"], 8)).then_inc(s["side"], 16)
                    act.wait_ge(s["side"], 64)

                @block.vector
                def _(dve):
                    dve.wait_ge(s["side"], 64)
                    for t, chunk, m, ps in work:
                        dve.wait_ge(s["tile"], t + 1)
                        a, b = chunk["col"], chunk["col"] + chunk["width"]
                        nc.vector.tensor_tensor(target(chunk, m), ps, bias[:, a:b], ALU.add).then_inc(s["free"], 1)

            token_gemm_stage(nc, "proj", chunks, ring, evacuate, extra=("side",), then=gate_weights(d))

        qT = sb("q_turned", [P, 2, 4, SEQ])
        keyT = sb("k_turned", [P, SEQ])
        kcT = sb("kcT", [P, CTX])
        rope_turn(nc, g, qkv, kvc, rope, qT, keyT, kcT)
        items = []
        for b in range(NT_X):
            for h in range(8):
                kv = h // 4
                lo, hi = max(0, b - 1), min(NT_X, b + 2)
                mask = {0: masks[:, 640:1152], NT_X - 1: masks[:, 0:512]}.get(b, masks[:, 0:640])
                items.append(dict(
                    q=qT[:, kv, h % 4, b * P:(b + 1) * P], keys=[kcT[:, :], keyT[:, lo * P:hi * P]],
                    v=[kvc[:, t, P + HD * kv:P + HD * kv + HD] for t in range(NT_C)] +
                      [qkv[:, t, 640 + HD * kv:640 + HD * kv + HD] for t in range(lo, hi)],
                    mask=mask, sink=sinks[:, h:h + 1], half=h % 2,
                    out=attT[HD * (h % 2):HD * (h % 2) + HD, h // 2, b * P:(b + 1) * P], gate=None))
        attention_stage(nc, "window", items, HD ** -0.5, ident, early=early)


def rope_turn(nc, g, qkv, kvc, rope, qT, keyT, kcT):
    ident = g.ident[:, :]
    with ExitStack() as held:
        rot = held.enter_context(nc.sbuf_tensor("rot", [P, NT_X, 640], F32))
        tmp = held.enter_context(nc.sbuf_tensor("rot_tmp", [P, 2, 4, 320], F32))
        ps = held.enter_context(nc.psum_tensor("rot_ps", [P, 2, 1024], F32))
        with stage(nc, "rot", "parts", "rotated", "turned", "copied", "zero") as (s, block):
            @block.vector
            def _(dve):
                for m in range(NT_X):
                    src = qkv[:, m, 0:640].rearrange("p (h a b c) -> p b h a c", h=10, a=2, b=2)
                    dst = rot[:, m, :].rearrange("p (h a b c) -> p b h a c", h=10, a=2, b=2)
                    cos = rope[:, m, 0].unsqueeze(1).to_broadcast([P, 10, 2, 16])
                    sin = rope[:, m, 1].unsqueeze(1).to_broadcast([P, 10, 2, 16])
                    if m >= 2:
                        dve.wait_ge(s["rotated"], 2 * (m - 1))
                    part = [tmp[:, m % 2, i, :].rearrange("p (h a c) -> p h a c", h=10, a=2) for i in range(4)]
                    for i, (x, y) in enumerate(((0, cos), (1, sin), (1, cos), (0, sin))):
                        nc.vector.tensor_tensor(part[i], src[:, x], y, ALU.mult).then_inc(s["parts"], 1)
                    dve.wait_ge(s["parts"], 4 * m + 4)
                    nc.vector.tensor_tensor(dst[:, 0], part[0], part[1], ALU.subtract).then_inc(s["rotated"], 1)
                    nc.vector.tensor_tensor(dst[:, 1], part[2], part[3], ALU.add).then_inc(s["rotated"], 1)

            @block.gpsimd
            def _(pool):
                for kv in range(2):
                    rows = slice(HD * (1 - kv), HD * (1 - kv) + HD)
                    nc.gpsimd.memset(qT[rows, kv], 0.0).then_inc(s["zero"], 1)
                    pool.wait_ge(s["zero"], kv + 1)

            @block.tensor
            def _(pe):
                for m in range(NT_X + 1):
                    if m >= 2:
                        pe.wait_ge(s["copied"], m - 1)
                    if m < NT_X:
                        pe.wait_ge(s["rotated"], 2 * m + 2)
                        for j in range(5):
                            last = nc.tensor.transpose(ps[:, m % 2, j * P:(j + 1) * P], rot[:, m, j * P:(j + 1) * P], ident)
                    else:
                        for t in range(NT_C):
                            last = nc.tensor.transpose(ps[:, m % 2, t * P:(t + 1) * P], kvc[:, t, 0:P], ident)
                    last.then_inc(s["turned"], 1)

            @block.scalar
            def _(act):
                for m in range(NT_X + 1):
                    act.wait_ge(s["turned"], m + 1)
                    if m < NT_X:
                        for kv in range(2):
                            rows = slice(HD * kv, HD * kv + HD)
                            nc.scalar.copy(qT[rows, kv, :, m * P:(m + 1) * P],
                                           ps[rows, m % 2, 0:512].rearrange("p (j t) -> p j t", j=4))
                        nc.scalar.copy(keyT[:, m * P:(m + 1) * P], ps[:, m % 2, 512:640]).then_inc(s["copied"], 1)
                    else:
                        nc.scalar.copy(kcT[:, :], ps[:, m % 2, 0:CTX]).then_inc(s["copied"], 1)


def merge_gates(nc, d, ring, hT, gates):
    with ExitStack() as held:
        bias = held.enter_context(nc.sbuf_tensor("gates_bias", [P, 2 * D], F32))

        def tok(t):
            return lambda k: hT[:, k, t * P:(t + 1) * P]

        chunks = [dict(c, lhs=[tok(NT_C + m) for m in range(NT_X)]) for c in gate_weights(d)]

        def evacuate(s, block, work):
            @block.vector
            def _(dve):
                dve.wait_ge(s["side"], 16)
                for t, chunk, m, ps in work:
                    dve.wait_ge(s["tile"], t + 1)
                    a = chunk["col"]
                    nc.vector.tensor_tensor(gates[:, m, a:a + 512], ps, bias[:, a:a + 512], ALU.add).then_inc(s["free"], 1)

            @block.scalar
            def _(act):
                act.dma_start(bias[:, :], row_to_all(d["b_gates"], 2 * D)).then_inc(s["side"], 16)
                for t, chunk, m, ps in work:
                    act.wait_ge(s["free"], t + 1)
                    gate = gates[:, m, chunk["col"]:chunk["col"] + 512]
                    nc.scalar.activation(gate, gate, ACT.Sigmoid)

        token_gemm_stage(nc, "gates", chunks, ring, evacuate, extra=("side",), then=up_weights((d["w_up_att"], d["w_up_rwkv"])))


def rows_stage(nc, g, name, columns, rows, ones):
    with ExitStack() as held:
        diag = held.enter_context(nc.sbuf_tensor(f"{name}_diag", [P, 2, KD, P], F32))
        ps = held.enter_context(nc.psum_tensor(f"{name}_ps", [P, 2, 1024], F32))
        with stage(nc, name, "diag", "made", "copied") as (s, block):
            @block.vector
            def _(dve):
                for i, col in enumerate(columns):
                    if i >= 2:
                        dve.wait_ge(s["made"], i - 1)
                    for k in range(KD):
                        last = nc.vector.tensor_scalar(diag[:, i % 2, k, :], g.ident[:, :], col[:, k:k + 1], None, ALU.mult)
                    last.then_inc(s["diag"], 1)

            @block.tensor
            def _(pe):
                for i in range(len(columns)):
                    pe.wait_ge(s["diag"], i + 1)
                    if i >= 2:
                        pe.wait_ge(s["copied"], i - 1)
                    for half in range(2):
                        last = nc.tensor.matmul(ps[:, i % 2, 512 * half:512 * half + 512], ones,
                                                diag[:, i % 2, 4 * half:4 * half + 4, :].rearrange("p k n -> p (k n)"),
                                                start=True, stop=True)
                    last.then_inc(s["made"], 1)

            @block.scalar
            def _(act):
                for i, row in enumerate(rows):
                    act.wait_ge(s["made"], i + 1)
                    nc.scalar.copy(row, ps[:, i % 2, :]).then_inc(s["copied"], 1)


def add_normed_stage(nc, g, name, branch, x, row, early=None):
    n = len(x)
    with ExitStack() as held:
        squares = held.enter_context(nc.sbuf_tensor(f"{name}_sq", [P, D], F32))
        stat = held.enter_context(nc.sbuf_tensor(f"{name}_stat", [P, 3, n], F32))
        with stage(nc, name, "squared", "root", "inverse", "scaled", "added") as (s, block):
            if early is not None:
                @block.sync
                def _(sp):
                    early(sp)

            @block.scalar
            def _(act):
                for m in range(n):
                    if m:
                        act.wait_ge(s["squared"], m)
                    nc.scalar.activation(squares[:, :], branch[m], ACT.Square,
                                         accum_out=stat[:, 0, m:m + 1]).then_inc(s["squared"], 1)
                    act.wait_ge(s["squared"], m + 1)
                    nc.scalar.activation(stat[:, 1, m:m + 1], stat[:, 0, m:m + 1], ACT.Sqrt, scale=1.0 / D,
                                         bias=g.eps_col[:, 0:1]).then_inc(s["root"], 1)

            @block.vector
            def _(dve):
                for m in range(n):
                    dve.wait_ge(s["root"], m + 1)
                    nc.vector.reciprocal(stat[:, 2, m:m + 1], stat[:, 1, m:m + 1]).then_inc(s["inverse"], 1)
                    dve.wait_ge(s["inverse"], m + 1)
                    nc.vector.scalar_tensor_tensor(branch[m], branch[m], stat[:, 2, m:m + 1], row, ALU.mult,
                                                   ALU.mult).then_inc(s["scaled"], 1)
                    if m >= 1:
                        dve.wait_ge(s["scaled"], m)
                        nc.vector.tensor_tensor(x[m - 1], x[m - 1], branch[m - 1], ALU.add).then_inc(s["added"], 1)
                dve.wait_ge(s["scaled"], n)
                nc.vector.tensor_tensor(x[n - 1], x[n - 1], branch[n - 1], ALU.add).then_inc(s["added"], 1)


def up_weights(w_up):
    return [dict(w=w_up[b][:, 512 * c:512 * c + 512], width=512, k=4, b=b, c=c) for b in range(2) for c in range(2)]


def merge_and_out(nc, d, g, name, ring, branches, gates, w_up, w_out, mix, finish=None):
    with ExitStack() as held:
        merged = held.enter_context(nc.sbuf_tensor(f"{name}_merged", [P, NT_X, D], F32))
        tmp = held.enter_context(nc.sbuf_tensor(f"{name}_tmp", [P, 2, 512], F32))

        def tok(t, m):
            return lambda k: t[:, k, m * P:(m + 1) * P]

        chunks = [dict(c, lhs=[tok(branches[c["b"]], m) for m in range(NT_X)]) for c in up_weights(w_up)]
        out_weights = [dict(w=w_out[:, 512 * c:512 * c + 512], width=512, k=KD, c=c) for c in range(2)]

        def gated(s, block, work):
            @block.vector
            def _(dve):
                for t, chunk, m, ps in work:
                    dve.wait_ge(s["tile"], t + 1)
                    at = slice(512 * chunk["c"], 512 * chunk["c"] + 512)
                    gate = gates[:, m, D * chunk["b"] + at.start:D * chunk["b"] + at.stop]
                    if chunk["b"] == 0:
                        nc.vector.tensor_tensor(merged[:, m, at], ps, gate, ALU.mult).then_inc(s["free"], 1)
                    else:
                        if t > 8:
                            dve.wait_ge(s["chain"], t - 8)
                        nc.vector.tensor_tensor(tmp[:, t % 2, :], ps, gate, ALU.mult).then_inc(s["free"], 1)
                        dve.wait_ge(s["free"], t + 1)
                        nc.vector.tensor_tensor(merged[:, m, at], merged[:, m, at], tmp[:, t % 2, :],
                                                ALU.add).then_inc(s["chain"], 1)

        token_gemm_stage(nc, f"{name}_up", chunks, ring, gated, then=out_weights)
        mergedT = held.enter_context(nc.sbuf_tensor(f"{name}_mergedT", [P, KD, SEQ], F32))
        turn_stage(nc, f"{name}_turn", [merged[:, m, k * P:(k + 1) * P] for m in range(NT_X) for k in range(KD)],
                   [mergedT[:, k, m * P:(m + 1) * P] for m in range(NT_X) for k in range(KD)], g.ident[:, :])
        chunks = [dict(c, lhs=[tok(mergedT, m) for m in range(NT_X)]) for c in out_weights]

        def keep(s, block, work):
            @block.vector
            def _(dve):
                for t, chunk, m, ps in work:
                    dve.wait_ge(s["tile"], t + 1)
                    nc.vector.tensor_copy(mix[:, m, 512 * chunk["c"]:512 * chunk["c"] + 512], ps).then_inc(s["free"], 1)

        token_gemm_stage(nc, f"{name}_out", chunks, ring, finish or keep, extra=("out",))


N_EXP = 32
TOP_K = 4
SLOTS = P
MAX_BLOCKS = 48
LISTED = 50
LIMIT, ALPHA = 7.0, 1.702


def route_stage(nc, d, g, hT, ones, weights, xn, rows, weight, slot_of, token_of, table, n_blocks):
    with ExitStack() as held:
        def sb(name, shape, dtype=F32):
            return held.enter_context(nc.sbuf_tensor(name, shape, dtype))

        w = sb("router_w", [P, KD, N_EXP])
        bias = sb("router_b", [P, N_EXP])
        iota = sb("router_iota", [P, P])
        part = sb("router_part", [P, 1])
        before = sb("router_before", [P, P])
        logits = sb("router_logits", [P, NT_X, N_EXP])
        top = sb("router_top", [P, NT_X, 8])
        index = sb("router_index", [P, NT_X, 8], U32)
        indexf = sb("router_indexf", [P, NT_X, 8])
        number = sb("router_number", [P, NT_X, N_EXP])
        at_choice = sb("router_at_choice", [P, NT_X, TOP_K, N_EXP])
        hit = sb("router_hit", [P, NT_X, N_EXP])
        slotf = sb("router_slotf", [P, NT_X, TOP_K])
        place, home = (sb(f"router_{x}", [P, NT_X, TOP_K]) for x in ("place", "home"))
        in_block = sb("router_in_block", [P, NT_X * TOP_K, SLOTS])
        of_block = sb("router_of_block", [P, NT_X * TOP_K, LISTED])
        tokenf = sb("router_tokenf", [P, NT_X])
        negtop = sb("router_negtop", [P, NT_X])
        total = sb("router_total", [P, NT_X])
        chosen = sb("router_chosen", [P, NT_X, N_EXP])
        blocks, ends, starts, tmp = (sb(f"router_{x}", [P, N_EXP]) for x in ("blocks", "ends", "starts", "tmp"))
        expert = sb("router_expert", [P, 4])
        experti = sb("router_experti", [P, 1], I32)
        ps = held.enter_context(nc.psum_tensor("router_ps", [P, NT_X, 512], F32))
        ps_r = held.enter_context(nc.psum_tensor("router_rank", [P, 1, 512], F32))
        with stage(nc, "route", "loaded", "logits", "negtop", "weight", "chosen", "rank", "chain", "expert",
                   "table", "slots", "hot", "listed", "rows", "at", "top") as (s, block):
            @block.sync
            def _(sp):
                sp.dma_start(w[:, :, :], d["w_router"].rearrange("(k p) e -> p k e", p=P)).then_inc(s["loaded"], 16)
                sp.dma_start(bias[:, :], row_to_all(d["b_router"], N_EXP)).then_inc(s["loaded"], 16)
                sp.dma_start(iota[:, :], row_to_all(d["iota"], P)).then_inc(s["loaded"], 16)
                sp.dma_start(part[:, :], d["iota"].rearrange("(p a) -> p a", a=1)).then_inc(s["loaded"], 16)
                sp.dma_start(before[:, :], d["before"]).then_inc(s["loaded"], 16)
                sp.wait_ge(s["expert"], 2)
                sp.dma_start(table[0:1, :], experti[:, 0:1]).then_inc(s["table"], 16)
                sp.wait_ge(s["table"], 16)
                first = sp.value_load(table[0:1, 0:1], min_val=0, max_val=N_EXP - 1)
                for what in range(3 * GROUPS):
                    weights.load(sp, first, what, "a")

            @block.tensor
            def _(pe):
                pe.wait_ge(s["loaded"], 80)
                for m in range(NT_X):
                    for k in range(KD):
                        last = nc.tensor.matmul(ps[:, m, 0:N_EXP], hT[:, k, m * P:(m + 1) * P], w[:, k, :],
                                                start=(k == 0), stop=(k == KD - 1))
                    last.then_inc(s["logits"], 1)
                pe.wait_ge(s["chosen"], 1)
                nc.tensor.matmul(ps_r[:, 0, 0:NT_X * N_EXP], before[:, :], chosen[:, :, :].rearrange("p m e -> p (m e)"),
                                 start=True, stop=False, skip_group_check=True)
                for back in range(1, NT_X):
                    nc.tensor.matmul(ps_r[:, 0, back * N_EXP:NT_X * N_EXP], ones,
                                     chosen[:, 0:NT_X - back, :].rearrange("p m e -> p (m e)"), start=False,
                                     stop=(back == NT_X - 1), skip_group_check=True)
                for q in range(NT_X):
                    last = nc.tensor.matmul(ps_r[:, 0, 128:160], ones, chosen[:, q, :], start=False,
                                            stop=(q == NT_X - 1), skip_group_check=True)
                last.then_inc(s["rank"], 1)
                pe.wait_ge(s["hot"], 1)
                for c in range(NT_X * TOP_K):
                    last = nc.tensor.matmul(ps[:, 0, 0:LISTED], in_block[:, c, :], of_block[:, c, :], start=(c == 0),
                                            stop=(c == NT_X * TOP_K - 1))
                last.then_inc(s["listed"], 1)

            @block.scalar
            def _(act):
                act.wait_ge(s["loaded"], 80)
                act.dma_start(rows.rearrange("(m p) n -> p m n", p=P), xn[:, :, :]).then_inc(s["rows"], 16)
                for m in range(NT_X):
                    if m == 0:
                        act.wait_ge(s["negtop"], 1)
                    nc.scalar.activation(weight[:, m, :], top[:, m, 0:TOP_K], ACT.Exp, bias=negtop[:, m:m + 1],
                                         accum_out=total[:, m:m + 1]).then_inc(s["weight"], 1)
                act.wait_ge(s["rows"], 16)

            @block.vector
            def _(dve):
                step = chained(dve, s["chain"])
                dve.wait_ge(s["loaded"], 80)
                def per_expert(columns):
                    return columns.unsqueeze(2).to_broadcast([P, NT_X, N_EXP])

                experts_row = iota[:, 0:N_EXP].unsqueeze(1).to_broadcast([P, NT_X, N_EXP])
                dve.wait_ge(s["logits"], NT_X)
                step(nc.vector.tensor_tensor(logits[:, :, :], ps[:, :, 0:N_EXP],
                                             bias[:, :].unsqueeze(1).to_broadcast([P, NT_X, N_EXP]), ALU.add))
                for m in range(NT_X):
                    nc.vector.max(top[:, m, :], logits[:, m, :]).then_inc(s["top"], 1)
                dve.wait_ge(s["top"], NT_X)
                nc.vector.tensor_scalar(negtop[:, :].unsqueeze(2), top[:, :, 0:1], -1.0, None, ALU.mult) \
                    .then_inc(s["negtop"], 1)
                for m in range(NT_X):
                    nc.vector.max_index(index[:, m, :], top[:, m, :], logits[:, m, :]).then_inc(s["top"], 1)
                dve.wait_ge(s["top"], 2 * NT_X)
                step(nc.vector.tensor_copy(indexf[:, :, :], index[:, :, :]))
                step(nc.vector.tensor_tensor(chosen[:, :, :], experts_row, per_expert(indexf[:, :, 0]), ALU.is_equal))
                for j in range(1, TOP_K):
                    step(nc.vector.tensor_tensor(hit[:, :, :], experts_row, per_expert(indexf[:, :, j]), ALU.is_equal))
                    if j < TOP_K - 1:
                        step(nc.vector.tensor_tensor(chosen[:, :, :], chosen[:, :, :], hit[:, :, :], ALU.add))
                nc.vector.tensor_tensor(chosen[:, :, :], chosen[:, :, :], hit[:, :, :], ALU.add) \
                    .then_inc(s["chosen"], 1)
                dve.wait_ge(s["weight"], NT_X)
                step(nc.vector.reciprocal(total[:, :], total[:, :]))
                step(nc.vector.tensor_tensor(weight[:, :, :], weight[:, :, :],
                                             total[:, :].unsqueeze(2).to_broadcast([P, NT_X, TOP_K]), ALU.mult))
                dve.wait_ge(s["chosen"], 1)
                dve.wait_ge(s["rank"], 1)
                counts = ps_r[:, 0, 128:160]
                step(nc.vector.tensor_scalar(blocks[:, :], counts, 0.0, None, ALU.is_gt))
                for j in range(1, SEQ // SLOTS):
                    step(nc.vector.scalar_tensor_tensor(blocks[:, :], counts, float(SLOTS * j), blocks[:, :],
                                                        ALU.is_gt, ALU.add))
                step(nc.vector.memset(tmp[:, :], 1.0))
                step(nc.vector.tensor_tensor_scan(ends[:, :], tmp[:, :], blocks[:, :], 0.0, ALU.mult, ALU.add))
                step(nc.vector.tensor_tensor(starts[:, :], ends[:, :], blocks[:, :], ALU.subtract))
                step(nc.vector.tensor_scalar(tmp[:, :], ends[:, :], part[:, 0:1], None, ALU.is_le))
                step(nc.vector.tensor_reduce(expert[:, 0:1], tmp[:, :], AX.X, ALU.add))
                step(nc.vector.tensor_scalar(expert[:, 0:1], expert[:, 0:1], float(N_EXP - 1), None, ALU.min))
                nc.vector.tensor_copy(experti[:, :], expert[:, 0:1]).then_inc(s["expert"], 1)
                step(nc.vector.tensor_scalar(tmp[:, :], iota[:, 0:N_EXP], 2.0, None, ALU.mult))
                step(nc.vector.tensor_scalar(tmp[:, :], tmp[:, :], ends[:, N_EXP - 1:N_EXP], None, ALU.is_lt))
                step(nc.vector.tensor_reduce(expert[:, 1:2], tmp[:, :], AX.X, ALU.add))
                nc.vector.tensor_copy(n_blocks[0:1, :], expert[0:1, 1:2]).then_inc(s["expert"], 1)
                step(nc.vector.tensor_scalar(starts[:, :], starts[:, :], float(SLOTS), float(SLOTS), ALU.mult, ALU.add))
                ranks = ps_r[:, 0, 0:NT_X * N_EXP].rearrange("p (m e) -> p m e", e=N_EXP)
                step(nc.vector.tensor_tensor(number[:, :, :], ranks,
                                             starts[:, :].unsqueeze(1).to_broadcast([P, NT_X, N_EXP]), ALU.add))
                step(nc.vector.tensor_tensor(number[:, :, :], number[:, :, :], chosen[:, :, :], ALU.mult))
                for m in range(NT_X):
                    nc.vector.tensor_tensor(at_choice[:, m, :, :],
                                            iota[:, 0:N_EXP].unsqueeze(1).to_broadcast([P, TOP_K, N_EXP]),
                                            indexf[:, m, 0:TOP_K].unsqueeze(2).to_broadcast([P, TOP_K, N_EXP]),
                                            ALU.is_equal).then_inc(s["at"], 1)
                    nc.vector.tensor_scalar(tokenf[:, m:m + 1], part[:, 0:1], float(P * m), None,
                                            ALU.add).then_inc(s["at"], 1)
                dve.wait_ge(s["at"], 2 * NT_X)
                for m in range(NT_X):
                    nc.vector.tensor_tensor(at_choice[:, m, :, :], at_choice[:, m, :, :],
                                            number[:, m, :].unsqueeze(1).to_broadcast([P, TOP_K, N_EXP]),
                                            ALU.mult).then_inc(s["at"], 1)
                dve.wait_ge(s["at"], 3 * NT_X)
                step(nc.vector.tensor_reduce(slotf[:, :, :].rearrange("p m j -> p (m j)"),
                                             at_choice[:, :, :, :].rearrange("p m j e -> p (m j) e"), AX.X, ALU.add))
                step(nc.vector.tensor_scalar(home[:, :, :], slotf[:, :, :], 1.0 / SLOTS, -(SLOTS - 1) / (2.0 * SLOTS),
                                             ALU.mult, ALU.add))
                step(nc.vector.tensor_scalar(home[:, :, :], home[:, :, :], ROUND, None, ALU.add))
                step(nc.vector.tensor_scalar(home[:, :, :], home[:, :, :], -ROUND, None, ALU.add))
                step(nc.vector.scalar_tensor_tensor(place[:, :, :], home[:, :, :], -float(SLOTS), slotf[:, :, :],
                                                    ALU.mult, ALU.add))
                step(nc.vector.tensor_scalar(home[:, :, :], home[:, :, :], -1.0, None, ALU.add))
                step(nc.vector.tensor_tensor(in_block[:, :, :],
                                             iota[:, :].unsqueeze(1).to_broadcast([P, NT_X * TOP_K, SLOTS]),
                                             place[:, :, :].rearrange("p m j -> p (m j)").unsqueeze(2)
                                             .to_broadcast([P, NT_X * TOP_K, SLOTS]), ALU.is_equal))
                step(nc.vector.tensor_tensor(of_block[:, :, :],
                                             iota[:, 0:LISTED].unsqueeze(1).to_broadcast([P, NT_X * TOP_K, LISTED]),
                                             home[:, :, :].rearrange("p m j -> p (m j)").unsqueeze(2)
                                             .to_broadcast([P, NT_X * TOP_K, LISTED]), ALU.is_equal))
                for m in range(NT_X):
                    part_of = of_block[:, m * TOP_K:(m + 1) * TOP_K, :]
                    step(nc.vector.tensor_scalar(part_of, part_of, tokenf[:, m:m + 1], None, ALU.mult))
                nc.vector.tensor_copy(slot_of[:, :, :], slotf[:, :, :]).then_inc(s["hot"], 1)
                dve.wait_ge(s["listed"], 1)
                nc.vector.tensor_copy(token_of[:, :], ps[:, 0, 0:LISTED]).then_inc(s["slots"], 1)


def spread(row, n):
    return row.unsqueeze(0).to_broadcast([P, n])


GROUPS = 4


class ExpertWeights:

    def __init__(self, nc, d, held):
        self.gu = held.enter_context(nc.sbuf_tensor("w_gu", [P, KD, 2 * D], F32))
        self.dn = held.enter_context(nc.sbuf_tensor("w_dn", [P, KD, D], F32))
        self.arrived = {p: [held.enter_context(nc.semaphore(f"w_{p}{i}")) for i in range(3 * GROUPS)] for p in "ab"}
        self.gu_v = d["w_gate_up"].rearrange("e (k p) n -> e p k n", p=P)
        self.dn_v = d["w_down"].rearrange("e (k p) n -> e p k n", p=P)

    def load(self, sp, expert, what, parity):
        k = slice(2 * (what % 4), 2 * (what % 4) + 2)
        if what < 8:
            half = slice(D * (what // 4), D * (what // 4) + D)
            to, src = self.gu[:, k, half], self.gu_v[expert][:, k, half]
        else:
            to, src = self.dn[:, k, :], self.dn_v[expert][:, k, :]
        sp.dma_start(to, src).then_inc(self.arrived[parity][what], 16)


def experts(nc, d, g, weights, rows, gain, shift, token_of, table, n_blocks):
    ident = g.ident[:, :]
    gu, dn, arrived, load = weights.gu, weights.dn, weights.arrived, weights.load
    slot_rows = nc.dram_tensor("slot_rows", ((MAX_BLOCKS + 1) * SLOTS, D), I32).ap()
    with ExitStack() as held:
        def sb(name, shape, dtype=F32):
            return held.enter_context(nc.sbuf_tensor(name, shape, dtype))

        b_gu = sb("b_gu", [P, 2 * D])
        b_dn = {p: sb(f"b_dn_{p}", [P, D]) for p in "ab"}
        tokens = sb("tokens", [P, 1], U32)
        xg = sb("xg", [P, D])
        xgT = sb("xgT", [P, KD, SLOTS])
        biased = sb("biased", [P, 512])
        ga, up, sg = (sb(x, [P, 256]) for x in ("ga", "up", "sg"))
        act_sb = sb("act_sb", [P, D])
        actT = sb("actT", [P, KD, SLOTS])
        yb = sb("yb", [P, D])
        ps_dn = held.enter_context(nc.psum_tensor("moe_down_ps", [P, 2, 512], F32))
        gathered = held.enter_context(nc.semaphore("gathered"))
        stored = {p: held.enter_context(nc.semaphore(f"rows_stored_{p}")) for p in "ab"}
        def turn_gathered(ps, half, signal):
            for k in range(4):
                last = nc.tensor.transpose(ps[:, 1 - half, k * P:(k + 1) * P],
                                           xg[:, (4 * half + k) * P:(4 * half + k + 1) * P], ident)
            last.then_inc(signal, 1)

        def modulate(ps, half, signal):
            for k in range(4 * half, 4 * half + 4):
                last = nc.scalar.activation(xgT[:, k, :], ps[:, 1 - half, (k % 4) * P:(k % 4 + 1) * P], ACT.Identity,
                                            scale=gain[:, k:k + 1], bias=shift[:, k:k + 1])
            last.then_inc(signal, 1)

        def keep_rows(dve, before, signal):
            dve.wait_ge(stored[before], 32)
            for n in range(2):
                nc.vector.tensor_tensor(yb[:, 512 * n:512 * n + 512], ps_dn[:, n, :],
                                        b_dn[before][:, 512 * n:512 * n + 512], ALU.add).then_inc(signal, 1)

        def store_rows(act, v, signal, parity):
            for n in range(2):
                act.wait_ge(signal, n + 1)
                act.dma_start(slot_rows[bass.ds(v * SLOTS, SLOTS), 512 * n:512 * n + 512],
                              yb[:, 512 * n:512 * n + 512].bitcast(I32)).then_inc(stored[parity], 16)

        def expert_block(parity, other, v):
            w_here = arrived[parity]
            with nc.psum_tensor(f"moe_ps_{parity}", [P, 6, 512], F32) as ps, \
                    stage(nc, f"moe_{parity}", "bias", "tokens", "gu_used", "chain", "ga", "sig", "acted", "turned", "actT",
                          "dn_used", "yb", "xg_turned", "xgT", clear=w_here + [stored[other]], pool_dma=(gathered,)) as (s, block):
                @block.sync
                def _(sp):
                    after = sp.value_load(table[0:1, bass.ds(v + 1, 1)], min_val=0, max_val=N_EXP - 1)
                    for what in range(3 * GROUPS):
                        if what < 2 * GROUPS:
                            sp.wait_ge(s["gu_used"], what + 1)
                        else:
                            sp.wait_ge(s["dn_used"], what - 2 * GROUPS + 1)
                        load(sp, after, what, other)

                @block.gpsimd
                def _(pool):
                    pool.wait_ge(s["tokens"], 1)
                    nc.gpsimd.indirect_dma_start(xg[:, :], None, rows,
                                                 bass.IndirectOffsetOnAxis(ap=tokens[:, 0:1], axis=0)) \
                        .then_inc(gathered, 16)
                    pool.wait_ge(gathered, 16)

                @block.tensor
                def _(pe):
                    for half in range(2):
                        for k in range(KD):
                            if k % 2 == 0:
                                pe.wait_ge(w_here[half * GROUPS + k // 2], 16)
                            for n in range(2):
                                at = D * half + 512 * n
                                last = nc.tensor.matmul(ps[:, 2 + 2 * half + n, :], xgT[:, k, :], gu[:, k, at:at + 512],
                                                        start=(k == 0), stop=(k == KD - 1))
                            if k % 2:
                                last.then_inc(s["gu_used"], 1)

                    def turn_act(half):
                        pe.wait_ge(s["acted"], 2 * half + 2)
                        for k in range(4):
                            last = nc.tensor.transpose(ps[:, half, k * P:(k + 1) * P],
                                                       act_sb[:, (4 * half + k) * P:(4 * half + k + 1) * P], ident)
                        last.then_inc(s["turned"], 1)

                    def down(half):
                        pe.wait_ge(s["actT"], half + 1)
                        for k in range(4 * half, 4 * half + 4):
                            if k % 2 == 0:
                                pe.wait_ge(w_here[2 * GROUPS + k // 2], 16)
                            for n in range(2):
                                last = nc.tensor.matmul(ps_dn[:, n, :], actT[:, k, :], dn[:, k, 512 * n:512 * n + 512],
                                                        start=(k == 0), stop=(k == KD - 1))
                            if k % 2:
                                last.then_inc(s["dn_used"], 1)

                    turn_act(0)
                    pe.wait_ge(gathered, 16)
                    turn_gathered(ps, 0, s["xg_turned"])
                    pe.wait_ge(s["yb"], 2)
                    down(0)
                    pe.wait_ge(s["xgT"], 1)
                    turn_act(1)
                    turn_gathered(ps, 1, s["xg_turned"])
                    down(1)

                @block.scalar
                def _(act):
                    here = act.value_load(table[0:1, bass.ds(v, 1)], min_val=0, max_val=N_EXP - 1)
                    act.dma_start(b_gu[:, :], spread(d["b_gate_up"][here], 2 * D)).then_inc(s["bias"], 16)
                    act.dma_start(b_dn[parity][:, :], spread(d["b_down"][here], D)).then_inc(s["bias"], 16)
                    store_rows(act, v, s["yb"], parity)
                    for n in range(2):
                        act.wait_ge(s["ga"], n + 1)
                        nc.scalar.activation(sg[:, :], ga[:, :], ACT.Sigmoid, scale=ALPHA).then_inc(s["sig"], 1)

                    def keep_turned(half):
                        act.wait_ge(s["turned"], half + 1)
                        nc.scalar.copy(actT[:, 4 * half:4 * half + 4, :],
                                       ps[:, half, :].rearrange("p (k t) -> p k t", k=4)).then_inc(s["actT"], 1)

                    keep_turned(0)
                    act.wait_ge(s["ga"], 3)
                    nc.scalar.activation(sg[:, :], ga[:, :], ACT.Sigmoid, scale=ALPHA).then_inc(s["sig"], 1)
                    act.wait_ge(s["ga"], 4)
                    nc.scalar.activation(sg[:, :], ga[:, :], ACT.Sigmoid, scale=ALPHA).then_inc(s["sig"], 1)
                    act.wait_ge(s["xg_turned"], 1)
                    modulate(ps, 0, s["xgT"])
                    keep_turned(1)
                    act.wait_ge(s["xg_turned"], 2)
                    modulate(ps, 1, s["xgT"])

                @block.vector
                def _(dve):
                    step = chained(dve, s["chain"])
                    nc.vector.tensor_copy(tokens[:, :], token_of[:, bass.ds(v + 1, 1)]).then_inc(s["tokens"], 1)
                    keep_rows(dve, other, s["yb"])
                    dve.wait_ge(s["bias"], 32)
                    for n in range(4):
                        dve.wait_ge(s["gu_used"], GROUPS * (n // 2 + 1))
                        pairs = biased[:, :].rearrange("p (c a) -> p c a", a=2)
                        step(nc.vector.tensor_tensor(biased[:, :], ps[:, 2 + n, :], b_gu[:, 512 * n:512 * n + 512], ALU.add))
                        nc.vector.tensor_scalar(ga[:, :], pairs[:, :, 0], LIMIT, None, ALU.min).then_inc(s["ga"], 1)
                        step(nc.vector.tensor_scalar(up[:, :], pairs[:, :, 1], LIMIT, -LIMIT, ALU.min, ALU.max))
                        dve.wait_ge(s["ga"], n + 1)
                        step(nc.vector.scalar_tensor_tensor(up[:, :], up[:, :], 1.0, ga[:, :], ALU.add, ALU.mult))
                        dve.wait_ge(s["sig"], n + 1)
                        nc.vector.tensor_tensor(act_sb[:, 256 * n:256 * n + 256], up[:, :], sg[:, :],
                                                ALU.mult).then_inc(s["acted"], 1)
                        dve.wait_ge(s["acted"], n + 1)

        with nc.psum_tensor("moe_ps_start", [P, 2, 512], F32) as ps, \
                stage(nc, "moe_start", "tokens", "zero", "xg_turned", "xgT", pool_dma=(gathered,)) as (s, block):
            @block.vector
            def _(dve):
                nc.vector.tensor_copy(tokens[:, :], token_of[:, 0:1]).then_inc(s["tokens"], 1)
                nc.vector.memset(ps_dn[:, :, :], 0.0).then_inc(s["zero"], 1)
                nc.vector.memset(b_dn["b"][:, :], 0.0).then_inc(s["zero"], 1)

            @block.gpsimd
            def _(pool):
                pool.wait_ge(s["tokens"], 1)
                nc.gpsimd.indirect_dma_start(xg[:, :], None, rows,
                                             bass.IndirectOffsetOnAxis(ap=tokens[:, 0:1], axis=0)).then_inc(gathered, 16)
                pool.wait_ge(gathered, 16)

            @block.tensor
            def _(pe):
                pe.wait_ge(gathered, 16)
                turn_gathered(ps, 0, s["xg_turned"])
                turn_gathered(ps, 1, s["xg_turned"])

            @block.scalar
            def _(act):
                for half in range(2):
                    act.wait_ge(s["xg_turned"], half + 1)
                    modulate(ps, half, s["xgT"])
                nc.scalar.copy(yb[:, 0:1], shift[:, 0:1]).then_inc(stored["b"], 32)

        turns = nc.values_load(n_blocks[0:1, 0:1], min_val=1, max_val=MAX_BLOCKS // 2)
        with nc.Fori(0, turns) as turn:
            for parity, other in ("ab", "ba"):
                expert_block(parity, other, turn * 2 + (parity == "b"))
        with stage(nc, "moe_end", "yb", clear=arrived["a"] + [stored["a"], stored["b"]]) as (s, block):
            @block.vector
            def _(dve):
                keep_rows(dve, "b", s["yb"])

            @block.scalar
            def _(act):
                store_rows(act, turns * 2, s["yb"], "a")
                act.wait_ge(stored["a"], 32)

            @block.sync
            def _(sp):
                for w in arrived["a"]:
                    sp.wait_ge(w, 16)
    return slot_rows


def combine(nc, slot_rows, weight, slot_of, y):
    n = NT_X * TOP_K
    with nc.sbuf_tensor("slot_in", [P, n, D], F32) as taken, ExitStack() as held:
        arrived = [held.enter_context(nc.semaphore(f"slot_rows_of_tile{m}")) for m in range(NT_X)]
        s, block = held.enter_context(stage(nc, "combine", "summed", pool_dma=arrived))

        @block.gpsimd
        def _(pool):
            for i in range(n):
                nc.gpsimd.indirect_dma_start(
                    taken[:, i, :].bitcast(I32), None, slot_rows,
                    bass.IndirectOffsetOnAxis(ap=slot_of[:, i // TOP_K, i % TOP_K:i % TOP_K + 1], axis=0)) \
                    .then_inc(arrived[i // TOP_K], 16)
            for m in range(NT_X):
                pool.wait_ge(arrived[m], 16 * TOP_K)

        @block.vector
        def _(dve):
            for m in range(NT_X):
                dve.wait_ge(arrived[m], 16 * TOP_K)
                for j in range(TOP_K):
                    row, w = taken[:, m * TOP_K + j, :], weight[:, m, j:j + 1]
                    if j == 0:
                        nc.vector.tensor_scalar(y[:, m, :], row, w, None, ALU.mult).then_inc(s["summed"], 1)
                    else:
                        dve.wait_ge(s["summed"], m * TOP_K + j)
                        nc.vector.scalar_tensor_tensor(y[:, m, :], row, w, y[:, m, :], ALU.mult,
                                                       ALU.add).then_inc(s["summed"], 1)


CH = 64
N_CHUNKS = NTOK // CH
SEG = 4
SEG_TOK = SEG * CH
LEVELS = 6
DECAY = float(-np.exp(np.float32(-0.5)))
GN_EPS = 64e-5
PAIR_COLS = ("b_r", "b_k", "b_v", "prev_r", "prev_k", "prev_v", "next_r", "next_k", "next_v", "w0_f", "w0_b",
             "a0_f", "a0_b", "k_k", "k_a", "r_k", "ln_w", "ln_b")
PC = {name: i for i, name in enumerate(PAIR_COLS)}


def shift_tokens(nc, step, zp, out_ctx, out_x, tmp, keep, prev, nxt):
    step(nc.vector.tensor_scalar(tmp[:, 0:769], zp[:, 1:770], keep, None, ALU.mult))
    step(nc.vector.scalar_tensor_tensor(tmp[:, 0:769], zp[:, 0:769], prev, tmp[:, 0:769], ALU.mult, ALU.add))
    nc.vector.scalar_tensor_tensor(out_ctx, zp[:, 2:258], nxt, tmp[:, 0:256], ALU.mult, ALU.add)
    step(nc.vector.scalar_tensor_tensor(out_x, zp[:, 259:771], nxt, tmp[:, 257:769], ALU.mult, ALU.add))


def channel_project(nc, name, w_sb, w_here, loads, hT, bias, finish, late=None):
    with nc.psum_tensor(f"{name}_ps", [P, 3, 1024], F32) as ps, \
            nc.sbuf_tensor(f"{name}_padded", [P, 3, NTOK + 4], F32) as zp, \
            nc.sbuf_tensor(f"{name}_tmp", [P, NTOK + 4], F32) as tmp, \
            nc.sbuf_tensor(f"{name}_keep", [P, 3], F32) as keep, \
            stage(nc, name, "w", "made", "biased", "chain", *(late.SIGNALS if late else ()), clear=(w_here,)) as (s, block):
        @block.sync
        def _(sp):
            for to, what in loads:
                sp.dma_start(to, what).then_inc(s["w"], 16)
            if late:
                late.loads(sp, s)

        @block.tensor
        def _(pe):
            pe.wait_ge(w_here, 16)
            for i in range(3):
                for lo, n, at in ((0, CTX, 0), (CTX, SEQ, 512)):
                    for k in range(KD):
                        last = nc.tensor.matmul(ps[:, i, at:at + n], w_sb[:, k, i * P:(i + 1) * P],
                                                hT[:, k, lo:lo + n], start=(k == 0), stop=(k == KD - 1))
                last.then_inc(s["made"], 1)
            if late:
                late.products(pe, s)

        @block.scalar
        def _(act):
            act.wait_ge(s["w"], 16 * len(loads))
            for i in range(3):
                act.wait_ge(s["made"], i + 1)
                nc.scalar.activation(zp[:, i, 1:1 + CTX], ps[:, i, 0:CTX], ACT.Identity, bias=bias(i))
                nc.scalar.activation(zp[:, i, 2 + CTX:2 + NTOK], ps[:, i, 512:1024], ACT.Identity,
                                     bias=bias(i)).then_inc(s["biased"], 1)
            if late:
                late.keep(act, s)

        @block.vector
        def _(dve):
            step = chained(dve, s["chain"])
            for zero in (0, 1 + CTX, 2 + NTOK):
                step(nc.vector.memset(zp[:, :, zero:zero + 1], 0.0))
            dve.wait_ge(s["w"], 16 * len(loads))
            finish(dve, step, s, zp, tmp, keep)


def rwkv_branch(nc, d, g, late, hT, scratch, rwkT):
    ident = g.ident[:, :]
    with ExitStack() as held:
        def sb(name, shape, dtype=F32):
            return held.enter_context(nc.sbuf_tensor(name, shape, dtype))

        w_sb = scratch[:, 0:KD * 384].rearrange("p (k n) -> p k n", n=384)
        lora = sb("lora", [P, 3, NTOK])
        segment = sb("segment", [P, NTOK])
        tri = sb("tri", [P, 2, 2, P])
        off = sb("off", [P, 2, LEVELS, P])
        heads = sb("heads", [P, 2, P])
        eps = sb("gn_eps", [P, 1])

        def lora_finish(dve, step, s, zp, tmp, keep):
            v = g.vec
            step(nc.vector.tensor_tensor(keep[:, :], v[:, VCOL["lora_mu_prev"]], v[:, VCOL["lora_mu_next"]], ALU.add))
            step(nc.vector.tensor_scalar(keep[:, :], keep[:, :], -1.0, 1.0, ALU.mult, ALU.add))
            step(nc.vector.memset(eps[:, :], GN_EPS))
            for i in range(3):
                dve.wait_ge(s["biased"], i + 1)
                p0, n0 = VCOL["lora_mu_prev"].start + i, VCOL["lora_mu_next"].start + i
                shift_tokens(nc, step, zp[:, i], lora[:, i, 0:CTX], lora[:, i, CTX:NTOK], tmp, keep[:, i:i + 1],
                             v[:, p0:p0 + 1], v[:, n0:n0 + 1])

        b0 = VCOL["lora_b_in"].start
        w_here = held.enter_context(nc.semaphore("rwkv_w_here"))
        with stage(nc, "lora_w", "none") as (s, block):
            @block.sync
            def _(sp):
                sp.dma_start(w_sb, d["w_lora_in"]).then_inc(w_here, 16)
        channel_project(nc, "lora_z", w_sb, w_here,
                        [(segment[:, :], d["segment"]), (tri[:, :, :, :], d["tri"]), (off[:, :, :, :], d["off"]), (heads[:, :, :], d["heads"])],
                        hT, lambda i: g.vec[:, b0 + i:b0 + i + 1], lora_finish)
        f = {n: sb(f"f_{n}", [P, NTOK]) for n in
             ("r", "k", "v", "a", "k0", "k1", "b0", "b1", "excl0", "excl1", "incl0", "incl1", "neg0", "neg1",
              "tail0", "tail1")}
        cols = sb("pair_cols", [P, len(PAIR_COLS)])
        at = KD * 384
        low = scratch[:, at:at + 5 * P].rearrange("p (q n) -> p q n", n=P)
        bonus = sb("bonus", [P, SEQ])
        gate = sb("gate", [P, SEQ])
        total = sb("total_decay", [P, 2, N_CHUNKS])
        y = sb("y", [P, SEQ])
        state = sb("state", [P, 2, 2, P])
        seg = {n: sb(f"bd_{n}", [P, 2, SEG, P]) for n in ("b", "k", "bt", "kt", "v")}
        seg["ar"] = sb("bd_ar", [P, 2, SEG, 2, P])
        with stage(nc, "lora_act", "done", "zero") as (s, block):
            @block.sync
            def _(sp):
                sp.dma_start(w_sb, d["w_rkv"][0]).then_inc(w_here, 16)

            @block.scalar
            def _(act):
                nc.scalar.activation(lora[:, 0, :], lora[:, 0, :], ACT.Tanh).then_inc(s["done"], 1)
                nc.scalar.activation(lora[:, 2, :], lora[:, 2, :], ACT.Sigmoid).then_inc(s["done"], 1)

            @block.gpsimd
            def _(pool):
                for t in seg.values():
                    nc.gpsimd.memset(t[:], 0.0).then_inc(s["zero"], 1)

        with nc.Fori(0, 4) as pair:
            def pair_finish(dve, step, s, zp, tmp, keep):
                step(nc.vector.tensor_tensor(keep[:, :], cols[:, 3:6], cols[:, 6:9], ALU.add))
                step(nc.vector.tensor_scalar(keep[:, :], keep[:, :], -1.0, 1.0, ALU.mult, ALU.add))
                for i, n in enumerate("rkv"):
                    late.sums(dve, s, ((0, 1), (2,), ())[i])
                    dve.wait_ge(s["biased"], i + 1)
                    shift_tokens(nc, step, zp[:, i], f[n][:, 0:CTX], f[n][:, CTX:NTOK], tmp, keep[:, i:i + 1],
                                 cols[:, 3 + i:4 + i], cols[:, 6 + i:7 + i])

            with ExitStack() as projecting:
                late.open(d, pair, projecting)
                channel_project(nc, "pair_z", w_sb, w_here,
                                [(cols[:, :], d["pair_cols"][pair]), (low, d["pair_low"][pair])],
                                hT, lambda i: cols[:, i:i + 1], pair_finish, late)
            pair_features(nc, g, f, cols, low, lora, heads, segment, bonus, gate, total)
            with stage(nc, "state0", "done") as (s, block):
                @block.sync
                def _(sp):
                    sp.dma_start(w_sb, d["w_rkv"][pair + 1]).then_inc(w_here, 16)

                @block.gpsimd
                def _(pool):
                    nc.gpsimd.memset(state[:, :, 0, :], 0.0).then_inc(s["done"], 1)
            for n in range(3):
                pair_segment(nc, g, n, f, seg, tri, off, total, state, y)
            pair_output(nc, g, pair, y, bonus, gate, cols, heads, eps, rwkT)
        with stage(nc, "rwkv_end", "none", clear=(w_here,)) as (s, block):
            @block.sync
            def _(sp):
                sp.wait_ge(w_here, 16)


def pair_features(nc, g, f, cols, low, lora, heads, segment, bonus, gate, total):
    def col(n):
        return cols[:, PC[n]:PC[n] + 1]

    halves = ((0, 512), (512, 256))
    with ExitStack() as held:
        ps = held.enter_context(nc.psum_tensor("feat_ps", [P, 4, 1024], F32))
        one_ka = held.enter_context(nc.sbuf_tensor("one_ka", [P, 1], F32))
        t1 = held.enter_context(nc.sbuf_tensor("feat_t1", [P, NTOK], F32))
        t2 = held.enter_context(nc.sbuf_tensor("feat_t2", [P, SEQ], F32))
        sg = [held.enter_context(nc.sbuf_tensor(f"feat_sg{i}", [P, NTOK], F32)) for i in range(2)]
        with stage(nc, "feat", "low", "rates", "squares", "sums", "rooted", "chain", "rk", "bonus", "gate", "gated",
                   "sums_in", "prep", "exped", "one_ka", "kdir") as (s, block):
            @block.gpsimd
            def _(pool):
                pool.wait_ge(s["one_ka"], 1)
                for i in range(2):
                    kd = f["k%d" % i]
                    pool.wait_ge(s["rates"], 3 + i)
                    nc.gpsimd.tensor_scalar(kd[:, :], f["b%d" % i][:, :], col("k_a"), one_ka[:, :], ALU.mult,
                                            ALU.add).then_inc(s["kdir"], 1)
                    pool.wait_ge(s["kdir"], 2 * i + 1)
                    nc.gpsimd.tensor_tensor(kd[:, :], kd[:, :], f["k"][:, :], ALU.mult).then_inc(s["kdir"], 1)

            @block.tensor
            def _(pe):
                for q in range(4):
                    for at, n in halves:
                        last = nc.tensor.matmul(ps[:, q, at:at + n], low[:, q, :], lora[:, q // 2, at:at + n],
                                                start=True, stop=True)
                    last.then_inc(s["low"], 1)
                pe.wait_ge(s["rates"], 2)
                pe.wait_ge(s["squares"], 1)
                for at, n in halves:
                    last = nc.tensor.matmul(ps[:, 0, at:at + n], heads[:, 0, :], t1[:, at:at + n], start=True, stop=True)
                last.then_inc(s["sums"], 1)
                nc.tensor.matmul(ps[:, 1, 0:SEQ], low[:, 4, :], lora[:, 2, CTX:NTOK], start=True,
                                 stop=True).then_inc(s["gate"], 1)
                pe.wait_ge(s["rates"], 4)
                pe.wait_ge(s["rk"], 1)
                nc.tensor.matmul(ps[:, 2, 0:SEQ], heads[:, 0, :], t2[:, :], start=True, stop=True).then_inc(s["bonus"], 1)

            @block.scalar
            def _(act):
                rate = (sg[0], sg[1], f["b0"], f["b1"])
                for q, (to, bias) in enumerate(zip(rate, ("w0_f", "w0_b", "a0_f", "a0_b"))):
                    act.wait_ge(s["low"], q + 1)
                    nc.scalar.activation(to[:, :], ps[:, q, 0:NTOK], ACT.Sigmoid, bias=col(bias)).then_inc(s["rates"], 1)
                act.wait_ge(s["gate"], 1)
                nc.scalar.copy(gate[:, :], ps[:, 1, 0:SEQ]).then_inc(s["gated"], 1)
                act.wait_ge(s["sums"], 1)
                nc.scalar.activation(t1[:, :], ps[:, 0, 0:NTOK], ACT.Sqrt).then_inc(s["rooted"], 1)
                for i in range(2):
                    act.wait_ge(s["prep"], 1 + i)
                    for to, sign in ((f["neg%d" % i], -1.0),):
                        nc.scalar.activation(to[:, :], f["incl%d" % i][:, :], ACT.Exp, scale=-DECAY).then_inc(s["exped"], 1)
                    act.wait_ge(s["exped"], 4 * i + 1)
                    for n in ("incl%d" % i, "excl%d" % i, "tail%d" % i):
                        nc.scalar.activation(f[n][:, :], f[n][:, :], ACT.Exp, scale=DECAY).then_inc(s["exped"], 1)
                    nc.scalar.activation(total[:, i, :], total[:, i, :], ACT.Exp, scale=DECAY)

            @block.vector
            def _(dve):
                step = chained(dve, s["chain"])
                nc.vector.tensor_scalar(one_ka[:, :], col("k_a"), -1.0, 1.0, ALU.mult, ALU.add).then_inc(s["one_ka"], 1)
                step(nc.vector.tensor_scalar(f["a"][:, :], f["k"][:, :], col("k_k"), None, ALU.mult))
                nc.vector.tensor_tensor(t1[:, :], f["a"][:, :], f["a"][:, :], ALU.mult).then_inc(s["squares"], 1)
                for i in range(2):
                    dve.wait_ge(s["rates"], i + 1)
                    cp = f["incl0" if i == 0 else "tail1"]
                    step(nc.vector.tensor_tensor_scan(cp[:, :], segment[:, :], sg[i][:, :], 0.0, ALU.mult, ALU.add))
                    cp3 = cp[:, :].rearrange("p (c t) -> p c t", t=CH)
                    end = cp3[:, :, CH - 1:CH]
                    step(nc.vector.tensor_copy(total[:, i, :].unsqueeze(2), end))
                    tot = total[:, i, :].unsqueeze(2).to_broadcast([P, N_CHUNKS, CH])
                    rest = f["tail0" if i == 0 else "excl1"]
                    step(nc.vector.tensor_tensor(rest[:, :].rearrange("p (c t) -> p c t", t=CH), tot, cp3, ALU.subtract))
                    if i == 0:
                        nc.vector.tensor_tensor(f["excl0"][:, :], cp[:, :], sg[0][:, :], ALU.subtract).then_inc(s["prep"], 1)
                    else:
                        step(nc.vector.tensor_tensor(f["incl1"][:, :], rest[:, :], sg[1][:, :], ALU.add))
                        nc.vector.tensor_tensor(cp[:, :], cp[:, :], sg[1][:, :], ALU.subtract).then_inc(s["prep"], 1)
                dve.wait_ge(s["kdir"], 4)
                x = slice(CTX, NTOK)
                step(nc.vector.tensor_tensor(t2[:, :], f["k0"][:, x], f["k1"][:, x], ALU.add))
                nc.vector.scalar_tensor_tensor(t2[:, :], t2[:, :], col("r_k"), f["r"][:, x], ALU.mult,
                                               ALU.mult).then_inc(s["rk"], 1)
                dve.wait_ge(s["rooted"], 1)
                step(nc.vector.tensor_scalar(t1[:, :], t1[:, :], 1e-12, None, ALU.max))
                step(nc.vector.reciprocal(t1[:, :], t1[:, :]))
                step(nc.vector.tensor_tensor(f["a"][:, :], f["a"][:, :], t1[:, :], ALU.mult))
                for i in range(2):
                    step(nc.vector.tensor_tensor(f["b%d" % i][:, :], f["b%d" % i][:, :], f["a"][:, :], ALU.mult))
                step(nc.vector.tensor_scalar(f["a"][:, :], f["a"][:, :], -1.0, None, ALU.mult))
                dve.wait_ge(s["bonus"], 1)
                nc.vector.tensor_tensor(bonus[:, :], f["v"][:, x], ps[:, 2, 0:SEQ], ALU.mult).then_inc(s["sums_in"], 1)


def segment_tokens(n, direction):
    return (0, (CTX, CTX + SEG_TOK)[direction], (CTX + SEG_TOK, CTX)[direction])[n]


def pair_segment(nc, g, n, f, seg, tri, off, total, state, y):
    ident = g.ident[:, :]
    has_y = n > 0
    start = [segment_tokens(n, i) for i in range(2)]
    last_level = LEVELS - 1
    with ExitStack() as held:
        def sb(name, shape):
            return held.enter_context(nc.sbuf_tensor(f"{name}_{n}", shape, F32))

        gb, gk = sb("gb", [P, 2, SEG, 2, P]), sb("gk", [P, 2, SEG, 2, P])
        aoff = sb("aoff", [P, 2, 2, SEG, P])
        tmat, qmat, wmat = (sb(x, [P, 2, SEG, P]) for x in ("tmat", "qmat", "wmat"))
        btT, ktT, vbd = (sb(x, [P, 2, SEG, P]) for x in ("btT", "ktT", "vbd"))
        xs, us = sb("xs", [P, 2, P]), sb("us", [P, 2, P])
        with nc.psum_tensor(f"seg_ps{n}", [P, 2, 4, 512], F32) as ps, \
                stage(nc, f"seg{n}", "built0", "built1", "v0", "v1", "made0", "made1", "dve0", "dve1", "act0", "act1",
                      "off0", "off1", "t_in", "chain", "q_in") as (s, block):
            built, vin, made = (s["built0"], s["built1"]), (s["v0"], s["v1"]), (s["made0"], s["made1"])
            out = {"dve": (s["dve0"], s["dve1"]), "act": (s["act0"], s["act1"])}
            offs = (s["off0"], s["off1"])
            jobs = [("gb0", "dve"), ("gb1", "dve"), ("gk0", "dve"), ("gk1", "dve"), ("n", "dve"), ("bt", "act"),
                    ("kt", "act"), ("v", "act")]
            for l in range(1, last_level):
                jobs += [(f"w{l}", "act"), (f"t{l}", "dve"), (f"q{l}", "act")]
            jobs += [(f"w{last_level}", "act"), (f"q{last_level}", "dve")]
            names = [j for j, _ in jobs]

            def evacuated(j):
                who = jobs[j][1]
                return who, sum(w == who for _, w in jobs[:j + 1])

            def wait_out(engine, name, i):
                who, count = evacuated(names.index(name))
                engine.wait_ge(out[who][i], count)

            arrays = [("b", "b", "neg"), ("ar0", "a", "excl"), ("k", "k", "neg"), ("bt", "b", "tail"),
                      ("kt", "k", "tail")] if not has_y else [("ar0", "a", "excl"), ("ar1", "r", "incl")]
            order = [x[0] for x in arrays]

            def wait_built(pe, i, *which):
                here = [order.index(w) for w in which if w in order]
                if here:
                    pe.wait_ge(built[i], 2 * (1 + max(here)))

            @block.tensor
            def _(pe):
                width = 256 if has_y else P
                for j, name in enumerate(names):
                    for i in range(2):
                        bank = ps[:, i, j % 4, :]
                        if j >= 4:
                            who, count = evacuated(j - 4)
                            pe.wait_ge(out[who][i], count)
                        if name[:2] in ("gb", "gk"):
                            wait_built(pe, i, "b", "ar1" if has_y else "ar0", "k" if name[1] == "k" else "b")
                            for c2 in range(2):
                                c = 2 * int(name[2]) + c2
                                last = nc.tensor.matmul(bank[:, 256 * c2:256 * c2 + width], seg[name[1]][:, i, c, :],
                                                        seg["ar"][:, i, c, 0:width // P, :], start=True, stop=True)
                        elif name == "n":
                            for c in range(SEG):
                                last = nc.tensor.matmul(bank[:, c * P:(c + 1) * P], seg["ar"][:, i, c, 0, :],
                                                        seg["b"][:, i, c, :], start=True, stop=True)
                        elif name in ("bt", "kt", "v"):
                            if name == "v":
                                pe.wait_ge(vin[i], 2)
                            else:
                                wait_built(pe, i, name)
                            for c in range(SEG):
                                last = nc.tensor.transpose(bank[:, c * P:(c + 1) * P], seg[name][:, i, c, :], ident)
                        elif name[0] == "w":
                            l = int(name[1:])
                            pe.wait_ge(offs[i], l + 1)
                            wait_out(pe, "n" if l == 1 else f"t{l - 1}", i)
                            for c in range(SEG):
                                last = nc.tensor.matmul(bank[:, c * P:(c + 1) * P], aoff[:, i, l % 2, c, :],
                                                        tmat[:, i, c, :], start=True, stop=True)
                        elif name[0] == "t":
                            l = int(name[1:])
                            wait_out(pe, f"w{l}", i)
                            if l > 1:
                                wait_out(pe, f"q{l - 1}", i)
                            for c in range(SEG):
                                last = nc.tensor.matmul(bank[:, c * P:(c + 1) * P], qmat[:, i, c, :],
                                                        wmat[:, i, c, :], start=True, stop=True)
                        else:
                            l = int(name[1:])
                            if l < last_level:
                                wait_out(pe, f"t{l}", i)
                            else:
                                wait_out(pe, f"w{l}", i)
                                wait_out(pe, f"q{l - 1}", i)
                            for c in range(SEG):
                                if l < last_level:
                                    last = nc.tensor.transpose(bank[:, c * P:(c + 1) * P], tmat[:, i, c, :], ident)
                                else:
                                    last = nc.tensor.matmul(bank[:, c * P:(c + 1) * P], wmat[:, i, c, :],
                                                            qmat[:, i, c, :], start=True, stop=True)
                        last.then_inc(made[i], 1)

            def four(t):
                return t.unsqueeze(1).to_broadcast([P, SEG, P])

            @block.vector
            def _(dve):
                step = chained(dve, s["chain"])
                for q, array in enumerate(arrays):
                    build_array(nc.vector, f, seg, array, 0, start[0], built[0])
                for j, (name, who) in enumerate(jobs):
                    if who != "dve":
                        continue
                    for i in range(2):
                        bank = ps[:, i, j % 4, :]
                        dve.wait_ge(made[i], j + 1)
                        if name[:2] in ("gb", "gk"):
                            to = gb if name[1] == "b" else gk
                            c = 2 * int(name[2])
                            if has_y:
                                mask = tri[:, i].rearrange("p a t -> p (a t)").unsqueeze(1).to_broadcast([P, 2, 256])
                                nc.vector.tensor_tensor(to[:, i, c:c + 2].rearrange("p c a t -> p c (a t)"),
                                                        bank.rearrange("p (c t) -> p c t", c=2), mask,
                                                        ALU.mult).then_inc(s_out(out, i), 1)
                            else:
                                mask = tri[:, i, 0, :].unsqueeze(1).to_broadcast([P, 2, P])
                                nc.vector.tensor_tensor(to[:, i, c:c + 2, 0, :],
                                                        bank.rearrange("p (c t) -> p c t", c=2)[:, :, 0:P], mask,
                                                        ALU.mult).then_inc(s_out(out, i), 1)
                        elif name == "n":
                            step(nc.vector.tensor_tensor(tmat[:, i], bank.rearrange("p (c t) -> p c t", c=SEG),
                                                         four(off[:, 1 - i, 0, :]), ALU.mult))
                            nc.vector.tensor_tensor(tmat[:, i], tmat[:, i], four(ident), ALU.add).then_inc(s_out(out, i), 1)
                        elif name[0] == "t":
                            nc.vector.tensor_tensor(tmat[:, i], bank.rearrange("p (c t) -> p c t", c=SEG), tmat[:, i],
                                                    ALU.add).then_inc(s_out(out, i), 1)
                        else:
                            nc.vector.tensor_tensor(qmat[:, i], bank.rearrange("p (c t) -> p c t", c=SEG), qmat[:, i],
                                                    ALU.add).then_inc(s_out(out, i), 1)

            @block.scalar
            def _(act):
                for i in range(2):
                    for h in range(2):
                        rows = slice(64 * h, 64 * h + 64)
                        nc.scalar.copy(seg["v"][rows, i, :, 64 * h:64 * h + 64],
                                       f["v"][rows, start[i]:start[i] + SEG_TOK].rearrange("p (c t) -> p c t", t=CH)) \
                            .then_inc(vin[i], 1)
                for j, (name, who) in enumerate(jobs):
                    if who != "act":
                        continue
                    for i in range(2):
                        act.wait_ge(made[i], j + 1)
                        to = {"bt": btT, "kt": ktT, "v": vbd}.get(name) or {"w": wmat, "q": qmat}[name[0]]
                        nc.scalar.copy(to[:, i], ps[:, i, j % 4, :].rearrange("p (c t) -> p c t", c=SEG)) \
                            .then_inc(out["act"][i], 1)

            @block.gpsimd
            def _(pool):
                for q, array in enumerate(arrays):
                    build_array(nc.gpsimd, f, seg, array, 1, start[1], built[1], pool, 2 * q)
                for i in range(2):
                    pool.wait_ge(out["dve"][i], 2)
                    nc.gpsimd.tensor_tensor(qmat[:, i], gb[:, i, :, 0, :], four(off[:, i, 0, :]), ALU.mult) \
                        .then_inc(s["t_in"], 1)
                    pool.wait_ge(s["t_in"], i + 1)
                    nc.gpsimd.tensor_tensor(qmat[:, i], qmat[:, i], four(ident), ALU.add).then_inc(offs[i], 1)
                for l in range(1, LEVELS):
                    for i in range(2):
                        if l > 2:
                            pool.wait_ge(made[i], names.index(f"w{l - 2}") + 1)
                        nc.gpsimd.tensor_tensor(aoff[:, i, l % 2], gb[:, i, :, 0, :], four(off[:, i, l, :]), ALU.mult) \
                            .then_inc(offs[i], 1)

        scan_segment(nc, n, start, f, seg, gb, gk, qmat, btT, ktT, vbd, xs, us, total, state, y)


def s_out(out, i):
    return out["dve"][i]


def build_array(ops, f, seg, array, i, start, signal, engine=None, count=0):
    to, what, decay = array
    src = f[what if what in "ar" else what + str(i)]
    dec = f[decay + str(i)]
    cut = slice(start, start + SEG_TOK)
    for h in range(2):
        rows = slice(64 * h, 64 * h + 64)
        dst = seg[to][rows, i, :, 64 * h:64 * h + 64] if to[:2] != "ar" else \
            seg["ar"][rows, i, :, int(to[2]), 64 * h:64 * h + 64]
        ops.tensor_tensor(dst, src[rows, cut].rearrange("p (c t) -> p c t", t=CH),
                          dec[rows, cut].rearrange("p (c t) -> p c t", t=CH), ALU.mult).then_inc(signal, 1)
        if engine is not None:
            engine.wait_ge(signal, count + h + 1)


EARLY_ARRAYS = [("b", "b", "neg"), ("k", "k", "neg"), ("bt", "b", "tail"), ("kt", "k", "tail")]


def scan_segment(nc, n, start, f, seg, gb, gk, qmat, btT, ktT, vbd, xs, us, total, state, y):
    has_y = n > 0
    with nc.psum_tensor(f"scan_ps{n}", [P, 2, 4, 512], F32) as ps, \
            stage(nc, f"scan{n}", "x0", "x1", "xs0", "xs1", "u0", "u1", "us0", "us1", "s0", "s1", "st0", "st1", "y0", "y1",
                  "yo0", "yo1", "early0", "early1") as (s, block):
        X, XS, U, US = (s["x0"], s["x1"]), (s["xs0"], s["xs1"]), (s["u0"], s["u1"]), (s["us0"], s["us1"])
        S_, ST, Y, YO = (s["s0"], s["s1"]), (s["st0"], s["st1"]), (s["y0"], s["y1"]), (s["yo0"], s["yo1"])

        def chunk(step_no, i):
            return step_no if i == 0 else SEG - 1 - step_no

        @block.tensor
        def _(pe):
            for q in range(SEG):
                for i in range(2):
                    c = chunk(q, i)
                    if q:
                        pe.wait_ge(ST[i], q)
                    nc.tensor.matmul(ps[:, i, 0, 0:P], gk[:, i, c, 0, :], vbd[:, i, c, :], start=True, stop=False)
                    nc.tensor.matmul(ps[:, i, 0, 0:P], seg["ar"][:, i, c, 0, :], state[:, i, q % 2, :], start=False,
                                     stop=True).then_inc(X[i], 1)
                for i in range(2):
                    c = chunk(q, i)
                    pe.wait_ge(XS[i], q + 1)
                    nc.tensor.matmul(ps[:, i, 1, 0:P], qmat[:, i, c, :], xs[:, i, :], start=True,
                                     stop=True).then_inc(U[i], 1)
                for i in range(2):
                    c = chunk(q, i)
                    nc.tensor.matmul(ps[:, i, 2, 0:P], ktT[:, i, c, :], vbd[:, i, c, :], start=True, stop=False)
                    pe.wait_ge(US[i], q + 1)
                    nc.tensor.matmul(ps[:, i, 2, 0:P], btT[:, i, c, :], us[:, i, :], start=False,
                                     stop=True).then_inc(S_[i], 1)
                if has_y:
                    for i in range(2):
                        c = chunk(q, i)
                        if q:
                            pe.wait_ge(YO[i], 2 * q)
                        nc.tensor.matmul(ps[:, i, 3, 0:P], vbd[:, i, c, :], gk[:, i, c, 1, :], start=True, stop=False)
                        nc.tensor.matmul(ps[:, i, 3, 0:P], state[:, i, q % 2, :], seg["ar"][:, i, c, 1, :], start=False,
                                         stop=False)
                        nc.tensor.matmul(ps[:, i, 3, 0:P], us[:, i, :], gb[:, i, c, 1, :], start=False,
                                         stop=True).then_inc(Y[i], 1)

        def put_y(ops, copy, i, q, signal):
            c = chunk(q, i)
            at = start[i] - CTX + c * CH
            for h in range(2):
                rows = slice(64 * h, 64 * h + 64)
                src = ps[rows, i, 3, 64 * h:64 * h + 64]
                if n == 1:
                    copy(y[rows, at:at + CH], src).then_inc(signal, 1)
                else:
                    ops.tensor_tensor(y[rows, at:at + CH], src, y[rows, at:at + CH], ALU.add).then_inc(signal, 1)

        next_start = [segment_tokens(n + 1, i) for i in range(2)] if n < 2 else None

        if next_start:
            @block.gpsimd
            def _(pool):
                for q, array in enumerate(EARLY_ARRAYS):
                    build_array(nc.gpsimd, f, seg, array, 1, next_start[1], s["early1"], pool, 2 * q)

        @block.vector
        def _(dve):
            for q in range(SEG):
                if next_start and q:
                    build_array(nc.vector, f, seg, EARLY_ARRAYS[q - 1], 0, next_start[0], s["early0"])
                dve.wait_ge(X[0], q + 1)
                if q:
                    dve.wait_ge(U[0], q)
                nc.vector.tensor_copy(xs[:, 0, :], ps[:, 0, 0, 0:P]).then_inc(XS[0], 1)
                dve.wait_ge(U[0], q + 1)
                if has_y and q:
                    dve.wait_ge(Y[0], q)
                nc.vector.tensor_copy(us[:, 0, :], ps[:, 0, 1, 0:P]).then_inc(US[0], 1)
                for i in range(2):
                    c = start[i] // CH + chunk(q, i)
                    dve.wait_ge(S_[i], q + 1)
                    if has_y and q:
                        dve.wait_ge(Y[i], q)
                    nc.vector.scalar_tensor_tensor(state[:, i, (q + 1) % 2, :], state[:, i, q % 2, :],
                                                   total[:, i, c:c + 1], ps[:, i, 2, 0:P], ALU.mult,
                                                   ALU.add).then_inc(ST[i], 1)
                if has_y:
                    for i in range(2):
                        if n == 2 or i == 0:
                            dve.wait_ge(Y[i], q + 1)
                            put_y(nc.vector, nc.vector.tensor_copy, i, q, YO[i])
            if next_start:
                build_array(nc.vector, f, seg, EARLY_ARRAYS[SEG - 1], 0, next_start[0], s["early0"])

        @block.scalar
        def _(act):
            for q in range(SEG):
                act.wait_ge(X[1], q + 1)
                if q:
                    act.wait_ge(U[1], q)
                nc.scalar.copy(xs[:, 1, :], ps[:, 1, 0, 0:P]).then_inc(XS[1], 1)
                act.wait_ge(U[1], q + 1)
                if has_y and q:
                    act.wait_ge(Y[1], q)
                nc.scalar.copy(us[:, 1, :], ps[:, 1, 1, 0:P]).then_inc(US[1], 1)
                if n == 1:
                    act.wait_ge(Y[1], q + 1)
                    put_y(None, nc.scalar.copy, 1, q, YO[1])


def pair_output(nc, g, pair, y, bonus, gate, cols, heads, eps, rwkT):
    with ExitStack() as held:
        t = held.enter_context(nc.sbuf_tensor("out_t", [P, SEQ], F32))
        u = held.enter_context(nc.sbuf_tensor("out_u", [P, SEQ], F32))
        ps = held.enter_context(nc.psum_tensor("out_ps", [P, 2, 512], F32))
        with stage(nc, "out", "mean", "centred", "squared", "var", "root", "chain", repeats=True) as (s, block):
            @block.tensor
            def _(pe):
                nc.tensor.matmul(ps[:, 0, :], heads[:, 1, :], y[:, :], start=True, stop=True).then_inc(s["mean"], 1)
                pe.wait_ge(s["squared"], 1)
                nc.tensor.matmul(ps[:, 1, :], heads[:, 1, :], t[:, :], start=True, stop=True).then_inc(s["var"], 1)

            @block.scalar
            def _(act):
                act.wait_ge(s["centred"], 1)
                nc.scalar.activation(t[:, :], y[:, :], ACT.Square).then_inc(s["squared"], 1)
                act.wait_ge(s["var"], 1)
                nc.scalar.activation(u[:, :], ps[:, 1, :], ACT.Sqrt, bias=eps[:, 0:1]).then_inc(s["root"], 1)

            @block.vector
            def _(dve):
                step = chained(dve, s["chain"])
                dve.wait_ge(s["mean"], 1)
                nc.vector.tensor_tensor(y[:, :], y[:, :], ps[:, 0, :], ALU.subtract).then_inc(s["centred"], 1)
                dve.wait_ge(s["root"], 1)
                step(nc.vector.reciprocal(u[:, :], u[:, :]))
                step(nc.vector.tensor_tensor(u[:, :], u[:, :], y[:, :], ALU.mult))
                step(nc.vector.tensor_scalar(u[:, :], u[:, :], cols[:, PC["ln_w"]:PC["ln_w"] + 1],
                                             cols[:, PC["ln_b"]:PC["ln_b"] + 1], ALU.mult, ALU.add))
                step(nc.vector.tensor_tensor(u[:, :], u[:, :], bonus[:, :], ALU.add))
                step(nc.vector.tensor_tensor(rwkT[:, bass.ds(pair, 1), :].rearrange("p a t -> p (a t)"), u[:, :],
                                             gate[:, :], ALU.mult))


NH = 8
QL, KVL, RD = 384, 256, 32
LOWW = QL + KVL + RD + NH
TWO_PI_HI, TWO_PI_MID = 6.28125, 0.0019350051879882812
TWO_PI_LO = float(2 * np.pi - TWO_PI_HI - TWO_PI_MID)



class HeadNorms:
    SIGNALS = ("square", "sum", "root", "inverse", "scaled", "normed")

    def __init__(self, nc, g, held, name, s_first, jobs):
        self.nc, self.g, self.first, self.jobs = nc, g, s_first, jobs
        self.sq = held.enter_context(nc.sbuf_tensor(f"{name}_sq", [P, 2, 512], F32))
        self.tmp = held.enter_context(nc.sbuf_tensor(f"{name}_tmp", [P, 2, 512], F32))
        self.ss = held.enter_context(nc.sbuf_tensor(f"{name}_ss", [P, 3, len(jobs), NH + 1], F32))

    def view(self, t, src):
        return t[:, 0:src.shape[1] * src.shape[2]].rearrange("p (h n) -> p h n", n=src.shape[2])

    def act(self, act, s, t):
        nc, j = self.nc, t - self.first
        if 0 <= j < len(self.jobs):
            src = self.jobs[j]["src"]
            act.wait_ge(s["free"], t + 1)
            if j >= 2:
                act.wait_ge(s["sum"], j - 1)
            nc.scalar.activation(self.view(self.sq[:, j % 2], src), src, ACT.Square).then_inc(s["square"], 1)
        j -= 1
        if 0 <= j < len(self.jobs):
            h, n = self.jobs[j]["src"].shape[1:3]
            act.wait_ge(s["sum"], j + 1)
            nc.scalar.activation(self.ss[:, 1, j, 0:h], self.ss[:, 0, j, 0:h], ACT.Sqrt, scale=1.0 / n,
                                 bias=self.g.eps_col[:, 0:1]).then_inc(s["root"], 1)

    def dve(self, dve, s, t):
        nc, j = self.nc, t - self.first - 1
        if 0 <= j < len(self.jobs):
            src = self.jobs[j]["src"]
            dve.wait_ge(s["square"], j + 1)
            nc.vector.tensor_reduce(self.ss[:, 0, j, 0:src.shape[1]], self.view(self.sq[:, j % 2], src), AX.X,
                                    ALU.add).then_inc(s["sum"], 1)
        j -= 1
        if 0 <= j < len(self.jobs):
            src = self.jobs[j]["src"]
            h, n = src.shape[1:3]
            dve.wait_ge(s["root"], j + 1)
            nc.vector.reciprocal(self.ss[:, 2, j, 0:h], self.ss[:, 1, j, 0:h]).then_inc(s["inverse"], 1)
            dve.wait_ge(s["inverse"], j + 1)
            if j >= 2:
                dve.wait_ge(s["normed"], j - 1)
            nc.vector.tensor_tensor(self.view(self.tmp[:, j % 2], src), src,
                                    self.ss[:, 2, j, 0:h].unsqueeze(2).to_broadcast([P, h, n]),
                                    ALU.mult).then_inc(s["scaled"], 1)

    def pool(self, pool, s):
        for j, job in enumerate(self.jobs):
            n = job["src"].shape[2]
            pool.wait_ge(s["scaled"], j + 1)
            for heads, w in job["parts"]:
                last = self.nc.gpsimd.tensor_tensor(job["dst"][:, heads, :],
                                                    self.view(self.tmp[:, j % 2], job["src"])[:, heads, :],
                                                    w.unsqueeze(1).to_broadcast([P, heads.stop - heads.start, n]),
                                                    ALU.mult)
            last.then_inc(s["normed"], 1)


def second_weights(d):
    chunks = [dict(to="low", at=0, width=512), dict(to="low", at=512, width=LOWW - 512)]
    chunks += [dict(to="gate", at=i, width=512) for i in range(2)]
    chunks += [dict(to="wide", at=i, width=512) for i in range(3)]
    at = 0
    for c in chunks:
        c.update(w=d["w_in_2"][:, at:at + c["width"]], k=KD)
        at += c["width"]
    return chunks


def second_gate_weights(d):
    at = LOWW + 5 * 512
    return [dict(w=d["w_in_2"][:, at + 512 * c:at + 512 * c + 512], width=512, k=KD, col=512 * c) for c in range(4)]


def mla_weights(d):
    uq, ukv = d["w_uq_2"], d["w_ukv_2"]
    return [dict(w=uq[:, 0:512], width=512, k=3, to="qn"), dict(w=uq[:, 512:768], width=256, k=3, to="qr"),
            dict(w=ukv[:, 0:512], width=512, k=2, to="kn"), dict(w=ukv[:, 512:1024], width=512, k=2, to="v")]


def second_block(nc, d, g, ring, x, row_cols, ones, out):
    ident = g.ident[:, :]
    tiles = [x[:, m] for m in range(NT_X)]
    with ExitStack() as whole:
        def sb(name, shape, dtype=F32):
            return whole.enter_context(nc.sbuf_tensor(name, shape, dtype))

        hT = sb("b2_hT", [P, KD, SEQ])
        yT = [sb(f"y{i}T", [P, 4, SEQ]) for i in range(2)]
        with ExitStack() as branches:
            def bb(name, shape, dtype=F32):
                return branches.enter_context(nc.sbuf_tensor(name, shape, dtype))

            low = bb("b2_low", [P, NT_X, LOWW])
            wide = bb("b2_wide", [P, NT_X, 3, 512])
            gateT = bb("b2_gateT", [P, 2, 4, SEQ])
            norm_rows = bb("norm_rows", [P, 320])
            causal = bb("causal", [P, 2, SEQ])
            rope = bb("b2_rope", [P, 2, NT_X, 16])
            b_f = bb("b_f", [P, NH])
            project_second(nc, d, g, ring, tiles, hT, low, wide, gateT, norm_rows, causal, b_f)
            rope_tables(nc, d, g, rope)
            mla(nc, d, g, ring, low, gateT, norm_rows, causal, rope, yT[0])
            fox(nc, d, g, ring, low, wide, gateT, norm_rows, causal, b_f, ones, yT[1])
        mg = sb("b2_mg", [P, NT_X, 2 * D])
        second_gates(nc, d, ring, hT, mg)
        row, part = sb("b2_row", [P, D]), sb("b2_part", [P, 2, 512])
        rows_stage(nc, g, "b2_rows", [row_cols[:, 2]], [row[:, :]], ones)

        def add_and_store(s, block, work):
            @block.vector
            def _(dve):
                for t, c, m, ps in work:
                    at = slice(512 * c["c"], 512 * c["c"] + 512)
                    dve.wait_ge(s["tile"], t + 1)
                    if t >= 2:
                        dve.wait_ge(s["chain"], t - 1)
                    nc.vector.tensor_tensor(part[:, t % 2, :], ps, row[:, at], ALU.mult).then_inc(s["free"], 1)
                    dve.wait_ge(s["free"], t + 1)
                    nc.vector.tensor_tensor(x[:, m, at], x[:, m, at], part[:, t % 2, :], ALU.add) \
                        .then_inc(s["chain"], 1)

            @block.scalar
            def _(act):
                for t, c, m, ps in work:
                    at = slice(512 * c["c"], 512 * c["c"] + 512)
                    act.wait_ge(s["chain"], t + 1)
                    act.dma_start(out[0, m * P:(m + 1) * P, at], x[:, m, at]).then_inc(s["out"], 16)
                act.wait_ge(s["out"], 16 * len(work))

        merge_and_out(nc, d, g, "b2m", ring, yT, mg, (d["w_branch_a_2"], d["w_branch_b_2"]), d["w_out_2"], None,
                      add_and_store)


def project_second(nc, d, g, ring, tiles, hT, low, wide, gateT, norm_rows, causal, b_f):
    with ExitStack() as held:
        def sb(name, shape, dtype=F32):
            return held.enter_context(nc.sbuf_tensor(name, shape, dtype))

        gain = sb("b2_gain", [P, KD])
        with stage(nc, "b2_gain", "done") as (s, block):
            @block.vector
            def _(dve):
                nc.vector.scalar_tensor_tensor(gain[:, :], g.ada2[:, 8:16, 0], 1.0, g.vec[:, VCOL["norm_w_2"]],
                                               ALU.add, ALU.mult).then_inc(s["done"], 1)
        with nc.sbuf_tensor("b2_xn", [P, NT_X, D], F32) as xn:
            norm_turn_stage(nc, "b2n", tiles, None, [xn[:, m] for m in range(NT_X)], hT,
                            lambda m, k: (gain[:, k:k + 1], g.ada2[:, k, 0:1]), g.eps_col[:, 0:1], g.ident[:, :])
        sig = sb("b2_sig", [P, 2, 512])

        def tok(m):
            return lambda k: hT[:, k, m * P:(m + 1) * P]

        lhs = [tok(m) for m in range(NT_X)]
        chunks = [dict(c, rhs=lambda k: hT[:, k, :]) if c["to"] == "gate" else dict(c, lhs=lhs)
                  for c in second_weights(d)]

        def evacuate(s, block, work):
            silu = [t for t, c, m, ps in work if c["to"] == "gate"]

            @block.gpsimd
            def _(pool):
                pool.wait_ge(s["side"], 48)
                norms.pool(pool, s)

            @block.vector
            def _(dve):
                for t, c, m, ps in work:
                    dve.wait_ge(s["tile"], t + 1)
                    if t in silu:
                        dve.wait_ge(s["step2"], silu.index(t) + 1)
                        nc.vector.tensor_tensor(gateT[:, c["at"], m, :], ps, sig[:, t % 2, :], ALU.mult).then_inc(s["free"], 1)
                    else:
                        to = wide[:, m, c["at"], :] if c["to"] == "wide" else low[:, m, c["at"]:c["at"] + c["width"]]
                        nc.vector.tensor_copy(to, ps).then_inc(s["free"], 1)
                    norms.dve(dve, s, t)

            @block.scalar
            def _(act):
                act.dma_start(norm_rows[:, :], row_to_all(d["norm_rows_2"], 320)).then_inc(s["side"], 16)
                act.dma_start(causal[:, :, :], d["causal_masks"]).then_inc(s["side"], 16)
                act.dma_start(b_f[:, :], row_to_all(d["b_f_2"], NH)).then_inc(s["side"], 16)
                act.wait_ge(s["side"], 48)
                for t, c, m, ps in work:
                    if t in silu:
                        act.wait_ge(s["tile"], t + 1)
                        if t >= silu[0] + 2:
                            act.wait_ge(s["free"], t - 1)
                        nc.scalar.activation(sig[:, t % 2, :], ps, ACT.Sigmoid).then_inc(s["step2"], 1)
                    norms.act(act, s, t)

        jobs = [dict(src=x, dst=x, parts=[(slice(0, NH), norm_rows[:, 128 + HD * i:192 + HD * i])]) for i in range(2)
                for x in (wide[:, m, i, :].rearrange("p (h n) -> p h n", n=HD) for m in range(NT_X))]
        norms = HeadNorms(nc, g, held, "fox_norm", 4 * NT_X, jobs)
        token_gemm_stage(nc, "b2p", chunks, ring, evacuate, extra=("side",) + HeadNorms.SIGNALS,
                         then=mla_weights(d))


def second_gates(nc, d, ring, hT, mg):
    with ExitStack() as held:
        def tok(m):
            return lambda k: hT[:, k, m * P:(m + 1) * P]

        chunks = [dict(c, lhs=[tok(m) for m in range(NT_X)]) for c in second_gate_weights(d)]

        def evacuate(s, block, work):
            @block.scalar
            def _(act):
                for t, chunk, m, ps in work:
                    act.wait_ge(s["tile"], t + 1)
                    a = chunk["col"]
                    nc.scalar.activation(mg[:, m, a:a + 512], ps, ACT.Sigmoid).then_inc(s["free"], 1)

        token_gemm_stage(nc, "b2g", chunks, ring, evacuate, then=up_weights((d["w_branch_a_2"], d["w_branch_b_2"])))


def rope_tables(nc, d, g, rope):
    with ExitStack() as held:
        def sb(name, shape, dtype=F32):
            return held.enter_context(nc.sbuf_tensor(name, shape, dtype))

        pos, posf = sb("pos", [P, NT_X], I32), sb("posf", [P, NT_X])
        freq = sb("freq", [P, 16])
        ang, n, r, a = (sb(f"rope_{x}", [P, NT_X, 16]) for x in ("ang", "n", "r", "abs"))
        half_pi = sb("half_pi", [P, 1])
        with stage(nc, "rope2", "loaded", "chain", "angle") as (s, block):
            @block.sync
            def _(sp):
                sp.dma_start(pos[:, :], d["positions_2"]).then_inc(s["loaded"], 16)
                sp.dma_start(freq[:, :], row_to_all(d["rope_freq"], 16)).then_inc(s["loaded"], 16)

            @block.vector
            def _(dve):
                step = chained(dve, s["chain"])
                step(nc.vector.memset(half_pi[:, :], float(np.pi / 2)))
                dve.wait_ge(s["loaded"], 32)
                step(nc.vector.tensor_copy(posf[:, :], pos[:, :]))
                for m in range(NT_X):
                    step(nc.vector.tensor_scalar(ang[:, m, :], freq[:, :], posf[:, m:m + 1], None, ALU.mult))
                step(nc.vector.tensor_scalar(n[:, :, :], ang[:, :, :], float(1 / (2 * np.pi)), ROUND, ALU.mult, ALU.add))
                step(nc.vector.tensor_scalar(n[:, :, :], n[:, :, :], -ROUND, None, ALU.add))
                step(nc.vector.scalar_tensor_tensor(r[:, :, :], n[:, :, :], -TWO_PI_HI, ang[:, :, :], ALU.mult, ALU.add))
                step(nc.vector.scalar_tensor_tensor(r[:, :, :], n[:, :, :], -TWO_PI_MID, r[:, :, :], ALU.mult, ALU.add))
                step(nc.vector.scalar_tensor_tensor(r[:, :, :], n[:, :, :], -TWO_PI_LO, r[:, :, :], ALU.mult, ALU.add))
                for beyond, edge, turn in ((ALU.is_gt, np.pi, -2 * np.pi), (ALU.is_lt, -np.pi, 2 * np.pi)):
                    step(nc.vector.tensor_scalar(n[:, :, :], r[:, :, :], float(edge), None, beyond))
                    step(nc.vector.scalar_tensor_tensor(r[:, :, :], n[:, :, :], float(turn), r[:, :, :], ALU.mult, ALU.add))
                step(nc.vector.tensor_scalar(r[:, :, :], r[:, :, :], 3.1415925, -3.1415925, ALU.min, ALU.max))
                nc.vector.scalar_tensor_tensor(a[:, :, :], r[:, :, :], -1.0, r[:, :, :], ALU.mult,
                                               ALU.max).then_inc(s["angle"], 1)

            @block.scalar
            def _(act):
                act.wait_ge(s["angle"], 1)
                nc.scalar.activation(rope[:, 0], a[:, :, :], ACT.Sin, scale=-1.0, bias=half_pi[:, 0:1])
                nc.scalar.activation(rope[:, 1], r[:, :, :], ACT.Sin)


def heads_at(t, b, h):
    return t[HD * (h % 2):HD * (h % 2) + HD, h // 2, b * P:(b + 1) * P]


def mla(nc, d, g, ring, low, gateT, norm_rows, causal, rope, yT):
    ident = g.ident[:, :]
    K = HD + RD
    with ExitStack() as held:
        def sb(name, shape, dtype=F32):
            return held.enter_context(nc.sbuf_tensor(name, shape, dtype))

        qT, kT = ring.slots
        v = sb("mla_v", [P, NT_X, 512])
        with ExitStack() as making:
            def tb(name, shape, dtype=F32):
                return making.enter_context(nc.sbuf_tensor(name, shape, dtype))

            qcat, kcat = tb("qcat", [P, NT_X, NH, K]), tb("kcat", [P, NT_X, NH, K])
            rr, rn = tb("mla_rr", [P, NT_X, 9, RD]), tb("mla_rn", [P, NT_X, 9, RD])
            with ExitStack() as lowering:
                lowT = lowering.enter_context(nc.sbuf_tensor("lowT", [P, 5, SEQ], F32))
                low_norm_turn(nc, g, low, lowT)

                def tok(m, k0):
                    return lambda k: lowT[:, k0 + k, m * P:(m + 1) * P]

                chunks = [dict(c, lhs=[tok(m, 0 if c["k"] == 3 else 3) for m in range(NT_X)]) for c in mla_weights(d)]
                raw = lowering.enter_context(nc.sbuf_tensor("mla_raw", [P, NT_X, 512], F32))
                every, eight = slice(0, NH), [raw[:, m, :].rearrange("p (h n) -> p h n", n=HD) for m in range(NT_X)]
                jobs = [dict(src=eight[m], dst=qcat[:, m, :, 0:HD], parts=[(every, norm_rows[:, 0:64])])
                        for m in range(NT_X)]
                jobs += [dict(src=rr[:, m], dst=rn[:, m], parts=[(every, norm_rows[:, 256:288]),
                                                                 (slice(NH, NH + 1), norm_rows[:, 288:320])])
                         for m in range(NT_X)]
                jobs += [dict(src=eight[m], dst=kcat[:, m, :, 0:HD], parts=[(every, norm_rows[:, 64:128])])
                         for m in range(NT_X)]
                norms = HeadNorms(nc, g, lowering, "mla_norm", 0, jobs)

                def evacuate(s, block, work):
                    @block.gpsimd
                    def _(pool):
                        norms.pool(pool, s)

                    @block.vector
                    def _(dve):
                        for t, c, m, ps in work:
                            dve.wait_ge(s["tile"], t + 1)
                            if c["to"] == "qr":
                                nc.vector.tensor_copy(rr[:, m, 0:NH, :],
                                                      ps.rearrange("p (h n) -> p h n", n=RD)).then_inc(s["free"], 1)
                            else:
                                nc.vector.tensor_copy((v if c["to"] == "v" else raw)[:, m, :], ps) \
                                    .then_inc(s["free"], 1)
                            norms.dve(dve, s, t)

                    @block.scalar
                    def _(act):
                        for m in range(NT_X):
                            nc.scalar.copy(rr[:, m, NH, :], low[:, m, QL + KVL:QL + KVL + RD]) \
                                .then_inc(s["k_rope"], 1)
                        act.wait_ge(s["k_rope"], NT_X)
                        for t, c, m, ps in work:
                            norms.act(act, s, t)

                token_gemm_stage(nc, "mla_up", chunks, ring, evacuate, extra=("k_rope",) + HeadNorms.SIGNALS)
            rotate_second(nc, rn, rope, rr, qcat, kcat)
            turn_heads(nc, "mla_turn", [(qcat, qT), (kcat, kT)], K, ident)
        items = [dict(q=qT[0:K, h, b * P:(b + 1) * P], keys=[kT[0:K, h, 0:(b + 1) * P]],
                      v=[v[:, t, HD * h:HD * h + HD] for t in range(b + 1)], mask=causal[:, 0, (3 - b) * P:SEQ],
                      sink=None, half=h % 2, out=heads_at(yT, b, h), gate=heads_at(gateT[:, 0], b, h)) for b in range(NT_X) for h in range(NH)]
        attention_stage(nc, "mla", items, float(1.0 / np.sqrt(K)), ident)


def rotate_second(nc, rn, rope, rr, qcat, kcat):
    with nc.sbuf_tensor("rot2", [P, 4, NT_X, 9, 16], F32) as part, \
            stage(nc, "rot2", "parts", "rotated", "copied") as (s, block):
        @block.vector
        def _(dve):
            n = 0
            for m in range(NT_X):
                cos = rope[:, 0, m].unsqueeze(1).to_broadcast([P, 9, 16])
                sin = rope[:, 1, m].unsqueeze(1).to_broadcast([P, 9, 16])
                for i, (x, y) in enumerate(((0, cos), (16, sin), (16, cos), (0, sin))):
                    nc.vector.tensor_tensor(part[:, i, m], rn[:, m, :, x:x + 16], y, ALU.mult).then_inc(s["parts"], 1)
            for m in range(NT_X):
                dve.wait_ge(s["parts"], 4 * m + 4)
                nc.vector.tensor_tensor(rr[:, m, :, 0:16], part[:, 0, m], part[:, 1, m], ALU.subtract).then_inc(s["rotated"], 1)
                nc.vector.tensor_tensor(rr[:, m, :, 16:32], part[:, 2, m], part[:, 3, m], ALU.add).then_inc(s["rotated"], 1)

        @block.scalar
        def _(act):
            for m in range(NT_X):
                act.wait_ge(s["rotated"], 2 * m + 2)
                nc.scalar.copy(qcat[:, m, :, HD:HD + RD], rr[:, m, 0:NH, :])
                nc.scalar.copy(kcat[:, m, :, HD:HD + RD], rr[:, m, NH:NH + 1, :].to_broadcast([P, NH, RD]))


def turn_heads(nc, name, pairs, K, ident):
    groups = [(src, dst, m, h) for src, dst in pairs for m in range(NT_X) for h in (0, 4)]
    with nc.psum_tensor(f"{name}_ps", [P, 4, 512], F32) as ps, stage(nc, name, "turned", "even", "odd") as (s, block):
        @block.tensor
        def _(pe):
            for q, (src, dst, m, h) in enumerate(groups):
                if q >= 4:
                    pe.wait_ge(s["odd"] if q % 2 else s["even"], (q - 4) // 2 + 1)
                for j in range(4):
                    last = nc.tensor.transpose(ps[0:K, q % 4, j * P:(j + 1) * P], src[:, m, h + j, :], ident)
                last.then_inc(s["turned"], 1)

        def copies(engine, copy, odd, signal):
            for q, (src, dst, m, h) in enumerate(groups):
                if q % 2 == odd:
                    engine.wait_ge(s["turned"], q + 1)
                    copy(dst[0:K, h:h + 4, m * P:(m + 1) * P],
                         ps[0:K, q % 4, :].rearrange("p (j t) -> p j t", j=4)).then_inc(signal, 1)

        @block.vector
        def _(dve):
            copies(dve, nc.vector.tensor_copy, 0, s["even"])

        @block.scalar
        def _(act):
            copies(act, nc.scalar.copy, 1, s["odd"])


def low_norm_turn(nc, g, low, lowT):
    parts = ((0, QL), (QL, KVL))
    gains = VCOL["lora_norms_2"].start
    with ExitStack() as held:
        def sb(name, shape):
            return held.enter_context(nc.sbuf_tensor(name, shape, F32))

        sq, xn, stat = sb("low_sq", [P, QL]), sb("low_xn", [P, NT_X, QL + KVL]), sb("low_stat", [P, 3, 2, NT_X])
        ps = held.enter_context(nc.psum_tensor("low_ps", [P, 2, 1024], F32))
        with stage(nc, "low", "squared", "root", "inverse", "normed", "turned", "out") as (s, block):
            @block.scalar
            def _(act):
                n = 0
                for i, (at, w) in enumerate(parts):
                    for m in range(NT_X):
                        if n:
                            act.wait_ge(s["squared"], n)
                        nc.scalar.activation(sq[:, 0:w], low[:, m, at:at + w], ACT.Square,
                                             accum_out=stat[:, 0, i, m:m + 1]).then_inc(s["squared"], 1)
                        n += 1
                act.wait_ge(s["squared"], n)
                for i, (at, w) in enumerate(parts):
                    nc.scalar.activation(stat[:, 1, i, :], stat[:, 0, i, :], ACT.Sqrt, scale=1.0 / w,
                                         bias=g.eps_col[:, 0:1]).then_inc(s["root"], 1)
                for m in range(NT_X):
                    act.wait_ge(s["turned"], m + 1)
                    for k in range(5):
                        last = nc.scalar.activation(lowT[:, k, m * P:(m + 1) * P], ps[:, m % 2, k * P:(k + 1) * P],
                                                    ACT.Copy, scale=g.vec[:, gains + k:gains + k + 1])
                    last.then_inc(s["out"], 1)

            @block.vector
            def _(dve):
                dve.wait_ge(s["root"], 2)
                nc.vector.reciprocal(stat[:, 2], stat[:, 1]).then_inc(s["inverse"], 1)
                dve.wait_ge(s["inverse"], 1)
                for m in range(NT_X):
                    for i, (at, w) in enumerate(parts):
                        nc.vector.tensor_scalar(xn[:, m, at:at + w], low[:, m, at:at + w], stat[:, 2, i, m:m + 1], None,
                                                ALU.mult).then_inc(s["normed"], 1)

            @block.tensor
            def _(pe):
                for m in range(NT_X):
                    pe.wait_ge(s["normed"], 2 * m + 2)
                    if m >= 2:
                        pe.wait_ge(s["out"], m - 1)
                    for k in range(5):
                        last = nc.tensor.transpose(ps[:, m % 2, k * P:(k + 1) * P], xn[:, m, k * P:(k + 1) * P],
                                                   g.ident[:, :])
                    last.then_inc(s["turned"], 1)


def fox(nc, d, g, ring, low, wide, gateT, norm_rows, causal, b_f, ones, yT):
    ident = g.ident[:, :]
    K = HD + 2
    scale = HD ** -0.5
    with ExitStack() as held:
        def sb(name, shape, dtype=F32):
            return held.enter_context(nc.sbuf_tensor(name, shape, dtype))

        qT, kT = sb("fox_qT", [P, NH, SEQ]), sb("fox_kT", [P, NH, SEQ])
        with ExitStack() as making:
            def tb(name, shape, dtype=F32):
                return making.enter_context(nc.sbuf_tensor(name, shape, dtype))

            qcat, kcat = tb("fox_qcat", [P, NT_X, NH, K]), tb("fox_kcat", [P, NT_X, NH, K])

            def heads(i, m):
                return wide[:, m, i, :].rearrange("p (h n) -> p h n", n=HD)

            z, e, lf = (tb(f"fox_{x}", [P, NT_X, NH]) for x in ("z", "e", "lf"))
            upto = tb("upto", [P, P])
            with nc.psum_tensor("cum_ps", [P, 512], F32) as ps, \
                    stage(nc, "cum", "chain", "loaded", "abs", "log", "lf", "summed", "done") as (s, block):
                @block.sync
                def _(sp):
                    sp.dma_start(upto[:, :], d["before"]).then_inc(s["loaded"], 16)

                @block.vector
                def _(dve):
                    step = chained(dve, s["chain"])
                    for m in range(NT_X):
                        step(nc.vector.tensor_tensor(z[:, m, :], low[:, m, LOWW - NH:LOWW], b_f[:, :], ALU.add))
                    nc.vector.scalar_tensor_tensor(e[:, :, :], z[:, :, :], -1.0, z[:, :, :], ALU.mult,
                                                   ALU.max).then_inc(s["abs"], 1)
                    dve.wait_ge(s["log"], 2)
                    step(nc.vector.tensor_scalar(z[:, :, :], z[:, :, :], 0.0, None, ALU.min))
                    step(nc.vector.tensor_tensor(lf[:, :, :], z[:, :, :], e[:, :, :], ALU.subtract))
                    dve.wait_ge(s["loaded"], 16)
                    nc.vector.tensor_tensor(upto[:, :], upto[:, :], ident, ALU.add).then_inc(s["lf"], 1)
                    for cat, at in ((qcat, HD + 1), (kcat, HD)):
                        for m in range(NT_X):
                            nc.vector.memset(cat[:, m, :, at:at + 1], 1.0).then_inc(s["done"], 1)
                    dve.wait_ge(s["summed"], 1)
                    for m in range(NT_X):
                        cum = ps[:, m * NH:(m + 1) * NH].unsqueeze(2)
                        nc.vector.tensor_scalar(qcat[:, m, :, HD:HD + 1], cum, 1.0 / scale, None,
                                                ALU.mult).then_inc(s["done"], 1)
                        nc.vector.tensor_scalar(kcat[:, m, :, HD + 1:HD + 2], cum, -1.0 / scale, None,
                                                ALU.mult).then_inc(s["done"], 1)

                @block.gpsimd
                def _(pool):
                    for m in range(NT_X):
                        for i, cat in enumerate((qcat, kcat)):
                            nc.gpsimd.tensor_copy(cat[:, m, :, 0:HD], heads(i, m)).then_inc(s["done"], 1)

                @block.scalar
                def _(act):
                    act.wait_ge(s["abs"], 1)
                    nc.scalar.activation(e[:, :, :], e[:, :, :], ACT.Exp, scale=-1.0).then_inc(s["log"], 1)
                    act.wait_ge(s["log"], 1)
                    nc.scalar.activation(e[:, :, :], e[:, :, :], ACT.Ln, bias=1.0).then_inc(s["log"], 1)

                @block.tensor
                def _(pe):
                    pe.wait_ge(s["lf"], 1)
                    for m in range(NT_X):
                        for q in range(m):
                            nc.tensor.matmul(ps[:, m * NH:(m + 1) * NH], ones, lf[:, q, :], start=(q == 0), stop=False,
                                             skip_group_check=True)
                        last = nc.tensor.matmul(ps[:, m * NH:(m + 1) * NH], upto[:, :], lf[:, m, :], start=(m == 0),
                                                stop=True, skip_group_check=True)
                    last.then_inc(s["summed"], 1)
            turn_heads(nc, "fox_turn", [(qcat, qT), (kcat, kT)], K, ident)
        items = [dict(q=qT[0:K, h, b * P:(b + 1) * P], keys=[kT[0:K, h, 0:(b + 1) * P]],
                      v=[wide[:, t, 2, HD * h:HD * h + HD] for t in range(b + 1)], mask=causal[:, 1, (3 - b) * P:SEQ],
                      sink=None, half=h % 2, out=heads_at(yT, b, h), gate=heads_at(gateT[:, 1], b, h)) for b in range(NT_X) for h in range(NH)]
        attention_stage(nc, "fox", items, scale, ident,
                        early=lambda sp: ring.call_first(sp, second_gate_weights(d)))


def build_program(nc, d, out):
    with ExitStack() as whole:
        def sb(name, shape, dtype=F32):
            return whole.enter_context(nc.sbuf_tensor(name, shape, dtype))

        ident = sb("ident", [P, P])
        vec = sb("vec", [P, NVCOL])
        eps_col = sb("eps_col", [P, 1])
        ada = sb("ada", [P, 48, 2])
        ada2 = sb("ada2", [P, 24, 1])
        g = Shared(ident=ident, vec=vec, eps_col=eps_col, ada=ada, ada2=ada2)

        cond = sb("cond", [P, KD, 2])
        sig = sb("sig", [P, 2, KD])
        with stage(nc, "start", "loaded", "set", "sig", "cond") as (s, block):
            @block.sync
            def _(sp):
                sp.dma_start(ident[:, :], d["ident"]).then_inc(s["loaded"], 16)
                sp.dma_start(vec[:, :], d["vectors"]).then_inc(s["loaded"], 16)
                sp.wait_ge(s["loaded"], 32)

            @block.vector
            def _(dve):
                nc.vector.memset(eps_col[:, :], RMS_EPS).then_inc(s["set"], 1)
                dve.wait_ge(s["sig"], 1)
                for j, name in enumerate(("c", "c_ctx")):
                    nc.vector.tensor_tensor(cond[:, :, j], vec[:, VCOL[name]], sig[:, j, :], ALU.mult).then_inc(s["cond"], 1)

            @block.scalar
            def _(act):
                act.wait_ge(s["loaded"], 32)
                nc.scalar.activation(sig[:, :, :].rearrange("p a k -> p (a k)"),
                                     vec[:, VCOL["c"].start:VCOL["c_ctx"].stop], ACT.Sigmoid).then_inc(s["sig"], 1)

        ada_stage(nc, "ada", cond, 2, d["w_ada"], EARLY, vec[:, VCOL["b_ada"]], ada, ident[:, :])
        row_cols = sb("row_cols", [P, 3, KD])
        ones = sb("ones", [P, P])
        late = LateModulation(nc, whole, ones)
        with stage(nc, "late_cond", "done") as (s, block):
            @block.vector
            def _(dve):
                nc.vector.memset(ones[:, :], 1.0).then_inc(s["done"], 1)
                half = LATE // 2
                nc.vector.tensor_copy(late.cond[:, 0:half, :],
                                      cond[:, :, 0].unsqueeze(1).to_broadcast([P, half, KD])).then_inc(s["done"], 1)
                nc.vector.tensor_copy(late.cond[:, half:LATE, :],
                                      vec[:, VCOL["c_2"]].unsqueeze(1).to_broadcast([P, half, KD])).then_inc(s["done"], 1)
        x = sb("x", [P, NT_X, D])
        mixing_block(nc, d, g, late, x, row_cols, ones[:, :])
        ring = WeightRing(nc, "b2_w", whole)
        ffn_block(nc, d, g, ring, x, row_cols, ones[:, :])
        second_block(nc, d, g, ring, x, row_cols, ones[:, :], out)
        RESTING.pop().close()


def axial_tables():
    t = np.arange(SEQ)
    half = HD // 2
    inv = (np.float32(10000.0) ** (-np.arange(0, half, 2, dtype=np.float32) / np.float32(half))).astype(np.float32)
    ang = np.stack([(t // 64).astype(np.float32)[:, None] * inv, (t % 64).astype(np.float32)[:, None] * inv], 1)
    tab = np.stack([np.cos(ang), np.sin(ang)], 1).astype(np.float32)
    return np.ascontiguousarray(tab.reshape(NT_X, P, 2, 2, 16).transpose(1, 0, 2, 3, 4))


def window_mask_table():
    q, k = np.arange(P)[:, None], np.arange(P)[None, :]
    before = np.where(k >= q, 0.0, NEG)
    after = np.where(k <= q, 0.0, NEG)
    z = np.zeros((P, P))
    return np.concatenate([z, z, before, z, after, z, z, z, after], 1).astype(np.float32)


def rwkv_tables():
    s, t = np.arange(P)[:, None], np.arange(P)[None, :]
    same = s // CH == t // CH
    tri = np.zeros((P, 2, 2, P), np.float32)
    off = np.zeros((P, 2, LEVELS, P), np.float32)
    for i, (before, upto) in enumerate(((s < t, s <= t), (s > t, s >= t))):
        tri[:, i, 0], tri[:, i, 1] = same & before, same & upto
        for l in range(LEVELS):
            off[:, i, l] = before & (s // (2 << l) == t // (2 << l)) & (s // (1 << l) != t // (1 << l))
    heads = np.stack([same.astype(np.float32), same / np.float32(CH)], 1).astype(np.float32)
    segment = np.tile((np.arange(NTOK) % CH != 0).astype(np.float32), (P, 1))
    return {"tri": tri, "off": off, "heads": heads, "segment": segment}


def rwkv_layout(a):
    w, b, mp, mn = a["w_in"][0], a["b_in"][0], a["mu_prev"][0], a["mu_next"][0]

    def slices(m):
        return m.reshape(KD, P, -1).transpose(1, 0, 2)

    d = dict(rwkv_tables())
    d["w_lora_in"] = slices(w[:, 768 + 1536:768 + 1920])
    rkv, cols, low = [], [], []
    for pair in range(4):
        c = slice(P * pair, P * pair + P)
        at = [768 + 512 * i + P * pair for i in range(3)]
        rkv.append(slices(np.concatenate([w[:, x:x + P] for x in at], 1)))
        here = [b[x:x + P] for x in at] + [m[x - 768:x - 768 + P] for m in (mp, mn) for x in at]
        here += [a[n][0, c] for n in ("w0_f", "w0_b", "a0_f", "a0_b", "k_k", "k_a")]
        here += [a["r_k"][0].reshape(-1)[c], a["ln_x_w"][0, c], a["ln_x_b"][0, c]]
        cols.append(np.stack(here, 1))
        none = np.zeros((HD, P), np.float32)
        low.append(np.stack([np.concatenate(x, 0) for x in (
            (a["w2_f"][0][:, c], none), (none, a["w2_b"][0][:, c]), (a["a2_f"][0][:, c], none),
            (none, a["a2_b"][0][:, c]), (a["g2"][0][:, c],))], 1))
    d["w_rkv"], d["pair_cols"], d["pair_low"] = np.stack(rkv + rkv[:1]), np.stack(cols), np.stack(low)
    return d


def second_layout(a):
    at = dict(zip(("cq", "ckv", "kr", "ga", "q", "k", "v", "f", "gb", "mg"),
                  (0, 384, 640, 672, 1184, 1696, 2208, 2720, 2728, 3240)))
    size = dict(cq=384, ckv=256, kr=32, ga=512, q=512, k=512, v=512, f=8, gb=512, mg=2048)
    order = np.concatenate([np.arange(at[n], at[n] + size[n]) for n in
                            ("cq", "ckv", "kr", "f", "ga", "gb", "q", "k", "v", "mg")])
    uq = np.arange(NH * (HD + RD)).reshape(NH, HD + RD)
    ukv = np.arange(NH * 2 * HD).reshape(NH, 2 * HD)
    q, k = np.arange(P)[:, None], np.arange(P)[None, :]
    causal = np.zeros((P, 2, SEQ), np.float32)
    causal[:, 0, 384:] = np.where(k // 64 <= q // 64, 0.0, NEG)
    causal[:, 1, 384:] = np.where(k <= q, 0.0, NEG)
    half = np.arange(0, RD, 2, dtype=np.float32)
    return {"w_in_2": a["w_in_2"][0][:, order],
            "w_uq_2": a["w_uq_2"][0][:, np.concatenate([uq[:, :HD].ravel(), uq[:, HD:].ravel()])],
            "w_ukv_2": a["w_ukv_2"][0][:, np.concatenate([ukv[:, :HD].ravel(), ukv[:, HD:].ravel()])],
            "norm_rows_2": np.concatenate([a[n + "_2"][0] for n in ("qn_nope_a", "kn_nope_a", "qn_b", "kn_b",
                                                                    "qn_rope_a", "kn_rope_a")]),
            "b_f_2": a["b_f_2"][0], "w_branch_a_2": a["w_branch_a_2"][0], "w_branch_b_2": a["w_branch_b_2"][0],
            "w_out_2": a["w_out_2"][0], "causal_masks": causal,
            "positions_2": np.ascontiguousarray(a["positions_2"].reshape(NT_X, P).T),
            "rope_freq": (np.float32(10000.0) ** (-half / np.float32(RD))).astype(np.float32)}


def host_layout(inputs):
    a = {k: np.asarray(v) for k, v in inputs.items()}

    def columns(v):
        return np.ascontiguousarray(v.reshape(-1, P).T)

    lora = slice(768 + 1536, 768 + 1920)
    parts = {"c": a["c"][0], "c_ctx": a["c_ctx"], "c_2": a["c_2"][0], "b_ada": a["b_ada"][0],
             "g_pre_mix": a["g_pre_mix"][0], "g_post_mix": a["g_post_mix"][0], "g_pre_ffn": a["g_pre_ffn"][0],
             "g_post_ffn": a["g_post_ffn"][0], "b_ada_2": a["b_ada_2"][0], "norm_w_2": a["norm_w_2"][0],
             "lora_b_in": a["b_in"][0, lora], "lora_mu_prev": a["mu_prev"][0, 1536:], "lora_mu_next": a["mu_next"][0, 1536:],
             "lora_norms_2": np.concatenate([a["q_lora_norm_w_2"][0], a["kv_lora_norm_w_2"][0]])}
    d = {"vectors": np.concatenate([columns(parts[n]) for n in VCOL], 1)}
    d["ident"] = np.eye(P, dtype=np.float32)
    d["x"], d["ctx"] = a["x"], a["ctx"]
    early = EARLY * 512
    d["w_ada"] = a["w_ada"][0][:, :early]
    late = np.concatenate([a["w_ada"][0][:, early:], a["w_ada_2"][0]], 1)
    d["w_late"] = late.reshape(KD, P, LATE, 512).transpose(2, 1, 0, 3)
    w, b = a["w_in"][0], a["b_in"][0]
    order = np.concatenate([np.arange(HD) + HD * h for h in (0, 4, 1, 5, 2, 6, 3, 7)])
    tok = np.concatenate([order, np.arange(512, 768), np.arange(2688, 4736)])
    d["w_in_tok"], d["b_in_tok"], d["b_gates"] = w[:, tok], b[tok[:768]], b[tok[768:]]
    d["rope_axial"], d["window_masks"] = axial_tables(), window_mask_table()
    d.update(rwkv_layout(a))
    for n in ("w_up_att", "w_up_rwkv", "w_out", "w_router", "b_router", "w_gate_up", "b_gate_up", "w_down", "b_down"):
        d[n] = a[n][0]
    d.update(second_layout(a))
    d["iota"] = np.arange(P, dtype=np.float32)
    d["before"] = np.triu(np.ones((P, P), np.float32), 1)
    d["att_sinks"] = a["att_sinks"][0]
    return d


def kernel(**inputs):
    import numpy as _np
    import concourse.bacc as _bacc
    from concourse import mybir as _mybir
    from concourse.bass_utils import run_bass_kernel_spmd as _run

    nc = _bacc.Bacc("TRN2", target_bir_lowering=False, num_devices=1)
    arrays, d = {}, {}
    for name, array in host_layout(inputs).items():
        array = _np.ascontiguousarray(array)
        arrays[f"in_{name}"] = array
        d[name] = nc.dram_tensor(f"in_{name}", array.shape, _mybir.dt.from_np(array.dtype), kind="ExternalInput").ap()
    out = nc.dram_tensor("out_0", (1, SEQ, D), F32, kind="ExternalOutput").ap()
    build_program(nc, d, out)
    r = _run(nc, [arrays], core_ids=[0])
    return r.results[0]["out_0"]
```
